# Optimizing a Trainium2 kernel written in Bass

```python
import math
import jax
import jax.numpy as jnp
from jax import lax
import numpy as np

D_MODEL = 1024
BATCH = 1
SEQ = 1024
DEPTH = 2
DEC_BATCH = 8
DEC_SEQ = 4
PAST_LEN = 1024
PAGE_SIZE = 128

HEAD_DIM = 64
CONV_CH = D_MODEL // 2
CONV_WIDTH = 31
WINDOWS = (128, 512, 2048)
DILATIONS = (1, 4, 16)
B_HPG = 4
B_HEADS = B_HPG * len(WINDOWS)
SW_BLOCK = 128
GLA_HEADS = 4
GLA_DK = D_MODEL // 16
GLA_DV = D_MODEL // 8
GLA_GATE_RANK = 16
GLA_TAU = 16.0
GLA_CHUNK = 64
DSA_HEADS = D_MODEL // 128
IDX_HEADS = 4
IDX_DIM = 64
DSA_TOPK_MAX = 256
DSA_QBLOCK = 128
REL_BUCKETS = 32
REL_MAX_DIST = 2048
REL_HEADS = B_HEADS + DSA_HEADS
FFN_HIDDEN = ((8 * D_MODEL + 3 * 256 - 1) // (3 * 256)) * 256
EPS = 1e-6

N_AB = (DEPTH + 1) // 2
N_CD = DEPTH // 2
AB_SPLITS = (CONV_CH, CONV_CH, B_HEADS * HEAD_DIM, B_HEADS * HEAD_DIM, B_HEADS * HEAD_DIM)
AB_IN = sum(AB_SPLITS)
AB_OUT = CONV_CH + B_HPG * HEAD_DIM
CD_SPLITS = (GLA_HEADS * GLA_DK, GLA_HEADS * GLA_DK, GLA_HEADS * GLA_DV, GLA_GATE_RANK, GLA_HEADS * GLA_DV,
             DSA_HEADS * HEAD_DIM, DSA_HEADS * HEAD_DIM, DSA_HEADS * HEAD_DIM,
             IDX_HEADS * IDX_DIM, IDX_DIM, IDX_HEADS)
CD_IN = sum(CD_SPLITS)
CD_OUT = GLA_HEADS * GLA_DV + DSA_HEADS * HEAD_DIM

kernel_name = 'hybrid_conv_dilated_gla_dsa_decoder_step'

F32 = jnp.float32

def split_cols(z, sizes):
    return jnp.split(z, np.cumsum(sizes)[:-1].tolist(), axis=-1)

def rmsnorm(x, g):
    xf = x.astype(F32)
    y = xf * lax.rsqrt(jnp.mean(xf * xf, axis=-1, keepdims=True) + EPS)
    return (y * g.astype(F32)).astype(x.dtype)

def rel_bucket(dist):
    n = jnp.maximum(dist, 0)
    max_exact = REL_BUCKETS // 2
    nf = jnp.maximum(n, max_exact).astype(F32)
    large = max_exact + (jnp.log(nf / max_exact) / math.log(REL_MAX_DIST / max_exact)
                         * (REL_BUCKETS - max_exact)).astype(jnp.int32)
    large = jnp.minimum(large, REL_BUCKETS - 1)
    return jnp.where(n < max_exact, n, large)

def conv_module(u, hist, conv_w, conv_b, ln_g, ln_b):
    c = u.shape[-1]
    uh = jnp.concatenate([hist.astype(u.dtype), u], axis=1)
    y = lax.conv_general_dilated(uh, conv_w[:, None, :].astype(u.dtype), window_strides=(1,), padding='VALID',
                                 dimension_numbers=('NWC', 'WIO', 'NWC'), feature_group_count=c)
    yf = y.astype(F32) + conv_b.astype(F32)
    mu = jnp.mean(yf, axis=-1, keepdims=True)
    var = jnp.mean(jnp.square(yf - mu), axis=-1, keepdims=True)
    yn = (yf - mu) * lax.rsqrt(var + EPS) * ln_g.astype(F32) + ln_b.astype(F32)
    return jax.nn.silu(yn).astype(u.dtype), uh[:, -(CONV_WIDTH - 1):]

def dilated_window_prompt(q, k, v, dil, window, tab):
    n_b, s_len, h, dh = q.shape
    n = s_len // dil
    reach = window // dil
    nb = -(-n // SW_BLOCK)
    n_pad = nb * SW_BLOCK

    def to_blocks(t):
        t = t.reshape(n_b, n, dil, h, dh).transpose(0, 2, 1, 3, 4)
        t = jnp.pad(t, ((0, 0), (0, 0), (0, n_pad - n), (0, 0), (0, 0)))
        return t.reshape(n_b, dil, nb, SW_BLOCK, h, dh)

    def with_prev(t):
        prev = jnp.pad(t, ((0, 0), (0, 0), (1, 0), (0, 0), (0, 0), (0, 0)))[:, :, :-1]
        return jnp.concatenate([prev, t], axis=3)

    qb = to_blocks(q)
    kb = with_prev(to_blocks(k))
    vb = with_prev(to_blocks(v))
    ql = jnp.arange(SW_BLOCK)[:, None]
    kl = jnp.arange(2 * SW_BLOCK)[None, :] - SW_BLOCK
    rel = ql - kl
    key_sub = (jnp.arange(nb) * SW_BLOCK)[:, None, None] + kl[None]
    mask = ((rel >= 0) & (rel <= reach))[None] & (key_sub >= 0)
    bias = jnp.take(tab, rel_bucket(rel * dil), axis=0).transpose(2, 0, 1).astype(F32)
    s = jnp.einsum('nrbqhd,nrbkhd->nrbhqk', qb, kb).astype(F32) * HEAD_DIM ** -0.5 + bias
    s = jnp.where(mask[:, None], s, -jnp.inf)
    lse = jax.nn.logsumexp(s, axis=-1)
    o = jnp.einsum('nrbhqk,nrbkhd->nrbqhd', jnp.exp(s - lse[..., None]), vb.astype(F32))
    o = o.reshape(n_b, dil, n_pad, h, dh)[:, :, :n].transpose(0, 2, 1, 3, 4).reshape(n_b, s_len, h, dh)
    lse = lse.transpose(0, 1, 2, 4, 3).reshape(n_b, dil, n_pad, h)[:, :, :n]
    lse = lse.transpose(0, 2, 1, 3).reshape(n_b, s_len, h)
    return o, lse

def dilated_window_step(q, k, v, buf, dil, window, tab):
    n_b, l_new, h, dh = q.shape
    wb = buf.shape[1]
    kv = jnp.concatenate([buf, jnp.stack([k, v], axis=2).astype(buf.dtype)], axis=1)
    m = jnp.arange(window // dil + 1)
    idx = wb + jnp.arange(l_new)[:, None] - dil * m[None, :]
    valid = idx >= 0
    sel = kv[:, jnp.maximum(idx, 0)]
    bias = jnp.take(tab, rel_bucket(dil * m), axis=0).T.astype(F32)
    s = jnp.einsum('nlhd,nlmhd->nhlm', q, sel[:, :, :, 0]).astype(F32) * HEAD_DIM ** -0.5 + bias[None, :, None, :]
    s = jnp.where(valid[None, None], s, -jnp.inf)
    lse = jax.nn.logsumexp(s, axis=-1)
    o = jnp.einsum('nhlm,nlmhd->nlhd', jnp.exp(s - lse[..., None]), sel[:, :, :, 1].astype(F32))
    keep = min(window, wb + l_new)
    return o, lse.transpose(0, 2, 1), kv[:, -keep:]

def ab_mix(h, w_in, conv_w, conv_b, ln_g, ln_b, qn, kn, w_out, tab, conv_hist, win_bufs):
    n_b, l_len, _ = h.shape
    a_lin, a_gate, q, k, v = split_cols(h @ w_in, AB_SPLITS)
    a_out, conv_st = conv_module(a_lin * jax.nn.sigmoid(a_gate), conv_hist, conv_w, conv_b, ln_g, ln_b)
    shp = (n_b, l_len, B_HEADS, HEAD_DIM)
    q = rmsnorm(q.reshape(shp), qn)
    k = rmsnorm(k.reshape(shp), kn)
    v = v.reshape(shp)
    outs, lses, win_st = [], [], []
    for g, (window, dil) in enumerate(zip(WINDOWS, DILATIONS)):
        hs = slice(g * B_HPG, (g + 1) * B_HPG)
        tg = tab[:, hs]
        if win_bufs is None:
            o, lse = dilated_window_prompt(q[:, :, hs], k[:, :, hs], v[:, :, hs], dil, window, tg)
            st = jnp.stack([k[:, :, hs], v[:, :, hs]], axis=2)[:, -min(window, l_len):]
        else:
            o, lse, st = dilated_window_step(q[:, :, hs], k[:, :, hs], v[:, :, hs], win_bufs[g], dil, window, tg)
        outs.append(o)
        lses.append(lse)
        win_st.append(st)
    wts = jax.nn.softmax(jnp.stack(lses), axis=0)
    b_out = jnp.einsum('gnlh,gnlhd->nlhd', wts, jnp.stack(outs))
    merged = jnp.concatenate([a_out, b_out.reshape(n_b, l_len, -1).astype(h.dtype)], axis=-1)
    return merged @ w_out, conv_st, win_st

def gla_chunked(q, k, v, log_a, s0):
    n_b, l_len, h, dk = q.shape
    c = min(GLA_CHUNK, l_len)
    nc = -(-l_len // c)
    lp = nc * c

    def chunks(t):
        t = jnp.pad(t.astype(F32), ((0, 0), (0, lp - l_len), (0, 0), (0, 0)))
        return t.reshape(n_b, nc, c, h, t.shape[-1]).transpose(1, 0, 3, 2, 4)

    causal = jnp.tril(jnp.ones((c, c), bool))

    def step(s, inp):
        qi, ki, vi, gi = inp
        b = jnp.cumsum(gi, axis=2)
        o_inter = jnp.einsum('nhck,nhkv->nhcv', qi * jnp.exp(b), s)
        diff = b[:, :, :, None, :] - b[:, :, None, :, :]
        decay = jnp.exp(jnp.where(causal[:, :, None], diff, -jnp.inf))
        a_mat = jnp.einsum('nhik,nhjk,nhijk->nhij', qi, ki, decay)
        o_intra = jnp.einsum('nhij,nhjv->nhiv', a_mat, vi)
        b_last = b[:, :, -1:, :]
        s_new = jnp.exp(b_last[:, :, 0, :, None]) * s + jnp.einsum('nhck,nhcv->nhkv', ki * jnp.exp(b_last - b), vi)
        return s_new, o_inter + o_intra

    s_fin, o = lax.scan(step, s0.astype(F32), (chunks(q), chunks(k), chunks(v), chunks(log_a)))
    o = o.transpose(1, 0, 3, 2, 4).reshape(n_b, lp, h, v.shape[-1])[:, :l_len]
    return o, s_fin

def indexer_scores(qi, wi, ki):
    dots = jnp.einsum('nqhd,nkd->nqhk', qi, ki).astype(F32) * IDX_DIM ** -0.5
    return jnp.einsum('nqh,nqhk->nqk', wi.astype(F32) * IDX_HEADS ** -0.5, jax.nn.relu(dots))

def select_keys(scores, q_pos, topk):
    key_pos = jnp.arange(scores.shape[-1])
    s = jnp.where(key_pos[None, None, :] <= q_pos[None, :, None], scores, -jnp.inf)
    vals, idx = lax.top_k(s, topk)
    return idx, jnp.isfinite(vals)

def attend_selected(q, k_sel, v_sel, q_pos, key_idx, valid, tab):
    s = jnp.einsum('nqhd,nqkhd->nhqk', q, k_sel).astype(F32) * HEAD_DIM ** -0.5
    bias = jnp.take(tab, rel_bucket(q_pos[None, :, None] - key_idx), axis=0)
    s = s + bias.transpose(0, 3, 1, 2).astype(F32)
    s = jnp.where(valid[:, None], s, -jnp.inf)
    p = jax.nn.softmax(s, axis=-1)
    return jnp.einsum('nhqk,nqkhd->nqhd', p, v_sel.astype(F32))

def dsa_prompt(q, kv, qi, ki, wi, tab):
    n_b, s_len, h, dh = q.shape
    topk = min(DSA_TOPK_MAX, s_len // 4)
    nblk = s_len // DSA_QBLOCK
    gather = jax.vmap(lambda rows, i: rows[i])

    def block(bi):
        start = bi * DSA_QBLOCK
        q_pos = start + jnp.arange(DSA_QBLOCK)
        qb = lax.dynamic_slice_in_dim(q, start, DSA_QBLOCK, axis=1)
        qib = lax.dynamic_slice_in_dim(qi, start, DSA_QBLOCK, axis=1)
        wib = lax.dynamic_slice_in_dim(wi, start, DSA_QBLOCK, axis=1)
        idx, valid = select_keys(indexer_scores(qib, wib, ki), q_pos, topk)
        sel = gather(kv, idx)
        return attend_selected(qb, sel[:, :, :, 0], sel[:, :, :, 1], q_pos, idx, valid, tab)

    o = lax.map(block, jnp.arange(nblk))
    return o.transpose(1, 0, 2, 3, 4).reshape(n_b, s_len, h, dh)

def dsa_step(q, kv_new, qi, ki, wi, kv_pool, kidx_pool, page_table, tab):
    n_b, l_new = q.shape[:2]
    past = page_table.shape[1] * PAGE_SIZE
    topk = min(DSA_TOPK_MAX, (past + l_new) // 4)
    gather = jax.vmap(lambda rows, i: rows[i])
    ki_past = kidx_pool[page_table].reshape(n_b, past, IDX_DIM)
    ki_all = jnp.concatenate([ki_past, ki.astype(ki_past.dtype)], axis=1)
    q_pos = past + jnp.arange(l_new)
    idx, valid = select_keys(indexer_scores(qi, wi, ki_all), q_pos, topk)
    p_idx = jnp.minimum(idx, past - 1)
    phys = gather(page_table, p_idx // PAGE_SIZE) * PAGE_SIZE + p_idx % PAGE_SIZE
    past_sel = kv_pool.reshape((-1,) + kv_pool.shape[2:])[phys]
    new_sel = gather(kv_new.astype(kv_pool.dtype), jnp.clip(idx - past, 0, l_new - 1))
    sel = jnp.where((idx < past)[..., None, None, None], past_sel, new_sel)
    return attend_selected(q, sel[:, :, :, 0], sel[:, :, :, 1], q_pos, idx, valid, tab)

def cd_mix(h, w_in, wa2, ba, gla_g, qn, kn, w_out, tab, s0, pools):
    n_b, l_len, _ = h.shape
    cq, ck, cv, c_lr, c_gate, dq, dk, dv, iq, ik, iw = split_cols(h @ w_in, CD_SPLITS)
    gshp = (n_b, l_len, GLA_HEADS, GLA_DK)
    log_a = jax.nn.log_sigmoid((c_lr @ wa2 + ba).astype(F32)) / GLA_TAU
    o_c, s_c = gla_chunked(cq.reshape(gshp) * GLA_DK ** -0.5, ck.reshape(gshp),
                           cv.reshape(n_b, l_len, GLA_HEADS, GLA_DV), log_a.reshape(gshp), s0)
    o_c = rmsnorm(o_c, gla_g) * jax.nn.silu(c_gate.astype(F32).reshape(n_b, l_len, GLA_HEADS, GLA_DV))
    dshp = (n_b, l_len, DSA_HEADS, HEAD_DIM)
    dq = rmsnorm(dq.reshape(dshp), qn)
    dk = rmsnorm(dk.reshape(dshp), kn)
    kv_rows = jnp.stack([dk, dv.reshape(dshp)], axis=2)
    iq = iq.reshape(n_b, l_len, IDX_HEADS, IDX_DIM)
    if pools is None:
        o_d = dsa_prompt(dq, kv_rows, iq, ik, iw, tab)
        n_pg = l_len // PAGE_SIZE
        kv_st = kv_rows.reshape(n_b, n_pg, PAGE_SIZE, 2, DSA_HEADS, HEAD_DIM)
        ki_st = ik.reshape(n_b, n_pg, PAGE_SIZE, IDX_DIM)
    else:
        kv_pool, kidx_pool, page_table = pools
        o_d = dsa_step(dq, kv_rows, iq, ik, iw, kv_pool, kidx_pool, page_table, tab)
        kv_st, ki_st = kv_rows, ik
    merged = jnp.concatenate([o_c.reshape(n_b, l_len, -1).astype(h.dtype),
                              o_d.reshape(n_b, l_len, -1).astype(h.dtype)], axis=-1)
    return merged @ w_out, s_c.astype(h.dtype), kv_st, ki_st

def trunk(x, is_step, conv_state, win_states, gla_state, dsa_kv, dsa_kidx, page_table,
          norm_mix, norm_ffn, w_in_ab, conv_w, conv_b, conv_ln_g, conv_ln_b, qn_ab, kn_ab, w_out_ab,
          w_in_cd, gla_wa2, gla_ba, gla_norm, qn_cd, kn_cd, w_out_cd, rel_bias,
          w_ffn_gate, w_ffn_up, w_ffn_down):
    n_b = x.shape[0]
    conv_new, gla_new, kv_new, kidx_new = [], [], [], []
    win_new = [[] for _ in WINDOWS]
    for layer in range(DEPTH):
        i = layer // 2
        h = rmsnorm(x, norm_mix[layer])
        if layer % 2 == 0:
            hist = conv_state[i] if is_step else jnp.zeros((n_b, CONV_WIDTH - 1, CONV_CH), x.dtype)
            bufs = [ws[i] for ws in win_states] if is_step else None
            mix, c_st, w_st = ab_mix(h, w_in_ab[i], conv_w[i], conv_b[i], conv_ln_g[i], conv_ln_b[i],
                                     qn_ab[i], kn_ab[i], w_out_ab[i], rel_bias[:, :B_HEADS], hist, bufs)
            conv_new.append(c_st)
            for g in range(len(WINDOWS)):
                win_new[g].append(w_st[g])
        else:
            s0 = gla_state[i] if is_step else jnp.zeros((n_b, GLA_HEADS, GLA_DK, GLA_DV), F32)
            pools = (dsa_kv[i], dsa_kidx[i], page_table) if is_step else None
            mix, g_st, kv_st, ki_st = cd_mix(h, w_in_cd[i], gla_wa2[i], gla_ba[i], gla_norm[i], qn_cd[i], kn_cd[i],
                                             w_out_cd[i], rel_bias[:, B_HEADS:], s0, pools)
            gla_new.append(g_st)
            kv_new.append(kv_st)
            kidx_new.append(ki_st)
        x = x + mix
        hf = rmsnorm(x, norm_ffn[layer])
        x = x + (jax.nn.silu(hf @ w_ffn_gate[layer]) * (hf @ w_ffn_up[layer])) @ w_ffn_down[layer]
    states = (jnp.stack(conv_new), jnp.stack(win_new[0]), jnp.stack(win_new[1]), jnp.stack(win_new[2]),
              jnp.stack(gla_new), jnp.stack(kv_new), jnp.stack(kidx_new))
    return x, states

def setup_inputs(seed: int = 0) -> dict:
    key = jax.random.key(seed)
    ks = iter(jax.random.split(key, 48))

    def nrm(shape, scale=1.0):
        return scale * jax.random.normal(next(ks), shape, F32)

    def gain(shape):
        return 1.0 + nrm(shape, 0.02)

    n_pages = PAST_LEN // PAGE_SIZE
    n_pool = (5 * DEC_BATCH * n_pages + 3) // 4
    page_table = jax.random.permutation(next(ks), n_pool)[: DEC_BATCH * n_pages]
    page_table = page_table.reshape(DEC_BATCH, n_pages).astype(jnp.int32)
    return {
        'x_prompt': nrm((BATCH, SEQ, D_MODEL)),
        'x_sample': nrm((DEC_BATCH, DEC_SEQ, D_MODEL)),
        'state_conv': nrm((N_AB, DEC_BATCH, CONV_WIDTH - 1, CONV_CH), 0.5),
        'cache_win128': nrm((N_AB, DEC_BATCH, min(WINDOWS[0], PAST_LEN), 2, B_HPG, HEAD_DIM)),
        'cache_win512': nrm((N_AB, DEC_BATCH, min(WINDOWS[1], PAST_LEN), 2, B_HPG, HEAD_DIM)),
        'cache_win2048': nrm((N_AB, DEC_BATCH, min(WINDOWS[2], PAST_LEN), 2, B_HPG, HEAD_DIM)),
        'state_gla': nrm((N_CD, DEC_BATCH, GLA_HEADS, GLA_DK, GLA_DV), 0.3),
        'cache_dsa_kv': nrm((N_CD, n_pool, PAGE_SIZE, 2, DSA_HEADS, HEAD_DIM)),
        'cache_dsa_kidx': nrm((N_CD, n_pool, PAGE_SIZE, IDX_DIM)),
        'page_table': page_table,
        'norm_mix': gain((DEPTH, D_MODEL)),
        'norm_ffn': gain((DEPTH, D_MODEL)),
        'w_in_ab': nrm((N_AB, D_MODEL, AB_IN), D_MODEL ** -0.5),
        'conv_w': nrm((N_AB, CONV_WIDTH, CONV_CH), CONV_WIDTH ** -0.5),
        'conv_b': nrm((N_AB, CONV_CH), 0.02),
        'conv_ln_g': gain((N_AB, CONV_CH)),
        'conv_ln_b': nrm((N_AB, CONV_CH), 0.02),
        'qn_ab': gain((N_AB, HEAD_DIM)),
        'kn_ab': gain((N_AB, HEAD_DIM)),
        'w_out_ab': nrm((N_AB, AB_OUT, D_MODEL), AB_OUT ** -0.5),
        'w_in_cd': nrm((N_CD, D_MODEL, CD_IN), D_MODEL ** -0.5),
        'gla_wa2': nrm((N_CD, GLA_GATE_RANK, GLA_HEADS * GLA_DK), GLA_GATE_RANK ** -0.5),
        'gla_ba': nrm((N_CD, GLA_HEADS * GLA_DK), 0.02),
        'gla_norm': gain((N_CD, GLA_DV)),
        'qn_cd': gain((N_CD, HEAD_DIM)),
        'kn_cd': gain((N_CD, HEAD_DIM)),
        'w_out_cd': nrm((N_CD, CD_OUT, D_MODEL), CD_OUT ** -0.5),
        'rel_bias': nrm((REL_BUCKETS, REL_HEADS), 0.5),
        'w_ffn_gate': nrm((DEPTH, D_MODEL, FFN_HIDDEN), D_MODEL ** -0.5),
        'w_ffn_up': nrm((DEPTH, D_MODEL, FFN_HIDDEN), D_MODEL ** -0.5),
        'w_ffn_down': nrm((DEPTH, FFN_HIDDEN, D_MODEL), FFN_HIDDEN ** -0.5),
    }

def reference(x_prompt, x_sample, state_conv, cache_win128, cache_win512, cache_win2048, state_gla,
              cache_dsa_kv, cache_dsa_kidx, page_table,
              norm_mix, norm_ffn, w_in_ab, conv_w, conv_b, conv_ln_g, conv_ln_b, qn_ab, kn_ab, w_out_ab,
              w_in_cd, gla_wa2, gla_ba, gla_norm, qn_cd, kn_cd, w_out_cd, rel_bias,
              w_ffn_gate, w_ffn_up, w_ffn_down):
    weights = (norm_mix, norm_ffn, w_in_ab, conv_w, conv_b, conv_ln_g, conv_ln_b, qn_ab, kn_ab, w_out_ab,
               w_in_cd, gla_wa2, gla_ba, gla_norm, qn_cd, kn_cd, w_out_cd, rel_bias,
               w_ffn_gate, w_ffn_up, w_ffn_down)
    y_prompt, p_states = trunk(x_prompt, False, None, None, None, None, None, None, *weights)
    y_sample, s_states = trunk(x_sample, True, state_conv, (cache_win128, cache_win512, cache_win2048),
                               state_gla, cache_dsa_kv, cache_dsa_kidx, page_table, *weights)
    conv_p, win128_p, win512_p, win2048_p, gla_p, dsa_kv_p, dsa_kidx_p = p_states
    conv_s, win128_s, win512_s, win2048_s, gla_s, dsa_kv_s, dsa_kidx_s = s_states
    return (y_prompt, y_sample, conv_p, conv_s, win128_p, win128_s, win512_p, win512_s, win2048_p, win2048_s,
            gla_p, gla_s, dsa_kv_p, dsa_kv_s, dsa_kidx_p, dsa_kidx_s)


_drawn_inputs = setup_inputs


def setup_inputs(seed=0):
    import zlib

    import numpy as np

    out = dict(_drawn_inputs(seed))
    spreads = {}
    factors = {'conv_ln_g': 3.232,
     'conv_ln_b': 3.471,
     'qn_ab': 8.0,
     'kn_ab': 3.992,
     'gla_ba': 7.298,
     'gla_norm': 7.643,
     'qn_cd': 8.0,
     'kn_cd': 4.036}
    for name, (base, spread) in spreads.items():
        noise = np.random.default_rng([zlib.crc32(name.encode()), seed]).standard_normal(out[name].shape)
        drawn = base * np.exp(spread * noise) if base else spread * noise
        out[name] = jnp.asarray(drawn.astype(out[name].dtype))
    for name, factor in factors.items():
        out[name] = (out[name] * factor).astype(out[name].dtype)
    return out
```

```python
from contextlib import ExitStack

import numpy as np
import concourse.bass as bass
from concourse import mybir

F32 = mybir.dt.float32
I32 = mybir.dt.int32
ALU = mybir.AluOpType
ACT = mybir.ActivationFunctionType
AX = mybir.AxisListType

P = 128
D_MODEL = 1024
KD = D_MODEL // P
SEQ = 1024
QT = SEQ // P
N_SEQ, L_NEW = 8, 4
TS = N_SEQ * L_NEW
T = SEQ + TS
PAST = 1024
PAGE = 128
N_PAGES = PAST // PAGE
DH = 64
CONV_CH = 512
CC = CONV_CH // P
TAPS = 31
HIST = TAPS - 1
WINDOWS = (128, 512, 2048)
DILS = (1, 4, 16)
HPG = 4
GW = HPG * DH
GLA_H, GLA_DK, GLA_DV, GLA_RANK, GLA_TAU = 4, 64, 128, 16, 16.0
DSA_H = 8
IDX_H = 4
TOPK = 256
FFN = 2816
KF = FFN // P
EPS = 1e-6
BUCKETS, MAX_DIST = 32, 2048
NB = BUCKETS + 1
MASKED = -1e30
TAKEN = -3e38
CQ, CK, CV, CLR, CG, DQ, DK_, DV_, IQ, IK, IW = 0, 256, 512, 1024, 1040, 1552, 2064, 2576, 3088, 3344, 3408
AT_M, AT_L, HEAD_ROW = DH, DH + 1, DH + 2
BANK = 512
PIECES = ((0, 512), (512, 512), (1024, TS))


def rel_bucket(dist):
    n = np.maximum(dist, 0)
    half = BUCKETS // 2
    nf = np.maximum(n, half).astype(np.float32)
    large = half + (np.log(nf / np.float32(half)) / np.float32(np.log(MAX_DIST / half)) * np.float32(BUCKETS - half)).astype(np.int32)
    b = np.where(n < half, n, np.minimum(large, BUCKETS - 1))
    return np.where(dist < 0, BUCKETS, b)


def one_hot(bucket):
    return np.moveaxis(np.eye(NB, dtype=np.float32)[bucket], -1, 0)


def shape_constants():
    c = {}
    c["ident"] = np.eye(P, dtype=np.float32)
    c["head_ones"] = np.kron(np.eye(2, dtype=np.float32), np.ones((DH, DH), np.float32))
    for g, dil in enumerate(DILS[:2]):
        rel = 255 - np.arange(383)
        c[f"line{g}"] = one_hot(rel_bucket(np.where((rel >= 0) & (rel <= WINDOWS[g] // dil), rel * dil, -1)))
    rel = 127 - np.arange(255)
    c["line2"] = one_hot(rel_bucket(np.where((rel >= 0) & (rel % 2 == 0), rel * (DILS[2] // 2), -1)))
    c["line_dsa"] = one_hot(rel_bucket(1023 - np.arange(1151)))
    for g, dil in enumerate(DILS):
        nk = 64 if g == 2 else 128
        rows = []
        for l in range(L_NEW):
            j = np.arange(nk)
            cached = np.where(j >= l, 128 + l - j, -1) if g == 0 else dil * (nk - j)
            new = l - np.arange(L_NEW)
            if g:
                new = np.where(new == 0, 0, -1)
            rows.append(one_hot(rel_bucket(np.concatenate([cached, np.tile(new, N_SEQ)]))))
        c[f"sample_hot{g}"] = np.stack(rows, 1)
    n_of, l_of = np.arange(TS) // L_NEW, np.arange(TS) % L_NEW
    c["tri"] = np.where(np.arange(P)[None] <= np.arange(P)[:, None], 0, MASKED).astype(np.float32)
    c["causal_T"] = (np.arange(P)[:, None] <= np.arange(P)[None]).astype(np.float32)
    c["chunk_inside"] = np.concatenate([np.arange(SEQ) % P != 0, l_of != 0]).astype(np.float32)[None]
    c["sample_causal_T"] = ((n_of[:, None] == n_of[None]) & (l_of[:, None] <= l_of[None])).astype(np.float32)
    c["seq_of"] = (n_of[:, None] == np.arange(N_SEQ)[None]).astype(np.float32)
    row = np.arange(P)
    tok = lambda half, l: (4 * half + row // 32) * L_NEW + l
    c["index_rows"] = np.stack([((np.arange(TS)[:, None] == tok(g, row % 4)[None]) & (row % 32 < 16)[None]) for g in range(2)], 1).astype(np.float32)
    c["dsa_rows"] = np.stack([np.arange(TS)[:, None] == tok(g, row % 4)[None] for g in range(2)], 1).astype(np.float32)
    c["dsa_other"] = np.stack([np.where(n_of[None] == (4 * g + row // 32)[:, None], 0, MASKED) for g in range(2)], 1).astype(np.float32)
    c["new_mask"] = np.where(np.arange(L_NEW)[None] <= l_of[:, None], 0, MASKED).astype(np.float32)
    key = np.arange(PAST)
    c["dsa_hot"] = np.stack([one_hot(rel_bucket(PAST + l - key)) for l in range(L_NEW)], 1)
    c["dsa_hot_new"] = np.stack([one_hot(rel_bucket(np.tile(l - np.arange(L_NEW), N_SEQ))) for l in range(L_NEW)], 1)
    row_n = np.arange(P) // (L_NEW * HPG)
    c["other_seq"] = np.where(row_n[:, None] == np.arange(TS)[None] // L_NEW, 0, MASKED).astype(np.float32)
    f = np.arange(GW) // DH
    c["feat_head"] = (f[:, None] == np.arange(HPG)[None]).astype(np.float32).reshape(2, P, HPG).transpose(1, 0, 2).copy()
    c["row_head"] = (np.arange(P)[:, None] % HPG == np.arange(HPG)[None]).astype(np.float32)
    return c


class Stage:
    pass


LIVE_SEMAPHORES = []


def add_sems(nc, *names):
    sems = [nc.alloc_semaphore(n) for n in names]
    LIVE_SEMAPHORES.extend(sems)
    return sems


def recycle_semaphores(nc):
    nc.clear_and_free_semaphores(list(LIVE_SEMAPHORES))
    LIVE_SEMAPHORES.clear()
    nc.all_engine_barrier()


def chain(eng, sem):
    count = [0]

    def done(ins):
        count[0] += 1
        ins.then_inc(sem, 1)
        eng.wait_ge(sem, count[0])
        return ins
    return done


def load_inputs(nc, S):
    with ExitStack() as ctx:
        xrow = ctx.enter_context(nc.sbuf_tensor("xrow", [P, QT + 1, D_MODEL], F32))
        loaded, gains, transposed, evacuated = add_sems(nc, "x_loaded", "gains_loaded", "x_transposed", "x_evacuated")
        ps = S.ps[:, 0:3072].rearrange("p (b c) -> p b c", b=2)
        block = ctx.enter_context(nc.Block())

        @block.sync
        def _(sp):
            sp.dma_start(S.ident[:, :], S.c["ident"]).then_inc(loaded, 16)
            for t in range(QT):
                sp.dma_start(xrow[:, t, :], S.d["x_prompt"][0, t * P:(t + 1) * P, :]).then_inc(loaded, 16)
            sp.dma_start(xrow[0:TS, QT, :], S.d["x_sample"].rearrange("n l d -> (n l) d")).then_inc(loaded, 16)
            sp.dma_start(S.head_ones[:, :], S.c["head_ones"]).then_inc(gains, 16)
            for name, dst in (("norm_mix", S.g_mix), ("norm_ffn", S.g_ffn)):
                for layer in range(2):
                    sp.dma_start(dst[:, layer, :], S.d[name][layer].rearrange("(k p) -> p k", p=P)).then_inc(gains, 16)
            for i, name in enumerate(("qn_ab", "kn_ab", "qn_cd", "kn_cd")):
                for half in range(2):
                    sp.dma_start(S.g_qk[half * DH:(half + 1) * DH, i:i + 1], S.d[name].rearrange("a d -> d a")).then_inc(gains, 16)
            sp.dma_start(S.tab[0:BUCKETS, :], S.d["rel_bias"]).then_inc(gains, 16)
            sp.wait_ge(gains, 16 * 14)

        @block.gpsimd
        def _(pool):
            pool.memset(S.ones[:, :], 1.0)

        @block.tensor
        def _(pe):
            pe.wait_ge(loaded, 16 * (QT + 2))
            for k in range(KD):
                if k >= 2:
                    pe.wait_ge(evacuated, k - 1)
                for t in range(QT + 1):
                    n = P if t < QT else TS
                    last = pe.transpose(ps[:, k % 2, t * P:t * P + n], xrow[0:n, t, k * P:(k + 1) * P], S.ident[0:n, 0:n])
                last.then_inc(transposed, 1)

        @block.vector
        def _(dve):
            dve.memset(S.tab[BUCKETS:NB, :], MASKED)
            dve.memset(S.eps[:, :], EPS)
            dve.wait_ge(gains, 16 * 14)
            dve.tensor_scalar(S.g_qk[:, 2:3], S.g_qk[:, 2:3], DH ** -0.5, None, ALU.mult)
            for k in range(KD):
                dve.wait_ge(transposed, k + 1)
                dve.tensor_copy(S.xT[:, k, :], ps[:, k % 2, 0:T]).then_inc(evacuated, 1)


def rms_norm(nc, S, tag, gain, hT):
    with ExitStack() as ctx:
        sq = ctx.enter_context(nc.sbuf_tensor(f"sq_{tag}", [P, 2, T], F32))
        rstd = ctx.enter_context(nc.sbuf_tensor(f"rstd_{tag}", [P, T], F32))
        squared, summed, mean_ready, rstd_ready = add_sems(
            nc, f"squared_{tag}", f"summed_{tag}", f"mean_ready_{tag}", f"rstd_ready_{tag}")
        block = ctx.enter_context(nc.Block())

        @block.scalar
        def _(act):
            for k in range(KD):
                if k >= 2:
                    act.wait_ge(summed, k - 1)
                act.activation(sq[:, k % 2, :], S.xT[:, k, :], ACT.Square).then_inc(squared, 1)
            act.wait_ge(summed, KD)
            act.activation(rstd[:, :], S.ps[:, 0:T], ACT.Ln, scale=1.0 / D_MODEL, bias=S.eps[:, :]).then_inc(mean_ready, 1)
            act.wait_ge(mean_ready, 1)
            act.activation(rstd[:, :], rstd[:, :], ACT.Exp, scale=-0.5).then_inc(rstd_ready, 1)

        @block.tensor
        def _(pe):
            for k in range(KD):
                pe.wait_ge(squared, k + 1)
                for at, n in PIECES:
                    last = pe.matmul(S.ps[:, at:at + n], S.ones[:, :], sq[:, k % 2, at:at + n], start=k == 0, stop=k == KD - 1)
                last.then_inc(summed, 1)

        @block.vector
        def _(dve):
            dve.wait_ge(rstd_ready, 1)
            for k in range(KD):
                dve.scalar_tensor_tensor(hT[:, k, :], S.xT[:, k, :], gain[:, k:k + 1], rstd[:, :], ALU.mult, ALU.mult)


class Weights:

    def __init__(self, nc, ctx, tag, kt):
        self.slots = ctx.enter_context(nc.sbuf_tensor(f"w_{tag}", [P, 2, kt, P], F32))
        self.loaded = add_sems(nc, f"w0_loaded_{tag}", f"w1_loaded_{tag}")


def product_sems(nc, tag):
    return [add_sems(nc, *(f"{what}{j}_{tag}" for j in range(2))) for what in ("product", "slot_free")]


def load_weight_pairs(sp, W, product, kt, iters, src_a, src_b, before=0):
    with sp.Fori(1, iters + 1) as i:
        for j, (w, step, col) in enumerate((src_a, src_b)):
            sp.wait_ge(product[j], i + before)
            sp.dma_start(W.slots[:, j, 0:kt, :], w[:, :, bass.ds(i * step + (col - step), P)]).then_inc(W.loaded[j], 16)


def multiply_pairs(pe, S, W, product, free, kt, iters, rhs, before=0):
    for j in range(0 if before else 2):
        pe.sem_inc(product[j], 1)
    with pe.Fori(0, iters) as i:
        for j in range(2):
            pe.wait_ge(W.loaded[j], i * 16 + 16 * (before + 1))
            pe.wait_ge(free[j], i + (before + 1))
            for k in range(kt):
                for n, (at, size) in enumerate(PIECES):
                    last = pe.matmul(S.ps[:, j * 1536 + at:j * 1536 + at + size], W.slots[:, j, k, :], rhs(k)[:, at:at + size],
                                     start=k == 0, stop=k == kt - 1)
                    if k == kt - 1 and n == 2:
                        last.then_inc(product[j], 1)


def w_cols(w, col):
    return w.rearrange("(k p) m -> p k m", p=P), P, col


def w_pairs(w, col):
    v = w.rearrange("(k p) m -> p k m", p=P)
    return (v, 2 * P, col), (v, 2 * P, col + P)


def slot(S, j, n=T):
    return S.ps[:, j * 1536:j * 1536 + n]


LINES = ((0, 383), (383, 383), (766, 255))
AB_LINE, DSA_LINE = 1021, 1151


def bias_lines(nc, S):
    with ExitStack() as ctx:
        sb = lambda n, s: ctx.enter_context(nc.sbuf_tensor(n, s, F32))
        hot, hot_d = sb("hot", [NB, AB_LINE]), sb("hot_dsa", [NB, DSA_LINE])
        line, line_d = sb("line", [HPG, 3, BANK]), sb("line_dsa", [DSA_H, DSA_LINE])
        loaded, product, kept, out = add_sems(nc, "hot_loaded", "lines_product", "lines_kept", "lines_out")
        block = ctx.enter_context(nc.Block())

        @block.sync
        def _(sp):
            for g, (at, n) in enumerate(LINES):
                sp.dma_start(hot[:, at:at + n], S.c[f"line{g}"]).then_inc(loaded, 16)
            sp.dma_start(hot_d[:, :], S.c["line_dsa"]).then_inc(loaded, 16)
            sp.wait_ge(kept, 2)
            for g, (at, n) in enumerate(LINES):
                sp.dma_start(S.ab_line[:, at:at + n], line[:, g, 0:n]).then_inc(out, 16)
            sp.dma_start(S.dsa_line, line_d[:, :]).then_inc(out, 16)
            sp.wait_ge(out, 64)
            for h in range(HPG):
                sp.dma_start(S.ab_copies[h], S.ab_line[h:h + 1, :].broadcast_to([P, AB_LINE])).then_inc(S.ab_lines, 16)
            for h in range(DSA_H):
                sp.dma_start(S.dsa_copies[h], S.dsa_line[h:h + 1, :].broadcast_to([P, DSA_LINE])).then_inc(S.dsa_lines, 16)

        @block.tensor
        def _(pe):
            pe.wait_ge(loaded, 64)
            for g, (at, n) in enumerate(LINES):
                last = pe.matmul(S.ps[0:HPG, g * BANK:g * BANK + n], S.tab[:, g * HPG:(g + 1) * HPG], hot[:, at:at + n], start=True, stop=True)
            for at in range(0, DSA_LINE, BANK):
                n = min(BANK, DSA_LINE - at)
                last = pe.matmul(S.ps[0:DSA_H, 1536 + at:1536 + at + n], S.tab[:, 12:12 + DSA_H], hot_d[:, at:at + n], start=True, stop=True)
            last.then_inc(product, 1)

        @block.vector
        def _(dve):
            dve.wait_ge(product, 1)
            for g, (at, n) in enumerate(LINES):
                last = dve.tensor_copy(line[:, g, 0:n], S.ps[0:HPG, g * BANK:g * BANK + n])
            last.then_inc(kept, 1)
            dve.tensor_copy(line_d[:, :], S.ps[0:DSA_H, 1536:1536 + DSA_LINE]).then_inc(kept, 1)


def toeplitz(copies, line, at, heads, step, n):
    return bass.AP(copies.tensor, heads.start * P * line + at + P - 1, [[line - 1, P], [step * P * line, (heads.stop - heads.start) // step], [1, n]])


U_PROMPT = HIST + SEQ
U_SEQ = HIST + L_NEW
U_LEN = U_PROMPT + N_SEQ * U_SEQ


def glu_products(nc, S, hT, uT, taps):
    with ExitStack() as ctx:
        W = Weights(nc, ctx, "glu", KD)
        gate = ctx.enter_context(nc.sbuf_tensor("glu_gate", [P, T], F32))
        hist = ctx.enter_context(nc.sbuf_tensor("glu_hist", [120, 2, CONV_CH], F32))
        tap_rows = ctx.enter_context(nc.sbuf_tensor("tap_rows", [TAPS, CONV_CH], F32))
        product, free = product_sems(nc, "glu")
        hist_loaded, turned, placed = add_sems(nc, "hist_loaded", "hist_turned", "hist_placed")
        w = S.d["w_in_ab"][0]
        us = uT[:, :, U_PROMPT:].rearrange("p c (n u) -> p c n u", n=N_SEQ)
        turn = S.ps[:, 3072:3584]
        block = ctx.enter_context(nc.Block())

        @block.sync
        def _(sp):
            for half in range(2):
                sp.dma_start(hist[:, half, :], S.d["state_conv"][0, 4 * half:4 * half + 4].rearrange("n r c -> (n r) c")).then_inc(hist_loaded, 16)
            sp.dma_start(tap_rows[:, :], S.d["conv_w"][0]).then_inc(hist_loaded, 16)
            load_weight_pairs(sp, W, product, KD, CC, w_cols(w, CONV_CH), w_cols(w, 0))

        @block.tensor
        def _(pe):
            pe.wait_ge(hist_loaded, 48)
            for c in range(CC):
                last = pe.transpose(turn[:, 256 + c * TAPS:256 + (c + 1) * TAPS], tap_rows[:, c * P:(c + 1) * P], S.ident[0:TAPS, 0:TAPS])
            last.then_inc(turned, 1)
            for c in range(CC):
                pe.wait_ge(placed, 2 * c + 1)
                for half in range(2):
                    last = pe.transpose(turn[:, 120 * half:120 * half + 120], hist[:, half, c * P:(c + 1) * P], S.ident[0:120, 0:120])
                last.then_inc(turned, 1)
            multiply_pairs(pe, S, W, product, free, KD, CC, lambda k: hT[:, k, :])

        @block.scalar
        def _(act):
            act.sem_inc(free[0], 1)
            with act.Fori(0, CC) as i:
                act.wait_ge(product[0], i + 2)
                act.wait_ge(free[1], i + 1)
                act.activation(gate[:, :], slot(S, 0), ACT.Sigmoid).then_inc(free[0], 1)

        @block.vector
        def _(dve):
            dve.memset(uT[:, :, 0:HIST], 0.0)
            dve.wait_ge(turned, 1)
            dve.tensor_copy(taps[:, :, :], turn[:, 256:256 + CC * TAPS].rearrange("p (c t) -> p c t", c=CC)).then_inc(placed, 1)
            for c in range(CC):
                dve.wait_ge(turned, c + 2)
                for half in range(2):
                    dve.tensor_copy(us[:, c, 4 * half:4 * half + 4, 0:HIST],
                                    turn[:, 120 * half:120 * half + 120].rearrange("p (n r) -> p n r", n=4)).then_inc(placed, 1)
            dve.sem_inc(free[1], 1)
            with dve.Fori(0, CC) as i:
                dve.wait_ge(product[1], i + 2)
                dve.wait_ge(free[0], i + 2)
                dve.tensor_tensor(us[:, bass.ds(i, 1), :, HIST:].rearrange("p a n u -> p (a n) u"),
                                  S.ps[:, 1536 + SEQ:1536 + T].rearrange("p (n u) -> p n u", n=N_SEQ),
                                  gate[:, SEQ:T].rearrange("p (n u) -> p n u", n=N_SEQ), ALU.mult)
                dve.tensor_tensor(uT[:, bass.ds(i, 1), HIST:U_PROMPT].rearrange("p a t -> p (a t)"), slot(S, 1, SEQ), gate[:, 0:SEQ],
                                  ALU.mult).then_inc(free[1], 1)


def qkv_products(nc, S, hT, uT, taps, yT, vS, v_new):
    with ExitStack() as ctx:
        W = Weights(nc, ctx, "qk", KD)
        wv = ctx.enter_context(nc.sbuf_tensor("wv", [P, KD, GW], F32))
        conv_bias = ctx.enter_context(nc.sbuf_tensor("conv_bias", [P, CC], F32))
        product, free = product_sems(nc, "qk")
        wv_loaded, v_product, v_kept, bias_loaded, conv_step = add_sems(nc, "wv_loaded", "v_product", "v_kept", "bias_loaded", "conv_step")
        w = S.d["w_in_ab"][0]
        vps = S.ps[:, 3072:4096].rearrange("p (b c) -> p b c", b=2)
        us = uT[:, :, U_PROMPT:].rearrange("p c (n u) -> p c n u", n=N_SEQ)
        block = ctx.enter_context(nc.Block())
        srcs = w_pairs(w, 2 * CONV_CH)

        @block.sync
        def _(sp):
            sp.dma_start(conv_bias[:, :], S.d["conv_b"][0].rearrange("(c p) -> p c", p=P)).then_inc(bias_loaded, 16)
            load_weight_pairs(sp, W, product, KD, 6, *srcs)
            for g in range(3):
                if g:
                    sp.wait_ge(v_product, 9 * g)
                sp.dma_start(wv[:, :, :], w[:, 2560 + g * GW:2560 + (g + 1) * GW].rearrange("(k p) m -> p k m", p=P)).then_inc(wv_loaded, 16)

        @block.tensor
        def _(pe):
            multiply_pairs(pe, S, W, product, free, KD, 6, lambda k: hT[:, k, :])
            for g in range(3):
                pe.wait_ge(wv_loaded, 16 * (g + 1))
                for b in range(QT + 1):
                    n = 9 * g + b
                    if n >= 2:
                        pe.wait_ge(v_kept, n - 1)
                    for k in range(KD):
                        tok = block_tokens(g, b, hT[:, k, 0:SEQ]) if b < QT else hT[:, k, SEQ:T]
                        last = pe.matmul(vps[0:P if b < QT else TS, n % 2, 0:GW], tok, wv[:, k, :], start=k == 0, stop=k == KD - 1)
                    last.then_inc(v_product, 1)

        @block.scalar
        def _(act):
            for j in range(2):
                act.sem_inc(free[j], 1)
            with act.Fori(0, 6) as i:
                for j in range(2):
                    act.wait_ge(product[j], i + 2)
                    act.activation(S.qk[:, bass.ds(i * 2 + j, 1), :].rearrange("p a t -> p (a t)"), slot(S, j), ACT.Copy).then_inc(free[j], 1)
            for n in range(27):
                act.wait_ge(v_product, n + 1)
                g, b = n // 9, n % 9
                if b < QT:
                    act.activation(vS[:, g, b, :], vps[:, n % 2, 0:GW], ACT.Copy).then_inc(v_kept, 1)
                else:
                    act.activation(v_new[:, g, :], vps[0:TS, n % 2, 0:GW], ACT.Copy).then_inc(v_kept, 1)

        @block.vector
        def _(dve):
            ysmp = yT[:, :, SEQ:T].rearrange("p c (n l) -> p c n l", n=N_SEQ)
            dve.wait_ge(bias_loaded, 16)
            for c in range(CC):
                dve.tensor_scalar(yT[:, c, 0:SEQ], uT[:, c, 0:SEQ], taps[:, c, 0:1], conv_bias[:, c:c + 1], ALU.mult, ALU.add).then_inc(conv_step, 1)
                dve.tensor_scalar(ysmp[:, c], us[:, c, :, 0:L_NEW], taps[:, c, 0:1], conv_bias[:, c:c + 1], ALU.mult, ALU.add).then_inc(conv_step, 1)
            with dve.Fori(1, TAPS) as t:
                for c in range(CC):
                    dve.wait_ge(conv_step, t * (2 * CC) + (2 * c + 2 - 2 * CC))
                    dve.scalar_tensor_tensor(yT[:, c, 0:SEQ], uT[:, c, bass.ds(t, SEQ)], taps[:, c, bass.ds(t, 1)], yT[:, c, 0:SEQ],
                                             ALU.mult, ALU.add).then_inc(conv_step, 1)
                    dve.scalar_tensor_tensor(ysmp[:, c], us[:, c, :, bass.ds(t, L_NEW)], taps[:, c, bass.ds(t, 1)], ysmp[:, c],
                                             ALU.mult, ALU.add).then_inc(conv_step, 1)


def block_tokens(g, b, line):
    if g == 0:
        return line[:, b * P:(b + 1) * P]
    if g == 1:
        r, half = b // 2, b % 2
        return line.rearrange("p (j r) -> p r j", r=4)[:, r, half * P:(half + 1) * P]
    return line.rearrange("p (j r) -> p r j", r=8)[:, b, :]


def block_keys(g, b, line):
    if g == 0 and b:
        return line[:, (b - 1) * P:(b + 1) * P]
    if g == 1 and b % 2:
        return line.rearrange("p (j r) -> p r j", r=4)[:, b // 2, :]
    return block_tokens(g, b, line)


def has_previous(g, b):
    return (g == 0 and b > 0) or (g == 1 and b % 2 == 1)


def dram_rows(g, b, rows):
    if g == 0:
        return rows[b * P:(b + 1) * P, :]
    if g == 1:
        return rows.rearrange("(j r) x -> r j x", r=4)[b // 2, (b % 2) * P:(b % 2 + 1) * P, :]
    return rows.rearrange("(j r) x -> r j x", r=8)[b]


def head_norms(nc, S, tag, src, tiles, gains, ones, dim):
    n = len(tiles)
    with ExitStack() as ctx:
        sq = ctx.enter_context(nc.sbuf_tensor(f"hsq_{tag}", [P, 2, T], F32))
        rstd = ctx.enter_context(nc.sbuf_tensor(f"hrstd_{tag}", [P, 2, T], F32))
        squared, summed, logged, rstd_ready, scaled = add_sems(
            nc, *(f"{x}_{tag}" for x in ("hsquared", "hsummed", "hlogged", "hrstd_ready", "hscaled")))
        block = ctx.enter_context(nc.Block())

        @block.scalar
        def _(act):
            def square(i):
                if i >= 2:
                    act.wait_ge(summed, i - 1)
                act.activation(sq[:, i % 2, :], src[:, tiles[i], :], ACT.Square).then_inc(squared, 1)

            square(0)
            for i in range(n):
                if i + 1 < n:
                    square(i + 1)
                act.wait_ge(summed, i + 1)
                if i >= 2:
                    act.wait_ge(scaled, i - 1)
                act.activation(rstd[:, i % 2, :], slot(S, i % 2), ACT.Ln, scale=1.0 / dim, bias=S.eps[:, :]).then_inc(logged, 1)
                act.wait_ge(logged, i + 1)
                act.activation(rstd[:, i % 2, :], rstd[:, i % 2, :], ACT.Exp, scale=-0.5).then_inc(rstd_ready, 1)

        @block.tensor
        def _(pe):
            for i in range(n):
                pe.wait_ge(squared, i + 1)
                if i >= 2:
                    pe.wait_ge(logged, i - 1)
                for at, m in PIECES:
                    last = pe.matmul(S.ps[:, (i % 2) * 1536 + at:(i % 2) * 1536 + at + m], ones[:, :], sq[:, i % 2, at:at + m],
                                     start=True, stop=True)
                last.then_inc(summed, 1)

        @block.vector
        def _(dve):
            for i in range(n):
                dve.wait_ge(rstd_ready, i + 1)
                dve.scalar_tensor_tensor(src[:, tiles[i], :], src[:, tiles[i], :], gains[i], rstd[:, i % 2, :],
                                         ALU.mult, ALU.mult).then_inc(scaled, 1)


def turn_and_store(nc, S, tag, jobs, direct):
    with ExitStack() as ctx:
        stage = ctx.enter_context(nc.sbuf_tensor(f"turn_stage_{tag}", [P, 4, 512], F32))
        turned, copied, rows_out = add_sems(nc, f"turned_{tag}", f"turn_copied_{tag}", f"direct_out_{tag}")
        stored = add_sems(nc, *(f"turn_stored{i}_{tag}" for i in range(4)))
        stores_before = lambda i: sum(len(jobs[j][2]) for j in range(i % 4, i, 4))
        block = ctx.enter_context(nc.Block())

        @block.tensor
        def _(pe):
            for i, (tiles, n, _) in enumerate(jobs):
                if i >= 2:
                    pe.wait_ge(copied, i - 1)
                for f, tile in enumerate(tiles):
                    last = pe.transpose(S.ps[0:n, (i % 2) * BANK + f * P:(i % 2) * BANK + (f + 1) * P], tile, S.ident[:, :])
                last.then_inc(turned, 1)

        @block.vector
        def _(dve):
            for i, (tiles, n, _) in enumerate(jobs):
                dve.wait_ge(turned, i + 1)
                if i >= 4:
                    dve.wait_ge(stored[i % 4], 16 * stores_before(i))
                dve.tensor_copy(stage[0:n, i % 4, 0:P * len(tiles)], S.ps[0:n, (i % 2) * BANK:(i % 2) * BANK + P * len(tiles)]).then_inc(copied, 1)

        @block.sync
        def _(sp):
            for i, (tiles, n, outs) in enumerate(jobs):
                sp.wait_ge(copied, i + 1)
                for first, end, width, dst in outs:
                    sp.dma_start(dst, stage[first:end, i % 4, 0:width]).then_inc(stored[i % 4], 16)
            for s in range(4):
                sp.wait_ge(stored[s], 16 * stores_before(len(jobs) + (s - len(jobs)) % 4))

        @block.scalar
        def _(act):
            for dst, src in direct:
                act.dma_start(dst, src).then_inc(rows_out, 16)
            act.wait_ge(rows_out, 16 * len(direct))


def layer0_states(nc, S, uT, vS, v_new, q_rows, k_rows, v_rows):
    o = S.o
    jobs = []
    jobs.append(([uT[:, c, U_PROMPT - HIST:U_PROMPT] for c in range(CC)], HIST, [(0, HIST, 512, o["conv_p"][0, 0])]))
    for n0 in range(0, N_SEQ, 3):
        ns = min(3, N_SEQ - n0)
        at = U_PROMPT + n0 * U_SEQ
        jobs.append(([uT[:, c, at:at + ns * U_SEQ] for c in range(CC)], ns * U_SEQ,
                     [(i * U_SEQ + L_NEW, (i + 1) * U_SEQ, 512, o["conv_s"][0, n0 + i]) for i in range(ns)]))
    for src, dst in ((0, q_rows), (6, k_rows)):
        jobs.append(([S.qk[:, src + f, SEQ:T] for f in range(4)], TS, [(0, TS, 512, dst[:, 0:512])]))
        jobs.append(([S.qk[:, src + f, SEQ:T] for f in range(4, 6)], TS, [(0, TS, 256, dst[:, 512:768])]))
    for g, name in enumerate(("win128_p", "win512_p", "win2048_p")):
        keep = min(WINDOWS[g], SEQ)
        rows = o[name][0, 0].rearrange("t a h d -> t a (h d)")
        for t in range(keep // P):
            at = SEQ - keep + t * P
            jobs.append(([S.qk[:, 6 + 2 * g + f, at:at + P] for f in range(2)], P, [(0, P, 256, rows[t * P:(t + 1) * P, 0, :])]))
    direct = [(v_rows.rearrange("t (g x) -> t g x", g=3), v_new[:, :, :])]
    for g, name in enumerate(("win128_p", "win512_p", "win2048_p")):
        rows = o[name][0, 0].rearrange("t a h d -> t a (h d)")
        if g == 0:
            direct.append((rows[:, 1, :], vS[:, 0, QT - 1, :]))
        elif g == 1:
            direct += [(rows.rearrange("(j r) a x -> r j a x", r=4)[r, :, 1, :], vS[:, 1, 2 * r + 1, :]) for r in range(4)]
        else:
            direct += [(rows.rearrange("(j r) a x -> r j a x", r=8)[r, :, 1, :], vS[:, 2, r, :]) for r in range(8)]
    for g, name in enumerate(("win128_s", "win512_s", "win2048_s")):
        cache = S.d[("cache_win128", "cache_win512", "cache_win2048")[g]][0]
        old = cache.shape[1]
        keep = min(WINDOWS[g], old + L_NEW)
        direct.append((o[name][0, :, 0:keep - L_NEW].rearrange("n t a h d -> n t (a h d)"),
                       cache[:, old - (keep - L_NEW):old].rearrange("n t a h d -> n t (a h d)")))
    turn_and_store(nc, S, "ab", jobs, direct)

    with ExitStack() as ctx:
        (new_rows,) = add_sems(nc, "new_rows_out")
        block = ctx.enter_context(nc.Block())

        @block.sync
        def _(sp):
            count = 0
            for g, name in enumerate(("win128_s", "win512_s", "win2048_s")):
                out = o[name][0].rearrange("n t a h d -> n t a (h d)")
                keep = out.shape[1]
                for a, rows in ((0, k_rows), (1, v_rows)):
                    sp.dma_start(out[:, keep - L_NEW:keep, a, :], rows[:, g * GW:(g + 1) * GW].rearrange("(n l) x -> n l x", n=N_SEQ)).then_inc(new_rows, 16)
                    count += 1
            sp.wait_ge(new_rows, 16 * count)


def dilated_prompt(nc, S, vS):
    with ExitStack() as ctx:
        sb = lambda n, s: ctx.enter_context(nc.sbuf_tensor(n, s, F32))
        toep = sb("toep", [P, 3, HPG, 256])
        sc = sb("sc", [P, 2, HPG, 256])
        pT = sb("pT", [P, 2, HPG, 256])
        row = sb("part_row", [P, 2, HPG, HEAD_ROW])
        toep_in, scored, biased, row_in = add_sems(nc, "toep_in", "scored", "biased", "maxima_ready")
        exps, turned, kept, summed, sums_copied = add_sems(nc, "exps_done", "probs_turned", "probs_kept", "pv_summed", "sums_copied")
        stored = add_sems(nc, "part_stored0", "part_stored1")
        s_ps = S.ps[:, 0:1024].rearrange("p (h k) -> p h k", h=HPG)
        t_ps = S.ps[:, 1024:3072].rearrange("p (b h k) -> p b h k", b=2, h=HPG)
        o_ps = S.ps[:, 3072:4096].rearrange("p (b c) -> p b c", b=2)
        blocks = [(g, b) for g in range(3) for b in range(QT)]
        place = lambda h: 2 * (h % 2) + h // 2
        block = ctx.enter_context(nc.Block())

        @block.sync
        def _(sp):
            sp.wait_ge(S.ab_lines, 16 * HPG)
            for g, n in enumerate((256, 256, P)):
                for odd in range(2):
                    sp.dma_start(toep[:, g, 2 * odd:2 * odd + 2, 0:n],
                                 toeplitz(S.ab_copies, AB_LINE, LINES[g][0], slice(odd, odd + 4), 2, n)).then_inc(toep_in, 16)
            for i, (g, b) in enumerate(blocks):
                sp.wait_ge(sums_copied, i + 1)
                sp.wait_ge(exps, i + 1)
                dst = dram_rows(g, b, S.part_rows[g, 0:SEQ].rearrange("t h x -> t (h x)"))
                sp.dma_start(dst, row[:, i % 2, :, :].rearrange("p h x -> p (h x)")).then_inc(stored[i % 2], 16)
            for j in range(2):
                sp.wait_ge(stored[j], 16 * len(blocks) // 2)

        @block.tensor
        def _(pe):
            def scores(i):
                g, b = blocks[i]
                nk = 256 if has_previous(g, b) else P
                if i:
                    pe.wait_ge(biased, i)
                for h in range(HPG):
                    f, base = 2 * g + h // 2, DH * (h % 2)
                    last = pe.matmul(s_ps[:, place(h), 0:nk], block_tokens(g, b, S.qk[base:base + DH, f, 0:SEQ]),
                                     block_keys(g, b, S.qk[base:base + DH, 6 + f, 0:SEQ]), start=True, stop=True)
                last.then_inc(scored, 1)

            scores(0)
            for i, (g, b) in enumerate(blocks):
                if i + 1 < len(blocks):
                    scores(i + 1)
                pe.wait_ge(exps, i + 1)
                if i >= 2:
                    pe.wait_ge(kept, i - 1)
                kts = 2 if has_previous(g, b) else 1
                for h in range(HPG):
                    for kt in range(kts):
                        last = pe.transpose(t_ps[:, i % 2, h, kt * P:(kt + 1) * P], sc[:, i % 2, place(h), kt * P:(kt + 1) * P], S.ident[:, :])
                last.then_inc(turned, 1)
                pe.wait_ge(kept, i + 1)
                if i >= 2:
                    pe.wait_ge(sums_copied, i - 1)
                for h in range(HPG):
                    for kt in range(kts):
                        v = vS[:, g, b - (kts - 1) + kt, h * DH:(h + 1) * DH]
                        last = pe.matmul(o_ps[:, i % 2, h * DH:(h + 1) * DH], pT[:, i % 2, h, kt * P:(kt + 1) * P], v,
                                         start=kt == 0, stop=kt == kts - 1)
                last.then_inc(summed, 1)

        @block.vector
        def _(dve):
            def copy_sums(i):
                dve.wait_ge(summed, i + 1)
                dve.tensor_copy(row[:, i % 2, :, 0:DH], o_ps[:, i % 2, 0:GW].rearrange("p (h d) -> p h d", h=HPG)).then_inc(sums_copied, 1)

            dve.wait_ge(toep_in, 96)
            for i, (g, b) in enumerate(blocks):
                nk = 256 if has_previous(g, b) else P
                off = 0 if nk == 256 or g == 2 else P
                dve.wait_ge(scored, i + 1)
                if i >= 2:
                    dve.wait_ge(turned, i - 1)
                dve.scalar_tensor_tensor(sc[:, i % 2, :, 0:nk], s_ps[:, :, 0:nk], DH ** -0.5, toep[:, g, :, off:off + nk],
                                         ALU.mult, ALU.add).then_inc(biased, 1)
                dve.wait_ge(biased, i + 1)
                if i >= 2:
                    dve.wait_ge(stored[i % 2], 16 * (i // 2))
                dve.tensor_reduce(row[:, i % 2, :, AT_M].rearrange("p (b a) -> p a b", a=2), sc[:, i % 2, :, 0:nk], AX.X, ALU.max, negate=True).then_inc(row_in, 1)
                if i >= 1:
                    copy_sums(i - 1)
            copy_sums(len(blocks) - 1)

        @block.scalar
        def _(act):
            for i, (g, b) in enumerate(blocks):
                kts = 2 if has_previous(g, b) else 1
                act.wait_ge(row_in, i + 1)
                for h in range(HPG):
                    last = act.activation(sc[:, i % 2, place(h), 0:kts * P], sc[:, i % 2, place(h), 0:kts * P], ACT.Exp,
                                          bias=row[:, i % 2, h, AT_M:AT_M + 1], accum_out=row[:, i % 2, h, AT_L:AT_L + 1])
                    if h == HPG - 1:
                        last.then_inc(exps, 1)
                act.wait_ge(turned, i + 1)
                if i >= 2:
                    act.wait_ge(summed, i - 1)
                act.activation(pT[:, i % 2, :, 0:kts * P], t_ps[:, i % 2, :, 0:kts * P], ACT.Copy).then_inc(kept, 1)


def dilated_sample(nc, S, g, q_rows, v_rows_sb):
    nk = 64 if g == 2 else P
    dil = DILS[g]
    cache = S.d[("cache_win128", "cache_win512", "cache_win2048")[g]][0]
    with ExitStack() as ctx:
        tag = f"g{g}"
        sb = lambda n, s: ctx.enter_context(nc.sbuf_tensor(f"{n}_{tag}", s, F32))
        lk = 1 if g == 0 else L_NEW
        HN = N_SEQ // 2
        kt = sb("kt", [nk, HN, lk, GW])
        vt = sb("vt", [nk, N_SEQ, lk, GW])
        qb = sb("qb", [nk, HN, L_NEW, GW])
        hot = sb("shot", [NB, L_NEW, nk + TS])
        tabr = sb("tabr", [NB, L_NEW, P])
        other = sb("other", [P, TS])
        fh = sb("fh", [P, 2, HPG])
        rh = sb("rh", [P, HPG])
        qx = sb("qx", [P, 2, P])
        cs = sb("cs", [nk, P])
        bias = sb("bias", [P, nk + TS])
        sc = sb("ssc", [P, nk + TS])
        pT = sb("spT", [P, 2, P])
        oT = sb("soT", [DH, P])
        new = sb("snew", [P, HPG, DH])
        row = sb("srow", [P, HEAD_ROW])
        u, neg_max, sum_p = row[:, 0:DH], row[:, AT_M:AT_M + 1], row[:, AT_L:AT_L + 1]
        cin, kin, qin, vin, step, pstep, astep, out_done, others_masked = add_sems(
            nc, *(f"{x}_{tag}" for x in ("consts_in", "keys_in", "queries_in", "values_in", "vector_step", "tensor_step", "exps_step", "rows_out", "others_masked")))
        block = ctx.enter_context(nc.Block())
        b_ps = S.ps[:, 0:nk + TS]
        s_ps = S.ps[:, 512:512 + nk + TS]
        t_ps = S.ps[:, 1024:1024 + 2 * P]
        o_ps = S.ps[0:DH, 1536:1536 + P]
        n_ps = S.ps[:, 2048:2048 + GW]
        u_ps = S.ps[:, 2560:2560 + DH]

        def rows_of(n, a):
            c = cache[n].rearrange("t a h d -> t a (h d)")[:, a, :]
            if g == 0:
                return c
            return c.rearrange("(j r) x -> j r x", r=dil)[:, 0:L_NEW, :]

        @block.sync
        def _(sp):
            sp.dma_start(hot[:, :, :], S.c[f"sample_hot{g}"]).then_inc(cin, 16)
            sp.dma_start(other[:, :], S.c["other_seq"]).then_inc(cin, 16)
            sp.dma_start(fh[:, :, :], S.c["feat_head"]).then_inc(cin, 16)
            sp.dma_start(rh[:, :], S.c["row_head"]).then_inc(cin, 16)
            for half in range(2):
                if half:
                    sp.wait_ge(step, 2)
                for n in range(HN):
                    sp.dma_start(kt[:, n, 0, :] if g == 0 else kt[:, n, :, :], rows_of(half * HN + n, 0)).then_inc(kin, 16)
                src = q_rows[half * HN * L_NEW:(half + 1) * HN * L_NEW, g * GW:(g + 1) * GW]
                sp.dma_start(qb[:, :, :, :].rearrange("k n l x -> k (n l) x"),
                             bass.AP(src.tensor, src.offset, [[0, nk]] + [list(x) for x in src.ap])).then_inc(qin, 16)

        @block.scalar
        def _(act):
            for n in range(N_SEQ):
                act.dma_start(vt[:, n, 0, :] if g == 0 else vt[:, n, :, :], rows_of(n, 1)).then_inc(vin, 16)
            act.wait_ge(step, 9)
            act.activation(sc[:, :], sc[:, :], ACT.Exp, bias=neg_max, accum_out=sum_p).then_inc(astep, 1)
            act.wait_ge(step, 14)
            act.wait_ge(astep, 1)
            act.dma_start(S.part_rows[g, SEQ:T].rearrange("t h x -> (t h) x"), row[:, :]).then_inc(out_done, 16)
            act.wait_ge(out_done, 16)

        @block.vector
        def _(dve):
            done = chain(dve, step)
            for half in range(2):
                dve.wait_ge(kin, 16 * HN * (half + 1))
                dve.wait_ge(qin, 16 * (half + 1))
                kk = kt[:, :, 0:1, :].broadcast_to([nk, HN, L_NEW, GW]) if g == 0 else kt[:, :, :, :]
                done(dve.tensor_tensor(qb[:, :, :, :], qb[:, :, :, :], kk, ALU.mult))
                if half == 0:
                    done(dve.tensor_reduce(cs[:, 0:64], qb[:, :, :, :].rearrange("k n l (h d) -> k (n l h) d", h=HPG), AX.X, ALU.add))
                    dve.wait_ge(cin, 64)
                    done(dve.memset(tabr[:, :, :], 0.0))
                else:
                    done(dve.tensor_reduce(cs[:, 64:128], qb[:, :, :, :].rearrange("k n l (h d) -> k (n l h) d", h=HPG), AX.X, ALU.add))
            for l in range(L_NEW):
                dve.tensor_copy(tabr[:, l, :].rearrange("b (n l h) -> b n l h", n=N_SEQ, l=L_NEW)[:, :, l, :],
                                S.tab[:, g * HPG:(g + 1) * HPG].unsqueeze(1).broadcast_to([NB, N_SEQ, HPG]))
            for f in range(2):
                ins = dve.tensor_tensor(qx[:, f, :].rearrange("p (t h) -> p t h", h=HPG),
                                        S.qk[:, 2 * g + f, SEQ:T].unsqueeze(2).broadcast_to([P, TS, HPG]),
                                        fh[:, f:f + 1, :].broadcast_to([P, TS, HPG]), ALU.mult)
            done(ins)
            dve.wait_ge(pstep, 2)
            done(dve.tensor_copy(bias[:, :], b_ps))
            done(dve.scalar_tensor_tensor(sc[:, :], s_ps, DH ** -0.5, bias[:, :], ALU.mult, ALU.add))
            dve.tensor_tensor(sc[:, nk:], sc[:, nk:], other[:, :], ALU.add).then_inc(others_masked, 1)
            dve.wait_ge(others_masked, 1)
            done(dve.tensor_reduce(neg_max, sc[:, :], AX.X, ALU.max, negate=True))
            dve.wait_ge(pstep, 3)
            dve.tensor_copy(pT[0:nk, 0, :], t_ps[0:nk, 0:P])
            done(dve.tensor_copy(pT[0:TS, 1, :], t_ps[0:TS, P:2 * P]))
            dve.wait_ge(pstep, 4)
            done(dve.tensor_copy(oT[:, :], o_ps))
            done(dve.tensor_tensor(new[:, :, :], n_ps.rearrange("p (h d) -> p h d", h=HPG),
                                   rh[:, :].unsqueeze(2).broadcast_to([P, HPG, DH]), ALU.mult))
            done(dve.tensor_reduce(u, new[:, :, :].rearrange("p h d -> p d h"), AX.X, ALU.add))
            dve.wait_ge(pstep, 5)
            done(dve.tensor_tensor(u, u, u_ps, ALU.add))

        @block.tensor
        def _(pe):
            pe.wait_ge(step, 6)
            for l in range(L_NEW):
                last = pe.matmul(b_ps, tabr[:, l, :], hot[:, l, :], start=l == 0, stop=l == L_NEW - 1)
            last.then_inc(pstep, 1)
            pe.transpose(s_ps[:, 0:nk], cs[:, :], S.ident[0:nk, 0:nk])
            for f in range(2):
                last = pe.matmul(s_ps[:, nk:], qx[:, f, :], S.qk[:, 6 + 2 * g + f, SEQ:T], start=f == 0, stop=f == 1)
            last.then_inc(pstep, 1)
            pe.wait_ge(astep, 1)
            pe.transpose(t_ps[0:nk, 0:P], sc[:, 0:nk], S.ident[:, :])
            pe.transpose(t_ps[0:TS, P:2 * P], sc[:, nk:], S.ident[:, :]).then_inc(pstep, 1)
            pe.wait_ge(step, 10)
            pe.wait_ge(vin, 16 * N_SEQ)
            pc = pT[0:nk, 0, :].rearrange("k (n l h) -> k n l h", n=N_SEQ, l=L_NEW)
            oc = o_ps.rearrange("d (n l h) -> d n l h", n=N_SEQ, l=L_NEW)
            for n in range(N_SEQ):
                for h in range(HPG):
                    if g == 0:
                        pe.matmul(oc[:, n, :, h], vt[:, n, 0, h * DH:(h + 1) * DH], pc[:, n, :, h], start=True, stop=True)
                    else:
                        for l in range(L_NEW):
                            pe.matmul(oc[:, n, l, h:h + 1], vt[:, n, l, h * DH:(h + 1) * DH], pc[:, n, l, h:h + 1], start=True, stop=True)
            pe.matmul(n_ps, pT[0:TS, 1, :], v_rows_sb[:, g, :], start=True, stop=True).then_inc(pstep, 1)
            pe.wait_ge(step, 11)
            pe.transpose(u_ps, oT[:, :], S.ident[0:DH, 0:DH]).then_inc(pstep, 1)


def combine_windows(nc, S, bT):
    with ExitStack() as ctx:
        sb = lambda n, s: ctx.enter_context(nc.sbuf_tensor(n, s, F32))
        rows = sb("cw_rows", [P, 3, 3, HPG, HEAD_ROW])
        nM = sb("cw_max", [P, HPG])
        e = sb("cw_e", [P, 2, 3, HPG])
        el = sb("cw_el", [P, 3, HPG])
        den = sb("cw_den", [P, HPG])
        b = sb("cw_b", [P, 2, GW])
        diffed, exped, mixed, turned, kept, step = add_sems(nc, *("cw_" + x for x in ("diffed", "exped", "mixed", "turned", "kept", "step")))
        loaded = add_sems(nc, "cw_loaded0", "cw_loaded1", "cw_loaded2")
        block = ctx.enter_context(nc.Block())
        N = [P] * QT + [TS]

        @block.sync
        def _(sp):
            for t, n in enumerate(N):
                if t >= 3:
                    sp.wait_ge(mixed, t - 2)
                sp.dma_start(rows[0:n, t % 3].rearrange("t g h x -> t g (h x)"),
                             S.part_rows[:, t * P:t * P + n].rearrange("g t h x -> t g (h x)")).then_inc(loaded[t % 3], 16)

        @block.vector
        def _(dve):
            done = chain(dve, step)
            for t, n in enumerate(N):
                r = rows[0:n, t % 3]
                dve.wait_ge(loaded[t % 3], 16 * (t // 3 + 1))
                m = r[:, :, :, AT_M]
                done(dve.tensor_reduce(nM[0:n, :], m.rearrange("p g h -> p h g"), AX.X, ALU.min))
                dve.tensor_tensor(e[0:n, t % 2], nM[0:n, :].unsqueeze(1).broadcast_to([n, 3, HPG]), m, ALU.subtract).then_inc(diffed, 1)
                dve.wait_ge(exped, t + 1)
                done(dve.tensor_tensor(el[0:n], e[0:n, t % 2], r[:, :, :, AT_L], ALU.mult))
                done(dve.tensor_reduce(den[0:n, :], el[0:n].rearrange("p g h -> p h g"), AX.X, ALU.add))
                done(dve.reciprocal(den[0:n, :], den[0:n, :]))
                done(dve.tensor_tensor(el[0:n], e[0:n, t % 2], den[0:n, :].unsqueeze(1).broadcast_to([n, 3, HPG]), ALU.mult))
                for g in range(3):
                    u = r[:, g, :, 0:DH]
                    ins = dve.tensor_tensor(u, u, el[0:n, g, :].unsqueeze(2).broadcast_to([n, HPG, DH]), ALU.mult)
                done(ins)
                if t >= 2:
                    dve.wait_ge(turned, t - 1)
                bt = b[0:n, t % 2, :].rearrange("p (h d) -> p h d", h=HPG)
                done(dve.tensor_tensor(bt, r[:, 0, :, 0:DH], r[:, 1, :, 0:DH], ALU.add))
                dve.tensor_tensor(bt, bt, r[:, 2, :, 0:DH], ALU.add).then_inc(mixed, 1)

        @block.tensor
        def _(pe):
            for t, n in enumerate(N):
                pe.wait_ge(mixed, t + 1)
                if t >= 2:
                    pe.wait_ge(kept, t - 1)
                for f in range(2):
                    last = pe.transpose(S.ps[:, (t % 2) * BANK + f * P:(t % 2) * BANK + f * P + n], b[0:n, t % 2, f * P:(f + 1) * P], S.ident[0:n, 0:n])
                last.then_inc(turned, 1)

        @block.scalar
        def _(act):
            for t, n in enumerate(N):
                act.wait_ge(diffed, t + 1)
                act.activation(e[0:n, t % 2], e[0:n, t % 2], ACT.Exp).then_inc(exped, 1)
                act.wait_ge(turned, t + 1)
                act.activation(bT[:, :, t * P:t * P + n],
                               S.ps[:, (t % 2) * BANK:(t % 2) * BANK + 2 * P].rearrange("p (f t) -> p f t", f=2)[:, :, 0:n], ACT.Copy).then_inc(kept, 1)


def conv_norm(nc, S, yT):
    with ExitStack() as ctx:
        sb = lambda n, s: ctx.enter_context(nc.sbuf_tensor(n, s, F32))
        sq = sb("ln_sq", [P, 2, T])
        mean = sb("ln_mean", [P, T])
        rstd = sb("ln_rstd", [P, T])
        gb = sb("ln_gb", [P, 2, CC])
        loaded, meaned, centred, squared, varied, astep, scaled, sig, done_s = add_sems(
            nc, *("ln_" + x for x in ("loaded", "meaned", "centred", "squared", "varied", "rstd_step", "scaled", "sigmoid", "mean_kept")))
        block = ctx.enter_context(nc.Block())

        @block.sync
        def _(sp):
            for i, name in enumerate(("conv_ln_g", "conv_ln_b")):
                sp.dma_start(gb[:, i, :], S.d[name][0].rearrange("(c p) -> p c", p=P)).then_inc(loaded, 16)

        @block.tensor
        def _(pe):
            for c in range(CC):
                for at, n in PIECES:
                    last = pe.matmul(S.ps[:, at:at + n], S.ones[:, :], yT[:, c, at:at + n], start=c == 0, stop=c == CC - 1)
            last.then_inc(meaned, 1)
            for c in range(CC):
                pe.wait_ge(squared, c + 1)
                for at, n in PIECES:
                    last = pe.matmul(S.ps[:, 1536 + at:1536 + at + n], S.ones[:, :], sq[:, c % 2, at:at + n], start=c == 0, stop=c == CC - 1)
                last.then_inc(varied, 1)

        @block.vector
        def _(dve):
            dve.wait_ge(meaned, 1)
            dve.tensor_scalar(mean[:, :], slot(S, 0), 1.0 / CONV_CH, None, ALU.mult).then_inc(done_s, 1)
            dve.wait_ge(done_s, 1)
            for c in range(CC):
                dve.tensor_tensor(yT[:, c, :], yT[:, c, :], mean[:, :], ALU.subtract).then_inc(centred, 1)
            dve.wait_ge(astep, 2)
            dve.wait_ge(loaded, 32)
            for c in range(CC):
                dve.wait_ge(centred, c + 1)
                dve.tensor_tensor(yT[:, c, :], yT[:, c, :], rstd[:, :], ALU.mult).then_inc(centred, 1)
                dve.wait_ge(centred, CC + c + 1)
                dve.tensor_scalar(yT[:, c, :], yT[:, c, :], gb[:, 0, c:c + 1], gb[:, 1, c:c + 1], ALU.mult, ALU.add).then_inc(scaled, 1)
            for c in range(CC):
                dve.wait_ge(sig, c + 1)
                dve.tensor_tensor(yT[:, c, :], yT[:, c, :], sq[:, c % 2, :], ALU.mult).then_inc(scaled, 1)

        @block.scalar
        def _(act):
            for c in range(CC):
                act.wait_ge(centred, c + 1)
                if c >= 2:
                    act.wait_ge(varied, c - 1)
                act.activation(sq[:, c % 2, :], yT[:, c, :], ACT.Square).then_inc(squared, 1)
            act.wait_ge(varied, CC)
            act.activation(rstd[:, :], slot(S, 1), ACT.Ln, scale=1.0 / CONV_CH, bias=S.eps[:, :]).then_inc(astep, 1)
            act.wait_ge(astep, 1)
            act.activation(rstd[:, :], rstd[:, :], ACT.Exp, scale=-0.5).then_inc(astep, 1)
            for c in range(CC):
                act.wait_ge(scaled, c + 1 if c < 2 else CC + c - 1)
                act.activation(sq[:, c % 2, :], yT[:, c, :], ACT.Sigmoid).then_inc(sig, 1)


def project_back(nc, S, tag, w, kt, rhs):
    with ExitStack() as ctx:
        W = Weights(nc, ctx, tag, kt)
        product, free = product_sems(nc, tag)
        block = ctx.enter_context(nc.Block())
        srcs = w_pairs(w, 0)

        @block.sync
        def _(sp):
            load_weight_pairs(sp, W, product, kt, KD // 2, *srcs)

        @block.tensor
        def _(pe):
            multiply_pairs(pe, S, W, product, free, kt, KD // 2, rhs)

        @block.vector
        def _(dve):
            for j in range(2):
                dve.sem_inc(free[j], 1)
            with dve.Fori(0, KD // 2) as i:
                for j in range(2):
                    dve.wait_ge(product[j], i + 2)
                    x = S.xT[:, bass.ds(i * 2 + j, 1), :].rearrange("p a t -> p (a t)")
                    dve.tensor_tensor(x, x, slot(S, j), ALU.add).then_inc(free[j], 1)


def ffn(nc, S, layer):
    with ExitStack() as outer:
        act_T = outer.enter_context(nc.sbuf_tensor(f"hidden{layer}", [P, KF, T], F32))
        with ExitStack() as ctx:
            hT = ctx.enter_context(nc.sbuf_tensor(f"hf{layer}", [P, KD, T], F32))
            rms_norm(nc, S, f"ffn{layer}", S.g_ffn[:, layer, :], hT)
            tag = f"up{layer}"
            W = Weights(nc, ctx, tag, KD)
            gate = ctx.enter_context(nc.sbuf_tensor(f"gate{layer}", [P, T], F32))
            product, free = product_sems(nc, tag)
            sig, gated = add_sems(nc, f"sigmoid{layer}", f"gated{layer}")
            block = ctx.enter_context(nc.Block())

            @block.sync
            def _(sp):
                load_weight_pairs(sp, W, product, KD, KF, w_cols(S.d["w_ffn_gate"][layer], 0), w_cols(S.d["w_ffn_up"][layer], 0))

            @block.tensor
            def _(pe):
                multiply_pairs(pe, S, W, product, free, KD, KF, lambda k: hT[:, k, :])

            @block.scalar
            def _(act):
                with act.Fori(0, KF) as i:
                    act.wait_ge(product[0], i + 2)
                    act.wait_ge(free[1], i + 1)
                    act.activation(gate[:, :], slot(S, 0), ACT.Sigmoid).then_inc(sig, 1)

            @block.vector
            def _(dve):
                for j in range(2):
                    dve.sem_inc(free[j], 1)
                with dve.Fori(0, KF) as i:
                    dve.wait_ge(sig, i + 1)
                    dve.tensor_tensor(gate[:, :], gate[:, :], slot(S, 0), ALU.mult).then_inc(free[0], 1)
                    dve.wait_ge(product[1], i + 2)
                    dve.wait_ge(free[0], i + 2)
                    dve.tensor_tensor(act_T[:, bass.ds(i, 1), :].rearrange("p a t -> p (a t)"), gate[:, :], slot(S, 1), ALU.mult).then_inc(free[1], 1)
        project_back(nc, S, f"down{layer}", S.d["w_ffn_down"][layer], KF, lambda k: act_T[:, k, :])


def store_y(nc, S):
    with ExitStack() as ctx:
        rows = ctx.enter_context(nc.sbuf_tensor("y_rows", [P, 3, D_MODEL], F32))
        turned, kept = add_sems(nc, "y_turned", "y_kept")
        stored = add_sems(nc, "y_stored0", "y_stored1", "y_stored2")
        block = ctx.enter_context(nc.Block())
        N = [P] * QT + [TS]

        @block.tensor
        def _(pe):
            for t, n in enumerate(N):
                if t >= 2:
                    pe.wait_ge(kept, t - 1)
                for k in range(KD):
                    last = pe.transpose(S.ps[0:n, (t % 2) * D_MODEL + k * P:(t % 2) * D_MODEL + (k + 1) * P], S.xT[:, k, t * P:t * P + n], S.ident[:, :])
                last.then_inc(turned, 1)

        @block.vector
        def _(dve):
            for t, n in enumerate(N):
                dve.wait_ge(turned, t + 1)
                if t >= 3:
                    dve.wait_ge(stored[t % 3], 16 * (t // 3))
                dve.tensor_copy(rows[0:n, t % 3, :], S.ps[0:n, (t % 2) * D_MODEL:(t % 2 + 1) * D_MODEL]).then_inc(kept, 1)

        @block.sync
        def _(sp):
            for t, n in enumerate(N):
                sp.wait_ge(kept, t + 1)
                dst = S.o["y_prompt"][0, t * P:(t + 1) * P, :] if t < QT else S.o["y_sample"].rearrange("n l d -> (n l) d")
                sp.dma_start(dst, rows[0:n, t % 3, :]).then_inc(stored[t % 3], 16)
            for s in range(3):
                sp.wait_ge(stored[s], 48)


WORK_AT = [None, None] + [sum((t + 1) * P for t in range(2, u)) for u in range(2, QT)]
WORK = sum((t + 1) * P for t in range(2, QT))
S_KEYS = PAST + L_NEW
NEW_AT = PAST
S_COLS = PAST + TS


def index_products(nc, S, hT, iqT, ikT, iw, lrT):
    with ExitStack() as ctx:
        sb = lambda n, s: ctx.enter_context(nc.sbuf_tensor(n, s, F32))
        wq, wk, wt, wl = sb("wiq", [P, KD, GW]), sb("wik", [P, KD, P]), sb("wit", [P, KD, DH + IDX_H]), sb("wlr", [P, KD, GLA_RANK])
        loaded, product, kept, stored = add_sems(nc, "index_w_loaded", "index_product", "index_kept", "kidx_stored")
        w = S.d["w_in_cd"][0].rearrange("(k p) m -> p k m", p=P)
        block = ctx.enter_context(nc.Block())

        @block.sync
        def _(sp):
            sp.dma_start(wq[:, :, :], w[:, :, IQ:IQ + GW]).then_inc(loaded, 16)
            for half in range(2):
                sp.dma_start(wk[:, :, half * DH:(half + 1) * DH], w[:, :, IK:IK + DH]).then_inc(loaded, 16)
            sp.dma_start(wt[:, :, :], w[:, :, IK:IK + DH + IDX_H]).then_inc(loaded, 16)
            sp.dma_start(wl[:, :, :], w[:, :, CLR:CLR + GLA_RANK]).then_inc(loaded, 16)
            sp.wait_ge(kept, 4 + QT + 1)
            sp.dma_start(S.o["dsa_kidx_p"][0, 0].rearrange("t p d -> p t d"), iw[:, 0:QT, 0:DH]).then_inc(stored, 16)
            sp.dma_start(S.o["dsa_kidx_s"][0].rearrange("n l d -> (n l) d"), iw[0:TS, QT, 0:DH]).then_inc(stored, 16)
            sp.wait_ge(stored, 32)

        @block.tensor
        def _(pe):
            pe.wait_ge(loaded, 80)
            for n, (wgt, m) in enumerate(((wq[:, :, 0:P], P), (wq[:, :, P:2 * P], P), (wk, P), (wl, GLA_RANK))):
                if n >= 2:
                    pe.wait_ge(kept, n - 1)
                for k in range(KD):
                    for at, size in PIECES:
                        last = pe.matmul(S.ps[0:m, (n % 2) * 1536 + at:(n % 2) * 1536 + at + size], wgt[:, k, :], hT[:, k, at:at + size],
                                         start=k == 0, stop=k == KD - 1)
                last.then_inc(product, 1)
            for t in range(QT + 1):
                n = P if t < QT else TS
                if t >= 2:
                    pe.wait_ge(kept, 4 + t - 1)
                for k in range(KD):
                    last = pe.matmul(S.ps[0:n, 3072 + (t % 2) * BANK:3072 + (t % 2) * BANK + DH + IDX_H], hT[:, k, t * P:t * P + n], wt[:, k, :],
                                     start=k == 0, stop=k == KD - 1)
                last.then_inc(product, 1)

        @block.scalar
        def _(act):
            for n, (dst, m) in enumerate(((iqT[:, 0, :], P), (iqT[:, 1, :], P), (ikT[:, :], P), (lrT[:, :], GLA_RANK))):
                act.wait_ge(product, n + 1)
                act.activation(dst, S.ps[0:m, (n % 2) * 1536:(n % 2) * 1536 + T], ACT.Copy).then_inc(kept, 1)
            for t in range(QT + 1):
                n = P if t < QT else TS
                act.wait_ge(product, 4 + t + 1)
                act.activation(iw[0:n, t, :], S.ps[0:n, 3072 + (t % 2) * BANK:3072 + (t % 2) * BANK + DH + IDX_H], ACT.Copy).then_inc(kept, 1)


def index_scores_prompt(nc, S, iqT, ikT, iw, work):
    with ExitStack() as ctx:
        sb = lambda n, s: ctx.enter_context(nc.sbuf_tensor(n, s, F32))
        relu = sb("relu", [P, 2, SEQ])
        wgt = sb("head_w", [P, QT, IDX_H])
        tri = sb("tri", [P, P])
        loaded, dots, rectified, step = add_sems(nc, "tri_loaded", "dots_done", "rectified", "index_step")
        units = [(t, h) for t in range(2, QT) for h in range(IDX_H)]
        block = ctx.enter_context(nc.Block())

        @block.sync
        def _(sp):
            sp.dma_start(tri[:, :], S.c["tri"]).then_inc(loaded, 16)

        @block.tensor
        def _(pe):
            for u, (t, h) in enumerate(units):
                if u >= 4:
                    pe.wait_ge(rectified, u - 3)
                base = DH * (h % 2)
                for at in range(0, (t + 1) * P, BANK):
                    n = min(BANK, (t + 1) * P - at)
                    last = pe.matmul(S.ps[:, (u % 4) * 1024 + at:(u % 4) * 1024 + at + n], iqT[base:base + DH, h // 2, t * P:(t + 1) * P],
                                     ikT[base:base + DH, at:at + n], start=True, stop=True)
                last.then_inc(dots, 1)

        @block.scalar
        def _(act):
            for u, (t, h) in enumerate(units):
                act.wait_ge(dots, u + 1)
                if u >= 2:
                    act.wait_ge(step, u)
                act.activation(relu[:, u % 2, 0:(t + 1) * P], S.ps[:, (u % 4) * 1024:(u % 4) * 1024 + (t + 1) * P], ACT.Relu).then_inc(rectified, 1)

        @block.vector
        def _(dve):
            done = chain(dve, step)
            done(dve.tensor_scalar(wgt[:, :, :], iw[:, 0:QT, DH:DH + IDX_H], DH ** -0.5 * IDX_H ** -0.5, None, ALU.mult))
            for u, (t, h) in enumerate(units):
                n = (t + 1) * P
                dst = work[:, WORK_AT[t]:WORK_AT[t] + n]
                dve.wait_ge(rectified, u + 1)
                if h == 0:
                    done(dve.tensor_scalar(dst, relu[:, u % 2, 0:n], wgt[:, t, h:h + 1], None, ALU.mult))
                else:
                    done(dve.scalar_tensor_tensor(dst, relu[:, u % 2, 0:n], wgt[:, t, h:h + 1], dst, ALU.mult, ALU.add))
            dve.wait_ge(loaded, 16)
            for t in range(2, QT):
                own = work[:, WORK_AT[t] + t * P:WORK_AT[t] + (t + 1) * P]
                dve.tensor_tensor(own, own, tri[:, :], ALU.add)


def index_scores_sample(nc, S, iqT, ikT, iw, work_s):
    with ExitStack() as ctx:
        sb = lambda n, s: ctx.enter_context(nc.sbuf_tensor(n, s, F32))
        pages = ctx.enter_context(nc.sbuf_tensor("pages_i", [1, N_SEQ * N_PAGES], I32))
        keys = sb("kidx", [P, 4, N_PAGES, DH])
        kT = sb("kidx_T", [P, 2, 4, P])
        iqs = sb("iq_s", [P, N_SEQ, 32])
        rows = sb("index_rows", [TS, 2, P])
        wx = sb("wx", [TS, 2, P])
        wsel = sb("wsel", [P, 2, TS])
        relu = sb("relu_s", [P, S_KEYS])
        nmask = sb("new_mask", [TS, L_NEW])
        consts, table_in, spread, turned, copied, dotted, relued, wstep, summed, final = add_sems(
            nc, *("is_" + x for x in ("consts", "table_in", "queries_spread", "keys_turned", "keys_copied", "dots", "rectified",
                                      "weights_step", "summed", "kept")))
        loaded = add_sems(nc, *(f"is_loaded{i}" for i in range(4)))
        pool_keys = S.d["cache_dsa_kidx"][0]
        dots_ps = S.ps[:, 0:1536]
        sum_ps = S.ps[0:TS, 1536:3072]
        turn_ps = S.ps[:, 3072:4096].rearrange("p (b x) -> p b x", b=2)
        block = ctx.enter_context(nc.Block())

        @block.sync
        def _(sp):
            sp.dma_start(pages[:, :], S.d["page_table"].rearrange("n (a g) -> a (n g)", a=1)).then_inc(table_in, 16)
            sp.dma_start(rows[:, :, :], S.c["index_rows"]).then_inc(consts, 16)
            sp.dma_start(nmask[:, :], S.c["new_mask"]).then_inc(consts, 16)
            sp.wait_ge(table_in, 16)
            for n in range(N_SEQ):
                if n >= 4:
                    sp.wait_ge(turned, n - 3)
                for g in range(N_PAGES):
                    page = sp.value_load(pages[0:1, n * N_PAGES + g:n * N_PAGES + g + 1], min_val=0, max_val=pool_keys.shape[0] - 1)
                    sp.dma_start(keys[:, n % 4, g, :], pool_keys[bass.ds(page, 1)].rearrange("a s d -> s (a d)")).then_inc(loaded[n % 4], 16)

        @block.vector
        def _(dve):
            dve.memset(iqs[:, :, :], 0.0).then_inc(spread, 1)
            dve.wait_ge(spread, 1)
            for h in range(IDX_H):
                src = iqT[DH * (h % 2):DH * (h % 2) + DH, h // 2, SEQ:T].rearrange("p (n l) -> p n l", l=L_NEW)
                for half in range(2):
                    ins = dve.tensor_copy(iqs[half * DH:(half + 1) * DH, :, h * L_NEW:(h + 1) * L_NEW], src)
            ins.then_inc(spread, 1)
            dve.wait_ge(consts, 32)
            for g in range(2):
                for h in range(IDX_H):
                    v = lambda x: x[:, g, :].rearrange("t (n a h l) -> t n a h l", n=4, a=2, h=4)
                    ins = dve.tensor_scalar(v(wx)[:, :, :, h, :], v(rows)[:, :, :, h, :], iw[0:TS, QT, DH + h:DH + h + 1], DH ** -0.5 * IDX_H ** -0.5,
                                            ALU.mult, ALU.mult)
            ins.then_inc(wstep, 1)
            dve.wait_ge(wstep, 2)
            dve.tensor_copy(wsel[:, :, :], turn_ps[:, 0, 0:2 * TS].rearrange("p (g t) -> p g t", g=2)).then_inc(wstep, 1)
            for n in range(N_SEQ):
                dve.wait_ge(turned, n + 1)
                if n >= 2:
                    dve.wait_ge(dotted, n - 1)
                dve.tensor_copy(kT[:, n % 2, :, :], turn_ps[:, n % 2, :].rearrange("p (c s) -> p c s", c=4)).then_inc(copied, 1)
            dve.wait_ge(summed, 1)
            dve.tensor_copy(work_s[:, 0:PAST], sum_ps[:, 0:PAST])
            dve.tensor_tensor(work_s[:, PAST:S_KEYS], sum_ps[:, PAST:S_KEYS], nmask[:, :], ALU.add)

        @block.tensor
        def _(pe):
            pe.wait_ge(wstep, 1)
            for g in range(2):
                last = pe.transpose(turn_ps[:, 0, g * TS:(g + 1) * TS], wx[:, g, :], S.ident[0:TS, 0:TS])
            last.then_inc(wstep, 1)
            pe.wait_ge(wstep, 3)
            pe.wait_ge(spread, 2)

            def turn(n):
                pe.wait_ge(loaded[n % 4], 16 * N_PAGES * (n // 4 + 1))
                if n >= 2:
                    pe.wait_ge(copied, n - 1)
                for c in range(4):
                    last = pe.transpose(turn_ps[:, n % 2, c * P:(c + 1) * P], keys[:, n % 4, 2 * c:2 * c + 2, :].rearrange("s g d -> s (g d)"), S.ident[:, :])
                last.then_inc(turned, 1)

            turn(0)
            for n in range(N_SEQ):
                if n + 1 < N_SEQ:
                    turn(n + 1)
                pe.wait_ge(copied, n + 1)
                if n == 4:
                    pe.wait_ge(relued, 1)
                q = 32 * (n % 4)
                for half in range(2):
                    for c in range(4):
                        at = half * BANK + c * P
                        pe.matmul(dots_ps[q:q + 32, at:at + P], iqs[half * DH:(half + 1) * DH, n, :], kT[half * DH:(half + 1) * DH, n % 2, c, :],
                                  start=True, stop=True)
                pe.matmul(dots_ps[q:q + 32, PAST:S_KEYS], iqs[0:DH, n, :], ikT[0:DH, SEQ + n * L_NEW:SEQ + (n + 1) * L_NEW],
                          start=True, stop=True).then_inc(dotted, 1)
                if n % 4 == 3:
                    g = n // 4
                    pe.wait_ge(relued, g + 1)
                    for at, size in ((0, BANK), (BANK, BANK), (PAST, L_NEW)):
                        last = pe.matmul(sum_ps[:, at:at + size], wsel[:, g, :], relu[:, at:at + size], start=g == 0, stop=g == 1)
                    last.then_inc(summed if g else final, 1)

        @block.scalar
        def _(act):
            for g in range(2):
                act.wait_ge(dotted, 4 * g + 4)
                if g:
                    act.wait_ge(final, 1)
                act.activation(relu[:, 0:PAST].rearrange("p (c b s) -> p b c s", b=2, s=P),
                               dots_ps[:, 0:PAST].rearrange("p (b c s) -> p b c s", b=2, s=P), ACT.Relu)
                act.activation(relu[:, PAST:S_KEYS], dots_ps[:, PAST:S_KEYS], ACT.Relu).then_inc(relued, 1)


def big_products(nc, S, hT, gT, big, gvS, work, work_s):
    with ExitStack() as ctx:
        W = Weights(nc, ctx, "cd", KD)
        wv = ctx.enter_context(nc.sbuf_tensor("wcv", [P, KD, GW], F32))
        best = ctx.enter_context(nc.sbuf_tensor("best", [P, 7, 8], F32))
        tick = ctx.enter_context(nc.sbuf_tensor("tick", [1, 2], F32))
        product, free = product_sems(nc, "cd")
        wv_loaded, v_product, v_kept, round_step = add_sems(nc, "cv_w_loaded", "cv_product", "cv_kept", "topk_step")
        w = S.d["w_in_cd"][0]
        vps = S.ps[:, 3072:4096].rearrange("p (b c) -> p b c", b=2)
        lines = [work[:, WORK_AT[t]:WORK_AT[t] + (t + 1) * P] for t in range(QT - 1, 1, -1)] + [work_s[:, :]]
        rows = [P] * 6 + [TS]
        NL = len(lines)
        block = ctx.enter_context(nc.Block())

        @block.sync
        def _(sp):
            load_weight_pairs(sp, W, product, KD, 2, *w_pairs(w, CQ))
            load_weight_pairs(sp, W, product, KD, 6, *w_pairs(w, CG), before=2)
            for half in range(2):
                if half:
                    sp.wait_ge(v_product, 9)
                sp.dma_start(wv[:, :, :], w[:, CV + half * GW:CV + (half + 1) * GW].rearrange("(k p) m -> p k m", p=P)).then_inc(wv_loaded, 16)

        @block.tensor
        def _(pe):
            rhs = lambda k: hT[:, k, :]
            multiply_pairs(pe, S, W, product, free, KD, 2, rhs)
            multiply_pairs(pe, S, W, product, free, KD, 6, rhs, before=2)
            value_products(pe, vps, hT, wv, wv_loaded, v_product, v_kept)

        @block.scalar
        def _(act):
            for j in range(2):
                act.sem_inc(free[j], 1)
            for dst, iters, before in ((gT, 2, 0), (big, 6, 2)):
                with act.Fori(0, iters) as i:
                    for j in range(2):
                        act.wait_ge(product[j], i + (2 + before))
                        act.activation(dst[:, bass.ds(i * 2 + j, 1), :].rearrange("p a t -> p (a t)"), slot(S, j), ACT.Copy).then_inc(free[j], 1)
            keep_values(act, vps, gvS, v_product, v_kept)

        @block.vector
        def _(dve):
            dve.memset(tick[:, :], 0.0).then_inc(round_step, NL)
            with dve.Fori(0, TOPK // 8) as i:
                dve.wait_ge(round_step, i * (2 * NL) + NL)
                dve.tensor_copy(tick[:, 0:1], tick[:, 1:2])
                for j, line in enumerate(lines):
                    dve.max(best[0:rows[j], j, :], line).then_inc(round_step, 1)
                dve.wait_ge(round_step, i * (2 * NL) + 2 * NL)
                dve.tensor_copy(tick[:, 0:1], tick[:, 1:2])
                for j, line in enumerate(lines):
                    dve.match_replace(line, best[0:rows[j], j, :], line, TAKEN).then_inc(round_step, 1)
            for j, line in enumerate(lines):
                dve.wait_ge(round_step, NL + (TOPK // 8 - 1) * 2 * NL + NL + j + 1)
                dve.tensor_scalar(line, line, TAKEN, MASKED, ALU.not_equal, ALU.mult)


def value_products(pe, vps, hT, wv, loaded, product, kept):
    for n in range(2 * (QT + 1)):
        half, t = divmod(n, QT + 1)
        if t == 0:
            pe.wait_ge(loaded, 16 * (half + 1))
        if n >= 2:
            pe.wait_ge(kept, n - 1)
        m = P if t < QT else TS
        for k in range(KD):
            last = pe.matmul(vps[0:m, n % 2, 0:GW], hT[:, k, t * P:t * P + m], wv[:, k, :], start=k == 0, stop=k == KD - 1)
        last.then_inc(product, 1)


def keep_values(act, vps, dst, product, kept):
    for n in range(2 * (QT + 1)):
        half, t = divmod(n, QT + 1)
        act.wait_ge(product, n + 1)
        m = P if t < QT else TS
        act.activation(dst[0:m, t, half * GW:(half + 1) * GW], vps[0:m, n % 2, 0:GW], ACT.Copy).then_inc(kept, 1)


def dsa_value_products(nc, S, hT, dvS):
    with ExitStack() as ctx:
        wv = ctx.enter_context(nc.sbuf_tensor("wdv", [P, KD, GW], F32))
        loaded, product, kept = add_sems(nc, "dv_w_loaded", "dv_product", "dv_kept")
        w = S.d["w_in_cd"][0]
        vps = S.ps[:, 3072:4096].rearrange("p (b c) -> p b c", b=2)
        block = ctx.enter_context(nc.Block())

        @block.sync
        def _(sp):
            for half in range(2):
                if half:
                    sp.wait_ge(product, 9)
                sp.dma_start(wv[:, :, :], w[:, DV_ + half * GW:DV_ + (half + 1) * GW].rearrange("(k p) m -> p k m", p=P)).then_inc(loaded, 16)

        @block.tensor
        def _(pe):
            value_products(pe, vps, hT, wv, loaded, product, kept)

        @block.scalar
        def _(act):
            keep_values(act, vps, dvS, product, kept)


def gla_decays(nc, S, lrT, bT):
    with ExitStack() as ctx:
        sb = lambda n, s: ctx.enter_context(nc.sbuf_tensor(n, s, F32))
        wa, ba, inside, e = sb("wa2", [GLA_RANK, 2, P]), sb("ba", [P, 2]), sb("inside", [P, T]), sb("gla_e", [P, T])
        loaded, product, z_ready, a_step, v_step = add_sems(nc, "gate_loaded", "gate_product", "gate_z", "gate_log_step", "gate_step")
        block = ctx.enter_context(nc.Block())

        @block.sync
        def _(sp):
            sp.dma_start(wa[:, :, :], S.d["gla_wa2"][0].rearrange("r (f p) -> r f p", p=P)).then_inc(loaded, 16)
            sp.dma_start(ba[:, :], S.d["gla_ba"][0].rearrange("(f p) -> p f", p=P)).then_inc(loaded, 16)
            sp.dma_start(inside[:, :], S.c["chunk_inside"].broadcast_to([P, T])).then_inc(loaded, 16)

        @block.tensor
        def _(pe):
            pe.wait_ge(loaded, 48)
            for f in range(2):
                for at, n in PIECES:
                    last = pe.matmul(S.ps[:, f * 1536 + at:f * 1536 + at + n], wa[:, f, :], lrT[:, at:at + n], start=True, stop=True)
                last.then_inc(product, 1)

        @block.scalar
        def _(act):
            for f in range(2):
                act.wait_ge(z_ready, f + 1)
                if f:
                    act.wait_ge(v_step, 1)
                for func, scale, bias in ((ACT.Abs, 1.0, 0.0), (ACT.Exp, -1.0, 0.0), (ACT.Ln, 1.0, S.ones[:, 0:1])):
                    act.activation(e[:, :], bT[:, f, :] if func is ACT.Abs else e[:, :], func, scale=scale, bias=bias).then_inc(a_step, 1)
                    act.wait_ge(a_step, 3 * f + {ACT.Abs: 1, ACT.Exp: 2}.get(func, 3))

        @block.vector
        def _(dve):
            for f in range(2):
                dve.wait_ge(product, f + 1)
                dve.tensor_scalar(bT[:, f, :], slot(S, f), ba[:, f:f + 1], None, ALU.add).then_inc(z_ready, 1)
            for f in range(2):
                dve.wait_ge(a_step, 3 * f + 3)
                dve.scalar_tensor_tensor(bT[:, f, :], bT[:, f, :], 0.0, e[:, :], ALU.min, ALU.subtract).then_inc(v_step, 1)
                dve.wait_ge(v_step, 3 * f + 1)
                dve.tensor_scalar(bT[:, f, :], bT[:, f, :], 1.0 / GLA_TAU, None, ALU.mult).then_inc(v_step, 1)
                dve.wait_ge(v_step, 3 * f + 2)
                dve.tensor_tensor_scan(bT[:, f, :], inside[:, :], bT[:, f, :], 0.0, ALU.mult, ALU.add).then_inc(v_step, 1)


SUB = 32


def gla_prompt(nc, S, gT, bT, gvS):
    with ExitStack() as ctx:
        sb = lambda n, s: ctx.enter_context(nc.sbuf_tensor(n, s, F32))
        NS = P // SUB
        nb = sb("neg_mid", [P, 2, QT * NS])
        eq, ek = sb("eq", [P, 2, P]), sb("ek", [P, 2, NS, P])
        ei, ed = sb("ei", [P, 2, P]), sb("ed", [P, 2, P])
        el = sb("el", [P, 2, QT])
        A = sb("A_T", [P, GLA_H, P])
        kd = sb("kd", [P, 2, P])
        st = sb("gla_state", [P, 2, GLA_DV])
        causal = sb("causal_T", [P, P])
        loaded, ready, exps, mixed, scored, masked, turned, copied, outs, states, stepped, stored = add_sems(
            nc, *("gp_" + x for x in ("loaded", "start", "exps", "mixed", "scored", "masked", "turned", "kd_copied", "outs",
                                      "state_sums", "stepped", "stored")))
        a_ps = S.ps[:, 0:1024].rearrange("p (b f i) -> p b f i", b=2, f=4)
        o_ps = S.ps[:, 1024:2048].rearrange("p (b f i) -> p b f i", b=2, f=4)
        k_ps = S.ps[:, 2048:2048 + 2 * P].rearrange("p (f x) -> p f x", f=2)
        s_ps = S.ps[:, 2560:2560 + 2 * P].rearrange("p (f x) -> p f x", f=2)
        block = ctx.enter_context(nc.Block())

        @block.sync
        def _(sp):
            sp.dma_start(causal[:, :], S.c["causal_T"]).then_inc(loaded, 16)
            sp.wait_ge(stepped, QT + 1)
            for f in range(2):
                sp.dma_start(S.o["gla_p"][0, 0, 2 * f:2 * f + 2].rearrange("h k v -> (h k) v"), st[:, f, :]).then_inc(stored, 16)
            sp.wait_ge(stored, 32)

        @block.scalar
        def _(act):
            act.wait_ge(ready, 1)
            act.activation(el[:, :, :], bT[:, :, P - 1:SEQ:P], ACT.Exp)
            for c in range(QT):
                if c:
                    act.wait_ge(outs, c)
                for f in range(2):
                    b = lambda at, n: bT[:, f, c * P + at:c * P + at + n]
                    for s in range(NS):
                        at = s * SUB
                        act.activation(eq[:, f, at:at + SUB], b(at, SUB), ACT.Exp, bias=nb[:, f, c * NS + s:c * NS + s + 1])
                        act.activation(ek[:, f, s, 0:at + SUB], b(0, at + SUB), ACT.Exp, scale=-1.0, bias=b(at + SUB // 2, 1))
                    act.activation(ei[:, f, :], b(0, P), ACT.Exp)
                    last = act.activation(ed[:, f, :], b(0, P), ACT.Exp, scale=-1.0, bias=b(P - 1, 1))
                last.then_inc(exps, 1)
                act.wait_ge(turned, c + 1)
                if c:
                    act.wait_ge(states, c)
                act.activation(kd[:, :, :], k_ps, ACT.Copy).then_inc(copied, 1)

        @block.vector
        def _(dve):
            dve.tensor_scalar(nb[:, :, :], bT[:, :, SUB // 2:SEQ:SUB], -1.0, None, ALU.mult)
            dve.memset(st[:, :, :], 0.0).then_inc(stepped, 1)
            dve.memset(ek[:, :, :, :], 0.0).then_inc(ready, 1)
            dve.wait_ge(loaded, 16)
            for c in range(QT):
                cols = slice(c * P, (c + 1) * P)
                dve.wait_ge(exps, c + 1)
                q, k = gT[:, 0:2, cols], gT[:, 2:4, cols]
                dve.scalar_tensor_tensor(eq[:, :, :], eq[:, :, :], GLA_DK ** -0.5, q, ALU.mult, ALU.mult)
                for f in range(2):
                    dve.tensor_tensor(ek[:, f], ek[:, f], gT[:, 2 + f, cols].unsqueeze(1).broadcast_to([P, NS, P]), ALU.mult)
                dve.scalar_tensor_tensor(ei[:, :, :], ei[:, :, :], GLA_DK ** -0.5, q, ALU.mult, ALU.mult)
                dve.tensor_tensor(ed[:, :, :], ed[:, :, :], k, ALU.mult).then_inc(mixed, 1)
                dve.wait_ge(scored, c + 1)
                for b in range(2):
                    last = dve.tensor_tensor(A[:, :, :].rearrange("p (f b) i -> p b f i", b=2)[:, b], a_ps[:, b, 0:2, :],
                                             causal[:, :].unsqueeze(1).broadcast_to([P, 2, P]), ALU.mult)
                last.then_inc(masked, 1)
                dve.wait_ge(outs, c + 1)
                for b in range(2):
                    last = dve.tensor_copy(gT[:, b:4:2, cols], o_ps[:, b, 0:2, :])
                dve.wait_ge(states, c + 1)
                for f in range(2):
                    last = dve.scalar_tensor_tensor(st[:, f, :], st[:, f, :], el[:, f, c:c + 1], s_ps[:, f, :], ALU.mult, ALU.add)
                last.then_inc(stepped, 1)

        @block.tensor
        def _(pe):
            for c in range(QT):
                pe.wait_ge(mixed, c + 1)
                if c:
                    pe.wait_ge(masked, c)
                for h in range(GLA_H):
                    f, b = h // 2, h % 2
                    half = slice(b * DH, b * DH + DH)
                    for s in range(NS):
                        last = pe.matmul(a_ps[:, b, f, s * SUB:(s + 1) * SUB], ek[half, f, s, :], eq[half, f, s * SUB:(s + 1) * SUB], start=True, stop=True)
                last.then_inc(scored, 1)
                if c:
                    pe.wait_ge(copied, c)
                for f in range(2):
                    last = pe.transpose(k_ps[:, f, :], ed[:, f, :], S.ident[:, :])
                last.then_inc(turned, 1)
                pe.wait_ge(masked, c + 1)
                pe.wait_ge(stepped, c + 1)
                for h in range(GLA_H):
                    f, b = h // 2, h % 2
                    half = slice(b * DH, b * DH + DH)
                    pe.matmul(o_ps[:, b, f, :], st[half, f, :], ei[half, f, :], start=True, stop=False)
                    last = pe.matmul(o_ps[:, b, f, :], gvS[:, c, h * P:(h + 1) * P], A[:, h, :], start=False, stop=True)
                last.then_inc(outs, 1)
                pe.wait_ge(copied, c + 1)
                for h in range(GLA_H):
                    f, b = h // 2, h % 2
                    last = pe.matmul(s_ps[b * DH:(b + 1) * DH, f, :], kd[:, f, b * DH:(b + 1) * DH], gvS[:, c, h * P:(h + 1) * P], start=True, stop=True)
                last.then_inc(states, 1)


def gla_sample(nc, S, gT, bT, gvS):
    with ExitStack() as ctx:
        sb = lambda n, s: ctx.enter_context(nc.sbuf_tensor(n, s, F32))
        s0 = sb("s0", [P, 2, N_SEQ, GLA_DV])
        new = s0
        e, q, k, kd, diff = sb("gs_e", [P, 4, 2, TS]), sb("gs_q", [P, 2, TS]), sb("gs_k", [P, 2, TS]), sb("gs_kd", [P, 2, TS]), sb("gs_diff", [P, 2, TS])
        el = sb("gs_el", [P, 2, N_SEQ])
        A = sb("gs_A", [TS, GLA_H, TS])
        kdT = sb("gs_kdT", [TS, 2, P])
        km = sb("gs_km", [TS, N_SEQ, P])
        mask, seq = sb("gs_mask", [TS, TS]), sb("gs_seq", [TS, N_SEQ])
        loaded, diffed, exped, mixed, scored, step, outs, kept, states, finished, stored = add_sems(
            nc, *("gs_" + x for x in ("loaded", "diffed", "exped", "mixed", "scored", "step", "outs", "kept", "states", "finished", "stored")))
        a_ps = S.ps[0:TS, 0:1024].rearrange("p (b f i) -> p b f i", b=2, f=16)
        k_ps = S.ps[0:TS, 1024:1024 + 2 * P].rearrange("p (f x) -> p f x", f=2)
        inter_ps = S.ps[:, 1536:2560].rearrange("p (b f i) -> p b f i", b=2, f=16)
        intra_ps = S.ps[:, 2560:2560 + GLA_H * TS].rearrange("p (h i) -> p h i", h=GLA_H)
        s_ps = S.ps[:, 3072:4096].rearrange("p (n v) -> p n v", n=N_SEQ)
        block = ctx.enter_context(nc.Block())
        last_b = bT[:, :, SEQ + L_NEW - 1:T:L_NEW]

        @block.sync
        def _(sp):
            for n in range(N_SEQ):
                sp.dma_start(s0[:, :, n, :], S.d["state_gla"][0, n].rearrange("(f b) k v -> (b k) f v", b=2)).then_inc(loaded, 16)
            sp.dma_start(mask[:, :], S.c["sample_causal_T"]).then_inc(loaded, 16)
            sp.dma_start(seq[:, :], S.c["seq_of"]).then_inc(loaded, 16)
            sp.wait_ge(finished, 2)
            for n in range(N_SEQ):
                sp.dma_start(S.o["gla_s"][0, n].rearrange("(f b) k v -> (b k) f v", b=2), new[:, :, n, :]).then_inc(stored, 16)
            sp.wait_ge(stored, 16 * N_SEQ)

        @block.scalar
        def _(act):
            b = bT[:, :, SEQ:T]
            act.activation(e[:, 0], b, ACT.Exp)
            act.activation(e[:, 1], b, ACT.Exp, scale=-1.0)
            act.activation(el[:, :, :], last_b, ACT.Exp)
            act.wait_ge(diffed, 1)
            act.activation(e[:, 2], diff[:, :, :], ACT.Exp).then_inc(exped, 1)
            act.wait_ge(outs, 1)
            for b in range(2):
                last = act.activation(gT[:, b:4:2, SEQ:T], inter_ps[:, b, 0:2, :], ACT.Copy)
            last.then_inc(kept, 1)

        @block.vector
        def _(dve):
            done = chain(dve, step)
            dve.tensor_tensor(diff[:, :, :].rearrange("p f (n l) -> p f n l", l=L_NEW), last_b.unsqueeze(3).broadcast_to([P, 2, N_SEQ, L_NEW]),
                              bT[:, :, SEQ:T].rearrange("p f (n l) -> p f n l", l=L_NEW), ALU.subtract).then_inc(diffed, 1)
            dve.wait_ge(exped, 1)
            dve.scalar_tensor_tensor(q[:, :, :], e[:, 0], GLA_DK ** -0.5, gT[:, 0:2, SEQ:T], ALU.mult, ALU.mult)
            dve.tensor_tensor(k[:, :, :], e[:, 1], gT[:, 2:4, SEQ:T], ALU.mult)
            dve.tensor_tensor(kd[:, :, :], e[:, 2], gT[:, 2:4, SEQ:T], ALU.mult).then_inc(mixed, 1)
            dve.wait_ge(loaded, 16 * (N_SEQ + 2))
            dve.wait_ge(scored, 1)
            for b in range(2):
                dve.tensor_tensor(A[:, :, :].rearrange("p (f b) i -> p b f i", b=2)[:, b], a_ps[:, b, 0:2, :], mask[:, :].unsqueeze(1).broadcast_to([TS, 2, TS]), ALU.mult)
            done(dve.tensor_copy(kdT[:, :, :], k_ps))
            keys_of_sequences = lambda f: dve.tensor_tensor(km[:, :, :], kdT[:, f, :].unsqueeze(1).broadcast_to([TS, N_SEQ, P]),
                                                            seq[:, :].unsqueeze(2).broadcast_to([TS, N_SEQ, P]), ALU.mult)
            done(keys_of_sequences(0))
            dve.wait_ge(kept, 1)
            for f in range(2):
                ins = dve.tensor_tensor(new[:, f], s0[:, f], el[:, f, :].unsqueeze(2).broadcast_to([P, N_SEQ, GLA_DV]), ALU.mult)
            done(ins)
            dve.tensor_tensor(gT[:, :, SEQ:T], gT[:, :, SEQ:T], intra_ps, ALU.add)
            for f in range(2):
                dve.wait_ge(states, f + 1)
                if f == 0:
                    done(keys_of_sequences(1))
                dve.tensor_tensor(new[:, f], new[:, f], s_ps, ALU.add).then_inc(finished, 1)

        @block.tensor
        def _(pe):
            pe.wait_ge(mixed, 1)
            for h in range(GLA_H):
                f, b = h // 2, h % 2
                half = slice(b * DH, b * DH + DH)
                pe.matmul(a_ps[:, b, f, :], k[half, f, :], q[half, f, :], start=True, stop=True)
            for f in range(2):
                last = pe.transpose(k_ps[:, f, :], kd[:, f, :], S.ident[:, :])
            last.then_inc(scored, 1)
            pe.wait_ge(loaded, 16 * (N_SEQ + 2))
            for h in range(GLA_H):
                f, b = h // 2, h % 2
                half = slice(b * DH, b * DH + DH)
                for n in range(N_SEQ):
                    pe.matmul(inter_ps[:, b, f, n * L_NEW:(n + 1) * L_NEW], s0[half, f, n, :], q[half, f, n * L_NEW:(n + 1) * L_NEW], start=True, stop=True)
            pe.wait_ge(step, 2)
            for h in range(GLA_H):
                last = pe.matmul(intra_ps[:, h, :], gvS[0:TS, QT, h * P:(h + 1) * P], A[:, h, :], start=True, stop=True)
            last.then_inc(outs, 1)
            for f in range(2):
                if f:
                    pe.wait_ge(finished, 1)
                    pe.wait_ge(step, 4)
                for n in range(N_SEQ):
                    for b in range(2):
                        last = pe.matmul(s_ps[b * DH:(b + 1) * DH, n, :], km[:, n, b * DH:(b + 1) * DH],
                                         gvS[0:TS, QT, (2 * f + b) * P:(2 * f + b + 1) * P], start=True, stop=True)
                last.then_inc(states, 1)


def gate_outputs(nc, S, gT, cg):
    with ExitStack() as ctx:
        sig = ctx.enter_context(nc.sbuf_tensor("cg_sig", [P, 2, T], F32))
        made, gated = add_sems(nc, "cg_sigmoid", "cg_gated")
        block = ctx.enter_context(nc.Block())

        @block.scalar
        def _(act):
            for h in range(GLA_H):
                if h >= 2:
                    act.wait_ge(gated, 2 * (h - 1))
                act.activation(sig[:, h % 2, :], cg[:, h, :], ACT.Sigmoid).then_inc(made, 1)

        @block.vector
        def _(dve):
            for h in range(GLA_H):
                dve.wait_ge(made, h + 1)
                dve.tensor_tensor(cg[:, h, :], cg[:, h, :], sig[:, h % 2, :], ALU.mult).then_inc(gated, 1)
                dve.wait_ge(gated, 2 * h + 1)
                dve.tensor_tensor(cg[:, h, :], cg[:, h, :], gT[:, h, :], ALU.mult).then_inc(gated, 1)


def dsa_prompt(nc, S, big, work, dvS):
    with ExitStack() as ctx:
        sb = lambda n, s: ctx.enter_context(nc.sbuf_tensor(n, s, F32))
        toep = sb("toep_dsa", [P, 4, SEQ])
        sc = sb("sc_dsa", [P, 2, SEQ])
        pT = sb("pT_dsa", [P, 2, BANK])
        osb = sb("o_dsa", [P, 2, P])
        stat = sb("stat_dsa", [P, 2, 4])
        scored, biased, vstep, maxed, exps, turned, kept, summed, scaled, pair_turned, pair_kept = add_sems(
            nc, *("dp_" + x for x in ("scored", "biased", "vector_step", "maxima", "exps", "turned",
                                      "probs_kept", "summed", "scaled", "pair_turned", "pair_kept")))
        toep_in = add_sems(nc, *(f"dp_toep_in{i}" for i in range(4)))
        units = [(f, t, b) for f in range(DSA_H // 2) for t in range(QT) for b in range(2)]
        groups = [(u, list(range(at, min(at + 4, units[u][1] + 1)))) for u in range(len(units)) for at in range(0, units[u][1] + 1, 4)]
        groups_to = [sum(1 for g in groups if g[0] <= u) for u in range(len(units))]
        s_ps = S.ps[:, 0:2048].rearrange("p (b k) -> p b k", b=2)
        t_ps = S.ps[:, 2048:3072].rearrange("p (b k) -> p b k", b=2)
        o_ps = S.ps[:, 3072:4096].rearrange("p (b d) -> p b d", b=2)[:, :, 0:DH]
        oT_ps = S.ps[:, 3584 + P:3584 + 2 * P]
        block = ctx.enter_context(nc.Block())

        @block.sync
        def _(sp):
            sp.wait_ge(S.dsa_lines, 16 * DSA_H)
            for h in range(DSA_H):
                if h >= 4:
                    sp.wait_ge(biased, (h - 4) // 2 * 2 * QT + 2 * QT)
                sp.dma_start(toep[:, h % 4:h % 4 + 1, :], toeplitz(S.dsa_copies, DSA_LINE, 0, slice(h, h + 1), 1, SEQ)).then_inc(toep_in[h % 4], 16)

        @block.tensor
        def _(pe):
            def scores(u):
                f, t, b = units[u]
                if u >= 2:
                    pe.wait_ge(biased, u - 1)
                half = slice(b * DH, b * DH + DH)
                for at in range(0, (t + 1) * P, BANK):
                    n = min(BANK, (t + 1) * P - at)
                    last = pe.matmul(s_ps[:, u % 2, at:at + n], big[half, 4 + f, t * P:(t + 1) * P], big[half, 8 + f, at:at + n], start=True, stop=True)
                last.then_inc(scored, 1)

            def turn_probs(g):
                u, kts = groups[g]
                pe.wait_ge(exps, u + 1)
                if g >= 2:
                    pe.wait_ge(kept, g - 1)
                for i, kt in enumerate(kts):
                    last = pe.transpose(t_ps[:, g % 2, i * P:(i + 1) * P], sc[:, u % 2, kt * P:(kt + 1) * P], S.ident[:, :])
                last.then_inc(turned, 1)

            def weigh_values(g):
                u, kts = groups[g]
                f, t, b = units[u]
                pe.wait_ge(kept, g + 1)
                if kts[0] == 0 and u >= 2:
                    pe.wait_ge(scaled, u - 1)
                if kts[0] == 0 and u % 2 == 1 and u >= 3:
                    pe.wait_ge(pair_kept, (u - 3) // 2 + 1)
                h = 2 * f + b
                for i, kt in enumerate(kts):
                    last = pe.matmul(o_ps[:, u % 2, :], pT[:, g % 2, i * P:(i + 1) * P], dvS[:, kt, h * DH:(h + 1) * DH], start=kt == 0, stop=kt == t)
                if kts[-1] == t:
                    last.then_inc(summed, 1)

            def turn_pair(k):
                pe.wait_ge(scaled, 2 * k + 2)
                if k:
                    pe.wait_ge(pair_kept, k)
                pe.transpose(oT_ps, osb[:, k % 2, :], S.ident[:, :]).then_inc(pair_turned, 1)

            scores(0)
            for g, (u, kts) in enumerate(groups):
                if kts[0] == 0:
                    if u + 1 < len(units):
                        scores(u + 1)
                turn_probs(g)
                if g:
                    weigh_values(g - 1)
                if kts[0] == 0 and u % 2 == 1 and u >= 3:
                    turn_pair((u - 3) // 2)
            weigh_values(len(groups) - 1)
            turn_pair(len(units) // 2 - 1)

        @block.vector
        def _(dve):
            done = chain(dve, vstep)
            def scale(u):
                dve.wait_ge(summed, u + 1)
                if u % 2 == 0 and u >= 4:
                    dve.wait_ge(pair_turned, (u - 4) // 2 + 1)
                dve.tensor_scalar(osb[:, (u // 2) % 2, (u % 2) * DH:(u % 2 + 1) * DH], o_ps[:, u % 2, :], stat[:, u % 2, 3:4], None,
                                  ALU.mult).then_inc(scaled, 1)

            for u, (f, t, b) in enumerate(units):
                h, n = 2 * f + b, (t + 1) * P
                if t == 0:
                    dve.wait_ge(toep_in[h % 4], 16 * (h // 4 + 1))
                dve.wait_ge(scored, u + 1)
                if u >= 2:
                    dve.wait_ge(turned, groups_to[u - 2])
                bias = toep[:, h % 4, SEQ - n:SEQ]
                st = stat[:, u % 2, :]
                if t < 2:
                    dve.tensor_tensor_reduce(sc[:, u % 2, 0:n], s_ps[:, u % 2, 0:n], bias, 1.0, TAKEN, ALU.add, ALU.max, st[:, 0:1]).then_inc(biased, 1)
                    dve.wait_ge(biased, u + 1)
                else:
                    dve.tensor_tensor(sc[:, u % 2, 0:n], s_ps[:, u % 2, 0:n], bias, ALU.add).then_inc(biased, 1)
                    dve.wait_ge(biased, u + 1)
                    done(dve.tensor_tensor_reduce(sc[:, u % 2, 0:n], sc[:, u % 2, 0:n], work[:, WORK_AT[t]:WORK_AT[t] + n], 1.0, TAKEN,
                                                  ALU.add, ALU.max, st[:, 0:1]))
                dve.tensor_scalar(st[:, 1:2], st[:, 0:1], -1.0, None, ALU.mult).then_inc(maxed, 1)
                if u:
                    dve.wait_ge(exps, u)
                    done(dve.reciprocal(stat[:, (u - 1) % 2, 3:4], stat[:, (u - 1) % 2, 2:3]))
                    scale(u - 1)
            dve.wait_ge(exps, len(units))
            done(dve.reciprocal(stat[:, (len(units) - 1) % 2, 3:4], stat[:, (len(units) - 1) % 2, 2:3]))
            scale(len(units) - 1)

        @block.scalar
        def _(act):
            def keep_pair(k):
                f, t, _ = units[2 * k]
                act.wait_ge(pair_turned, k + 1)
                act.activation(big[:, 4 + f, t * P:(t + 1) * P], oT_ps, ACT.Copy).then_inc(pair_kept, 1)

            g = 0
            for u, (f, t, b) in enumerate(units):
                act.wait_ge(maxed, u + 1)
                n = (t + 1) * P
                act.activation(sc[:, u % 2, 0:n], sc[:, u % 2, 0:n], ACT.Exp, bias=stat[:, u % 2, 1:2], accum_out=stat[:, u % 2, 2:3]).then_inc(exps, 1)
                while g < len(groups) and groups[g][0] == u:
                    m = len(groups[g][1]) * P
                    act.wait_ge(turned, g + 1)
                    if g >= 2:
                        act.wait_ge(kept, g - 1)
                    act.activation(pT[:, g % 2, 0:m], t_ps[:, g % 2, 0:m], ACT.Copy).then_inc(kept, 1)
                    g += 1
                if u % 2 == 1 and u >= 3:
                    keep_pair((u - 3) // 2)
            keep_pair(len(units) // 2 - 1)


def dsa_sample(nc, S, big, work, work_s, dvS, space):
    sc, bias = work[:, 0:S_COLS], work[:, S_COLS:2 * S_COLS]
    mask = work[0:TS, 2 * S_COLS:3 * S_COLS]
    with ExitStack() as outer:
        sb = lambda n, s: outer.enter_context(nc.sbuf_tensor(n, s, F32))
        pages = outer.enter_context(nc.sbuf_tensor("pages_kv", [1, N_SEQ * N_PAGES], I32))
        qb = sb("qb_dsa", [P, 4, N_SEQ, 32])
        tabr = sb("tabr_dsa", [NB, L_NEW, P])
        third = sb("kv_slot", [P, N_PAGES, BANK])
        slots = [space[:, i * 4096:(i + 1) * 4096].rearrange("p (g x) -> p g x", g=N_PAGES) for i in range(2)] + [third[:, :, :]]
        for half in range(2):
            with ExitStack() as ctx:
                tag = f"ds{half}"
                sb2 = lambda n, s: ctx.enter_context(nc.sbuf_tensor(f"{n}_{tag}", s, F32))
                hot = sb2("hot_s", [NB, L_NEW, BANK])
                sel = sb2("dsa_rows", [TS, P])
                other = sb2("dsa_other", [P, TS])
                kT = sb2("kT", [P, 2, BANK])
                pT = sb2("pT_s", [P, N_PAGES + 1, P])
                stat = sb2("stat_s", [P, 3])
                consts, table_in, prep, hot_in, biased, scored, step, exps, turned, copied, probs_turned, probs_kept, summed = add_sems(
                    nc, *(f"{x}_{tag}" for x in ("consts", "table_in", "prepared", "hot_in", "bias_made", "scored", "step", "exps", "keys_turned",
                                                 "keys_copied", "probs_turned", "probs_kept", "summed")))
                kv_in = add_sems(nc, *(f"kv_in{i}_{tag}" for i in range(3)))
                (kv_used,) = add_sems(nc, f"kv_used_{tag}")
                s_ps = S.ps[:, 0:S_COLS]
                b_ps = S.ps[:, 1536:1536 + S_COLS]
                t_ps = S.ps[:, 3072:4096].rearrange("p (b x) -> p b x", b=2)
                p_ps = S.ps[:, 0:(N_PAGES + 1) * P].rearrange("p (g x) -> p g x", g=N_PAGES + 1)
                o_ps = S.ps[:, 1536:1536 + P].rearrange("p (n f x) -> p n f x", n=4, f=4)
                pool_kv = S.d["cache_dsa_kv"][0]
                block = ctx.enter_context(nc.Block())

                @block.sync
                def _(sp):
                    if half == 0:
                        sp.dma_start(pages[:, :], S.d["page_table"].rearrange("n (a g) -> a (n g)", a=1)).then_inc(table_in, 16)
                    sp.dma_start(sel[:, :], S.c["dsa_rows"][:, half, :]).then_inc(consts, 16)
                    sp.dma_start(other[:, :], S.c["dsa_other"][:, half, :]).then_inc(consts, 16)
                    sp.dma_start(hot[:, :, :], S.c["dsa_hot"][:, :, 0:BANK]).then_inc(hot_in, 16)
                    if half == 0:
                        sp.wait_ge(table_in, 16)
                    for i in range(8):
                        n, what = 4 * half + i % 4, i // 4
                        if 3 <= i < 7:
                            sp.wait_ge(turned, N_PAGES * (i - 2))
                        elif i >= 7:
                            sp.wait_ge(kv_used, i - 6)
                        for g in range(N_PAGES):
                            page = sp.value_load(pages[0:1, n * N_PAGES + g:n * N_PAGES + g + 1], min_val=0, max_val=pool_kv.shape[0] - 1)
                            sp.dma_start(slots[i % 3][:, g, :], pool_kv[bass.ds(page, 1)].rearrange("a s c h d -> s (a c) (h d)")[:, what, :]).then_inc(kv_in[i % 3], 16)

                @block.scalar
                def _(act):
                    act.wait_ge(biased, 1)
                    act.dma_start(hot[:, :, :], S.c["dsa_hot"][:, :, BANK:PAST]).then_inc(hot_in, 16)
                    act.wait_ge(biased, 2)
                    act.dma_start(hot[:, :, 0:TS], S.c["dsa_hot_new"]).then_inc(hot_in, 16)
                    for i in range(4 * N_PAGES):
                        act.wait_ge(turned, i + 1)
                        if i >= 2:
                            act.wait_ge(scored, i - 1)
                        act.activation(kT[:, i % 2, :], t_ps[:, i % 2, :], ACT.Copy).then_inc(copied, 1)
                    act.wait_ge(step, 3)
                    act.activation(sc, sc, ACT.Exp, bias=stat[:, 0:1], accum_out=stat[:, 1:2]).then_inc(exps, 1)

                @block.vector
                def _(dve):
                    done = chain(dve, step)
                    if half == 0:
                        dve.memset(qb[:, :, :, :], 0.0).then_inc(prep, 1)
                        dve.memset(tabr[:, :, :], 0.0).then_inc(prep, 1)
                        dve.wait_ge(prep, 2)
                        for h in range(DSA_H):
                            rows, f = slice(DH * (h % 2), DH * (h % 2) + DH), h // 2
                            dve.tensor_copy(qb[rows, f, :, h * L_NEW:(h + 1) * L_NEW],
                                            big[rows, 4 + f, SEQ:T].rearrange("p (n l) -> p n l", l=L_NEW))
                        for l in range(L_NEW):
                            dve.tensor_copy(tabr[:, l, :].rearrange("b (n h l) -> b n h l", n=4, h=DSA_H)[:, :, :, l],
                                            S.tab[:, 12:12 + DSA_H].unsqueeze(1).broadcast_to([NB, 4, DSA_H]))
                        dve.tensor_copy(mask[:, 0:PAST], work_s[:, 0:PAST])
                        dve.tensor_copy(mask[:, PAST:S_COLS].rearrange("t (n l) -> t n l", n=N_SEQ),
                                        work_s[:, PAST:S_KEYS].unsqueeze(1).broadcast_to([TS, N_SEQ, L_NEW])).then_inc(prep, 1)
                    dve.wait_ge(consts, 32)
                    dve.wait_ge(biased, 3)
                    dve.tensor_copy(bias[:, 0:PAST], b_ps[:, 0:PAST])
                    done(dve.tensor_tensor(bias[:, PAST:S_COLS], b_ps[:, PAST:S_COLS], other[:, :], ALU.add))
                    dve.wait_ge(scored, 4 * N_PAGES + 1)
                    done(dve.tensor_tensor(sc, s_ps, bias, ALU.add))
                    done(dve.tensor_reduce(stat[:, 0:1], sc, AX.X, ALU.max, negate=True))
                    dve.wait_ge(exps, 1)
                    done(dve.reciprocal(stat[:, 2:3], stat[:, 1:2]))
                    done(dve.tensor_scalar(sc, sc, stat[:, 2:3], None, ALU.mult))
                    dve.wait_ge(probs_turned, 1)
                    dve.tensor_copy(pT[:, 0:N_PAGES, :], p_ps[:, 0:N_PAGES, :])
                    dve.tensor_copy(pT[0:TS, N_PAGES, :], p_ps[0:TS, N_PAGES, :]).then_inc(probs_kept, 1)
                    dve.wait_ge(summed, 1)
                    for b in range(2):
                        rows = slice(b * DH, b * DH + DH)
                        dve.tensor_copy(big[rows, 4:8, SEQ + 16 * half:SEQ + 16 * (half + 1)].rearrange("p f (n l) -> p f n l", n=4),
                                        o_ps[rows, :, :, b * L_NEW:(b + 1) * L_NEW].rearrange("p n f l -> p f n l"))

                @block.tensor
                def _(pe):
                    if half == 0:
                        pe.wait_ge(prep, 3)
                    pe.wait_ge(consts, 32)
                    for i, (at, n) in enumerate(((0, BANK), (BANK, BANK), (PAST, TS))):
                        pe.wait_ge(hot_in, 16 * (i + 1))
                        for l in range(L_NEW):
                            pe.matmul(b_ps[:, at:at + n], tabr[:, l, :], hot[:, l, 0:n], start=l == 0, stop=False)
                        pe.matmul(b_ps[:, at:at + n], sel[:, :], mask[:, at:at + n], start=False, stop=True).then_inc(biased, 1)

                    def turn_keys(i):
                        n, g = divmod(i, N_PAGES)
                        pe.wait_ge(kv_in[n % 3], 16 * N_PAGES * (n // 3 + 1))
                        if i >= 2:
                            pe.wait_ge(copied, i - 1)
                        for f in range(4):
                            last = pe.transpose(t_ps[:, i % 2, f * P:(f + 1) * P], slots[n % 3][:, g, f * P:(f + 1) * P], S.ident[:, :])
                        last.then_inc(turned, 1)
                        if g == N_PAGES - 1:
                            return last
                    turn_keys(0)
                    for i in range(4 * N_PAGES):
                        if i + 1 < 4 * N_PAGES:
                            turn_keys(i + 1)
                        pe.wait_ge(copied, i + 1)
                        n, g = divmod(i, N_PAGES)
                        for f in range(4):
                            last = pe.matmul(s_ps[32 * n:32 * n + 32, g * P:(g + 1) * P], qb[:, f, 4 * half + n, :], kT[:, i % 2, f * P:(f + 1) * P],
                                             start=f == 0, stop=f == 3)
                        last.then_inc(scored, 1)
                    for n in range(4):
                        for f in range(4):
                            last = pe.matmul(s_ps[32 * n:32 * n + 32, NEW_AT:NEW_AT + TS], qb[:, f, 4 * half + n, :], big[:, 8 + f, SEQ:T],
                                             start=f == 0, stop=f == 3)
                    last.then_inc(scored, 1)
                    pe.wait_ge(step, 5)
                    for g in range(N_PAGES):
                        pe.transpose(p_ps[:, g, :], sc[:, g * P:(g + 1) * P], S.ident[:, :])
                    pe.transpose(p_ps[0:TS, N_PAGES, :], sc[:, PAST:S_COLS], S.ident[:, :]).then_inc(probs_turned, 1)
                    pe.wait_ge(probs_kept, 1)
                    for n in range(4):
                        i = 4 + n
                        pe.wait_ge(kv_in[i % 3], 16 * N_PAGES * (i // 3 + 1))
                        for f in range(4):
                            own = slice(n * 32 + f * 8, n * 32 + f * 8 + 8)
                            for g in range(N_PAGES):
                                last = pe.matmul(o_ps[:, n, f, :], slots[i % 3][:, g, f * P:(f + 1) * P], pT[:, g, own], start=g == 0, stop=False)
                            if f == 3:
                                last.then_inc(kv_used, 1)
                            last = pe.matmul(o_ps[:, n, f, :], dvS[0:TS, QT, f * P:(f + 1) * P], pT[0:TS, N_PAGES, own], start=False, stop=True)
                    last.then_inc(summed, 1)


def layer1_states(nc, S, big, dvS):
    o = S.o
    rows_p = o["dsa_kv_p"][0, 0].rearrange("t p c h d -> t p c (h d)")
    rows_s = o["dsa_kv_s"][0].rearrange("n l c h d -> (n l) c (h d)")
    jobs = [([big[:, 8 + f, t * P:(t + 1) * P] for f in range(4)], P, [(0, P, 512, rows_p[t, :, 0, :])]) for t in range(QT)]
    jobs.append(([big[:, 8 + f, SEQ:T] for f in range(4)], TS, [(0, TS, 512, rows_s[:, 0, :])]))
    direct = [(rows_p[t, :, 1, :], dvS[:, t, :]) for t in range(QT)] + [(rows_s[:, 1, :], dvS[0:TS, QT, :])]
    turn_and_store(nc, S, "cd", jobs, direct)


def layer1(nc, S):
    with ExitStack() as layer:
        keep = lambda n, s: layer.enter_context(nc.sbuf_tensor(n, s, F32))
        big = keep("big", [P, 12, T])
        iw = keep("iw", [P, QT + 1, DH + IDX_H])
        work, work_s = keep("work", [P, WORK]), keep("work_s", [TS, S_KEYS])
        hT = keep("h1", [P, KD, T])
        rms_norm(nc, S, "mix1", S.g_mix[:, 1, :], hT)
        with ExitStack() as gla:
            keep2 = lambda n, s: gla.enter_context(nc.sbuf_tensor(n, s, F32))
            bT = keep2("decays", [P, 2, T])
            lrT = bT[0:GLA_RANK, 1, :]
            with ExitStack() as index:
                iqT = index.enter_context(nc.sbuf_tensor("iqT", [P, 2, T], F32))
                ikT = index.enter_context(nc.sbuf_tensor("ikT", [P, T], F32))
                index_products(nc, S, hT, iqT, ikT, iw, lrT)
                index_scores_prompt(nc, S, iqT, ikT, iw, work)
                index_scores_sample(nc, S, iqT, ikT, iw, work_s)
            gT = keep2("gT", [P, 4, T])
            gvS = keep2("gvS", [P, QT + 1, BANK])
            big_products(nc, S, hT, gT, big, gvS, work, work_s)
            gla_decays(nc, S, lrT, bT)
            gla_prompt(nc, S, gT, bT, gvS)
            gla_sample(nc, S, gT, bT, gvS)
            with nc.sbuf_tensor("g_gla", [P, 1], F32) as g_gla:
                (g_in,) = add_sems(nc, "g_gla_in")
                with nc.Block() as block:
                    @block.sync
                    def _(sp):
                        sp.dma_start(g_gla[:, :], S.d["gla_norm"].rearrange("a v -> v a")).then_inc(g_in, 16)
                        sp.wait_ge(g_in, 16)
                head_norms(nc, S, "gla", gT, [0, 1, 2, 3], [g_gla[:, 0:1]] * 4, S.ones, GLA_DV)
            gate_outputs(nc, S, gT, big)
        dvS = keep("dvS", [P, QT + 1, BANK])
        dsa_value_products(nc, S, hT, dvS)
        head_norms(nc, S, "qk1", big, list(range(4, 12)), [S.g_qk[:, 2:3]] * 4 + [S.g_qk[:, 3:4]] * 4, S.head_ones, DH)
        layer1_states(nc, S, big, dvS)
        dsa_prompt(nc, S, big, work, dvS)
        dsa_sample(nc, S, big, work, work_s, dvS, hT[:, :, :].rearrange("p k t -> p (k t)"))
        project_back(nc, S, "out1", S.d["w_out_cd"][0], KD, lambda k: big[:, k, :])


def build_kernel(nc, d, c, o, stop=99):
    S = Stage()
    LIVE_SEMAPHORES.clear()
    S.d, S.c, S.o = d, c, o
    dram = lambda n, s: nc.dram_tensor(n, s, F32, kind="Internal").ap()
    S.part_rows = dram("part_rows", [3, T, HPG, HEAD_ROW])
    S.ab_line, S.dsa_line = dram("ab_line", [HPG, AB_LINE]), dram("dsa_line", [DSA_H, DSA_LINE])
    S.ab_copies, S.dsa_copies = dram("ab_copies", [HPG, P, AB_LINE]), dram("dsa_copies", [DSA_H, P, DSA_LINE])
    S.ab_lines, S.dsa_lines = nc.alloc_semaphore("ab_lines_copied"), nc.alloc_semaphore("dsa_lines_copied")
    q_rows, k_rows, v_rows = (dram(n, [TS, 3 * GW]) for n in ("q_rows", "k_rows", "v_rows"))
    with ExitStack() as ctx, nc.allow_non_contiguous_dma(reason="columns of gains and rows of a few floats"):
        sb = lambda n, s: ctx.enter_context(nc.sbuf_tensor(n, s, F32))
        S.ps = ctx.enter_context(nc.psum_tensor("ps", [P, 4096], F32))
        S.xT = sb("xT", [P, KD, T])
        S.ident, S.head_ones, S.ones = sb("ident", [P, P]), sb("head_ones", [P, P]), sb("ones", [P, P])
        S.g_mix, S.g_ffn, S.g_qk = sb("g_mix", [P, 2, KD]), sb("g_ffn", [P, 2, KD]), sb("g_qk", [P, 4])
        S.tab, S.eps = sb("tab", [NB, 20]), sb("eps", [P, 1])
        load_inputs(nc, S)
        bias_lines(nc, S)
        with ExitStack() as layer0:
            keep = lambda n, s: layer0.enter_context(nc.sbuf_tensor(n, s, F32))
            yT = keep("yT", [P, CC, T])
            v_new = keep("v_new", [TS, 3, GW])
            with ExitStack() as attention:
                keep2 = lambda n, s: attention.enter_context(nc.sbuf_tensor(n, s, F32))
                S.qk = keep2("qk", [P, 12, T])
                vS = keep2("vS", [P, 3, QT, GW])
                with ExitStack() as projections:
                    uT = projections.enter_context(nc.sbuf_tensor("uT", [P, CC, U_LEN], F32))
                    taps = projections.enter_context(nc.sbuf_tensor("taps", [P, CC, TAPS], F32))
                    with nc.sbuf_tensor("h0", [P, KD, T], F32) as hT:
                        rms_norm(nc, S, "mix0", S.g_mix[:, 0, :], hT)
                        glu_products(nc, S, hT, uT, taps)
                        qkv_products(nc, S, hT, uT, taps, yT, vS, v_new)
                    head_norms(nc, S, "qk0", S.qk, list(range(12)), [S.g_qk[:, 0:1]] * 6 + [S.g_qk[:, 1:2]] * 6, S.head_ones, DH)
                    layer0_states(nc, S, uT, vS, v_new, q_rows, k_rows, v_rows)
                dilated_prompt(nc, S, vS)
                for g in range(3):
                    dilated_sample(nc, S, g, q_rows, v_new)
            merged = keep("bT", [P, 2, T])
            combine_windows(nc, S, merged)
            conv_norm(nc, S, yT)
            project_back(nc, S, "out0", S.d["w_out_ab"][0], 6, lambda k: yT[:, k, :] if k < CC else merged[:, k - CC, :])
        ffn(nc, S, 0)
        recycle_semaphores(nc)
        if stop > 1:
            layer1(nc, S)
            recycle_semaphores(nc)
            ffn(nc, S, 1)
        store_y(nc, S)


_OUTS = [("y_prompt", (1, SEQ, D_MODEL)), ("y_sample", (N_SEQ, L_NEW, D_MODEL)),
         ("conv_p", (1, 1, HIST, CONV_CH)), ("conv_s", (1, N_SEQ, HIST, CONV_CH)),
         ("win128_p", (1, 1, 128, 2, HPG, DH)), ("win128_s", (1, N_SEQ, 128, 2, HPG, DH)),
         ("win512_p", (1, 1, 512, 2, HPG, DH)), ("win512_s", (1, N_SEQ, 512, 2, HPG, DH)),
         ("win2048_p", (1, 1, SEQ, 2, HPG, DH)), ("win2048_s", (1, N_SEQ, PAST + L_NEW, 2, HPG, DH)),
         ("gla_p", (1, 1, GLA_H, GLA_DK, GLA_DV)), ("gla_s", (1, N_SEQ, GLA_H, GLA_DK, GLA_DV)),
         ("dsa_kv_p", (1, 1, QT, PAGE, 2, DSA_H, DH)), ("dsa_kv_s", (1, N_SEQ, L_NEW, 2, DSA_H, DH)),
         ("dsa_kidx_p", (1, 1, QT, PAGE, DH)), ("dsa_kidx_s", (1, N_SEQ, L_NEW, DH))]


def kernel(**inputs):
    import concourse.bacc as _bacc
    from concourse.bass_utils import run_bass_kernel_spmd as _run

    nc = _bacc.Bacc("TRN2", target_bir_lowering=False, num_devices=1)
    arrays, d, c, o = {}, {}, {}, {}
    for name, a in inputs.items():
        arrays[f"in_{name}"] = np.ascontiguousarray(a)
        d[name] = nc.dram_tensor(f"in_{name}", a.shape, mybir.dt.from_np(arrays[f"in_{name}"].dtype), kind="ExternalInput").ap()
    for name, a in shape_constants().items():
        arrays[f"const_{name}"] = np.ascontiguousarray(a)
        c[name] = nc.dram_tensor(f"const_{name}", a.shape, mybir.dt.from_np(a.dtype), kind="ExternalInput").ap()
    for name, shape in _OUTS:
        o[name] = nc.dram_tensor(f"out_{name}", shape, F32, kind="ExternalOutput").ap()
    build_kernel(nc, d, c, o)
    r = _run(nc, [arrays], core_ids=[0])
    return tuple(r.results[0][f"out_{name}"] for name, _ in _OUTS)
```

```python
from contextlib import ExitStack

import numpy as np
import concourse.bass as bass
from concourse import mybir

F32 = mybir.dt.float32
F32R = mybir.dt.float32r
I32 = mybir.dt.int32
ALU = mybir.AluOpType
ACT = mybir.ActivationFunctionType
AX = mybir.AxisListType

P = 128
D_MODEL = 1024
KD = D_MODEL // P
SEQ = 1024
QT = SEQ // P
N_SEQ, L_NEW = 8, 4
TS = N_SEQ * L_NEW
T = SEQ + TS
PAST = 1024
PAGE = 128
N_PAGES = PAST // PAGE
DH = 64
CONV_CH = 512
CC = CONV_CH // P
TAPS = 31
HIST = TAPS - 1
WINDOWS = (128, 512, 2048)
DILS = (1, 4, 16)
HPG = 4
GW = HPG * DH
GLA_H, GLA_DK, GLA_DV, GLA_RANK, GLA_TAU = 4, 64, 128, 16, 16.0
DSA_H = 8
IDX_H = 4
TOPK = 256
FFN = 2816
KF = FFN // P
EPS = 1e-6
BUCKETS, MAX_DIST = 32, 2048
NB = BUCKETS + 1
MASKED = -1e30
TAKEN = -3e38
CQ, CK, CV, CLR, CG, DQ, DK_, DV_, IQ, IK, IW = 0, 256, 512, 1024, 1040, 1552, 2064, 2576, 3088, 3344, 3408
AT_M, AT_L, HEAD_ROW = DH, DH + 1, DH + 2
BANK = 512
PIECE = T // 3
PIECES = tuple((c * BANK, c * PIECE, PIECE) for c in range(3))


def rel_bucket(dist):
    n = np.maximum(dist, 0)
    half = BUCKETS // 2
    nf = np.maximum(n, half).astype(np.float32)
    large = half + (np.log(nf / np.float32(half)) / np.float32(np.log(MAX_DIST / half)) * np.float32(BUCKETS - half)).astype(np.int32)
    b = np.where(n < half, n, np.minimum(large, BUCKETS - 1))
    return np.where(dist < 0, BUCKETS, b)


def one_hot(bucket):
    return np.moveaxis(np.eye(NB, dtype=np.float32)[bucket], -1, 0)


def shape_constants():
    c = {}
    c["ident"] = np.eye(P, dtype=np.float32)
    c["head_ones"] = np.kron(np.eye(2, dtype=np.float32), np.ones((DH, DH), np.float32))
    for g, dil in enumerate(DILS[:2]):
        rel = 255 - np.arange(383)
        c[f"line{g}"] = one_hot(rel_bucket(np.where((rel >= 0) & (rel <= WINDOWS[g] // dil), rel * dil, -1)))
    rel = 127 - np.arange(255)
    c["line2"] = one_hot(rel_bucket(np.where((rel >= 0) & (rel % 2 == 0), rel * (DILS[2] // 2), -1)))
    c["line_dsa"] = one_hot(rel_bucket(1023 - np.arange(1151)))
    for g, dil in enumerate(DILS):
        nk = 64 if g == 2 else 128
        rows = []
        for l in range(L_NEW):
            j = np.arange(nk)
            cached = np.where(j >= l, 128 + l - j, -1) if g == 0 else dil * (nk - j)
            new = l - np.arange(L_NEW)
            if g:
                new = np.where(new == 0, 0, -1)
            rows.append(one_hot(rel_bucket(np.concatenate([cached, np.tile(new, N_SEQ)]))))
        c[f"sample_hot{g}"] = np.stack(rows, 1)
    n_of, l_of = np.arange(TS) // L_NEW, np.arange(TS) % L_NEW
    c["tri"] = np.where(np.arange(P)[None] <= np.arange(P)[:, None], 0, MASKED).astype(np.float32)
    c["causal_T"] = (np.arange(P)[:, None] <= np.arange(P)[None]).astype(np.float32)
    c["chunk_inside"] = np.concatenate([np.arange(SEQ) % P != 0, l_of != 0]).astype(np.float32)[None]
    c["sample_causal_T"] = ((n_of[:, None] == n_of[None]) & (l_of[:, None] <= l_of[None])).astype(np.float32)
    c["seq_of"] = (n_of[:, None] == np.arange(N_SEQ)[None]).astype(np.float32)
    row = np.arange(P)
    tok = lambda half, l: (4 * half + row // 32) * L_NEW + l
    c["index_rows"] = np.stack([((np.arange(TS)[:, None] == tok(g, row % 4)[None]) & (row % 32 < 16)[None]) for g in range(2)], 1).astype(np.float32)
    c["dsa_rows"] = np.stack([np.arange(TS)[:, None] == tok(g, row % 4)[None] for g in range(2)], 1).astype(np.float32)
    c["dsa_other"] = np.stack([np.where(n_of[None] == (4 * g + row // 32)[:, None], 0, MASKED) for g in range(2)], 1).astype(np.float32)
    c["new_mask"] = np.where(np.arange(L_NEW)[None] <= l_of[:, None], 0, MASKED).astype(np.float32)
    key = np.arange(PAST)
    c["dsa_hot"] = np.stack([one_hot(rel_bucket(PAST + l - key)) for l in range(L_NEW)], 1)
    c["dsa_hot_new"] = np.stack([one_hot(rel_bucket(np.tile(l - np.arange(L_NEW), N_SEQ))) for l in range(L_NEW)], 1)
    row_n = np.arange(P) // (L_NEW * HPG)
    c["other_seq"] = np.where(row_n[:, None] == np.arange(TS)[None] // L_NEW, 0, MASKED).astype(np.float32)
    f = np.arange(GW) // DH
    c["feat_head"] = (f[:, None] == np.arange(HPG)[None]).astype(np.float32).reshape(2, P, HPG).transpose(1, 0, 2).copy()
    c["row_head"] = (np.arange(P)[:, None] % HPG == np.arange(HPG)[None]).astype(np.float32)
    return c


class Stage:
    pass


LIVE_SEMAPHORES = []


def add_sems(nc, *names):
    sems = [nc.alloc_semaphore(n) for n in names]
    LIVE_SEMAPHORES.extend(sems)
    return sems


def recycle_semaphores(nc):
    nc.clear_and_free_semaphores(list(LIVE_SEMAPHORES))
    LIVE_SEMAPHORES.clear()
    nc.all_engine_barrier()


def chain(eng, sem):
    count = [0]

    def done(ins):
        count[0] += 1
        ins.then_inc(sem, 1)
        eng.wait_ge(sem, count[0])
        return ins
    return done


def load_inputs(nc, S, xT):
    with ExitStack() as ctx:
        xrow = ctx.enter_context(nc.sbuf_tensor("xrow", [P, QT + 1, D_MODEL], F32))
        loaded, gains, transposed, evacuated = add_sems(nc, "x_loaded", "gains_loaded", "x_transposed", "x_evacuated")
        ps = S.ps[:, 0:3072].rearrange("p (b c) -> p b c", b=2)
        block = ctx.enter_context(nc.Block())

        @block.sync
        def _(sp):
            sp.dma_start(S.ident[:, :], S.c["ident"]).then_inc(loaded, 16)
            for t in range(QT):
                sp.dma_start(xrow[:, t, :], S.d["x_prompt"][0, t * P:(t + 1) * P, :]).then_inc(loaded, 16)
            sp.dma_start(xrow[0:TS, QT, :], S.d["x_sample"].rearrange("n l d -> (n l) d")).then_inc(loaded, 16)
            sp.dma_start(S.head_ones[:, :], S.c["head_ones"]).then_inc(gains, 16)
            for name, dst in (("norm_mix", S.g_mix), ("norm_ffn", S.g_ffn)):
                for layer in range(2):
                    sp.dma_start(dst[:, layer, :], S.d[name][layer].rearrange("(k p) -> p k", p=P)).then_inc(gains, 16)
            for i, name in enumerate(("qn_ab", "kn_ab", "qn_cd", "kn_cd")):
                for half in range(2):
                    sp.dma_start(S.g_qk[half * DH:(half + 1) * DH, i:i + 1], S.d[name].rearrange("a d -> d a")).then_inc(gains, 16)
            sp.dma_start(S.tab[0:BUCKETS, :], S.d["rel_bias"]).then_inc(gains, 16)
            sp.wait_ge(gains, 16 * 14)

        @block.gpsimd
        def _(pool):
            pool.memset(S.ones[:, :], 1.0)

        @block.tensor
        def _(pe):
            pe.wait_ge(loaded, 16 * (QT + 2))
            for k in range(KD):
                if k >= 2:
                    pe.wait_ge(evacuated, k - 1)
                for t in range(QT + 1):
                    n = P if t < QT else TS
                    last = pe.transpose(ps[:, k % 2, t * P:t * P + n], xrow[0:n, t, k * P:(k + 1) * P], S.ident[0:n, 0:n])
                last.then_inc(transposed, 1)

        @block.vector
        def _(dve):
            dve.memset(S.tab[BUCKETS:NB, :], MASKED)
            dve.memset(S.eps[:, :], EPS)
            dve.wait_ge(gains, 16 * 14)
            dve.tensor_scalar(S.g_qk[:, 2:3], S.g_qk[:, 2:3], DH ** -0.5, None, ALU.mult)
            for k in range(KD):
                dve.wait_ge(transposed, k + 1)
                dve.tensor_copy(xT[:, k, :], ps[:, k % 2, 0:T]).then_inc(evacuated, 1)


class Parts:

    def __init__(self, nc, ctx, name, shape):
        tile = ctx.enter_context(nc.sbuf_tensor(name, [P, 2, *shape], F32R))
        self.hi, self.lo = tile[:, 0], tile[:, 1]


def passes(stationary, moving):
    return (stationary.lo, moving.hi), (stationary.hi, moving.lo), (stationary.hi, moving.hi)


def rms_norm(nc, S, tag, gain, xT, h, scratch, spill=None):
    sq, rstd, normed = scratch[:, 0:2, :], scratch[:, 2, :], scratch[:, 3:5, :]
    with ExitStack() as ctx:
        squared, summed, mean_ready, rstd_ready, normalised, hi_made, lo_made, spilled = add_sems(
            nc, *(f"{x}_{tag}" for x in ("squared", "summed", "mean_ready", "rstd_ready", "normalised", "h_hi_made", "h_lo_made", "x_spilled")))
        block = ctx.enter_context(nc.Block())

        @block.sync
        def _(sp):
            if spill is not None:
                sp.dma_start(spill, xT).then_inc(spilled, 16)
                sp.wait_ge(spilled, 16)

        @block.scalar
        def _(act):
            for k in range(KD):
                if k >= 2:
                    act.wait_ge(summed, k - 1)
                act.activation(sq[:, k % 2, :], xT[:, k, :], ACT.Square).then_inc(squared, 1)
            act.wait_ge(summed, KD)
            act.activation(by3(rstd), slot(S, 0), ACT.Ln, scale=1.0 / D_MODEL, bias=S.eps[:, :]).then_inc(mean_ready, 1)
            act.wait_ge(mean_ready, 1)
            act.activation(rstd, rstd, ACT.Exp, scale=-0.5).then_inc(rstd_ready, 1)
            for k in range(KD):
                act.wait_ge(normalised, k + 1)
                act.activation(h.hi[:, k, :], normed[:, k % 2, :], ACT.Copy).then_inc(hi_made, 1)

        @block.tensor
        def _(pe):
            for k in range(KD):
                pe.wait_ge(squared, k + 1)
                for at, t, n in PIECES:
                    last = pe.matmul(S.ps[:, at:at + n], S.ones[:, :], sq[:, k % 2, t:t + n], start=k == 0, stop=k == KD - 1)
                last.then_inc(summed, 1)

        @block.vector
        def _(dve):
            def low_part(k):
                dve.wait_ge(hi_made, k + 1)
                dve.tensor_tensor(h.lo[:, k, :], normed[:, k % 2, :], h.hi[:, k, :], ALU.subtract).then_inc(lo_made, 1)

            dve.wait_ge(rstd_ready, 1)
            for k in range(KD):
                if k >= 2:
                    dve.wait_ge(lo_made, k - 1)
                dve.scalar_tensor_tensor(normed[:, k % 2, :], xT[:, k, :], gain[:, k:k + 1], rstd, ALU.mult, ALU.mult).then_inc(normalised, 1)
                if k:
                    low_part(k - 1)
            low_part(KD - 1)


class Weights:

    def __init__(self, nc, ctx, tag):
        self.raw = ctx.enter_context(nc.sbuf_tensor(f"w_{tag}", [P, KD, 2, P], F32))
        self.parts = Parts(nc, ctx, f"w_parts_{tag}", [KD, 2, P])
        self.loaded, self.hi_made, self.lo_made, self.product, self.free = (
            add_sems(nc, *(f"{what}{j}_{tag}" for j in range(2))) for what in ("w_loaded", "w_hi_made", "w_lo_made", "product", "slot_free"))

    def load(self, sp, j, n, kt, src):
        sp.wait_ge(self.lo_made[j], n)
        sp.dma_start(self.raw[:, 0:kt, j, :], src).then_inc(self.loaded[j], 16)

    def high(self, act, j, n, kt):
        act.wait_ge(self.loaded[j], n * 16)
        if type(n) is int and n == 1:
            act.sem_inc(self.product[j], 1)
        else:
            act.wait_ge(self.product[j], n)
        act.activation(self.parts.hi[:, 0:kt, j, :], self.raw[:, 0:kt, j, :], ACT.Copy).then_inc(self.hi_made[j], 1)

    def low(self, eng, j, n, kt):
        eng.wait_ge(self.hi_made[j], n)
        eng.tensor_tensor(self.parts.lo[:, 0:kt, j, :], self.raw[:, 0:kt, j, :], self.parts.hi[:, 0:kt, j, :], ALU.subtract).then_inc(self.lo_made[j], 1)


def load_weight_pairs(sp, W, kt, iters, src_a, src_b, before=0):
    with sp.Fori(1, iters + 1) as i:
        for j, (w, step, col) in enumerate((src_a, src_b)):
            W.load(sp, j, i + before, kt, w[:, 0:kt, bass.ds(i * step + (col - step), P)])


def multiply_pairs(pe, S, W, kt, iters, rhs, before=0, made=None):
    with pe.Fori(0, iters) as i:
        for j in range(2):
            pe.wait_ge(W.lo_made[j], i + (before + 2))
            pe.wait_ge(W.free[j], i + (before + 1))
            for k in range(kt):
                if made:
                    pe.wait_ge(made[0], made[1] + k + 1)
                for n, (w, x) in enumerate(passes(W.parts, rhs)):
                    for c, (at, t, size) in enumerate(PIECES):
                        last = pe.matmul(S.ps[:, j * 1536 + at:j * 1536 + at + size], w[:, k, j, :], x[:, k, t:t + size],
                                         start=k == 0 and n == 0, stop=k == kt - 1 and n == 2)
                        if k == kt - 1 and n == 2 and c == 2:
                            last.then_inc(W.product[j], 1)


def w_cols(w, col):
    return w.rearrange("(k p) m -> p k m", p=P), P, col


def w_pairs(w, col):
    v = w.rearrange("(k p) m -> p k m", p=P)
    return (v, 2 * P, col), (v, 2 * P, col + P)


def slot(S, j):
    return S.ps[:, j * 1536:(j + 1) * 1536].rearrange("p (c t) -> p c t", c=3)[:, :, 0:PIECE]


def by3(line):
    return line.rearrange("p (c t) -> p c t", c=3)


LINES = ((0, 383), (383, 383), (766, 255))
AB_LINE, DSA_LINE = 1021, 1151


def bias_lines(nc, S):
    with ExitStack() as ctx:
        sb = lambda n, s: ctx.enter_context(nc.sbuf_tensor(n, s, F32))
        hot, hot_d = sb("hot", [NB, AB_LINE]), sb("hot_dsa", [NB, DSA_LINE])
        line, line_d = sb("line", [HPG, 3, BANK]), sb("line_dsa", [DSA_H, DSA_LINE])
        loaded, product, kept, out = add_sems(nc, "hot_loaded", "lines_product", "lines_kept", "lines_out")
        block = ctx.enter_context(nc.Block())

        @block.sync
        def _(sp):
            for g, (at, n) in enumerate(LINES):
                sp.dma_start(hot[:, at:at + n], S.c[f"line{g}"]).then_inc(loaded, 16)
            sp.dma_start(hot_d[:, :], S.c["line_dsa"]).then_inc(loaded, 16)
            sp.wait_ge(kept, 2)
            for g, (at, n) in enumerate(LINES):
                sp.dma_start(S.ab_line[:, at:at + n], line[:, g, 0:n]).then_inc(out, 16)
            sp.dma_start(S.dsa_line, line_d[:, :]).then_inc(out, 16)
            sp.wait_ge(out, 64)
            for h in range(HPG):
                sp.dma_start(S.ab_copies[h], S.ab_line[h:h + 1, :].broadcast_to([P, AB_LINE])).then_inc(S.ab_lines, 16)
            for h in range(DSA_H):
                sp.dma_start(S.dsa_copies[h], S.dsa_line[h:h + 1, :].broadcast_to([P, DSA_LINE])).then_inc(S.dsa_lines, 16)

        @block.tensor
        def _(pe):
            pe.wait_ge(loaded, 64)
            for g, (at, n) in enumerate(LINES):
                last = pe.matmul(S.ps[0:HPG, g * BANK:g * BANK + n], S.tab[:, g * HPG:(g + 1) * HPG], hot[:, at:at + n], start=True, stop=True)
            for at in range(0, DSA_LINE, BANK):
                n = min(BANK, DSA_LINE - at)
                last = pe.matmul(S.ps[0:DSA_H, 1536 + at:1536 + at + n], S.tab[:, 12:12 + DSA_H], hot_d[:, at:at + n], start=True, stop=True)
            last.then_inc(product, 1)

        @block.vector
        def _(dve):
            dve.wait_ge(product, 1)
            for g, (at, n) in enumerate(LINES):
                last = dve.tensor_copy(line[:, g, 0:n], S.ps[0:HPG, g * BANK:g * BANK + n])
            last.then_inc(kept, 1)
            dve.tensor_copy(line_d[:, :], S.ps[0:DSA_H, 1536:1536 + DSA_LINE]).then_inc(kept, 1)


def toeplitz(copies, line, at, heads, step, n):
    return bass.AP(copies.tensor, heads.start * P * line + at + P - 1, [[line - 1, P], [step * P * line, (heads.stop - heads.start) // step], [1, n]])


U_PROMPT = HIST + SEQ
U_SEQ = HIST + L_NEW
U_LEN = U_PROMPT + N_SEQ * U_SEQ


def glu_products(nc, S, uT, taps, scratch):
    with ExitStack() as ctx:
        W = Weights(nc, ctx, "glu")
        gate = scratch[:, 0, :]
        hist = scratch[0:120, 1, 0:2 * CONV_CH].rearrange("p (a c) -> p a c", a=2)
        tap_rows = scratch[0:TAPS, 2, 0:CONV_CH]
        hist_loaded, turned, placed = add_sems(nc, "hist_loaded", "hist_turned", "hist_placed")
        w = S.d["w_in_ab"][0]
        us = uT[:, :, U_PROMPT:].rearrange("p c (n u) -> p c n u", n=N_SEQ)
        turn = S.ps[:, 3072:3584]
        in_third = SEQ - 2 * PIECE
        block = ctx.enter_context(nc.Block())

        @block.sync
        def _(sp):
            for half in range(2):
                sp.dma_start(hist[:, half, :], S.d["state_conv"][0, 4 * half:4 * half + 4].rearrange("n r c -> (n r) c")).then_inc(hist_loaded, 16)
            sp.dma_start(tap_rows, S.d["conv_w"][0]).then_inc(hist_loaded, 16)
            load_weight_pairs(sp, W, KD, CC, w_cols(w, CONV_CH), w_cols(w, 0))

        @block.tensor
        def _(pe):
            pe.wait_ge(hist_loaded, 48)
            for c in range(CC):
                last = pe.transpose(turn[:, 256 + c * TAPS:256 + (c + 1) * TAPS], tap_rows[:, c * P:(c + 1) * P], S.ident[0:TAPS, 0:TAPS])
            last.then_inc(turned, 1)
            for c in range(CC):
                pe.wait_ge(placed, 2 * c + 1)
                for half in range(2):
                    last = pe.transpose(turn[:, 120 * half:120 * half + 120], hist[:, half, c * P:(c + 1) * P], S.ident[0:120, 0:120])
                last.then_inc(turned, 1)
            multiply_pairs(pe, S, W, KD, CC, S.h)

        @block.scalar
        def _(act):
            def sigmoid(i):
                act.wait_ge(W.product[0], i + 2)
                act.wait_ge(W.free[1], i + 1)
                act.activation(by3(gate), slot(S, 0), ACT.Sigmoid).then_inc(W.free[0], 1)

            act.sem_inc(W.free[0], 1)
            for j in range(2):
                W.high(act, j, 1, KD)
            with act.Fori(0, CC - 1) as i:
                W.high(act, 0, i + 2, KD)
                sigmoid(i)
                W.high(act, 1, i + 2, KD)
            sigmoid(CC - 1)

        @block.vector
        def _(dve):
            def glu(i):
                dve.wait_ge(W.product[1], i + 2)
                dve.wait_ge(W.free[0], i + 2)
                dve.tensor_tensor(us[:, bass.ds(i, 1), :, HIST:].rearrange("p a n u -> p (a n) u"),
                                  S.ps[:, 1536 + 2 * BANK + in_third:1536 + 2 * BANK + PIECE].rearrange("p (n u) -> p n u", n=N_SEQ),
                                  gate[:, SEQ:T].rearrange("p (n u) -> p n u", n=N_SEQ), ALU.mult)
                u = uT[:, bass.ds(i, 1), HIST:U_PROMPT].rearrange("p a t -> p (a t)")
                dve.tensor_tensor(u[:, 2 * PIECE:SEQ], S.ps[:, 1536 + 2 * BANK:1536 + 2 * BANK + in_third], gate[:, 2 * PIECE:SEQ], ALU.mult)
                dve.tensor_tensor(u[:, 0:2 * PIECE].rearrange("p (c t) -> p c t", c=2), slot(S, 1)[:, 0:2, :],
                                  gate[:, 0:2 * PIECE].rearrange("p (c t) -> p c t", c=2), ALU.mult).then_inc(W.free[1], 1)

            for j in range(2):
                dve.sem_inc(W.lo_made[j], 1)
                W.low(dve, j, 1, KD)
            dve.memset(uT[:, :, 0:HIST], 0.0)
            dve.wait_ge(turned, 1)
            dve.tensor_copy(taps[:, :, :], turn[:, 256:256 + CC * TAPS].rearrange("p (c t) -> p c t", c=CC)).then_inc(placed, 1)
            for c in range(CC):
                dve.wait_ge(turned, c + 2)
                for half in range(2):
                    dve.tensor_copy(us[:, c, 4 * half:4 * half + 4, 0:HIST],
                                    turn[:, 120 * half:120 * half + 120].rearrange("p (n r) -> p n r", n=4)).then_inc(placed, 1)
            dve.sem_inc(W.free[1], 1)
            with dve.Fori(0, CC - 1) as i:
                W.low(dve, 0, i + 2, KD)
                W.low(dve, 1, i + 2, KD)
                glu(i)
            glu(CC - 1)


def qkv_products(nc, S, uT, taps, yT, vS, v_new):
    with ExitStack() as ctx:
        W = Weights(nc, ctx, "qk")
        conv_bias = ctx.enter_context(nc.sbuf_tensor("conv_bias", [P, CC], F32))
        v_product, v_kept, bias_loaded, conv_step = add_sems(nc, "v_product", "v_kept", "bias_loaded", "conv_step")
        w = S.d["w_in_ab"][0]
        vps = S.ps[:, 3072:4096].rearrange("p (b c) -> p b c", b=2)
        us = uT[:, :, U_PROMPT:].rearrange("p c (n u) -> p c n u", n=N_SEQ)
        QK_PAIRS, V_PAIRS = 6, 3
        block = ctx.enter_context(nc.Block())

        @block.sync
        def _(sp):
            sp.dma_start(conv_bias[:, :], S.d["conv_b"][0].rearrange("(c p) -> p c", p=P)).then_inc(bias_loaded, 16)
            load_weight_pairs(sp, W, KD, QK_PAIRS + V_PAIRS, *w_pairs(w, 2 * CONV_CH))

        @block.tensor
        def _(pe):
            multiply_pairs(pe, S, W, KD, QK_PAIRS, S.h)
            value_products(pe, S, W, vps, v_product, v_kept, V_PAIRS, QK_PAIRS,
                           lambda g, b, line: block_tokens(g, b, line[:, 0:SEQ]) if b < QT else line[:, SEQ:T])

        @block.scalar
        def _(act):
            def keep(i):
                for j in range(2):
                    act.wait_ge(W.product[j], i + 2)
                    act.activation(S.qk[:, bass.ds(i * 2 + j, 1), :].rearrange("p a (c t) -> p (a c) t", c=3), slot(S, j), ACT.Copy).then_inc(W.free[j], 1)
                    W.high(act, j, i + 2, KD)

            for j in range(2):
                act.sem_inc(W.free[j], 1)
                W.high(act, j, 1, KD)
            with act.Fori(0, QK_PAIRS - 1) as i:
                keep(i)
            keep(QK_PAIRS - 1)
            keep_values(act, W, vps, lambda g, b: vS[:, g, b, :] if b < QT else v_new[:, g, :], v_product, v_kept, V_PAIRS, QK_PAIRS)

        @block.gpsimd
        def _(pool):
            for j in range(2):
                pool.sem_inc(W.lo_made[j], 1)
            with pool.Fori(1, QK_PAIRS + V_PAIRS + 1) as n:
                for j in range(2):
                    W.low(pool, j, n, KD)

        @block.vector
        def _(dve):
            ysmp = yT[:, :, SEQ:T].rearrange("p c (n l) -> p c n l", n=N_SEQ)
            dve.wait_ge(bias_loaded, 16)
            for c in range(CC):
                dve.tensor_scalar(yT[:, c, 0:SEQ], uT[:, c, 0:SEQ], taps[:, c, 0:1], conv_bias[:, c:c + 1], ALU.mult, ALU.add).then_inc(conv_step, 1)
                dve.tensor_scalar(ysmp[:, c], us[:, c, :, 0:L_NEW], taps[:, c, 0:1], conv_bias[:, c:c + 1], ALU.mult, ALU.add).then_inc(conv_step, 1)
            with dve.Fori(1, TAPS) as t:
                for c in range(CC):
                    dve.wait_ge(conv_step, t * (2 * CC) + (2 * c + 2 - 2 * CC))
                    dve.scalar_tensor_tensor(yT[:, c, 0:SEQ], uT[:, c, bass.ds(t, SEQ)], taps[:, c, bass.ds(t, 1)], yT[:, c, 0:SEQ],
                                             ALU.mult, ALU.add).then_inc(conv_step, 1)
                    dve.scalar_tensor_tensor(ysmp[:, c], us[:, c, :, bass.ds(t, L_NEW)], taps[:, c, bass.ds(t, 1)], ysmp[:, c],
                                             ALU.mult, ALU.add).then_inc(conv_step, 1)


def value_products(pe, S, W, vps, product, kept, groups, before, tokens):
    for n in range(groups * (QT + 1)):
        g, b = divmod(n, QT + 1)
        if b == 0:
            for j in range(2):
                pe.wait_ge(W.lo_made[j], before + g + 2)
        if n >= 2:
            pe.wait_ge(kept, n - 1)
        m = P if b < QT else TS
        for k in range(KD):
            for i, (x, w) in enumerate(passes(S.h, W.parts)):
                last = pe.matmul(vps[0:m, n % 2, 0:GW], tokens(g, b, x[:, k, :]), w[:, k].rearrange("p j c -> p (j c)"),
                                 start=k == 0 and i == 0, stop=k == KD - 1 and i == 2)
        last.then_inc(product, 1)


def keep_values(act, W, vps, dst, product, kept, groups, before):
    for n in range(groups * (QT + 1)):
        g, b = divmod(n, QT + 1)
        act.wait_ge(product, n + 1)
        if b == QT and g + 1 < groups:
            for j in range(2):
                act.wait_ge(W.loaded[j], 16 * (before + g + 2))
                act.activation(W.parts.hi[:, :, j, :], W.raw[:, :, j, :], ACT.Copy).then_inc(W.hi_made[j], 1)
        m = P if b < QT else TS
        act.activation(dst(g, b)[0:m], vps[0:m, n % 2, 0:GW], ACT.Copy).then_inc(kept, 1)


def block_tokens(g, b, line):
    if g == 0:
        return line[:, b * P:(b + 1) * P]
    if g == 1:
        r, half = b // 2, b % 2
        return line.rearrange("p (j r) -> p r j", r=4)[:, r, half * P:(half + 1) * P]
    return line.rearrange("p (j r) -> p r j", r=8)[:, b, :]


def block_keys(g, b, line):
    if g == 0 and b:
        return line[:, (b - 1) * P:(b + 1) * P]
    if g == 1 and b % 2:
        return line.rearrange("p (j r) -> p r j", r=4)[:, b // 2, :]
    return block_tokens(g, b, line)


def has_previous(g, b):
    return (g == 0 and b > 0) or (g == 1 and b % 2 == 1)


def dram_rows(g, b, rows):
    if g == 0:
        return rows[b * P:(b + 1) * P, :]
    if g == 1:
        return rows.rearrange("(j r) x -> r j x", r=4)[b // 2, (b % 2) * P:(b % 2 + 1) * P, :]
    return rows.rearrange("(j r) x -> r j x", r=8)[b]


def head_norms(nc, S, tag, src, tiles, gains, ones, dim):
    n = len(tiles)
    with ExitStack() as ctx:
        sq = ctx.enter_context(nc.sbuf_tensor(f"hsq_{tag}", [P, 2, T], F32))
        rstd = ctx.enter_context(nc.sbuf_tensor(f"hrstd_{tag}", [P, 2, T], F32))
        squared, summed, logged, rstd_ready, scaled = add_sems(
            nc, *(f"{x}_{tag}" for x in ("hsquared", "hsummed", "hlogged", "hrstd_ready", "hscaled")))
        block = ctx.enter_context(nc.Block())

        @block.scalar
        def _(act):
            def square(i):
                if i >= 2:
                    act.wait_ge(summed, i - 1)
                act.activation(sq[:, i % 2, :], src[:, tiles[i], :], ACT.Square).then_inc(squared, 1)

            square(0)
            for i in range(n):
                if i + 1 < n:
                    square(i + 1)
                act.wait_ge(summed, i + 1)
                if i >= 2:
                    act.wait_ge(scaled, i - 1)
                act.activation(by3(rstd[:, i % 2, :]), slot(S, i % 2), ACT.Ln, scale=1.0 / dim, bias=S.eps[:, :]).then_inc(logged, 1)
                act.wait_ge(logged, i + 1)
                act.activation(rstd[:, i % 2, :], rstd[:, i % 2, :], ACT.Exp, scale=-0.5).then_inc(rstd_ready, 1)

        @block.tensor
        def _(pe):
            for i in range(n):
                pe.wait_ge(squared, i + 1)
                if i >= 2:
                    pe.wait_ge(logged, i - 1)
                for at, t, m in PIECES:
                    last = pe.matmul(S.ps[:, (i % 2) * 1536 + at:(i % 2) * 1536 + at + m], ones[:, :], sq[:, i % 2, t:t + m],
                                     start=True, stop=True)
                last.then_inc(summed, 1)

        @block.vector
        def _(dve):
            for i in range(n):
                dve.wait_ge(rstd_ready, i + 1)
                dve.scalar_tensor_tensor(src[:, tiles[i], :], src[:, tiles[i], :], gains[i], rstd[:, i % 2, :],
                                         ALU.mult, ALU.mult).then_inc(scaled, 1)


def turn_and_store(nc, S, tag, jobs, direct):
    with ExitStack() as ctx:
        stage = ctx.enter_context(nc.sbuf_tensor(f"turn_stage_{tag}", [P, 4, 512], F32))
        turned, copied, rows_out = add_sems(nc, f"turned_{tag}", f"turn_copied_{tag}", f"direct_out_{tag}")
        stored = add_sems(nc, *(f"turn_stored{i}_{tag}" for i in range(4)))
        stores_before = lambda i: sum(len(jobs[j][2]) for j in range(i % 4, i, 4))
        block = ctx.enter_context(nc.Block())

        @block.tensor
        def _(pe):
            for i, (tiles, n, _) in enumerate(jobs):
                if i >= 2:
                    pe.wait_ge(copied, i - 1)
                for f, tile in enumerate(tiles):
                    last = pe.transpose(S.ps[0:n, (i % 2) * BANK + f * P:(i % 2) * BANK + (f + 1) * P], tile, S.ident[:, :])
                last.then_inc(turned, 1)

        @block.vector
        def _(dve):
            for i, (tiles, n, _) in enumerate(jobs):
                dve.wait_ge(turned, i + 1)
                if i >= 4:
                    dve.wait_ge(stored[i % 4], 16 * stores_before(i))
                dve.tensor_copy(stage[0:n, i % 4, 0:P * len(tiles)], S.ps[0:n, (i % 2) * BANK:(i % 2) * BANK + P * len(tiles)]).then_inc(copied, 1)

        @block.sync
        def _(sp):
            for i, (tiles, n, outs) in enumerate(jobs):
                sp.wait_ge(copied, i + 1)
                for first, end, width, dst in outs:
                    sp.dma_start(dst, stage[first:end, i % 4, 0:width]).then_inc(stored[i % 4], 16)
            for s in range(4):
                sp.wait_ge(stored[s], 16 * stores_before(len(jobs) + (s - len(jobs)) % 4))

        @block.scalar
        def _(act):
            for dst, src in direct:
                act.dma_start(dst, src).then_inc(rows_out, 16)
            act.wait_ge(rows_out, 16 * len(direct))


def layer0_states(nc, S, uT, vS, v_new, q_rows, k_rows, v_rows):
    o = S.o
    jobs = []
    jobs.append(([uT[:, c, U_PROMPT - HIST:U_PROMPT] for c in range(CC)], HIST, [(0, HIST, 512, o["conv_p"][0, 0])]))
    for n0 in range(0, N_SEQ, 3):
        ns = min(3, N_SEQ - n0)
        at = U_PROMPT + n0 * U_SEQ
        jobs.append(([uT[:, c, at:at + ns * U_SEQ] for c in range(CC)], ns * U_SEQ,
                     [(i * U_SEQ + L_NEW, (i + 1) * U_SEQ, 512, o["conv_s"][0, n0 + i]) for i in range(ns)]))
    for src, dst in ((0, q_rows), (6, k_rows)):
        jobs.append(([S.qk[:, src + f, SEQ:T] for f in range(4)], TS, [(0, TS, 512, dst[:, 0:512])]))
        jobs.append(([S.qk[:, src + f, SEQ:T] for f in range(4, 6)], TS, [(0, TS, 256, dst[:, 512:768])]))
    for g, name in enumerate(("win128_p", "win512_p", "win2048_p")):
        keep = min(WINDOWS[g], SEQ)
        rows = o[name][0, 0].rearrange("t a h d -> t a (h d)")
        for t in range(keep // P):
            at = SEQ - keep + t * P
            jobs.append(([S.qk[:, 6 + 2 * g + f, at:at + P] for f in range(2)], P, [(0, P, 256, rows[t * P:(t + 1) * P, 0, :])]))
    direct = [(v_rows.rearrange("t (g x) -> t g x", g=3), v_new[:, :, :])]
    for g, name in enumerate(("win128_p", "win512_p", "win2048_p")):
        rows = o[name][0, 0].rearrange("t a h d -> t a (h d)")
        if g == 0:
            direct.append((rows[:, 1, :], vS[:, 0, QT - 1, :]))
        elif g == 1:
            direct += [(rows.rearrange("(j r) a x -> r j a x", r=4)[r, :, 1, :], vS[:, 1, 2 * r + 1, :]) for r in range(4)]
        else:
            direct += [(rows.rearrange("(j r) a x -> r j a x", r=8)[r, :, 1, :], vS[:, 2, r, :]) for r in range(8)]
    for g, name in enumerate(("win128_s", "win512_s", "win2048_s")):
        cache = S.d[("cache_win128", "cache_win512", "cache_win2048")[g]][0]
        old = cache.shape[1]
        keep = min(WINDOWS[g], old + L_NEW)
        direct.append((o[name][0, :, 0:keep - L_NEW].rearrange("n t a h d -> n t (a h d)"),
                       cache[:, old - (keep - L_NEW):old].rearrange("n t a h d -> n t (a h d)")))
    turn_and_store(nc, S, "ab", jobs, direct)

    with ExitStack() as ctx:
        (new_rows,) = add_sems(nc, "new_rows_out")
        block = ctx.enter_context(nc.Block())

        @block.sync
        def _(sp):
            count = 0
            for g, name in enumerate(("win128_s", "win512_s", "win2048_s")):
                out = o[name][0].rearrange("n t a h d -> n t a (h d)")
                keep = out.shape[1]
                for a, rows in ((0, k_rows), (1, v_rows)):
                    sp.dma_start(out[:, keep - L_NEW:keep, a, :], rows[:, g * GW:(g + 1) * GW].rearrange("(n l) x -> n l x", n=N_SEQ)).then_inc(new_rows, 16)
                    count += 1
            sp.wait_ge(new_rows, 16 * count)


def dilated_prompt(nc, S, vS):
    with ExitStack() as ctx:
        sb = lambda n, s: ctx.enter_context(nc.sbuf_tensor(n, s, F32))
        toep = sb("toep", [P, 3, HPG, 256])
        sc = sb("sc", [P, 2, HPG, 256])
        pT = sb("pT", [P, 2, HPG, 256])
        row = sb("part_row", [P, 2, HPG, HEAD_ROW])
        toep_in, scored, biased, row_in = add_sems(nc, "toep_in", "scored", "biased", "maxima_ready")
        exps, turned, kept, summed, sums_copied = add_sems(nc, "exps_done", "probs_turned", "probs_kept", "pv_summed", "sums_copied")
        stored = add_sems(nc, "part_stored0", "part_stored1")
        s_ps = S.ps[:, 0:1024].rearrange("p (h k) -> p h k", h=HPG)
        t_ps = S.ps[:, 1024:3072].rearrange("p (b h k) -> p b h k", b=2, h=HPG)
        o_ps = S.ps[:, 3072:4096].rearrange("p (b c) -> p b c", b=2)
        blocks = [(g, b) for g in range(3) for b in range(QT)]
        place = lambda h: 2 * (h % 2) + h // 2
        block = ctx.enter_context(nc.Block())

        @block.sync
        def _(sp):
            sp.wait_ge(S.ab_lines, 16 * HPG)
            for g, n in enumerate((256, 256, P)):
                for odd in range(2):
                    sp.dma_start(toep[:, g, 2 * odd:2 * odd + 2, 0:n],
                                 toeplitz(S.ab_copies, AB_LINE, LINES[g][0], slice(odd, odd + 4), 2, n)).then_inc(toep_in, 16)
            for i, (g, b) in enumerate(blocks):
                sp.wait_ge(sums_copied, i + 1)
                sp.wait_ge(exps, i + 1)
                dst = dram_rows(g, b, S.part_rows[g, 0:SEQ].rearrange("t h x -> t (h x)"))
                sp.dma_start(dst, row[:, i % 2, :, :].rearrange("p h x -> p (h x)")).then_inc(stored[i % 2], 16)
            for j in range(2):
                sp.wait_ge(stored[j], 16 * len(blocks) // 2)

        @block.tensor
        def _(pe):
            def scores(i):
                g, b = blocks[i]
                nk = 256 if has_previous(g, b) else P
                if i:
                    pe.wait_ge(biased, i)
                for h in range(HPG):
                    f, base = 2 * g + h // 2, DH * (h % 2)
                    last = pe.matmul(s_ps[:, place(h), 0:nk], block_tokens(g, b, S.qk[base:base + DH, f, 0:SEQ]),
                                     block_keys(g, b, S.qk[base:base + DH, 6 + f, 0:SEQ]), start=True, stop=True)
                last.then_inc(scored, 1)

            scores(0)
            for i, (g, b) in enumerate(blocks):
                if i + 1 < len(blocks):
                    scores(i + 1)
                pe.wait_ge(exps, i + 1)
                if i >= 2:
                    pe.wait_ge(kept, i - 1)
                kts = 2 if has_previous(g, b) else 1
                for h in range(HPG):
                    for kt in range(kts):
                        last = pe.transpose(t_ps[:, i % 2, h, kt * P:(kt + 1) * P], sc[:, i % 2, place(h), kt * P:(kt + 1) * P], S.ident[:, :])
                last.then_inc(turned, 1)
                pe.wait_ge(kept, i + 1)
                if i >= 2:
                    pe.wait_ge(sums_copied, i - 1)
                for h in range(HPG):
                    for kt in range(kts):
                        v = vS[:, g, b - (kts - 1) + kt, h * DH:(h + 1) * DH]
                        last = pe.matmul(o_ps[:, i % 2, h * DH:(h + 1) * DH], pT[:, i % 2, h, kt * P:(kt + 1) * P], v,
                                         start=kt == 0, stop=kt == kts - 1)
                last.then_inc(summed, 1)

        @block.vector
        def _(dve):
            def copy_sums(i):
                dve.wait_ge(summed, i + 1)
                dve.tensor_copy(row[:, i % 2, :, 0:DH], o_ps[:, i % 2, 0:GW].rearrange("p (h d) -> p h d", h=HPG)).then_inc(sums_copied, 1)

            dve.wait_ge(toep_in, 96)
            for i, (g, b) in enumerate(blocks):
                nk = 256 if has_previous(g, b) else P
                off = 0 if nk == 256 or g == 2 else P
                dve.wait_ge(scored, i + 1)
                if i >= 2:
                    dve.wait_ge(turned, i - 1)
                dve.scalar_tensor_tensor(sc[:, i % 2, :, 0:nk], s_ps[:, :, 0:nk], DH ** -0.5, toep[:, g, :, off:off + nk],
                                         ALU.mult, ALU.add).then_inc(biased, 1)
                dve.wait_ge(biased, i + 1)
                if i >= 2:
                    dve.wait_ge(stored[i % 2], 16 * (i // 2))
                dve.tensor_reduce(row[:, i % 2, :, AT_M].rearrange("p (b a) -> p a b", a=2), sc[:, i % 2, :, 0:nk], AX.X, ALU.max, negate=True).then_inc(row_in, 1)
                if i >= 1:
                    copy_sums(i - 1)
            copy_sums(len(blocks) - 1)

        @block.scalar
        def _(act):
            for i, (g, b) in enumerate(blocks):
                kts = 2 if has_previous(g, b) else 1
                act.wait_ge(row_in, i + 1)
                for h in range(HPG):
                    last = act.activation(sc[:, i % 2, place(h), 0:kts * P], sc[:, i % 2, place(h), 0:kts * P], ACT.Exp,
                                          bias=row[:, i % 2, h, AT_M:AT_M + 1], accum_out=row[:, i % 2, h, AT_L:AT_L + 1])
                    if h == HPG - 1:
                        last.then_inc(exps, 1)
                act.wait_ge(turned, i + 1)
                if i >= 2:
                    act.wait_ge(summed, i - 1)
                act.activation(pT[:, i % 2, :, 0:kts * P], t_ps[:, i % 2, :, 0:kts * P], ACT.Copy).then_inc(kept, 1)


def dilated_sample(nc, S, g, q_rows, v_rows_sb):
    nk = 64 if g == 2 else P
    dil = DILS[g]
    cache = S.d[("cache_win128", "cache_win512", "cache_win2048")[g]][0]
    with ExitStack() as ctx:
        tag = f"g{g}"
        sb = lambda n, s: ctx.enter_context(nc.sbuf_tensor(f"{n}_{tag}", s, F32))
        lk = 1 if g == 0 else L_NEW
        HN = N_SEQ // 2
        kt = sb("kt", [nk, HN, lk, GW])
        vt = sb("vt", [nk, N_SEQ, lk, GW])
        qb = sb("qb", [nk, HN, L_NEW, GW])
        hot = sb("shot", [NB, L_NEW, nk + TS])
        tabr = sb("tabr", [NB, L_NEW, P])
        other = sb("other", [P, TS])
        fh = sb("fh", [P, 2, HPG])
        rh = sb("rh", [P, HPG])
        qx = sb("qx", [P, 2, P])
        cs = sb("cs", [nk, P])
        bias = sb("bias", [P, nk + TS])
        sc = sb("ssc", [P, nk + TS])
        pT = sb("spT", [P, 2, P])
        oT = sb("soT", [DH, P])
        new = sb("snew", [P, HPG, DH])
        row = sb("srow", [P, HEAD_ROW])
        u, neg_max, sum_p = row[:, 0:DH], row[:, AT_M:AT_M + 1], row[:, AT_L:AT_L + 1]
        cin, kin, qin, vin, step, pstep, astep, out_done, others_masked = add_sems(
            nc, *(f"{x}_{tag}" for x in ("consts_in", "keys_in", "queries_in", "values_in", "vector_step", "tensor_step", "exps_step", "rows_out", "others_masked")))
        block = ctx.enter_context(nc.Block())
        b_ps = S.ps[:, 0:nk + TS]
        s_ps = S.ps[:, 512:512 + nk + TS]
        t_ps = S.ps[:, 1024:1024 + 2 * P]
        o_ps = S.ps[0:DH, 1536:1536 + P]
        n_ps = S.ps[:, 2048:2048 + GW]
        u_ps = S.ps[:, 2560:2560 + DH]

        def rows_of(n, a):
            c = cache[n].rearrange("t a h d -> t a (h d)")[:, a, :]
            if g == 0:
                return c
            return c.rearrange("(j r) x -> j r x", r=dil)[:, 0:L_NEW, :]

        @block.sync
        def _(sp):
            sp.dma_start(hot[:, :, :], S.c[f"sample_hot{g}"]).then_inc(cin, 16)
            sp.dma_start(other[:, :], S.c["other_seq"]).then_inc(cin, 16)
            sp.dma_start(fh[:, :, :], S.c["feat_head"]).then_inc(cin, 16)
            sp.dma_start(rh[:, :], S.c["row_head"]).then_inc(cin, 16)
            for half in range(2):
                if half:
                    sp.wait_ge(step, 2)
                for n in range(HN):
                    sp.dma_start(kt[:, n, 0, :] if g == 0 else kt[:, n, :, :], rows_of(half * HN + n, 0)).then_inc(kin, 16)
                src = q_rows[half * HN * L_NEW:(half + 1) * HN * L_NEW, g * GW:(g + 1) * GW]
                sp.dma_start(qb[:, :, :, :].rearrange("k n l x -> k (n l) x"),
                             bass.AP(src.tensor, src.offset, [[0, nk]] + [list(x) for x in src.ap])).then_inc(qin, 16)

        @block.scalar
        def _(act):
            for n in range(N_SEQ):
                act.dma_start(vt[:, n, 0, :] if g == 0 else vt[:, n, :, :], rows_of(n, 1)).then_inc(vin, 16)
            act.wait_ge(step, 9)
            act.activation(sc[:, :], sc[:, :], ACT.Exp, bias=neg_max, accum_out=sum_p).then_inc(astep, 1)
            act.wait_ge(step, 14)
            act.wait_ge(astep, 1)
            act.dma_start(S.part_rows[g, SEQ:T].rearrange("t h x -> (t h) x"), row[:, :]).then_inc(out_done, 16)
            act.wait_ge(out_done, 16)

        @block.vector
        def _(dve):
            done = chain(dve, step)
            for half in range(2):
                dve.wait_ge(kin, 16 * HN * (half + 1))
                dve.wait_ge(qin, 16 * (half + 1))
                kk = kt[:, :, 0:1, :].broadcast_to([nk, HN, L_NEW, GW]) if g == 0 else kt[:, :, :, :]
                done(dve.tensor_tensor(qb[:, :, :, :], qb[:, :, :, :], kk, ALU.mult))
                if half == 0:
                    done(dve.tensor_reduce(cs[:, 0:64], qb[:, :, :, :].rearrange("k n l (h d) -> k (n l h) d", h=HPG), AX.X, ALU.add))
                    dve.wait_ge(cin, 64)
                    done(dve.memset(tabr[:, :, :], 0.0))
                else:
                    done(dve.tensor_reduce(cs[:, 64:128], qb[:, :, :, :].rearrange("k n l (h d) -> k (n l h) d", h=HPG), AX.X, ALU.add))
            for l in range(L_NEW):
                dve.tensor_copy(tabr[:, l, :].rearrange("b (n l h) -> b n l h", n=N_SEQ, l=L_NEW)[:, :, l, :],
                                S.tab[:, g * HPG:(g + 1) * HPG].unsqueeze(1).broadcast_to([NB, N_SEQ, HPG]))
            for f in range(2):
                ins = dve.tensor_tensor(qx[:, f, :].rearrange("p (t h) -> p t h", h=HPG),
                                        S.qk[:, 2 * g + f, SEQ:T].unsqueeze(2).broadcast_to([P, TS, HPG]),
                                        fh[:, f:f + 1, :].broadcast_to([P, TS, HPG]), ALU.mult)
            done(ins)
            dve.wait_ge(pstep, 2)
            done(dve.tensor_copy(bias[:, :], b_ps))
            done(dve.scalar_tensor_tensor(sc[:, :], s_ps, DH ** -0.5, bias[:, :], ALU.mult, ALU.add))
            dve.tensor_tensor(sc[:, nk:], sc[:, nk:], other[:, :], ALU.add).then_inc(others_masked, 1)
            dve.wait_ge(others_masked, 1)
            done(dve.tensor_reduce(neg_max, sc[:, :], AX.X, ALU.max, negate=True))
            dve.wait_ge(pstep, 3)
            dve.tensor_copy(pT[0:nk, 0, :], t_ps[0:nk, 0:P])
            done(dve.tensor_copy(pT[0:TS, 1, :], t_ps[0:TS, P:2 * P]))
            dve.wait_ge(pstep, 4)
            done(dve.tensor_copy(oT[:, :], o_ps))
            done(dve.tensor_tensor(new[:, :, :], n_ps.rearrange("p (h d) -> p h d", h=HPG),
                                   rh[:, :].unsqueeze(2).broadcast_to([P, HPG, DH]), ALU.mult))
            done(dve.tensor_reduce(u, new[:, :, :].rearrange("p h d -> p d h"), AX.X, ALU.add))
            dve.wait_ge(pstep, 5)
            done(dve.tensor_tensor(u, u, u_ps, ALU.add))

        @block.tensor
        def _(pe):
            pe.wait_ge(step, 6)
            for l in range(L_NEW):
                last = pe.matmul(b_ps, tabr[:, l, :], hot[:, l, :], start=l == 0, stop=l == L_NEW - 1)
            last.then_inc(pstep, 1)
            pe.transpose(s_ps[:, 0:nk], cs[:, :], S.ident[0:nk, 0:nk])
            for f in range(2):
                last = pe.matmul(s_ps[:, nk:], qx[:, f, :], S.qk[:, 6 + 2 * g + f, SEQ:T], start=f == 0, stop=f == 1)
            last.then_inc(pstep, 1)
            pe.wait_ge(astep, 1)
            pe.transpose(t_ps[0:nk, 0:P], sc[:, 0:nk], S.ident[:, :])
            pe.transpose(t_ps[0:TS, P:2 * P], sc[:, nk:], S.ident[:, :]).then_inc(pstep, 1)
            pe.wait_ge(step, 10)
            pe.wait_ge(vin, 16 * N_SEQ)
            pc = pT[0:nk, 0, :].rearrange("k (n l h) -> k n l h", n=N_SEQ, l=L_NEW)
            oc = o_ps.rearrange("d (n l h) -> d n l h", n=N_SEQ, l=L_NEW)
            for n in range(N_SEQ):
                for h in range(HPG):
                    if g == 0:
                        pe.matmul(oc[:, n, :, h], vt[:, n, 0, h * DH:(h + 1) * DH], pc[:, n, :, h], start=True, stop=True)
                    else:
                        for l in range(L_NEW):
                            pe.matmul(oc[:, n, l, h:h + 1], vt[:, n, l, h * DH:(h + 1) * DH], pc[:, n, l, h:h + 1], start=True, stop=True)
            pe.matmul(n_ps, pT[0:TS, 1, :], v_rows_sb[:, g, :], start=True, stop=True).then_inc(pstep, 1)
            pe.wait_ge(step, 11)
            pe.transpose(u_ps, oT[:, :], S.ident[0:DH, 0:DH]).then_inc(pstep, 1)


def combine_windows(nc, S, bT):
    with ExitStack() as ctx:
        sb = lambda n, s: ctx.enter_context(nc.sbuf_tensor(n, s, F32))
        rows = sb("cw_rows", [P, 3, 3, HPG, HEAD_ROW])
        nM = sb("cw_max", [P, HPG])
        e = sb("cw_e", [P, 2, 3, HPG])
        el = sb("cw_el", [P, 3, HPG])
        den = sb("cw_den", [P, HPG])
        b = sb("cw_b", [P, 2, GW])
        diffed, exped, mixed, turned, kept, step = add_sems(nc, *("cw_" + x for x in ("diffed", "exped", "mixed", "turned", "kept", "step")))
        loaded = add_sems(nc, "cw_loaded0", "cw_loaded1", "cw_loaded2")
        block = ctx.enter_context(nc.Block())
        N = [P] * QT + [TS]

        @block.sync
        def _(sp):
            for t, n in enumerate(N):
                if t >= 3:
                    sp.wait_ge(mixed, t - 2)
                sp.dma_start(rows[0:n, t % 3].rearrange("t g h x -> t g (h x)"),
                             S.part_rows[:, t * P:t * P + n].rearrange("g t h x -> t g (h x)")).then_inc(loaded[t % 3], 16)

        @block.vector
        def _(dve):
            done = chain(dve, step)
            for t, n in enumerate(N):
                r = rows[0:n, t % 3]
                dve.wait_ge(loaded[t % 3], 16 * (t // 3 + 1))
                m = r[:, :, :, AT_M]
                done(dve.tensor_reduce(nM[0:n, :], m.rearrange("p g h -> p h g"), AX.X, ALU.min))
                dve.tensor_tensor(e[0:n, t % 2], nM[0:n, :].unsqueeze(1).broadcast_to([n, 3, HPG]), m, ALU.subtract).then_inc(diffed, 1)
                dve.wait_ge(exped, t + 1)
                done(dve.tensor_tensor(el[0:n], e[0:n, t % 2], r[:, :, :, AT_L], ALU.mult))
                done(dve.tensor_reduce(den[0:n, :], el[0:n].rearrange("p g h -> p h g"), AX.X, ALU.add))
                done(dve.reciprocal(den[0:n, :], den[0:n, :]))
                done(dve.tensor_tensor(el[0:n], e[0:n, t % 2], den[0:n, :].unsqueeze(1).broadcast_to([n, 3, HPG]), ALU.mult))
                for g in range(3):
                    u = r[:, g, :, 0:DH]
                    ins = dve.tensor_tensor(u, u, el[0:n, g, :].unsqueeze(2).broadcast_to([n, HPG, DH]), ALU.mult)
                done(ins)
                if t >= 2:
                    dve.wait_ge(turned, t - 1)
                bt = b[0:n, t % 2, :].rearrange("p (h d) -> p h d", h=HPG)
                done(dve.tensor_tensor(bt, r[:, 0, :, 0:DH], r[:, 1, :, 0:DH], ALU.add))
                dve.tensor_tensor(bt, bt, r[:, 2, :, 0:DH], ALU.add).then_inc(mixed, 1)

        @block.tensor
        def _(pe):
            for t, n in enumerate(N):
                pe.wait_ge(mixed, t + 1)
                if t >= 2:
                    pe.wait_ge(kept, t - 1)
                for f in range(2):
                    last = pe.transpose(S.ps[:, (t % 2) * BANK + f * P:(t % 2) * BANK + f * P + n], b[0:n, t % 2, f * P:(f + 1) * P], S.ident[0:n, 0:n])
                last.then_inc(turned, 1)

        @block.scalar
        def _(act):
            for t, n in enumerate(N):
                act.wait_ge(diffed, t + 1)
                act.activation(e[0:n, t % 2], e[0:n, t % 2], ACT.Exp).then_inc(exped, 1)
                act.wait_ge(turned, t + 1)
                act.activation(bT[:, :, t * P:t * P + n],
                               S.ps[:, (t % 2) * BANK:(t % 2) * BANK + 2 * P].rearrange("p (f t) -> p f t", f=2)[:, :, 0:n], ACT.Copy).then_inc(kept, 1)


def conv_norm(nc, S, yT):
    with ExitStack() as ctx:
        sb = lambda n, s: ctx.enter_context(nc.sbuf_tensor(n, s, F32))
        sq = sb("ln_sq", [P, 2, T])
        mean = sb("ln_mean", [P, T])
        rstd = sb("ln_rstd", [P, T])
        gb = sb("ln_gb", [P, 2, CC])
        loaded, meaned, centred, squared, varied, astep, scaled, sig, done_s = add_sems(
            nc, *("ln_" + x for x in ("loaded", "meaned", "centred", "squared", "varied", "rstd_step", "scaled", "sigmoid", "mean_kept")))
        block = ctx.enter_context(nc.Block())

        @block.sync
        def _(sp):
            for i, name in enumerate(("conv_ln_g", "conv_ln_b")):
                sp.dma_start(gb[:, i, :], S.d[name][0].rearrange("(c p) -> p c", p=P)).then_inc(loaded, 16)

        @block.tensor
        def _(pe):
            for c in range(CC):
                for at, t, n in PIECES:
                    last = pe.matmul(S.ps[:, at:at + n], S.ones[:, :], yT[:, c, t:t + n], start=c == 0, stop=c == CC - 1)
            last.then_inc(meaned, 1)
            for c in range(CC):
                pe.wait_ge(squared, c + 1)
                for at, t, n in PIECES:
                    last = pe.matmul(S.ps[:, 1536 + at:1536 + at + n], S.ones[:, :], sq[:, c % 2, t:t + n], start=c == 0, stop=c == CC - 1)
                last.then_inc(varied, 1)

        @block.vector
        def _(dve):
            dve.wait_ge(meaned, 1)
            dve.tensor_scalar(by3(mean[:, :]), slot(S, 0), 1.0 / CONV_CH, None, ALU.mult).then_inc(done_s, 1)
            dve.wait_ge(done_s, 1)
            for c in range(CC):
                dve.tensor_tensor(yT[:, c, :], yT[:, c, :], mean[:, :], ALU.subtract).then_inc(centred, 1)
            dve.wait_ge(astep, 2)
            dve.wait_ge(loaded, 32)
            for c in range(CC):
                dve.wait_ge(centred, c + 1)
                dve.tensor_tensor(yT[:, c, :], yT[:, c, :], rstd[:, :], ALU.mult).then_inc(centred, 1)
                dve.wait_ge(centred, CC + c + 1)
                dve.tensor_scalar(yT[:, c, :], yT[:, c, :], gb[:, 0, c:c + 1], gb[:, 1, c:c + 1], ALU.mult, ALU.add).then_inc(scaled, 1)
            for c in range(CC):
                dve.wait_ge(sig, c + 1)
                dve.tensor_tensor(yT[:, c, :], yT[:, c, :], sq[:, c % 2, :], ALU.mult).then_inc(scaled, 1)

        @block.scalar
        def _(act):
            for c in range(CC):
                act.wait_ge(centred, c + 1)
                if c >= 2:
                    act.wait_ge(varied, c - 1)
                act.activation(sq[:, c % 2, :], yT[:, c, :], ACT.Square).then_inc(squared, 1)
            act.wait_ge(varied, CC)
            act.activation(by3(rstd[:, :]), slot(S, 1), ACT.Ln, scale=1.0 / CONV_CH, bias=S.eps[:, :]).then_inc(astep, 1)
            act.wait_ge(astep, 1)
            act.activation(rstd[:, :], rstd[:, :], ACT.Exp, scale=-0.5).then_inc(astep, 1)
            for c in range(CC):
                act.wait_ge(scaled, c + 1 if c < 2 else CC + c - 1)
                act.activation(sq[:, c % 2, :], yT[:, c, :], ACT.Sigmoid).then_inc(sig, 1)


def project_back(nc, S, tag, w, kt, operand):
    with ExitStack() as ctx:
        S.h = Parts(nc, ctx, f"operand_{tag}", [kt, T])
        W = Weights(nc, ctx, tag)
        hi_made, lo_made, x_in = add_sems(nc, *(f"{x}_{tag}" for x in ("operand_hi_made", "operand_lo_made", "x_in")))
        block = ctx.enter_context(nc.Block())
        PAIRS = KD // 2
        v = w.rearrange("(k p) m -> p k m", p=P)

        @block.sync
        def _(sp):
            for j in range(2):
                W.load(sp, j, 1, kt, v[:, 0:kt, j * P:(j + 1) * P])
            sp.wait_ge(lo_made, kt)
            sp.dma_start(S.xT, S.x_spill).then_inc(x_in, 16)
            load_weight_pairs(sp, W, kt, PAIRS - 1, *w_pairs(w, 2 * P), before=1)

        @block.tensor
        def _(pe):
            multiply_pairs(pe, S, W, kt, PAIRS, S.h, made=(lo_made, 0))

        @block.scalar
        def _(act):
            for k in range(kt):
                act.activation(S.h.hi[:, k, :], operand(k), ACT.Copy).then_inc(hi_made, 1)
                if k < 2:
                    W.high(act, k, 1, kt)
            with act.Fori(0, PAIRS - 1) as i:
                for j in range(2):
                    W.high(act, j, i + 2, kt)

        @block.vector
        def _(dve):
            def add(i, j):
                dve.wait_ge(W.product[j], i + 2)
                x = S.xT[:, bass.ds(i * 2 + j, 1), :].rearrange("p a (c t) -> p (a c) t", c=3)
                dve.tensor_tensor(x, x, slot(S, j), ALU.add).then_inc(W.free[j], 1)

            for j in range(2):
                dve.sem_inc(W.free[j], 1)
                dve.sem_inc(W.lo_made[j], 1)
            for k in range(kt):
                dve.wait_ge(hi_made, k + 1)
                dve.tensor_tensor(S.h.lo[:, k, :], operand(k), S.h.hi[:, k, :], ALU.subtract).then_inc(lo_made, 1)
                if k < 2:
                    W.low(dve, k, 1, kt)
            dve.wait_ge(x_in, 16)
            with dve.Fori(0, PAIRS - 1) as i:
                for j in range(2):
                    add(i, j)
                    W.low(dve, j, i + 2, kt)
            for j in range(2):
                add(PAIRS - 1, j)


def ffn(nc, S, layer):
    RUNS = ((0, 8), (8, 7), (15, 7))
    PAIRS = KD // 2
    with ExitStack() as ctx:
        tag = f"ffn{layer}"
        S.h = Parts(nc, ctx, f"h_{tag}", [KD, T])
        with nc.sbuf_tensor(f"norm_{tag}", [P, 5, T], F32) as scratch:
            rms_norm(nc, S, tag, S.g_ffn[:, layer, :], S.xT, S.h, scratch)
        hidden = Parts(nc, ctx, f"hidden_{tag}", [KD, T])
        W = Weights(nc, ctx, tag)
        gate, whole = S.home[:, KD, :], S.home[:, KD + 1, :]
        sigmoid_made, hi_made, lo_made = add_sems(nc, *(f"{x}_{tag}" for x in ("sigmoid_made", "hidden_hi_made", "hidden_lo_made")))
        w_gate, w_up, w_down = (S.d[n][layer].rearrange("(k p) m -> p k m", p=P) for n in ("w_ffn_gate", "w_ffn_up", "w_ffn_down"))
        block = ctx.enter_context(nc.Block())

        @block.sync
        def _(sp):
            before = 0
            for first, tiles in RUNS:
                load_weight_pairs(sp, W, KD, tiles, (w_gate, P, first * P), (w_up, P, first * P), before)
                rows = w_down[:, first:first + tiles, :]
                load_weight_pairs(sp, W, tiles, PAIRS, (rows, 2 * P, 0), (rows, 2 * P, P), before + tiles)
                before += tiles + PAIRS

        @block.tensor
        def _(pe):
            before = 0
            for first, tiles in RUNS:
                multiply_pairs(pe, S, W, KD, tiles, S.h, before)
                multiply_pairs(pe, S, W, tiles, PAIRS, hidden, before + tiles, made=(lo_made, first + 1))
                before += tiles + PAIRS

        @block.scalar
        def _(act):
            def tile_of_hidden(i, before, first, next_kt):
                W.high(act, 0, i + (before + 2), next_kt)
                act.wait_ge(W.product[0], i + (before + 2))
                act.wait_ge(W.free[1], i + (before + 1))
                act.activation(by3(gate), slot(S, 0), ACT.Sigmoid).then_inc(sigmoid_made, 1)
                W.high(act, 1, i + (before + 2), next_kt)
                act.wait_ge(W.free[1], i + (before + 2))
                act.activation(hidden.hi[:, bass.ds(i, 1), :].rearrange("p a t -> p (a t)"), whole, ACT.Copy).then_inc(hi_made, 1)

            for j in range(2):
                W.high(act, j, 1, KD)
            before = 0
            for first, tiles in RUNS:
                with act.Fori(0, tiles - 1) as i:
                    tile_of_hidden(i, before, first, KD)
                tile_of_hidden(tiles - 1, before, first, tiles)
                before += tiles
                with act.Fori(0, PAIRS - 1) as i:
                    for j in range(2):
                        W.high(act, j, i + (before + 2), tiles)
                before += PAIRS
                if (first, tiles) != RUNS[-1]:
                    for j in range(2):
                        W.high(act, j, before + 1, KD)

        @block.vector
        def _(dve):
            def tile_of_hidden(i, before, first, next_kt):
                W.low(dve, 0, i + (before + 2), next_kt)
                dve.wait_ge(sigmoid_made, i + (first + 1))
                dve.tensor_tensor(by3(gate), by3(gate), slot(S, 0), ALU.mult).then_inc(W.free[0], 1)
                W.low(dve, 1, i + (before + 2), next_kt)
                dve.wait_ge(W.product[1], i + (before + 2))
                dve.wait_ge(W.free[0], i + (before + 2))
                dve.wait_ge(lo_made, i + (first + 1))
                dve.tensor_tensor(by3(whole), by3(gate), slot(S, 1), ALU.mult).then_inc(W.free[1], 1)
                dve.wait_ge(hi_made, i + (first + 1))
                dve.tensor_tensor(hidden.lo[:, bass.ds(i, 1), :].rearrange("p a t -> p (a t)"), whole,
                                  hidden.hi[:, bass.ds(i, 1), :].rearrange("p a t -> p (a t)"), ALU.subtract).then_inc(lo_made, 1)

            def add(i, j, before):
                dve.wait_ge(W.product[j], i + (before + 2))
                x = S.xT[:, bass.ds(i * 2 + j, 1), :].rearrange("p a (c t) -> p (a c) t", c=3)
                dve.tensor_tensor(x, x, slot(S, j), ALU.add).then_inc(W.free[j], 1)

            dve.sem_inc(lo_made, 1)
            for j in range(2):
                dve.sem_inc(W.free[j], 1)
                dve.sem_inc(W.lo_made[j], 1)
                W.low(dve, j, 1, KD)
            before = 0
            for first, tiles in RUNS:
                with dve.Fori(0, tiles - 1) as i:
                    tile_of_hidden(i, before, first, KD)
                tile_of_hidden(tiles - 1, before, first, tiles)
                before += tiles
                with dve.Fori(0, PAIRS - 1) as i:
                    for j in range(2):
                        add(i, j, before)
                        W.low(dve, j, i + (before + 2), tiles)
                for j in range(2):
                    add(PAIRS - 1, j, before)
                    if (first, tiles) != RUNS[-1]:
                        W.low(dve, j, before + PAIRS + 1, KD)
                before += PAIRS


def store_y(nc, S):
    with ExitStack() as ctx:
        rows = ctx.enter_context(nc.sbuf_tensor("y_rows", [P, 3, D_MODEL], F32))
        turned, kept = add_sems(nc, "y_turned", "y_kept")
        stored = add_sems(nc, "y_stored0", "y_stored1", "y_stored2")
        block = ctx.enter_context(nc.Block())
        N = [P] * QT + [TS]

        @block.tensor
        def _(pe):
            for t, n in enumerate(N):
                if t >= 2:
                    pe.wait_ge(kept, t - 1)
                for k in range(KD):
                    last = pe.transpose(S.ps[0:n, (t % 2) * D_MODEL + k * P:(t % 2) * D_MODEL + (k + 1) * P], S.xT[:, k, t * P:t * P + n], S.ident[:, :])
                last.then_inc(turned, 1)

        @block.vector
        def _(dve):
            for t, n in enumerate(N):
                dve.wait_ge(turned, t + 1)
                if t >= 3:
                    dve.wait_ge(stored[t % 3], 16 * (t // 3))
                dve.tensor_copy(rows[0:n, t % 3, :], S.ps[0:n, (t % 2) * D_MODEL:(t % 2 + 1) * D_MODEL]).then_inc(kept, 1)

        @block.sync
        def _(sp):
            for t, n in enumerate(N):
                sp.wait_ge(kept, t + 1)
                dst = S.o["y_prompt"][0, t * P:(t + 1) * P, :] if t < QT else S.o["y_sample"].rearrange("n l d -> (n l) d")
                sp.dma_start(dst, rows[0:n, t % 3, :]).then_inc(stored[t % 3], 16)
            for s in range(3):
                sp.wait_ge(stored[s], 48)


WORK_AT = [None, None] + [sum((t + 1) * P for t in range(2, u)) for u in range(2, QT)]
WORK = sum((t + 1) * P for t in range(2, QT))
S_KEYS = PAST + L_NEW
NEW_AT = PAST
S_COLS = PAST + TS


LR_AT = 96


def index_products(nc, S, iqT, ikT, iw, bT):
    with ExitStack() as ctx:
        W = Weights(nc, ctx, "index")
        gap_zeroed, kept, turned, rows_kept, doubled, stored = add_sems(
            nc, *("index_" + x for x in ("gap_zeroed", "key_kept", "turned", "rows_kept", "key_doubled", "kidx_stored")))
        w = S.d["w_in_cd"][0].rearrange("(k p) m -> p k m", p=P)
        KW, M = DH + IDX_H, LR_AT + GLA_RANK
        turn = S.ps[:, 3072:4096].rearrange("p (b c) -> p b c", b=2)
        block = ctx.enter_context(nc.Block())

        @block.sync
        def _(sp):
            for j in range(2):
                W.load(sp, j, 1, KD, w[:, :, IQ + j * P:IQ + (j + 1) * P])
            sp.wait_ge(gap_zeroed, 1)
            sp.dma_start(W.raw[:, :, 0, 0:KW], w[:, :, IK:IK + KW]).then_inc(W.loaded[0], 16)
            sp.dma_start(W.raw[:, :, 0, LR_AT:M], w[:, :, CLR:CLR + GLA_RANK]).then_inc(W.loaded[0], 16)
            sp.wait_ge(turned, QT + 1)
            sp.dma_start(ikT[DH:P, :], ikT[0:DH, :]).then_inc(doubled, 16)
            sp.wait_ge(rows_kept, QT + 1)
            sp.dma_start(S.o["dsa_kidx_p"][0, 0].rearrange("t p d -> p t d"), iw[:, 0:QT, 0:DH]).then_inc(stored, 16)
            sp.dma_start(S.o["dsa_kidx_s"][0].rearrange("n l d -> (n l) d"), iw[0:TS, QT, 0:DH]).then_inc(stored, 16)
            sp.wait_ge(stored, 32)
            sp.wait_ge(doubled, 16)

        @block.gpsimd
        def _(pool):
            pool.wait_ge(W.lo_made[0], 2)
            pool.memset(W.raw[:, :, 0, KW:LR_AT], 0.0).then_inc(gap_zeroed, 1)

        @block.tensor
        def _(pe):
            for n, (j, m) in enumerate(((0, P), (1, P), (0, M))):
                pe.wait_ge(W.lo_made[j], n // 2 + 2)
                if n == 2:
                    pe.wait_ge(W.free[0], 1)
                for k in range(KD):
                    for i, (wp, xp) in enumerate(passes(W.parts, S.h)):
                        for c, (at, t, size) in enumerate(PIECES):
                            last = pe.matmul(S.ps[0:m, j * 1536 + at:j * 1536 + at + size], wp[:, k, j, 0:m], xp[:, k, t:t + size],
                                             start=k == 0 and i == 0, stop=k == KD - 1 and i == 2)
                last.then_inc(W.product[j], 1)
            pe.wait_ge(kept, 1)
            for t in range(QT + 1):
                n = P if t < QT else TS
                if t >= 2:
                    pe.wait_ge(rows_kept, t - 1)
                pe.transpose(turn[0:n, t % 2, 0:KW], ikT[0:KW, t * P:t * P + n], S.ident[0:KW, 0:KW]).then_inc(turned, 1)

        @block.scalar
        def _(act):
            for j in range(2):
                W.high(act, j, 1, KD)
            act.wait_ge(W.loaded[0], 48)
            act.wait_ge(W.product[0], 2)
            act.activation(W.parts.hi[:, :, 0, 0:M], W.raw[:, :, 0, 0:M], ACT.Copy).then_inc(W.hi_made[0], 1)
            act.activation(by3(iqT[:, 0, :]), slot(S, 0), ACT.Copy).then_inc(W.free[0], 1)
            act.wait_ge(W.product[1], 2)
            act.activation(by3(iqT[:, 1, :]), slot(S, 1), ACT.Copy)
            act.wait_ge(W.product[0], 3)
            act.activation(by3(ikT[0:KW, :]), slot(S, 0)[0:KW], ACT.Copy).then_inc(kept, 1)
            act.activation(by3(bT[LR_AT:M, 1, :]), slot(S, 0)[LR_AT:M], ACT.Copy)
            for t in range(QT + 1):
                n = P if t < QT else TS
                act.wait_ge(turned, t + 1)
                act.activation(iw[0:n, t, :], turn[0:n, t % 2, 0:KW], ACT.Copy).then_inc(rows_kept, 1)

        @block.vector
        def _(dve):
            for j in range(2):
                dve.sem_inc(W.lo_made[j], 1)
                W.low(dve, j, 1, KD)
            dve.wait_ge(W.hi_made[0], 2)
            dve.tensor_tensor(W.parts.lo[:, :, 0, 0:M], W.raw[:, :, 0, 0:M], W.parts.hi[:, :, 0, 0:M], ALU.subtract).then_inc(W.lo_made[0], 1)


def index_scores_prompt(nc, S, iqT, ikT, iw, work):
    with ExitStack() as ctx:
        sb = lambda n, s: ctx.enter_context(nc.sbuf_tensor(n, s, F32))
        relu = sb("relu", [P, 2, SEQ])
        wgt = sb("head_w", [P, QT, IDX_H])
        tri = sb("tri", [P, P])
        loaded, dots, rectified, step = add_sems(nc, "tri_loaded", "dots_done", "rectified", "index_step")
        units = [(t, h) for t in range(2, QT) for h in range(IDX_H)]
        block = ctx.enter_context(nc.Block())

        @block.sync
        def _(sp):
            sp.dma_start(tri[:, :], S.c["tri"]).then_inc(loaded, 16)

        @block.tensor
        def _(pe):
            for u, (t, h) in enumerate(units):
                if u >= 4:
                    pe.wait_ge(rectified, u - 3)
                base = DH * (h % 2)
                for at in range(0, (t + 1) * P, BANK):
                    n = min(BANK, (t + 1) * P - at)
                    last = pe.matmul(S.ps[:, (u % 4) * 1024 + at:(u % 4) * 1024 + at + n], iqT[base:base + DH, h // 2, t * P:(t + 1) * P],
                                     ikT[base:base + DH, at:at + n], start=True, stop=True)
                last.then_inc(dots, 1)

        @block.scalar
        def _(act):
            for u, (t, h) in enumerate(units):
                act.wait_ge(dots, u + 1)
                if u >= 2:
                    act.wait_ge(step, u)
                act.activation(relu[:, u % 2, 0:(t + 1) * P], S.ps[:, (u % 4) * 1024:(u % 4) * 1024 + (t + 1) * P], ACT.Relu).then_inc(rectified, 1)

        @block.vector
        def _(dve):
            done = chain(dve, step)
            done(dve.tensor_scalar(wgt[:, :, :], iw[:, 0:QT, DH:DH + IDX_H], DH ** -0.5 * IDX_H ** -0.5, None, ALU.mult))
            for u, (t, h) in enumerate(units):
                n = (t + 1) * P
                dst = work[:, WORK_AT[t]:WORK_AT[t] + n]
                dve.wait_ge(rectified, u + 1)
                if h == 0:
                    done(dve.tensor_scalar(dst, relu[:, u % 2, 0:n], wgt[:, t, h:h + 1], None, ALU.mult))
                else:
                    done(dve.scalar_tensor_tensor(dst, relu[:, u % 2, 0:n], wgt[:, t, h:h + 1], dst, ALU.mult, ALU.add))
            dve.wait_ge(loaded, 16)
            for t in range(2, QT):
                own = work[:, WORK_AT[t] + t * P:WORK_AT[t] + (t + 1) * P]
                dve.tensor_tensor(own, own, tri[:, :], ALU.add)


def index_scores_sample(nc, S, iqT, ikT, iw, work_s):
    with ExitStack() as ctx:
        sb = lambda n, s: ctx.enter_context(nc.sbuf_tensor(n, s, F32))
        pages = ctx.enter_context(nc.sbuf_tensor("pages_i", [1, N_SEQ * N_PAGES], I32))
        keys = sb("kidx", [P, 4, N_PAGES, DH])
        kT = sb("kidx_T", [P, 2, 4, P])
        iqs = sb("iq_s", [P, N_SEQ, 32])
        rows = sb("index_rows", [TS, 2, P])
        wx = sb("wx", [TS, 2, P])
        wsel = sb("wsel", [P, 2, TS])
        relu = sb("relu_s", [P, S_KEYS])
        nmask = sb("new_mask", [TS, L_NEW])
        consts, table_in, spread, turned, copied, dotted, relued, wstep, summed, final = add_sems(
            nc, *("is_" + x for x in ("consts", "table_in", "queries_spread", "keys_turned", "keys_copied", "dots", "rectified",
                                      "weights_step", "summed", "kept")))
        loaded = add_sems(nc, *(f"is_loaded{i}" for i in range(4)))
        pool_keys = S.d["cache_dsa_kidx"][0]
        dots_ps = S.ps[:, 0:1536]
        sum_ps = S.ps[0:TS, 1536:3072]
        turn_ps = S.ps[:, 3072:4096].rearrange("p (b x) -> p b x", b=2)
        block = ctx.enter_context(nc.Block())

        @block.sync
        def _(sp):
            sp.dma_start(pages[:, :], S.d["page_table"].rearrange("n (a g) -> a (n g)", a=1)).then_inc(table_in, 16)
            sp.dma_start(rows[:, :, :], S.c["index_rows"]).then_inc(consts, 16)
            sp.dma_start(nmask[:, :], S.c["new_mask"]).then_inc(consts, 16)
            sp.wait_ge(table_in, 16)
            for n in range(N_SEQ):
                if n >= 4:
                    sp.wait_ge(turned, n - 3)
                for g in range(N_PAGES):
                    page = sp.value_load(pages[0:1, n * N_PAGES + g:n * N_PAGES + g + 1], min_val=0, max_val=pool_keys.shape[0] - 1)
                    sp.dma_start(keys[:, n % 4, g, :], pool_keys[bass.ds(page, 1)].rearrange("a s d -> s (a d)")).then_inc(loaded[n % 4], 16)

        @block.vector
        def _(dve):
            dve.memset(iqs[:, :, :], 0.0).then_inc(spread, 1)
            dve.wait_ge(spread, 1)
            for h in range(IDX_H):
                src = iqT[DH * (h % 2):DH * (h % 2) + DH, h // 2, SEQ:T].rearrange("p (n l) -> p n l", l=L_NEW)
                for half in range(2):
                    ins = dve.tensor_copy(iqs[half * DH:(half + 1) * DH, :, h * L_NEW:(h + 1) * L_NEW], src)
            ins.then_inc(spread, 1)
            dve.wait_ge(consts, 32)
            for g in range(2):
                for h in range(IDX_H):
                    v = lambda x: x[:, g, :].rearrange("t (n a h l) -> t n a h l", n=4, a=2, h=4)
                    ins = dve.tensor_scalar(v(wx)[:, :, :, h, :], v(rows)[:, :, :, h, :], iw[0:TS, QT, DH + h:DH + h + 1], DH ** -0.5 * IDX_H ** -0.5,
                                            ALU.mult, ALU.mult)
            ins.then_inc(wstep, 1)
            dve.wait_ge(wstep, 2)
            dve.tensor_copy(wsel[:, :, :], turn_ps[:, 0, 0:2 * TS].rearrange("p (g t) -> p g t", g=2)).then_inc(wstep, 1)
            for n in range(N_SEQ):
                dve.wait_ge(turned, n + 1)
                if n >= 2:
                    dve.wait_ge(dotted, n - 1)
                dve.tensor_copy(kT[:, n % 2, :, :], turn_ps[:, n % 2, :].rearrange("p (c s) -> p c s", c=4)).then_inc(copied, 1)
            dve.wait_ge(summed, 1)
            dve.tensor_copy(work_s[:, 0:PAST], sum_ps[:, 0:PAST])
            dve.tensor_tensor(work_s[:, PAST:S_KEYS], sum_ps[:, PAST:S_KEYS], nmask[:, :], ALU.add)

        @block.tensor
        def _(pe):
            pe.wait_ge(wstep, 1)
            for g in range(2):
                last = pe.transpose(turn_ps[:, 0, g * TS:(g + 1) * TS], wx[:, g, :], S.ident[0:TS, 0:TS])
            last.then_inc(wstep, 1)
            pe.wait_ge(wstep, 3)
            pe.wait_ge(spread, 2)

            def turn(n):
                pe.wait_ge(loaded[n % 4], 16 * N_PAGES * (n // 4 + 1))
                if n >= 2:
                    pe.wait_ge(copied, n - 1)
                for c in range(4):
                    last = pe.transpose(turn_ps[:, n % 2, c * P:(c + 1) * P], keys[:, n % 4, 2 * c:2 * c + 2, :].rearrange("s g d -> s (g d)"), S.ident[:, :])
                last.then_inc(turned, 1)

            turn(0)
            for n in range(N_SEQ):
                if n + 1 < N_SEQ:
                    turn(n + 1)
                pe.wait_ge(copied, n + 1)
                if n == 4:
                    pe.wait_ge(relued, 1)
                q = 32 * (n % 4)
                for half in range(2):
                    for c in range(4):
                        at = half * BANK + c * P
                        pe.matmul(dots_ps[q:q + 32, at:at + P], iqs[half * DH:(half + 1) * DH, n, :], kT[half * DH:(half + 1) * DH, n % 2, c, :],
                                  start=True, stop=True)
                pe.matmul(dots_ps[q:q + 32, PAST:S_KEYS], iqs[0:DH, n, :], ikT[0:DH, SEQ + n * L_NEW:SEQ + (n + 1) * L_NEW],
                          start=True, stop=True).then_inc(dotted, 1)
                if n % 4 == 3:
                    g = n // 4
                    pe.wait_ge(relued, g + 1)
                    for at, size in ((0, BANK), (BANK, BANK), (PAST, L_NEW)):
                        last = pe.matmul(sum_ps[:, at:at + size], wsel[:, g, :], relu[:, at:at + size], start=g == 0, stop=g == 1)
                    last.then_inc(summed if g else final, 1)

        @block.scalar
        def _(act):
            for g in range(2):
                act.wait_ge(dotted, 4 * g + 4)
                if g:
                    act.wait_ge(final, 1)
                act.activation(relu[:, 0:PAST].rearrange("p (c b s) -> p b c s", b=2, s=P),
                               dots_ps[:, 0:PAST].rearrange("p (b c s) -> p b c s", b=2, s=P), ACT.Relu)
                act.activation(relu[:, PAST:S_KEYS], dots_ps[:, PAST:S_KEYS], ACT.Relu).then_inc(relued, 1)


def big_products(nc, S, gT, big, gvS, work, work_s):
    with ExitStack() as ctx:
        W = Weights(nc, ctx, "cd")
        best = ctx.enter_context(nc.sbuf_tensor("best", [P, 7, 8], F32))
        tick = ctx.enter_context(nc.sbuf_tensor("tick", [1, 2], F32))
        v_product, v_kept, round_step = add_sems(nc, "cv_product", "cv_kept", "topk_step")
        w = S.d["w_in_cd"][0]
        vps = S.ps[:, 3072:4096].rearrange("p (b c) -> p b c", b=2)
        lines = [work[:, WORK_AT[t]:WORK_AT[t] + (t + 1) * P] for t in range(QT - 1, 1, -1)] + [work_s[:, :]]
        rows = [P] * 6 + [TS]
        NL = len(lines)
        block = ctx.enter_context(nc.Block())

        @block.sync
        def _(sp):
            load_weight_pairs(sp, W, KD, 2, *w_pairs(w, CQ))
            load_weight_pairs(sp, W, KD, 6, *w_pairs(w, CG), before=2)
            load_weight_pairs(sp, W, KD, 2, *w_pairs(w, CV), before=8)

        @block.tensor
        def _(pe):
            multiply_pairs(pe, S, W, KD, 2, S.h)
            multiply_pairs(pe, S, W, KD, 6, S.h, before=2)
            value_products(pe, S, W, vps, v_product, v_kept, 2, 8, token_tile)

        @block.scalar
        def _(act):
            for j in range(2):
                act.sem_inc(W.free[j], 1)
                W.high(act, j, 1, KD)
            for dst, iters, before in ((gT, 2, 0), (big, 6, 2)):
                with act.Fori(0, iters) as i:
                    for j in range(2):
                        act.wait_ge(W.product[j], i + (2 + before))
                        act.activation(dst[:, bass.ds(i * 2 + j, 1), :].rearrange("p a (c t) -> p (a c) t", c=3), slot(S, j), ACT.Copy).then_inc(W.free[j], 1)
                        W.high(act, j, i + (2 + before), KD)
            keep_values(act, W, vps, lambda g, t: gvS[:, t, g * GW:(g + 1) * GW], v_product, v_kept, 2, 8)

        @block.gpsimd
        def _(pool):
            for j in range(2):
                pool.sem_inc(W.lo_made[j], 1)
            with pool.Fori(1, 11) as n:
                for j in range(2):
                    W.low(pool, j, n, KD)

        @block.vector
        def _(dve):
            dve.memset(tick[:, :], 0.0).then_inc(round_step, NL)
            with dve.Fori(0, TOPK // 8) as i:
                dve.wait_ge(round_step, i * (2 * NL) + NL)
                dve.tensor_copy(tick[:, 0:1], tick[:, 1:2])
                for j, line in enumerate(lines):
                    dve.max(best[0:rows[j], j, :], line).then_inc(round_step, 1)
                dve.wait_ge(round_step, i * (2 * NL) + 2 * NL)
                dve.tensor_copy(tick[:, 0:1], tick[:, 1:2])
                for j, line in enumerate(lines):
                    dve.match_replace(line, best[0:rows[j], j, :], line, TAKEN).then_inc(round_step, 1)
            for j, line in enumerate(lines):
                dve.wait_ge(round_step, NL + (TOPK // 8 - 1) * 2 * NL + NL + j + 1)
                dve.tensor_scalar(line, line, TAKEN, MASKED, ALU.not_equal, ALU.mult)


def token_tile(g, t, line):
    return line[:, t * P:t * P + P] if t < QT else line[:, SEQ:T]


def dsa_value_products(nc, S, dvS, dv_new):
    with ExitStack() as ctx:
        W = Weights(nc, ctx, "dv")
        product, kept = add_sems(nc, "dv_product", "dv_kept")
        vps = S.ps[:, 3072:4096].rearrange("p (b c) -> p b c", b=2)
        block = ctx.enter_context(nc.Block())

        @block.sync
        def _(sp):
            load_weight_pairs(sp, W, KD, 2, *w_pairs(S.d["w_in_cd"][0], DV_))

        @block.tensor
        def _(pe):
            value_products(pe, S, W, vps, product, kept, 2, 0, token_tile)

        @block.scalar
        def _(act):
            for j in range(2):
                W.high(act, j, 1, KD)
            keep_values(act, W, vps, lambda g, t: (dvS[:, t] if t < QT else dv_new)[:, g * GW:(g + 1) * GW], product, kept, 2, 0)

        @block.vector
        def _(dve):
            for j in range(2):
                dve.sem_inc(W.lo_made[j], 1)
            for n in range(2):
                for j in range(2):
                    W.low(dve, j, n + 1, KD)


def gla_decays(nc, S, bT):
    with ExitStack() as ctx:
        sb = lambda n, s: ctx.enter_context(nc.sbuf_tensor(n, s, F32))
        wa_all, ba, inside, e = sb("wa2", [LR_AT + GLA_RANK, 2, P]), sb("ba", [P, 2]), sb("inside", [P, T]), sb("gla_e", [P, T])
        low_rank = slice(LR_AT, LR_AT + GLA_RANK)
        wa, lrT = wa_all[low_rank], bT[low_rank, 1, :]
        loaded, product, z_ready, a_step, v_step = add_sems(nc, "gate_loaded", "gate_product", "gate_z", "gate_log_step", "gate_step")
        block = ctx.enter_context(nc.Block())

        @block.sync
        def _(sp):
            sp.dma_start(wa, S.d["gla_wa2"][0].rearrange("r (f p) -> r f p", p=P)).then_inc(loaded, 16)
            sp.dma_start(ba[:, :], S.d["gla_ba"][0].rearrange("(f p) -> p f", p=P)).then_inc(loaded, 16)
            sp.dma_start(inside[:, :], S.c["chunk_inside"].broadcast_to([P, T])).then_inc(loaded, 16)

        @block.tensor
        def _(pe):
            pe.wait_ge(loaded, 48)
            for f in range(2):
                for at, t, n in PIECES:
                    last = pe.matmul(S.ps[:, f * 1536 + at:f * 1536 + at + n], wa[:, f, :], lrT[:, t:t + n], start=True, stop=True)
                last.then_inc(product, 1)

        @block.scalar
        def _(act):
            for f in range(2):
                act.wait_ge(z_ready, f + 1)
                if f:
                    act.wait_ge(v_step, 1)
                for func, scale, bias in ((ACT.Abs, 1.0, 0.0), (ACT.Exp, -1.0, 0.0), (ACT.Ln, 1.0, S.ones[:, 0:1])):
                    act.activation(e[:, :], bT[:, f, :] if func is ACT.Abs else e[:, :], func, scale=scale, bias=bias).then_inc(a_step, 1)
                    act.wait_ge(a_step, 3 * f + {ACT.Abs: 1, ACT.Exp: 2}.get(func, 3))

        @block.vector
        def _(dve):
            for f in range(2):
                dve.wait_ge(product, 2)
                dve.tensor_scalar(by3(bT[:, f, :]), slot(S, f), ba[:, f:f + 1], None, ALU.add).then_inc(z_ready, 1)
            for f in range(2):
                dve.wait_ge(a_step, 3 * f + 3)
                dve.scalar_tensor_tensor(bT[:, f, :], bT[:, f, :], 0.0, e[:, :], ALU.min, ALU.subtract).then_inc(v_step, 1)
                dve.wait_ge(v_step, 3 * f + 1)
                dve.tensor_scalar(bT[:, f, :], bT[:, f, :], 1.0 / GLA_TAU, None, ALU.mult).then_inc(v_step, 1)
                dve.wait_ge(v_step, 3 * f + 2)
                dve.tensor_tensor_scan(bT[:, f, :], inside[:, :], bT[:, f, :], 0.0, ALU.mult, ALU.add).then_inc(v_step, 1)


SUB = 32


def gla_prompt(nc, S, gT, bT, gvS):
    with ExitStack() as ctx:
        sb = lambda n, s: ctx.enter_context(nc.sbuf_tensor(n, s, F32))
        NS = P // SUB
        nb = sb("neg_mid", [P, 2, QT * NS])
        eq, ek = sb("eq", [P, 2, P]), sb("ek", [P, 2, NS, P])
        ei, ed = sb("ei", [P, 2, P]), sb("ed", [P, 2, P])
        el = sb("el", [P, 2, QT])
        A = sb("A_T", [P, GLA_H, P])
        kd = sb("kd", [P, 2, P])
        st = sb("gla_state", [P, 2, GLA_DV])
        causal = sb("causal_T", [P, P])
        loaded, ready, exps, mixed, scored, masked, turned, copied, outs, states, stepped, stored = add_sems(
            nc, *("gp_" + x for x in ("loaded", "start", "exps", "mixed", "scored", "masked", "turned", "kd_copied", "outs",
                                      "state_sums", "stepped", "stored")))
        a_ps = S.ps[:, 0:1024].rearrange("p (b f i) -> p b f i", b=2, f=4)
        o_ps = S.ps[:, 1024:2048].rearrange("p (b f i) -> p b f i", b=2, f=4)
        k_ps = S.ps[:, 2048:2048 + 2 * P].rearrange("p (f x) -> p f x", f=2)
        s_ps = S.ps[:, 2560:2560 + 2 * P].rearrange("p (f x) -> p f x", f=2)
        block = ctx.enter_context(nc.Block())

        @block.sync
        def _(sp):
            sp.dma_start(causal[:, :], S.c["causal_T"]).then_inc(loaded, 16)
            sp.wait_ge(stepped, QT + 1)
            for f in range(2):
                sp.dma_start(S.o["gla_p"][0, 0, 2 * f:2 * f + 2].rearrange("h k v -> (h k) v"), st[:, f, :]).then_inc(stored, 16)
            sp.wait_ge(stored, 32)

        @block.scalar
        def _(act):
            act.wait_ge(ready, 1)
            act.activation(el[:, :, :], bT[:, :, P - 1:SEQ:P], ACT.Exp)
            for c in range(QT):
                if c:
                    act.wait_ge(outs, c)
                for f in range(2):
                    b = lambda at, n: bT[:, f, c * P + at:c * P + at + n]
                    for s in range(NS):
                        at = s * SUB
                        act.activation(eq[:, f, at:at + SUB], b(at, SUB), ACT.Exp, bias=nb[:, f, c * NS + s:c * NS + s + 1])
                        act.activation(ek[:, f, s, 0:at + SUB], b(0, at + SUB), ACT.Exp, scale=-1.0, bias=b(at + SUB // 2, 1))
                    act.activation(ei[:, f, :], b(0, P), ACT.Exp)
                    last = act.activation(ed[:, f, :], b(0, P), ACT.Exp, scale=-1.0, bias=b(P - 1, 1))
                last.then_inc(exps, 1)
                act.wait_ge(turned, c + 1)
                if c:
                    act.wait_ge(states, c)
                act.activation(kd[:, :, :], k_ps, ACT.Copy).then_inc(copied, 1)

        @block.vector
        def _(dve):
            dve.tensor_scalar(nb[:, :, :], bT[:, :, SUB // 2:SEQ:SUB], -1.0, None, ALU.mult)
            dve.memset(st[:, :, :], 0.0).then_inc(stepped, 1)
            dve.memset(ek[:, :, :, :], 0.0).then_inc(ready, 1)
            dve.wait_ge(loaded, 16)
            for c in range(QT):
                cols = slice(c * P, (c + 1) * P)
                dve.wait_ge(exps, c + 1)
                q, k = gT[:, 0:2, cols], gT[:, 2:4, cols]
                dve.scalar_tensor_tensor(eq[:, :, :], eq[:, :, :], GLA_DK ** -0.5, q, ALU.mult, ALU.mult)
                for f in range(2):
                    dve.tensor_tensor(ek[:, f], ek[:, f], gT[:, 2 + f, cols].unsqueeze(1).broadcast_to([P, NS, P]), ALU.mult)
                dve.scalar_tensor_tensor(ei[:, :, :], ei[:, :, :], GLA_DK ** -0.5, q, ALU.mult, ALU.mult)
                dve.tensor_tensor(ed[:, :, :], ed[:, :, :], k, ALU.mult).then_inc(mixed, 1)
                dve.wait_ge(scored, c + 1)
                for b in range(2):
                    last = dve.tensor_tensor(A[:, :, :].rearrange("p (f b) i -> p b f i", b=2)[:, b], a_ps[:, b, 0:2, :],
                                             causal[:, :].unsqueeze(1).broadcast_to([P, 2, P]), ALU.mult)
                last.then_inc(masked, 1)
                dve.wait_ge(outs, c + 1)
                for b in range(2):
                    last = dve.tensor_copy(gT[:, b:4:2, cols], o_ps[:, b, 0:2, :])
                dve.wait_ge(states, c + 1)
                for f in range(2):
                    last = dve.scalar_tensor_tensor(st[:, f, :], st[:, f, :], el[:, f, c:c + 1], s_ps[:, f, :], ALU.mult, ALU.add)
                last.then_inc(stepped, 1)

        @block.tensor
        def _(pe):
            for c in range(QT):
                pe.wait_ge(mixed, c + 1)
                if c:
                    pe.wait_ge(masked, c)
                for h in range(GLA_H):
                    f, b = h // 2, h % 2
                    half = slice(b * DH, b * DH + DH)
                    for s in range(NS):
                        last = pe.matmul(a_ps[:, b, f, s * SUB:(s + 1) * SUB], ek[half, f, s, :], eq[half, f, s * SUB:(s + 1) * SUB], start=True, stop=True)
                last.then_inc(scored, 1)
                if c:
                    pe.wait_ge(copied, c)
                for f in range(2):
                    last = pe.transpose(k_ps[:, f, :], ed[:, f, :], S.ident[:, :])
                last.then_inc(turned, 1)
                pe.wait_ge(masked, c + 1)
                pe.wait_ge(stepped, c + 1)
                for h in range(GLA_H):
                    f, b = h // 2, h % 2
                    half = slice(b * DH, b * DH + DH)
                    pe.matmul(o_ps[:, b, f, :], st[half, f, :], ei[half, f, :], start=True, stop=False)
                    last = pe.matmul(o_ps[:, b, f, :], gvS[:, c, h * P:(h + 1) * P], A[:, h, :], start=False, stop=True)
                last.then_inc(outs, 1)
                pe.wait_ge(copied, c + 1)
                for h in range(GLA_H):
                    f, b = h // 2, h % 2
                    last = pe.matmul(s_ps[b * DH:(b + 1) * DH, f, :], kd[:, f, b * DH:(b + 1) * DH], gvS[:, c, h * P:(h + 1) * P], start=True, stop=True)
                last.then_inc(states, 1)


def gla_sample(nc, S, gT, bT, gvS):
    with ExitStack() as ctx:
        sb = lambda n, s: ctx.enter_context(nc.sbuf_tensor(n, s, F32))
        s0 = sb("s0", [P, 2, N_SEQ, GLA_DV])
        new = s0
        e, q, k, kd, diff = sb("gs_e", [P, 4, 2, TS]), sb("gs_q", [P, 2, TS]), sb("gs_k", [P, 2, TS]), sb("gs_kd", [P, 2, TS]), sb("gs_diff", [P, 2, TS])
        el = sb("gs_el", [P, 2, N_SEQ])
        A = sb("gs_A", [TS, GLA_H, TS])
        kdT = sb("gs_kdT", [TS, 2, P])
        km = sb("gs_km", [TS, N_SEQ, P])
        mask, seq = sb("gs_mask", [TS, TS]), sb("gs_seq", [TS, N_SEQ])
        loaded, diffed, exped, mixed, scored, step, outs, kept, states, finished, stored = add_sems(
            nc, *("gs_" + x for x in ("loaded", "diffed", "exped", "mixed", "scored", "step", "outs", "kept", "states", "finished", "stored")))
        a_ps = S.ps[0:TS, 0:1024].rearrange("p (b f i) -> p b f i", b=2, f=16)
        k_ps = S.ps[0:TS, 1024:1024 + 2 * P].rearrange("p (f x) -> p f x", f=2)
        inter_ps = S.ps[:, 1536:2560].rearrange("p (b f i) -> p b f i", b=2, f=16)
        intra_ps = S.ps[:, 2560:2560 + GLA_H * TS].rearrange("p (h i) -> p h i", h=GLA_H)
        s_ps = S.ps[:, 3072:4096].rearrange("p (n v) -> p n v", n=N_SEQ)
        block = ctx.enter_context(nc.Block())
        last_b = bT[:, :, SEQ + L_NEW - 1:T:L_NEW]

        @block.sync
        def _(sp):
            for n in range(N_SEQ):
                sp.dma_start(s0[:, :, n, :], S.d["state_gla"][0, n].rearrange("(f b) k v -> (b k) f v", b=2)).then_inc(loaded, 16)
            sp.dma_start(mask[:, :], S.c["sample_causal_T"]).then_inc(loaded, 16)
            sp.dma_start(seq[:, :], S.c["seq_of"]).then_inc(loaded, 16)
            sp.wait_ge(finished, 2)
            for n in range(N_SEQ):
                sp.dma_start(S.o["gla_s"][0, n].rearrange("(f b) k v -> (b k) f v", b=2), new[:, :, n, :]).then_inc(stored, 16)
            sp.wait_ge(stored, 16 * N_SEQ)

        @block.scalar
        def _(act):
            b = bT[:, :, SEQ:T]
            act.activation(e[:, 0], b, ACT.Exp)
            act.activation(e[:, 1], b, ACT.Exp, scale=-1.0)
            act.activation(el[:, :, :], last_b, ACT.Exp)
            act.wait_ge(diffed, 1)
            act.activation(e[:, 2], diff[:, :, :], ACT.Exp).then_inc(exped, 1)
            act.wait_ge(outs, 1)
            for b in range(2):
                last = act.activation(gT[:, b:4:2, SEQ:T], inter_ps[:, b, 0:2, :], ACT.Copy)
            last.then_inc(kept, 1)

        @block.vector
        def _(dve):
            done = chain(dve, step)
            dve.tensor_tensor(diff[:, :, :].rearrange("p f (n l) -> p f n l", l=L_NEW), last_b.unsqueeze(3).broadcast_to([P, 2, N_SEQ, L_NEW]),
                              bT[:, :, SEQ:T].rearrange("p f (n l) -> p f n l", l=L_NEW), ALU.subtract).then_inc(diffed, 1)
            dve.wait_ge(exped, 1)
            dve.scalar_tensor_tensor(q[:, :, :], e[:, 0], GLA_DK ** -0.5, gT[:, 0:2, SEQ:T], ALU.mult, ALU.mult)
            dve.tensor_tensor(k[:, :, :], e[:, 1], gT[:, 2:4, SEQ:T], ALU.mult)
            dve.tensor_tensor(kd[:, :, :], e[:, 2], gT[:, 2:4, SEQ:T], ALU.mult).then_inc(mixed, 1)
            dve.wait_ge(loaded, 16 * (N_SEQ + 2))
            dve.wait_ge(scored, 1)
            for b in range(2):
                dve.tensor_tensor(A[:, :, :].rearrange("p (f b) i -> p b f i", b=2)[:, b], a_ps[:, b, 0:2, :], mask[:, :].unsqueeze(1).broadcast_to([TS, 2, TS]), ALU.mult)
            done(dve.tensor_copy(kdT[:, :, :], k_ps))
            keys_of_sequences = lambda f: dve.tensor_tensor(km[:, :, :], kdT[:, f, :].unsqueeze(1).broadcast_to([TS, N_SEQ, P]),
                                                            seq[:, :].unsqueeze(2).broadcast_to([TS, N_SEQ, P]), ALU.mult)
            done(keys_of_sequences(0))
            dve.wait_ge(kept, 1)
            for f in range(2):
                ins = dve.tensor_tensor(new[:, f], s0[:, f], el[:, f, :].unsqueeze(2).broadcast_to([P, N_SEQ, GLA_DV]), ALU.mult)
            done(ins)
            dve.tensor_tensor(gT[:, :, SEQ:T], gT[:, :, SEQ:T], intra_ps, ALU.add)
            for f in range(2):
                dve.wait_ge(states, f + 1)
                if f == 0:
                    done(keys_of_sequences(1))
                dve.tensor_tensor(new[:, f], new[:, f], s_ps, ALU.add).then_inc(finished, 1)

        @block.tensor
        def _(pe):
            pe.wait_ge(mixed, 1)
            for h in range(GLA_H):
                f, b = h // 2, h % 2
                half = slice(b * DH, b * DH + DH)
                pe.matmul(a_ps[:, b, f, :], k[half, f, :], q[half, f, :], start=True, stop=True)
            for f in range(2):
                last = pe.transpose(k_ps[:, f, :], kd[:, f, :], S.ident[:, :])
            last.then_inc(scored, 1)
            pe.wait_ge(loaded, 16 * (N_SEQ + 2))
            for h in range(GLA_H):
                f, b = h // 2, h % 2
                half = slice(b * DH, b * DH + DH)
                for n in range(N_SEQ):
                    pe.matmul(inter_ps[:, b, f, n * L_NEW:(n + 1) * L_NEW], s0[half, f, n, :], q[half, f, n * L_NEW:(n + 1) * L_NEW], start=True, stop=True)
            pe.wait_ge(step, 2)
            for h in range(GLA_H):
                last = pe.matmul(intra_ps[:, h, :], gvS[0:TS, QT, h * P:(h + 1) * P], A[:, h, :], start=True, stop=True)
            last.then_inc(outs, 1)
            for f in range(2):
                if f:
                    pe.wait_ge(finished, 1)
                    pe.wait_ge(step, 4)
                for n in range(N_SEQ):
                    for b in range(2):
                        last = pe.matmul(s_ps[b * DH:(b + 1) * DH, n, :], km[:, n, b * DH:(b + 1) * DH],
                                         gvS[0:TS, QT, (2 * f + b) * P:(2 * f + b + 1) * P], start=True, stop=True)
                last.then_inc(states, 1)


def gate_outputs(nc, S, gT, cg):
    with ExitStack() as ctx:
        sig = ctx.enter_context(nc.sbuf_tensor("cg_sig", [P, 2, T], F32))
        made, gated = add_sems(nc, "cg_sigmoid", "cg_gated")
        block = ctx.enter_context(nc.Block())

        @block.scalar
        def _(act):
            for h in range(GLA_H):
                if h >= 2:
                    act.wait_ge(gated, 2 * (h - 1))
                act.activation(sig[:, h % 2, :], cg[:, h, :], ACT.Sigmoid).then_inc(made, 1)

        @block.vector
        def _(dve):
            for h in range(GLA_H):
                dve.wait_ge(made, h + 1)
                dve.tensor_tensor(cg[:, h, :], cg[:, h, :], sig[:, h % 2, :], ALU.mult).then_inc(gated, 1)
                dve.wait_ge(gated, 2 * h + 1)
                dve.tensor_tensor(cg[:, h, :], cg[:, h, :], gT[:, h, :], ALU.mult).then_inc(gated, 1)


def dsa_prompt(nc, S, big, work, dvS):
    with ExitStack() as ctx:
        sb = lambda n, s: ctx.enter_context(nc.sbuf_tensor(n, s, F32))
        toep = sb("toep_dsa", [P, 4, SEQ])
        sc = sb("sc_dsa", [P, 2, SEQ])
        pT = sb("pT_dsa", [P, 2, BANK])
        osb = sb("o_dsa", [P, 2, P])
        stat = sb("stat_dsa", [P, 2, 4])
        scored, biased, vstep, maxed, exps, turned, kept, summed, scaled, pair_turned, pair_kept = add_sems(
            nc, *("dp_" + x for x in ("scored", "biased", "vector_step", "maxima", "exps", "turned",
                                      "probs_kept", "summed", "scaled", "pair_turned", "pair_kept")))
        toep_in = add_sems(nc, *(f"dp_toep_in{i}" for i in range(4)))
        units = [(f, t, b) for f in range(DSA_H // 2) for t in range(QT) for b in range(2)]
        groups = [(u, list(range(at, min(at + 4, units[u][1] + 1)))) for u in range(len(units)) for at in range(0, units[u][1] + 1, 4)]
        groups_to = [sum(1 for g in groups if g[0] <= u) for u in range(len(units))]
        s_ps = S.ps[:, 0:2048].rearrange("p (b k) -> p b k", b=2)
        t_ps = S.ps[:, 2048:3072].rearrange("p (b k) -> p b k", b=2)
        o_ps = S.ps[:, 3072:4096].rearrange("p (b d) -> p b d", b=2)[:, :, 0:DH]
        oT_ps = S.ps[:, 3584 + P:3584 + 2 * P]
        block = ctx.enter_context(nc.Block())

        @block.sync
        def _(sp):
            sp.wait_ge(S.dsa_lines, 16 * DSA_H)
            for h in range(DSA_H):
                if h >= 4:
                    sp.wait_ge(biased, (h - 4) // 2 * 2 * QT + 2 * QT)
                sp.dma_start(toep[:, h % 4:h % 4 + 1, :], toeplitz(S.dsa_copies, DSA_LINE, 0, slice(h, h + 1), 1, SEQ)).then_inc(toep_in[h % 4], 16)

        @block.tensor
        def _(pe):
            def scores(u):
                f, t, b = units[u]
                if u >= 2:
                    pe.wait_ge(biased, u - 1)
                half = slice(b * DH, b * DH + DH)
                for at in range(0, (t + 1) * P, BANK):
                    n = min(BANK, (t + 1) * P - at)
                    last = pe.matmul(s_ps[:, u % 2, at:at + n], big[half, 4 + f, t * P:(t + 1) * P], big[half, 8 + f, at:at + n], start=True, stop=True)
                last.then_inc(scored, 1)

            def turn_probs(g):
                u, kts = groups[g]
                pe.wait_ge(exps, u + 1)
                if g >= 2:
                    pe.wait_ge(kept, g - 1)
                for i, kt in enumerate(kts):
                    last = pe.transpose(t_ps[:, g % 2, i * P:(i + 1) * P], sc[:, u % 2, kt * P:(kt + 1) * P], S.ident[:, :])
                last.then_inc(turned, 1)

            def weigh_values(g):
                u, kts = groups[g]
                f, t, b = units[u]
                pe.wait_ge(kept, g + 1)
                if kts[0] == 0 and u >= 2:
                    pe.wait_ge(scaled, u - 1)
                if kts[0] == 0 and u % 2 == 1 and u >= 3:
                    pe.wait_ge(pair_kept, (u - 3) // 2 + 1)
                h = 2 * f + b
                for i, kt in enumerate(kts):
                    last = pe.matmul(o_ps[:, u % 2, :], pT[:, g % 2, i * P:(i + 1) * P], dvS[:, kt, h * DH:(h + 1) * DH], start=kt == 0, stop=kt == t)
                if kts[-1] == t:
                    last.then_inc(summed, 1)

            def turn_pair(k):
                pe.wait_ge(scaled, 2 * k + 2)
                if k:
                    pe.wait_ge(pair_kept, k)
                pe.transpose(oT_ps, osb[:, k % 2, :], S.ident[:, :]).then_inc(pair_turned, 1)

            scores(0)
            for g, (u, kts) in enumerate(groups):
                if kts[0] == 0:
                    if u + 1 < len(units):
                        scores(u + 1)
                turn_probs(g)
                if g:
                    weigh_values(g - 1)
                if kts[0] == 0 and u % 2 == 1 and u >= 3:
                    turn_pair((u - 3) // 2)
            weigh_values(len(groups) - 1)
            turn_pair(len(units) // 2 - 1)

        @block.vector
        def _(dve):
            done = chain(dve, vstep)
            def scale(u):
                dve.wait_ge(summed, u + 1)
                if u % 2 == 0 and u >= 4:
                    dve.wait_ge(pair_turned, (u - 4) // 2 + 1)
                dve.tensor_scalar(osb[:, (u // 2) % 2, (u % 2) * DH:(u % 2 + 1) * DH], o_ps[:, u % 2, :], stat[:, u % 2, 3:4], None,
                                  ALU.mult).then_inc(scaled, 1)

            for u, (f, t, b) in enumerate(units):
                h, n = 2 * f + b, (t + 1) * P
                if t == 0:
                    dve.wait_ge(toep_in[h % 4], 16 * (h // 4 + 1))
                dve.wait_ge(scored, u + 1)
                if u >= 2:
                    dve.wait_ge(turned, groups_to[u - 2])
                bias = toep[:, h % 4, SEQ - n:SEQ]
                st = stat[:, u % 2, :]
                if t < 2:
                    dve.tensor_tensor_reduce(sc[:, u % 2, 0:n], s_ps[:, u % 2, 0:n], bias, 1.0, TAKEN, ALU.add, ALU.max, st[:, 0:1]).then_inc(biased, 1)
                    dve.wait_ge(biased, u + 1)
                else:
                    dve.tensor_tensor(sc[:, u % 2, 0:n], s_ps[:, u % 2, 0:n], bias, ALU.add).then_inc(biased, 1)
                    dve.wait_ge(biased, u + 1)
                    done(dve.tensor_tensor_reduce(sc[:, u % 2, 0:n], sc[:, u % 2, 0:n], work[:, WORK_AT[t]:WORK_AT[t] + n], 1.0, TAKEN,
                                                  ALU.add, ALU.max, st[:, 0:1]))
                dve.tensor_scalar(st[:, 1:2], st[:, 0:1], -1.0, None, ALU.mult).then_inc(maxed, 1)
                if u:
                    dve.wait_ge(exps, u)
                    done(dve.reciprocal(stat[:, (u - 1) % 2, 3:4], stat[:, (u - 1) % 2, 2:3]))
                    scale(u - 1)
            dve.wait_ge(exps, len(units))
            done(dve.reciprocal(stat[:, (len(units) - 1) % 2, 3:4], stat[:, (len(units) - 1) % 2, 2:3]))
            scale(len(units) - 1)

        @block.scalar
        def _(act):
            def keep_pair(k):
                f, t, _ = units[2 * k]
                act.wait_ge(pair_turned, k + 1)
                act.activation(big[:, 4 + f, t * P:(t + 1) * P], oT_ps, ACT.Copy).then_inc(pair_kept, 1)

            g = 0
            for u, (f, t, b) in enumerate(units):
                act.wait_ge(maxed, u + 1)
                n = (t + 1) * P
                act.activation(sc[:, u % 2, 0:n], sc[:, u % 2, 0:n], ACT.Exp, bias=stat[:, u % 2, 1:2], accum_out=stat[:, u % 2, 2:3]).then_inc(exps, 1)
                while g < len(groups) and groups[g][0] == u:
                    m = len(groups[g][1]) * P
                    act.wait_ge(turned, g + 1)
                    if g >= 2:
                        act.wait_ge(kept, g - 1)
                    act.activation(pT[:, g % 2, 0:m], t_ps[:, g % 2, 0:m], ACT.Copy).then_inc(kept, 1)
                    g += 1
                if u % 2 == 1 and u >= 3:
                    keep_pair((u - 3) // 2)
            keep_pair(len(units) // 2 - 1)


def dsa_sample(nc, S, big, work, work_s, dv_new):
    sc, bias = work[:, 0:S_COLS], work[:, S_COLS:2 * S_COLS]
    mask = work[0:TS, 2 * S_COLS:3 * S_COLS]
    with ExitStack() as outer:
        sb = lambda n, s: outer.enter_context(nc.sbuf_tensor(n, s, F32))
        pages = outer.enter_context(nc.sbuf_tensor("pages_kv", [1, N_SEQ * N_PAGES], I32))
        qb = sb("qb_dsa", [P, 4, N_SEQ, 32])
        tabr = sb("tabr_dsa", [NB, L_NEW, P])
        slots = [sb(f"kv_slot{i}", [P, N_PAGES, BANK]) for i in range(3)]
        for half in range(2):
            with ExitStack() as ctx:
                tag = f"ds{half}"
                sb2 = lambda n, s: ctx.enter_context(nc.sbuf_tensor(f"{n}_{tag}", s, F32))
                hot = sb2("hot_s", [NB, L_NEW, BANK])
                sel = sb2("dsa_rows", [TS, P])
                other = sb2("dsa_other", [P, TS])
                kT = sb2("kT", [P, 2, BANK])
                pT = sb2("pT_s", [P, N_PAGES + 1, P])
                stat = sb2("stat_s", [P, 3])
                consts, table_in, prep, hot_in, biased, scored, step, exps, turned, copied, probs_turned, probs_kept, summed = add_sems(
                    nc, *(f"{x}_{tag}" for x in ("consts", "table_in", "prepared", "hot_in", "bias_made", "scored", "step", "exps", "keys_turned",
                                                 "keys_copied", "probs_turned", "probs_kept", "summed")))
                kv_in = add_sems(nc, *(f"kv_in{i}_{tag}" for i in range(3)))
                (kv_used,) = add_sems(nc, f"kv_used_{tag}")
                s_ps = S.ps[:, 0:S_COLS]
                b_ps = S.ps[:, 1536:1536 + S_COLS]
                t_ps = S.ps[:, 3072:4096].rearrange("p (b x) -> p b x", b=2)
                p_ps = S.ps[:, 0:(N_PAGES + 1) * P].rearrange("p (g x) -> p g x", g=N_PAGES + 1)
                o_ps = S.ps[:, 1536:1536 + P].rearrange("p (n f x) -> p n f x", n=4, f=4)
                pool_kv = S.d["cache_dsa_kv"][0]
                block = ctx.enter_context(nc.Block())

                @block.sync
                def _(sp):
                    if half == 0:
                        sp.dma_start(pages[:, :], S.d["page_table"].rearrange("n (a g) -> a (n g)", a=1)).then_inc(table_in, 16)
                    sp.dma_start(sel[:, :], S.c["dsa_rows"][:, half, :]).then_inc(consts, 16)
                    sp.dma_start(other[:, :], S.c["dsa_other"][:, half, :]).then_inc(consts, 16)
                    sp.dma_start(hot[:, :, :], S.c["dsa_hot"][:, :, 0:BANK]).then_inc(hot_in, 16)
                    if half == 0:
                        sp.wait_ge(table_in, 16)
                    for i in range(8):
                        n, what = 4 * half + i % 4, i // 4
                        if 3 <= i < 7:
                            sp.wait_ge(turned, N_PAGES * (i - 2))
                        elif i >= 7:
                            sp.wait_ge(kv_used, i - 6)
                        for g in range(N_PAGES):
                            page = sp.value_load(pages[0:1, n * N_PAGES + g:n * N_PAGES + g + 1], min_val=0, max_val=pool_kv.shape[0] - 1)
                            sp.dma_start(slots[i % 3][:, g, :], pool_kv[bass.ds(page, 1)].rearrange("a s c h d -> s (a c) (h d)")[:, what, :]).then_inc(kv_in[i % 3], 16)

                @block.scalar
                def _(act):
                    act.wait_ge(biased, 1)
                    act.dma_start(hot[:, :, :], S.c["dsa_hot"][:, :, BANK:PAST]).then_inc(hot_in, 16)
                    act.wait_ge(biased, 2)
                    act.dma_start(hot[:, :, 0:TS], S.c["dsa_hot_new"]).then_inc(hot_in, 16)
                    for i in range(4 * N_PAGES):
                        act.wait_ge(turned, i + 1)
                        if i >= 2:
                            act.wait_ge(scored, i - 1)
                        act.activation(kT[:, i % 2, :], t_ps[:, i % 2, :], ACT.Copy).then_inc(copied, 1)
                    act.wait_ge(step, 3)
                    act.activation(sc, sc, ACT.Exp, bias=stat[:, 0:1], accum_out=stat[:, 1:2]).then_inc(exps, 1)

                @block.vector
                def _(dve):
                    done = chain(dve, step)
                    if half == 0:
                        dve.memset(qb[:, :, :, :], 0.0).then_inc(prep, 1)
                        dve.memset(tabr[:, :, :], 0.0).then_inc(prep, 1)
                        dve.wait_ge(prep, 2)
                        for h in range(DSA_H):
                            rows, f = slice(DH * (h % 2), DH * (h % 2) + DH), h // 2
                            dve.tensor_copy(qb[rows, f, :, h * L_NEW:(h + 1) * L_NEW],
                                            big[rows, 4 + f, SEQ:T].rearrange("p (n l) -> p n l", l=L_NEW))
                        for l in range(L_NEW):
                            dve.tensor_copy(tabr[:, l, :].rearrange("b (n h l) -> b n h l", n=4, h=DSA_H)[:, :, :, l],
                                            S.tab[:, 12:12 + DSA_H].unsqueeze(1).broadcast_to([NB, 4, DSA_H]))
                        dve.tensor_copy(mask[:, 0:PAST], work_s[:, 0:PAST])
                        dve.tensor_copy(mask[:, PAST:S_COLS].rearrange("t (n l) -> t n l", n=N_SEQ),
                                        work_s[:, PAST:S_KEYS].unsqueeze(1).broadcast_to([TS, N_SEQ, L_NEW])).then_inc(prep, 1)
                    dve.wait_ge(consts, 32)
                    dve.wait_ge(biased, 3)
                    dve.tensor_copy(bias[:, 0:PAST], b_ps[:, 0:PAST])
                    done(dve.tensor_tensor(bias[:, PAST:S_COLS], b_ps[:, PAST:S_COLS], other[:, :], ALU.add))
                    dve.wait_ge(scored, 4 * N_PAGES + 1)
                    done(dve.tensor_tensor(sc, s_ps, bias, ALU.add))
                    done(dve.tensor_reduce(stat[:, 0:1], sc, AX.X, ALU.max, negate=True))
                    dve.wait_ge(exps, 1)
                    done(dve.reciprocal(stat[:, 2:3], stat[:, 1:2]))
                    done(dve.tensor_scalar(sc, sc, stat[:, 2:3], None, ALU.mult))
                    dve.wait_ge(probs_turned, 1)
                    dve.tensor_copy(pT[:, 0:N_PAGES, :], p_ps[:, 0:N_PAGES, :])
                    dve.tensor_copy(pT[0:TS, N_PAGES, :], p_ps[0:TS, N_PAGES, :]).then_inc(probs_kept, 1)
                    dve.wait_ge(summed, 1)
                    for b in range(2):
                        rows = slice(b * DH, b * DH + DH)
                        dve.tensor_copy(big[rows, 4:8, SEQ + 16 * half:SEQ + 16 * (half + 1)].rearrange("p f (n l) -> p f n l", n=4),
                                        o_ps[rows, :, :, b * L_NEW:(b + 1) * L_NEW].rearrange("p n f l -> p f n l"))

                @block.tensor
                def _(pe):
                    if half == 0:
                        pe.wait_ge(prep, 3)
                    pe.wait_ge(consts, 32)
                    for i, (at, n) in enumerate(((0, BANK), (BANK, BANK), (PAST, TS))):
                        pe.wait_ge(hot_in, 16 * (i + 1))
                        for l in range(L_NEW):
                            pe.matmul(b_ps[:, at:at + n], tabr[:, l, :], hot[:, l, 0:n], start=l == 0, stop=False)
                        pe.matmul(b_ps[:, at:at + n], sel[:, :], mask[:, at:at + n], start=False, stop=True).then_inc(biased, 1)

                    def turn_keys(i):
                        n, g = divmod(i, N_PAGES)
                        pe.wait_ge(kv_in[n % 3], 16 * N_PAGES * (n // 3 + 1))
                        if i >= 2:
                            pe.wait_ge(copied, i - 1)
                        for f in range(4):
                            last = pe.transpose(t_ps[:, i % 2, f * P:(f + 1) * P], slots[n % 3][:, g, f * P:(f + 1) * P], S.ident[:, :])
                        last.then_inc(turned, 1)
                        if g == N_PAGES - 1:
                            return last
                    turn_keys(0)
                    for i in range(4 * N_PAGES):
                        if i + 1 < 4 * N_PAGES:
                            turn_keys(i + 1)
                        pe.wait_ge(copied, i + 1)
                        n, g = divmod(i, N_PAGES)
                        for f in range(4):
                            last = pe.matmul(s_ps[32 * n:32 * n + 32, g * P:(g + 1) * P], qb[:, f, 4 * half + n, :], kT[:, i % 2, f * P:(f + 1) * P],
                                             start=f == 0, stop=f == 3)
                        last.then_inc(scored, 1)
                    for n in range(4):
                        for f in range(4):
                            last = pe.matmul(s_ps[32 * n:32 * n + 32, NEW_AT:NEW_AT + TS], qb[:, f, 4 * half + n, :], big[:, 8 + f, SEQ:T],
                                             start=f == 0, stop=f == 3)
                    last.then_inc(scored, 1)
                    pe.wait_ge(step, 5)
                    for g in range(N_PAGES):
                        pe.transpose(p_ps[:, g, :], sc[:, g * P:(g + 1) * P], S.ident[:, :])
                    pe.transpose(p_ps[0:TS, N_PAGES, :], sc[:, PAST:S_COLS], S.ident[:, :]).then_inc(probs_turned, 1)
                    pe.wait_ge(probs_kept, 1)
                    for n in range(4):
                        i = 4 + n
                        pe.wait_ge(kv_in[i % 3], 16 * N_PAGES * (i // 3 + 1))
                        for f in range(4):
                            own = slice(n * 32 + f * 8, n * 32 + f * 8 + 8)
                            for g in range(N_PAGES):
                                last = pe.matmul(o_ps[:, n, f, :], slots[i % 3][:, g, f * P:(f + 1) * P], pT[:, g, own], start=g == 0, stop=False)
                            if f == 3:
                                last.then_inc(kv_used, 1)
                            last = pe.matmul(o_ps[:, n, f, :], dv_new[:, f * P:(f + 1) * P], pT[0:TS, N_PAGES, own], start=False, stop=True)
                    last.then_inc(summed, 1)


def layer1_states(nc, S, big, dvS, dv_new):
    o = S.o
    rows_p = o["dsa_kv_p"][0, 0].rearrange("t p c h d -> t p c (h d)")
    rows_s = o["dsa_kv_s"][0].rearrange("n l c h d -> (n l) c (h d)")
    jobs = [([big[:, 8 + f, t * P:(t + 1) * P] for f in range(4)], P, [(0, P, 512, rows_p[t, :, 0, :])]) for t in range(QT)]
    jobs.append(([big[:, 8 + f, SEQ:T] for f in range(4)], TS, [(0, TS, 512, rows_s[:, 0, :])]))
    direct = [(rows_p[t, :, 1, :], dvS[:, t, :]) for t in range(QT)] + [(rows_s[:, 1, :], dv_new[:, :])]
    turn_and_store(nc, S, "cd", jobs, direct)


def layer1(nc, S):
    with ExitStack() as layer:
        keep = lambda n, s: layer.enter_context(nc.sbuf_tensor(n, s, F32))
        big = S.home
        with ExitStack() as mixing:
            keep1 = lambda n, s: mixing.enter_context(nc.sbuf_tensor(n, s, F32))
            dv_new = keep1("dv_new", [TS, BANK])
            work, work_s = keep1("work", [P, WORK]), keep1("work_s", [TS, S_KEYS])
            heads = mixing.enter_context(ExitStack())
            S.h = Parts(nc, heads, "h1", [KD, T])
            with nc.sbuf_tensor("norm1", [P, 5, T], F32) as scratch:
                rms_norm(nc, S, "mix1", S.g_mix[:, 1, :], S.xT, S.h, scratch, spill=S.x_spill)
            with ExitStack() as gla:
                keep2 = lambda n, s: gla.enter_context(nc.sbuf_tensor(n, s, F32))
                bT = keep2("decays", [P, 2, T])
                with ExitStack() as index:
                    iw = index.enter_context(nc.sbuf_tensor("iw", [P, QT + 1, DH + IDX_H], F32))
                    iqT = index.enter_context(nc.sbuf_tensor("iqT", [P, 2, T], F32))
                    ikT = index.enter_context(nc.sbuf_tensor("ikT", [P, T], F32))
                    index_products(nc, S, iqT, ikT, iw, bT)
                    index_scores_prompt(nc, S, iqT, ikT, iw, work)
                    index_scores_sample(nc, S, iqT, ikT, iw, work_s)
                gT = keep2("gT", [P, 4, T])
                gvS = keep2("gvS", [P, QT + 1, BANK])
                big_products(nc, S, gT, big, gvS, work, work_s)
                gla_decays(nc, S, bT)
                gla_prompt(nc, S, gT, bT, gvS)
                gla_sample(nc, S, gT, bT, gvS)
                with nc.sbuf_tensor("g_gla", [P, 1], F32) as g_gla:
                    (g_in,) = add_sems(nc, "g_gla_in")
                    with nc.Block() as block:
                        @block.sync
                        def _(sp):
                            sp.dma_start(g_gla[:, :], S.d["gla_norm"].rearrange("a v -> v a")).then_inc(g_in, 16)
                            sp.wait_ge(g_in, 16)
                    head_norms(nc, S, "gla", gT, [0, 1, 2, 3], [g_gla[:, 0:1]] * 4, S.ones, GLA_DV)
                gate_outputs(nc, S, gT, big)
            recycle_semaphores(nc)
            dvS = heads.enter_context(nc.sbuf_tensor("dvS", [P, QT, BANK], F32))
            dsa_value_products(nc, S, dvS, dv_new)
            head_norms(nc, S, "qk1", big, list(range(4, 12)), [S.g_qk[:, 2:3]] * 4 + [S.g_qk[:, 3:4]] * 4, S.head_ones, DH)
            layer1_states(nc, S, big, dvS, dv_new)
            dsa_prompt(nc, S, big, work, dvS)
            heads.close()
            dsa_sample(nc, S, big, work, work_s, dv_new)
        recycle_semaphores(nc)
        project_back(nc, S, "out1", S.d["w_out_cd"][0], KD, lambda k: big[:, k, :])


def build_kernel(nc, d, c, o, stop=99):
    S = Stage()
    LIVE_SEMAPHORES.clear()
    S.d, S.c, S.o = d, c, o
    dram = lambda n, s: nc.dram_tensor(n, s, F32, kind="Internal").ap()
    S.x_spill = dram("x_spill", [P, KD, T])
    S.part_rows = dram("part_rows", [3, T, HPG, HEAD_ROW])
    S.ab_line, S.dsa_line = dram("ab_line", [HPG, AB_LINE]), dram("dsa_line", [DSA_H, DSA_LINE])
    S.ab_copies, S.dsa_copies = dram("ab_copies", [HPG, P, AB_LINE]), dram("dsa_copies", [DSA_H, P, DSA_LINE])
    S.ab_lines, S.dsa_lines = nc.alloc_semaphore("ab_lines_copied"), nc.alloc_semaphore("dsa_lines_copied")
    q_rows, k_rows, v_rows = (dram(n, [TS, 3 * GW]) for n in ("q_rows", "k_rows", "v_rows"))
    with ExitStack() as ctx, nc.allow_non_contiguous_dma(reason="columns of gains and rows of a few floats"):
        sb = lambda n, s: ctx.enter_context(nc.sbuf_tensor(n, s, F32))
        S.ps = ctx.enter_context(nc.psum_tensor("ps", [P, 4096], F32))
        S.ident, S.head_ones, S.ones = sb("ident", [P, P]), sb("head_ones", [P, P]), sb("ones", [P, P])
        S.g_mix, S.g_ffn, S.g_qk = sb("g_mix", [P, 2, KD]), sb("g_ffn", [P, 2, KD]), sb("g_qk", [P, 4])
        S.tab, S.eps = sb("tab", [NB, 20]), sb("eps", [P, 1])
        S.home = sb("home", [P, 12, T])
        S.xT = S.home[:, 0:KD, :]
        load_inputs(nc, S, S.xT)
        bias_lines(nc, S)
        with ExitStack() as layer0:
            keep = lambda n, s: layer0.enter_context(nc.sbuf_tensor(n, s, F32))
            yT = keep("yT", [P, CC, T])
            v_new = keep("v_new", [TS, 3, GW])
            with ExitStack() as attention:
                keep2 = lambda n, s: attention.enter_context(nc.sbuf_tensor(n, s, F32))
                S.qk = S.home
                vS = keep2("vS", [P, 3, QT, GW])
                with ExitStack() as projections:
                    uT = projections.enter_context(nc.sbuf_tensor("uT", [P, CC, U_LEN], F32))
                    taps = projections.enter_context(nc.sbuf_tensor("taps", [P, CC, TAPS], F32))
                    scratch = vS[:, :, :, :].rearrange("p g b c -> p (g b c)")[:, 0:5 * T].rearrange("p (l t) -> p l t", l=5)
                    with ExitStack() as normed:
                        S.h = Parts(nc, normed, "h0", [KD, T])
                        rms_norm(nc, S, "mix0", S.g_mix[:, 0, :], S.xT, S.h, scratch, spill=S.x_spill)
                        glu_products(nc, S, uT, taps, S.home)
                        qkv_products(nc, S, uT, taps, yT, vS, v_new)
                    head_norms(nc, S, "qk0", S.qk, list(range(12)), [S.g_qk[:, 0:1]] * 6 + [S.g_qk[:, 1:2]] * 6, S.head_ones, DH)
                    layer0_states(nc, S, uT, vS, v_new, q_rows, k_rows, v_rows)
                dilated_prompt(nc, S, vS)
                for g in range(3):
                    dilated_sample(nc, S, g, q_rows, v_new)
            merged = keep("bT", [P, 2, T])
            combine_windows(nc, S, merged)
            conv_norm(nc, S, yT)
            project_back(nc, S, "out0", S.d["w_out_ab"][0], 6, lambda k: yT[:, k, :] if k < CC else merged[:, k - CC, :])
        ffn(nc, S, 0)
        recycle_semaphores(nc)
        if stop > 1:
            layer1(nc, S)
            recycle_semaphores(nc)
            ffn(nc, S, 1)
        store_y(nc, S)


_OUTS = [("y_prompt", (1, SEQ, D_MODEL)), ("y_sample", (N_SEQ, L_NEW, D_MODEL)),
         ("conv_p", (1, 1, HIST, CONV_CH)), ("conv_s", (1, N_SEQ, HIST, CONV_CH)),
         ("win128_p", (1, 1, 128, 2, HPG, DH)), ("win128_s", (1, N_SEQ, 128, 2, HPG, DH)),
         ("win512_p", (1, 1, 512, 2, HPG, DH)), ("win512_s", (1, N_SEQ, 512, 2, HPG, DH)),
         ("win2048_p", (1, 1, SEQ, 2, HPG, DH)), ("win2048_s", (1, N_SEQ, PAST + L_NEW, 2, HPG, DH)),
         ("gla_p", (1, 1, GLA_H, GLA_DK, GLA_DV)), ("gla_s", (1, N_SEQ, GLA_H, GLA_DK, GLA_DV)),
         ("dsa_kv_p", (1, 1, QT, PAGE, 2, DSA_H, DH)), ("dsa_kv_s", (1, N_SEQ, L_NEW, 2, DSA_H, DH)),
         ("dsa_kidx_p", (1, 1, QT, PAGE, DH)), ("dsa_kidx_s", (1, N_SEQ, L_NEW, DH))]


def kernel(**inputs):
    import concourse.bacc as _bacc
    from concourse.bass_utils import run_bass_kernel_spmd as _run

    nc = _bacc.Bacc("TRN2", target_bir_lowering=False, num_devices=1)
    arrays, d, c, o = {}, {}, {}, {}
    for name, a in inputs.items():
        arrays[f"in_{name}"] = np.ascontiguousarray(a)
        d[name] = nc.dram_tensor(f"in_{name}", a.shape, mybir.dt.from_np(arrays[f"in_{name}"].dtype), kind="ExternalInput").ap()
    for name, a in shape_constants().items():
        arrays[f"const_{name}"] = np.ascontiguousarray(a)
        c[name] = nc.dram_tensor(f"const_{name}", a.shape, mybir.dt.from_np(a.dtype), kind="ExternalInput").ap()
    for name, shape in _OUTS:
        o[name] = nc.dram_tensor(f"out_{name}", shape, F32, kind="ExternalOutput").ap()
    build_kernel(nc, d, c, o)
    r = _run(nc, [arrays], core_ids=[0])
    return tuple(r.results[0][f"out_{name}"] for name, _ in _OUTS)
```

```python
from contextlib import ExitStack

import numpy as np
import concourse.bass as bass
from concourse import mybir

F32 = mybir.dt.float32
F32R = mybir.dt.float32r
I32 = mybir.dt.int32
ALU = mybir.AluOpType
ACT = mybir.ActivationFunctionType
AX = mybir.AxisListType

P = 128
D_MODEL = 1024
KD = D_MODEL // P
SEQ = 1024
QT = SEQ // P
N_SEQ, L_NEW = 8, 4
TS = N_SEQ * L_NEW
T = SEQ + TS
PAST = 1024
PAGE = 128
N_PAGES = PAST // PAGE
DH = 64
CONV_CH = 512
CC = CONV_CH // P
TAPS = 31
HIST = TAPS - 1
WINDOWS = (128, 512, 2048)
DILS = (1, 4, 16)
HPG = 4
GW = HPG * DH
GLA_H, GLA_DK, GLA_DV, GLA_RANK, GLA_TAU = 4, 64, 128, 16, 16.0
DSA_H = 8
IDX_H = 4
TOPK = 256
FFN = 2816
KF = FFN // P
EPS = 1e-6
BUCKETS, MAX_DIST = 32, 2048
NB = BUCKETS + 1
MASKED = -1e30
TAKEN = -3e38
CQ, CK, CV, CLR, CG, DQ, DK_, DV_, IQ, IK, IW = 0, 256, 512, 1024, 1040, 1552, 2064, 2576, 3088, 3344, 3408
AT_M, AT_L, HEAD_ROW = DH, DH + 1, DH + 2
BANK = 512
PIECE = T // 3
PIECES = tuple((c * BANK, c * PIECE, PIECE) for c in range(3))


def rel_bucket(dist):
    n = np.maximum(dist, 0)
    half = BUCKETS // 2
    nf = np.maximum(n, half).astype(np.float32)
    large = half + (np.log(nf / np.float32(half)) / np.float32(np.log(MAX_DIST / half)) * np.float32(BUCKETS - half)).astype(np.int32)
    b = np.where(n < half, n, np.minimum(large, BUCKETS - 1))
    return np.where(dist < 0, BUCKETS, b)


def one_hot(bucket):
    return np.moveaxis(np.eye(NB, dtype=np.float32)[bucket], -1, 0)


def shape_constants():
    c = {}
    c["ident"] = np.eye(P, dtype=np.float32)
    c["head_ones"] = np.kron(np.eye(2, dtype=np.float32), np.ones((DH, DH), np.float32))
    for g, dil in enumerate(DILS[:2]):
        rel = 255 - np.arange(383)
        c[f"line{g}"] = one_hot(rel_bucket(np.where((rel >= 0) & (rel <= WINDOWS[g] // dil), rel * dil, -1)))
    rel = 127 - np.arange(255)
    c["line2"] = one_hot(rel_bucket(np.where((rel >= 0) & (rel % 2 == 0), rel * (DILS[2] // 2), -1)))
    c["line_dsa"] = one_hot(rel_bucket(1023 - np.arange(1151)))
    for g, dil in enumerate(DILS):
        nk = 64 if g == 2 else 128
        rows = []
        for l in range(L_NEW):
            j = np.arange(nk)
            cached = np.where(j >= l, 128 + l - j, -1) if g == 0 else dil * (nk - j)
            new = l - np.arange(L_NEW)
            if g:
                new = np.where(new == 0, 0, -1)
            rows.append(one_hot(rel_bucket(np.concatenate([cached, np.tile(new, N_SEQ)]))))
        c[f"sample_hot{g}"] = np.stack(rows, 1)
    n_of, l_of = np.arange(TS) // L_NEW, np.arange(TS) % L_NEW
    c["tri"] = np.where(np.arange(P)[None] <= np.arange(P)[:, None], 0, MASKED).astype(np.float32)
    c["causal_T"] = (np.arange(P)[:, None] <= np.arange(P)[None]).astype(np.float32)
    c["chunk_inside"] = np.concatenate([np.arange(SEQ) % P != 0, l_of != 0]).astype(np.float32)[None]
    c["sample_causal_T"] = ((n_of[:, None] == n_of[None]) & (l_of[:, None] <= l_of[None])).astype(np.float32)
    c["seq_of"] = (n_of[:, None] == np.arange(N_SEQ)[None]).astype(np.float32)
    row = np.arange(P)
    tok = lambda half, l: (4 * half + row // 32) * L_NEW + l
    c["index_rows"] = np.stack([((np.arange(TS)[:, None] == tok(g, row % 4)[None]) & (row % 32 < 16)[None]) for g in range(2)], 1).astype(np.float32)
    c["dsa_rows"] = np.stack([np.arange(TS)[:, None] == tok(g, row % 4)[None] for g in range(2)], 1).astype(np.float32)
    c["dsa_other"] = np.stack([np.where(n_of[None] == (4 * g + row // 32)[:, None], 0, MASKED) for g in range(2)], 1).astype(np.float32)
    c["new_mask"] = np.where(np.arange(L_NEW)[None] <= l_of[:, None], 0, MASKED).astype(np.float32)
    key = np.arange(PAST)
    c["dsa_hot"] = np.stack([one_hot(rel_bucket(PAST + l - key)) for l in range(L_NEW)], 1)
    c["dsa_hot_new"] = np.stack([one_hot(rel_bucket(np.tile(l - np.arange(L_NEW), N_SEQ))) for l in range(L_NEW)], 1)
    row_n = np.arange(P) // (L_NEW * HPG)
    c["other_seq"] = np.where(row_n[:, None] == np.arange(TS)[None] // L_NEW, 0, MASKED).astype(np.float32)
    f = np.arange(GW) // DH
    c["feat_head"] = (f[:, None] == np.arange(HPG)[None]).astype(np.float32).reshape(2, P, HPG).transpose(1, 0, 2).copy()
    c["dsa_row_head"] = (np.arange(P)[:, None] // L_NEW % DSA_H == np.arange(DSA_H)[None]).astype(np.float32)
    c["row_head"] = (np.arange(P)[:, None] % HPG == np.arange(HPG)[None]).astype(np.float32)
    return c


class Stage:
    pass


LIVE_SEMAPHORES = []


def add_sems(nc, *names):
    sems = [nc.alloc_semaphore(n) for n in names]
    LIVE_SEMAPHORES.extend(sems)
    return sems


def recycle_semaphores(nc):
    nc.clear_and_free_semaphores(list(LIVE_SEMAPHORES))
    LIVE_SEMAPHORES.clear()
    nc.all_engine_barrier()


def chain(eng, sem):
    count = [0]

    def done(ins):
        count[0] += 1
        ins.then_inc(sem, 1)
        eng.wait_ge(sem, count[0])
        return ins
    return done


def load_inputs(nc, S, xT):
    with ExitStack() as ctx:
        xrow = ctx.enter_context(nc.sbuf_tensor("xrow", [P, QT + 1, D_MODEL], F32))
        loaded, gains, transposed, evacuated = add_sems(nc, "x_loaded", "gains_loaded", "x_transposed", "x_evacuated")
        ps = S.ps[:, 0:3072].rearrange("p (b c) -> p b c", b=2)
        block = ctx.enter_context(nc.Block())

        @block.sync
        def _(sp):
            sp.dma_start(S.ident[:, :], S.c["ident"]).then_inc(loaded, 16)
            for t in range(QT):
                sp.dma_start(xrow[:, t, :], S.d["x_prompt"][0, t * P:(t + 1) * P, :]).then_inc(loaded, 16)
            sp.dma_start(xrow[0:TS, QT, :], S.d["x_sample"].rearrange("n l d -> (n l) d")).then_inc(loaded, 16)
            sp.dma_start(S.head_ones[:, :], S.c["head_ones"]).then_inc(gains, 16)
            for name, dst in (("norm_mix", S.g_mix), ("norm_ffn", S.g_ffn)):
                for layer in range(2):
                    sp.dma_start(dst[:, layer, :], S.d[name][layer].rearrange("(k p) -> p k", p=P)).then_inc(gains, 16)
            for i, name in enumerate(("qn_ab", "kn_ab", "qn_cd", "kn_cd")):
                for half in range(2):
                    sp.dma_start(S.g_qk[half * DH:(half + 1) * DH, i:i + 1], S.d[name].rearrange("a d -> d a")).then_inc(gains, 16)
            sp.dma_start(S.g_gla[:, :], S.d["gla_norm"].rearrange("a v -> v a")).then_inc(gains, 16)
            sp.dma_start(S.tab[0:BUCKETS, :], S.d["rel_bias"]).then_inc(gains, 16)
            sp.wait_ge(gains, 16 * 15)

        @block.gpsimd
        def _(pool):
            pool.memset(S.ones[:, :], 1.0)

        @block.tensor
        def _(pe):
            pe.wait_ge(loaded, 16 * (QT + 2))
            for k in range(KD):
                if k >= 2:
                    pe.wait_ge(evacuated, k - 1)
                for t in range(QT + 1):
                    n = P if t < QT else TS
                    last = pe.transpose(ps[:, k % 2, t * P:t * P + n], xrow[0:n, t, k * P:(k + 1) * P], S.ident[0:n, 0:n])
                last.then_inc(transposed, 1)

        @block.vector
        def _(dve):
            dve.memset(S.tab[BUCKETS:NB, :], MASKED)
            dve.memset(S.eps[:, :], EPS)
            dve.wait_ge(gains, 16 * 15)
            dve.tensor_scalar(S.g_qk[:, 2:3], S.g_qk[:, 2:3], DH ** -0.5, None, ALU.mult)
            for k in range(KD):
                dve.wait_ge(transposed, k + 1)
                dve.tensor_copy(xT[:, k, :], ps[:, k % 2, 0:T]).then_inc(evacuated, 1)


class Parts:

    def __init__(self, nc, ctx, name, shape):
        tile = ctx.enter_context(nc.sbuf_tensor(name, [P, 2, *shape], F32R))
        self.hi, self.lo = tile[:, 0], tile[:, 1]


def passes(stationary, moving):
    return (stationary.lo, moving.hi), (stationary.hi, moving.lo), (stationary.hi, moving.hi)


def rms_norm(nc, S, tag, gain, xT, h, scratch, spill=None, W=None, first=()):
    sq, rstd, normed = scratch[:, 0:2, :], scratch[:, 2, :], scratch[:, 3:5, :]
    with ExitStack() as ctx:
        squared, summed, mean_ready, rstd_ready, normalised, hi_made, lo_made, lo_made_odd, spilled = add_sems(
            nc, *(f"{x}_{tag}" for x in ("squared", "summed", "mean_ready", "rstd_ready", "normalised", "h_hi_made", "h_lo_made", "h_lo_made_odd", "x_spilled")))
        block = ctx.enter_context(nc.Block())

        @block.sync
        def _(sp):
            for j, src in enumerate(first):
                sp.dma_start(W.raw[:, :, j, :], src).then_inc(W.loaded[j], 16)
            if spill is not None:
                sp.dma_start(spill, xT).then_inc(spilled, 16)
                sp.wait_ge(spilled, 16)

        @block.scalar
        def _(act):
            for k in range(KD):
                if k >= 2:
                    act.wait_ge(summed, k - 1)
                act.activation(sq[:, k % 2, :], xT[:, k, :], ACT.Square).then_inc(squared, 1)
            for j in range(len(first)):
                W.high(act, j, 1, KD)
            act.wait_ge(summed, KD)
            act.activation(by3(rstd), slot(S, 0), ACT.Ln, scale=1.0 / D_MODEL, bias=S.eps[:, :]).then_inc(mean_ready, 1)
            act.wait_ge(mean_ready, 1)
            act.activation(rstd, rstd, ACT.Exp, scale=-0.5).then_inc(rstd_ready, 1)
            for k in range(KD):
                act.wait_ge(normalised, k + 1)
                act.activation(h.hi[:, k, :], normed[:, k % 2, :], ACT.Copy).then_inc(hi_made, 1)

        @block.tensor
        def _(pe):
            for k in range(KD):
                pe.wait_ge(squared, k + 1)
                for at, t, n in PIECES:
                    last = pe.matmul(S.ps[:, at:at + n], S.ones[:, :], sq[:, k % 2, t:t + n], start=k == 0, stop=k == KD - 1)
                last.then_inc(summed, 1)

        @block.gpsimd
        def _(pool):
            for j in range(len(first)):
                pool.sem_inc(W.lo_made[j], 1)
                W.low(pool, j, 1, KD)
            for k in range(1, KD, 2):
                pool.wait_ge(hi_made, k + 1)
                pool.tensor_tensor(h.lo[:, k, :], normed[:, k % 2, :], h.hi[:, k, :], ALU.subtract).then_inc(lo_made_odd, 1)

        @block.vector
        def _(dve):
            def low_part(k):
                if k % 2 == 0:
                    dve.wait_ge(hi_made, k + 1)
                    dve.tensor_tensor(h.lo[:, k, :], normed[:, k % 2, :], h.hi[:, k, :], ALU.subtract).then_inc(lo_made, 1)

            dve.wait_ge(rstd_ready, 1)
            for k in range(KD):
                if k >= 2:
                    dve.wait_ge(lo_made_odd if k % 2 else lo_made, k // 2)
                dve.scalar_tensor_tensor(normed[:, k % 2, :], xT[:, k, :], gain[:, k:k + 1], rstd, ALU.mult, ALU.mult).then_inc(normalised, 1)
                if k:
                    low_part(k - 1)
            low_part(KD - 1)


class Weights:

    def __init__(self, nc, ctx, tag):
        self.raw = ctx.enter_context(nc.sbuf_tensor(f"w_{tag}", [P, KD, 2, P], F32))
        self.parts = Parts(nc, ctx, f"w_parts_{tag}", [KD, 2, P])
        self.loaded, self.hi_made, self.lo_made, self.product, self.free = (
            add_sems(nc, *(f"{what}{j}_{tag}" for j in range(2))) for what in ("w_loaded", "w_hi_made", "w_lo_made", "product", "slot_free"))

    def load(self, sp, j, n, kt, src):
        sp.wait_ge(self.lo_made[j], n)
        sp.dma_start(self.raw[:, 0:kt, j, :], src).then_inc(self.loaded[j], 16)

    def high(self, act, j, n, kt):
        act.wait_ge(self.loaded[j], n * 16)
        if type(n) is int and n == 1:
            act.sem_inc(self.product[j], 1)
        else:
            act.wait_ge(self.product[j], n)
        act.activation(self.parts.hi[:, 0:kt, j, :], self.raw[:, 0:kt, j, :], ACT.Copy).then_inc(self.hi_made[j], 1)

    def low(self, eng, j, n, kt):
        eng.wait_ge(self.hi_made[j], n)
        eng.tensor_tensor(self.parts.lo[:, 0:kt, j, :], self.raw[:, 0:kt, j, :], self.parts.hi[:, 0:kt, j, :], ALU.subtract).then_inc(self.lo_made[j], 1)


def load_weight_pairs(sp, W, kt, iters, src_a, src_b, before=0, there=0):
    with sp.Fori(1 + there, iters + 1) as i:
        for j, (w, step, col) in enumerate((src_a, src_b)):
            W.load(sp, j, i + before, kt, w[:, 0:kt, bass.ds(i * step + (col - step), P)])


def multiply_pairs(pe, S, W, kt, iters, rhs, before=0, made=None):
    with pe.Fori(0, iters) as i:
        for j in range(2):
            pe.wait_ge(W.lo_made[j], i + (before + 2))
            pe.wait_ge(W.free[j], i + (before + 1))
            for k in range(kt):
                if made:
                    pe.wait_ge(made[0], made[1] + k + 1)
                for n, (w, x) in enumerate(passes(W.parts, rhs)):
                    for c, (at, t, size) in enumerate(PIECES):
                        last = pe.matmul(S.ps[:, j * 1536 + at:j * 1536 + at + size], w[:, k, j, :], x[:, k, t:t + size],
                                         start=k == 0 and n == 0, stop=k == kt - 1 and n == 2)
                        if k == kt - 1 and n == 2 and c == 2:
                            last.then_inc(W.product[j], 1)


def w_cols(w, col):
    return w.rearrange("(k p) m -> p k m", p=P), P, col


def w_pairs(w, col):
    v = w.rearrange("(k p) m -> p k m", p=P)
    return (v, 2 * P, col), (v, 2 * P, col + P)


def slot(S, j):
    return S.ps[:, j * 1536:(j + 1) * 1536].rearrange("p (c t) -> p c t", c=3)[:, :, 0:PIECE]


def by3(line):
    return line.rearrange("p (c t) -> p c t", c=3)


LINES = ((0, 383), (383, 383), (766, 255))
AB_LINE, DSA_LINE = 1021, 1151


def bias_lines(nc, S):
    with ExitStack() as ctx:
        sb = lambda n, s: ctx.enter_context(nc.sbuf_tensor(n, s, F32))
        hot, hot_d = sb("hot", [NB, AB_LINE]), sb("hot_dsa", [NB, DSA_LINE])
        line, line_d = sb("line", [HPG, 3, BANK]), sb("line_dsa", [DSA_H, DSA_LINE])
        loaded, product, kept, out = add_sems(nc, "hot_loaded", "lines_product", "lines_kept", "lines_out")
        block = ctx.enter_context(nc.Block())

        @block.sync
        def _(sp):
            for g, (at, n) in enumerate(LINES):
                sp.dma_start(hot[:, at:at + n], S.c[f"line{g}"]).then_inc(loaded, 16)
            sp.dma_start(hot_d[:, :], S.c["line_dsa"]).then_inc(loaded, 16)
            sp.wait_ge(kept, 2)
            for g, (at, n) in enumerate(LINES):
                sp.dma_start(S.ab_line[:, at:at + n], line[:, g, 0:n]).then_inc(out, 16)
            sp.dma_start(S.dsa_line, line_d[:, :]).then_inc(out, 16)
            sp.wait_ge(out, 64)
            for h in range(HPG):
                sp.dma_start(S.ab_copies[h], S.ab_line[h:h + 1, :].broadcast_to([P, AB_LINE])).then_inc(S.ab_lines, 16)
            for h in range(DSA_H):
                sp.dma_start(S.dsa_copies[h], S.dsa_line[h:h + 1, :].broadcast_to([P, DSA_LINE])).then_inc(S.dsa_lines, 16)

        @block.tensor
        def _(pe):
            pe.wait_ge(loaded, 64)
            for g, (at, n) in enumerate(LINES):
                last = pe.matmul(S.ps[0:HPG, g * BANK:g * BANK + n], S.tab[:, g * HPG:(g + 1) * HPG], hot[:, at:at + n], start=True, stop=True)
            for at in range(0, DSA_LINE, BANK):
                n = min(BANK, DSA_LINE - at)
                last = pe.matmul(S.ps[0:DSA_H, 1536 + at:1536 + at + n], S.tab[:, 12:12 + DSA_H], hot_d[:, at:at + n], start=True, stop=True)
            last.then_inc(product, 1)

        @block.vector
        def _(dve):
            dve.wait_ge(product, 1)
            for g, (at, n) in enumerate(LINES):
                last = dve.tensor_copy(line[:, g, 0:n], S.ps[0:HPG, g * BANK:g * BANK + n])
            last.then_inc(kept, 1)
            dve.tensor_copy(line_d[:, :], S.ps[0:DSA_H, 1536:1536 + DSA_LINE]).then_inc(kept, 1)


def toeplitz(copies, line, at, heads, step, n):
    return bass.AP(copies.tensor, heads.start * P * line + at + P - 1, [[line - 1, P], [step * P * line, (heads.stop - heads.start) // step], [1, n]])


U_PROMPT = HIST + SEQ
U_SEQ = HIST + L_NEW
U_LEN = U_PROMPT + N_SEQ * U_SEQ


def glu_products(nc, S, W, uT, taps, scratch):
    with ExitStack() as ctx:
        gate = scratch[:, 0, :]
        hist = scratch[0:120, 1, 0:2 * CONV_CH].rearrange("p (a c) -> p a c", a=2)
        tap_rows = scratch[0:TAPS, 2, 0:CONV_CH]
        hist_loaded, turned, placed = add_sems(nc, "hist_loaded", "hist_turned", "hist_placed")
        w = S.d["w_in_ab"][0]
        us = uT[:, :, U_PROMPT:].rearrange("p c (n u) -> p c n u", n=N_SEQ)
        turn = S.ps[:, 3072:3584]
        in_third = SEQ - 2 * PIECE
        block = ctx.enter_context(nc.Block())

        @block.sync
        def _(sp):
            for half in range(2):
                sp.dma_start(hist[:, half, :], S.d["state_conv"][0, 4 * half:4 * half + 4].rearrange("n r c -> (n r) c")).then_inc(hist_loaded, 16)
            sp.dma_start(tap_rows, S.d["conv_w"][0]).then_inc(hist_loaded, 16)
            load_weight_pairs(sp, W, KD, CC, w_cols(w, CONV_CH), w_cols(w, 0), there=1)

        @block.tensor
        def _(pe):
            pe.wait_ge(hist_loaded, 48)
            for c in range(CC):
                last = pe.transpose(turn[:, 256 + c * TAPS:256 + (c + 1) * TAPS], tap_rows[:, c * P:(c + 1) * P], S.ident[0:TAPS, 0:TAPS])
            last.then_inc(turned, 1)
            for c in range(CC):
                pe.wait_ge(placed, 2 * c + 1)
                for half in range(2):
                    last = pe.transpose(turn[:, 120 * half:120 * half + 120], hist[:, half, c * P:(c + 1) * P], S.ident[0:120, 0:120])
                last.then_inc(turned, 1)
            multiply_pairs(pe, S, W, KD, CC, S.h)

        @block.scalar
        def _(act):
            def sigmoid(i):
                act.wait_ge(W.product[0], i + 2)
                act.wait_ge(W.free[1], i + 1)
                act.activation(by3(gate), slot(S, 0), ACT.Sigmoid).then_inc(W.free[0], 1)

            act.sem_inc(W.free[0], 1)
            with act.Fori(0, CC - 1) as i:
                W.high(act, 0, i + 2, KD)
                sigmoid(i)
                W.high(act, 1, i + 2, KD)
            sigmoid(CC - 1)

        @block.vector
        def _(dve):
            def glu(i):
                dve.wait_ge(W.product[1], i + 2)
                dve.wait_ge(W.free[0], i + 2)
                dve.tensor_tensor(us[:, bass.ds(i, 1), :, HIST:].rearrange("p a n u -> p (a n) u"),
                                  S.ps[:, 1536 + 2 * BANK + in_third:1536 + 2 * BANK + PIECE].rearrange("p (n u) -> p n u", n=N_SEQ),
                                  gate[:, SEQ:T].rearrange("p (n u) -> p n u", n=N_SEQ), ALU.mult)
                u = uT[:, bass.ds(i, 1), HIST:U_PROMPT].rearrange("p a t -> p (a t)")
                dve.tensor_tensor(u[:, 2 * PIECE:SEQ], S.ps[:, 1536 + 2 * BANK:1536 + 2 * BANK + in_third], gate[:, 2 * PIECE:SEQ], ALU.mult)
                dve.tensor_tensor(u[:, 0:2 * PIECE].rearrange("p (c t) -> p c t", c=2), slot(S, 1)[:, 0:2, :],
                                  gate[:, 0:2 * PIECE].rearrange("p (c t) -> p c t", c=2), ALU.mult).then_inc(W.free[1], 1)

            dve.memset(uT[:, :, 0:HIST], 0.0)
            dve.wait_ge(turned, 1)
            dve.tensor_copy(taps[:, :, :], turn[:, 256:256 + CC * TAPS].rearrange("p (c t) -> p c t", c=CC)).then_inc(placed, 1)
            for c in range(CC):
                dve.wait_ge(turned, c + 2)
                for half in range(2):
                    dve.tensor_copy(us[:, c, 4 * half:4 * half + 4, 0:HIST],
                                    turn[:, 120 * half:120 * half + 120].rearrange("p (n r) -> p n r", n=4)).then_inc(placed, 1)
            dve.sem_inc(W.free[1], 1)
            with dve.Fori(0, CC - 1) as i:
                W.low(dve, 0, i + 2, KD)
                W.low(dve, 1, i + 2, KD)
                glu(i)
            glu(CC - 1)


def qkv_products(nc, S, uT, taps, yT, vS, v_new):
    with ExitStack() as ctx:
        W = Weights(nc, ctx, "qk")
        conv_bias = ctx.enter_context(nc.sbuf_tensor("conv_bias", [P, CC], F32))
        v_product, v_kept, bias_loaded, conv_step = add_sems(nc, "v_product", "v_kept", "bias_loaded", "conv_step")
        w = S.d["w_in_ab"][0]
        vps = S.ps[:, 3072:4096].rearrange("p (b c) -> p b c", b=2)
        us = uT[:, :, U_PROMPT:].rearrange("p c (n u) -> p c n u", n=N_SEQ)
        QK_PAIRS, V_PAIRS = 6, 3
        block = ctx.enter_context(nc.Block())

        @block.sync
        def _(sp):
            sp.dma_start(conv_bias[:, :], S.d["conv_b"][0].rearrange("(c p) -> p c", p=P)).then_inc(bias_loaded, 16)
            load_weight_pairs(sp, W, KD, QK_PAIRS + V_PAIRS, *w_pairs(w, 2 * CONV_CH))

        @block.tensor
        def _(pe):
            multiply_pairs(pe, S, W, KD, QK_PAIRS, S.h)
            value_products(pe, S, W, vps, v_product, v_kept, V_PAIRS, QK_PAIRS,
                           lambda g, b, line: block_tokens(g, b, line[:, 0:SEQ]) if b < QT else line[:, SEQ:T])

        @block.scalar
        def _(act):
            def keep(i):
                for j in range(2):
                    act.wait_ge(W.product[j], i + 2)
                    act.activation(S.qk[:, bass.ds(i * 2 + j, 1), :].rearrange("p a (c t) -> p (a c) t", c=3), slot(S, j), ACT.Copy).then_inc(W.free[j], 1)
                    W.high(act, j, i + 2, KD)

            for j in range(2):
                act.sem_inc(W.free[j], 1)
                W.high(act, j, 1, KD)
            with act.Fori(0, QK_PAIRS - 1) as i:
                keep(i)
            keep(QK_PAIRS - 1)
            keep_values(act, W, vps, lambda g, b: vS[:, g, b, :] if b < QT else v_new[:, g, :], v_product, v_kept, V_PAIRS, QK_PAIRS)

        @block.gpsimd
        def _(pool):
            for j in range(2):
                pool.sem_inc(W.lo_made[j], 1)
            with pool.Fori(1, QK_PAIRS + V_PAIRS + 1) as n:
                for j in range(2):
                    W.low(pool, j, n, KD)

        @block.vector
        def _(dve):
            ysmp = yT[:, :, SEQ:T].rearrange("p c (n l) -> p c n l", n=N_SEQ)
            dve.wait_ge(bias_loaded, 16)
            for c in range(CC):
                dve.tensor_scalar(yT[:, c, 0:SEQ], uT[:, c, 0:SEQ], taps[:, c, 0:1], conv_bias[:, c:c + 1], ALU.mult, ALU.add).then_inc(conv_step, 1)
                dve.tensor_scalar(ysmp[:, c], us[:, c, :, 0:L_NEW], taps[:, c, 0:1], conv_bias[:, c:c + 1], ALU.mult, ALU.add).then_inc(conv_step, 1)
            with dve.Fori(1, TAPS) as t:
                for c in range(CC):
                    dve.wait_ge(conv_step, t * (2 * CC) + (2 * c + 2 - 2 * CC))
                    dve.scalar_tensor_tensor(yT[:, c, 0:SEQ], uT[:, c, bass.ds(t, SEQ)], taps[:, c, bass.ds(t, 1)], yT[:, c, 0:SEQ],
                                             ALU.mult, ALU.add).then_inc(conv_step, 1)
                    dve.scalar_tensor_tensor(ysmp[:, c], us[:, c, :, bass.ds(t, L_NEW)], taps[:, c, bass.ds(t, 1)], ysmp[:, c],
                                             ALU.mult, ALU.add).then_inc(conv_step, 1)


def value_products(pe, S, W, vps, product, kept, groups, before, tokens):
    for n in range(groups * (QT + 1)):
        g, b = divmod(n, QT + 1)
        if b == 0:
            for j in range(2):
                pe.wait_ge(W.lo_made[j], before + g + 2)
        if n >= 2:
            pe.wait_ge(kept, n - 1)
        m = P if b < QT else TS
        for k in range(KD):
            for i, (x, w) in enumerate(passes(S.h, W.parts)):
                last = pe.matmul(vps[0:m, n % 2, 0:GW], tokens(g, b, x[:, k, :]), w[:, k].rearrange("p j c -> p (j c)"),
                                 start=k == 0 and i == 0, stop=k == KD - 1 and i == 2)
        last.then_inc(product, 1)


def keep_values(act, W, vps, dst, product, kept, groups, before):
    for n in range(groups * (QT + 1)):
        g, b = divmod(n, QT + 1)
        act.wait_ge(product, n + 1)
        if b == QT and g + 1 < groups:
            for j in range(2):
                act.wait_ge(W.loaded[j], 16 * (before + g + 2))
                act.activation(W.parts.hi[:, :, j, :], W.raw[:, :, j, :], ACT.Copy).then_inc(W.hi_made[j], 1)
        m = P if b < QT else TS
        act.activation(dst(g, b)[0:m], vps[0:m, n % 2, 0:GW], ACT.Copy).then_inc(kept, 1)


def block_tokens(g, b, line):
    if g == 0:
        return line[:, b * P:(b + 1) * P]
    if g == 1:
        r, half = b // 2, b % 2
        return line.rearrange("p (j r) -> p r j", r=4)[:, r, half * P:(half + 1) * P]
    return line.rearrange("p (j r) -> p r j", r=8)[:, b, :]


def block_keys(g, b, line):
    if g == 0 and b:
        return line[:, (b - 1) * P:(b + 1) * P]
    if g == 1 and b % 2:
        return line.rearrange("p (j r) -> p r j", r=4)[:, b // 2, :]
    return block_tokens(g, b, line)


def has_previous(g, b):
    return (g == 0 and b > 0) or (g == 1 and b % 2 == 1)


def dram_rows(g, b, rows):
    if g == 0:
        return rows[b * P:(b + 1) * P, :]
    if g == 1:
        return rows.rearrange("(j r) x -> r j x", r=4)[b // 2, (b % 2) * P:(b % 2 + 1) * P, :]
    return rows.rearrange("(j r) x -> r j x", r=8)[b]


def head_norms(nc, S, tag, src, tiles, gains, ones, dim):
    n = len(tiles)
    GROUP = 4
    R = min(n, 2 * GROUP)
    with ExitStack() as ctx:
        sq = ctx.enter_context(nc.sbuf_tensor(f"hsq_{tag}", [P, 2, T], F32))
        rstd = ctx.enter_context(nc.sbuf_tensor(f"hrstd_{tag}", [P, R, T], F32))
        squared, summed, logged, rstd_ready, scaled = add_sems(
            nc, *(f"{x}_{tag}" for x in ("hsquared", "hsummed", "hlogged", "hrstd_ready", "hscaled")))
        block = ctx.enter_context(nc.Block())

        @block.scalar
        def _(act):
            for first in range(0, n, GROUP):
                for i in range(first, first + GROUP):
                    act.wait_ge(summed, i + 1)
                    if i >= R:
                        act.wait_ge(scaled, i - R + 1)
                    act.activation(by3(rstd[:, i % R, :]), slot(S, i % 2), ACT.Ln, scale=1.0 / dim, bias=S.eps[:, :]).then_inc(logged, 1)
                for i in range(first, first + GROUP):
                    act.wait_ge(logged, i + 1)
                    act.activation(rstd[:, i % R, :], rstd[:, i % R, :], ACT.Exp, scale=-0.5).then_inc(rstd_ready, 1)

        @block.tensor
        def _(pe):
            for i in range(n):
                pe.wait_ge(squared, i + 1)
                if i >= 2:
                    pe.wait_ge(logged, i - 1)
                for at, t, m in PIECES:
                    last = pe.matmul(S.ps[:, (i % 2) * 1536 + at:(i % 2) * 1536 + at + m], ones[:, :], sq[:, i % 2, t:t + m],
                                     start=True, stop=True)
                last.then_inc(summed, 1)

        @block.vector
        def _(dve):
            def square(i):
                if i >= 2:
                    dve.wait_ge(summed, i - 1)
                dve.tensor_tensor(sq[:, i % 2, :], src[:, tiles[i], :], src[:, tiles[i], :], ALU.mult).then_inc(squared, 1)

            for i in range(min(n, GROUP)):
                square(i)
            for i in range(n):
                dve.wait_ge(rstd_ready, i + 1)
                dve.scalar_tensor_tensor(src[:, tiles[i], :], src[:, tiles[i], :], gains[i], rstd[:, i % R, :],
                                         ALU.mult, ALU.mult).then_inc(scaled, 1)
                if i + GROUP < n:
                    square(i + GROUP)


def turn_and_store(nc, S, tag, jobs, direct):
    with ExitStack() as ctx:
        stage = ctx.enter_context(nc.sbuf_tensor(f"turn_stage_{tag}", [P, 4, 512], F32))
        turned, copied, rows_out = add_sems(nc, f"turned_{tag}", f"turn_copied_{tag}", f"direct_out_{tag}")
        stored = add_sems(nc, *(f"turn_stored{i}_{tag}" for i in range(4)))
        stores_before = lambda i: sum(len(jobs[j][2]) for j in range(i % 4, i, 4))
        block = ctx.enter_context(nc.Block())

        @block.tensor
        def _(pe):
            for i, (tiles, n, _) in enumerate(jobs):
                if i >= 2:
                    pe.wait_ge(copied, i - 1)
                for f, tile in enumerate(tiles):
                    last = pe.transpose(S.ps[0:n, (i % 2) * BANK + f * P:(i % 2) * BANK + (f + 1) * P], tile, S.ident[:, :])
                last.then_inc(turned, 1)

        @block.vector
        def _(dve):
            for i, (tiles, n, _) in enumerate(jobs):
                dve.wait_ge(turned, i + 1)
                if i >= 4:
                    dve.wait_ge(stored[i % 4], 16 * stores_before(i))
                dve.tensor_copy(stage[0:n, i % 4, 0:P * len(tiles)], S.ps[0:n, (i % 2) * BANK:(i % 2) * BANK + P * len(tiles)]).then_inc(copied, 1)

        @block.sync
        def _(sp):
            for i, (tiles, n, outs) in enumerate(jobs):
                sp.wait_ge(copied, i + 1)
                for first, end, width, dst in outs:
                    sp.dma_start(dst, stage[first:end, i % 4, 0:width]).then_inc(stored[i % 4], 16)
            for s in range(4):
                sp.wait_ge(stored[s], 16 * stores_before(len(jobs) + (s - len(jobs)) % 4))

        @block.scalar
        def _(act):
            for dst, src in direct:
                act.dma_start(dst, src).then_inc(rows_out, 16)
            act.wait_ge(rows_out, 16 * len(direct))


def layer0_states(nc, S, uT, vS, v_new, q_rows, k_rows, v_rows):
    o = S.o
    jobs = []
    jobs.append(([uT[:, c, U_PROMPT - HIST:U_PROMPT] for c in range(CC)], HIST, [(0, HIST, 512, o["conv_p"][0, 0])]))
    for n0 in range(0, N_SEQ, 3):
        ns = min(3, N_SEQ - n0)
        at = U_PROMPT + n0 * U_SEQ
        jobs.append(([uT[:, c, at:at + ns * U_SEQ] for c in range(CC)], ns * U_SEQ,
                     [(i * U_SEQ + L_NEW, (i + 1) * U_SEQ, 512, o["conv_s"][0, n0 + i]) for i in range(ns)]))
    for src, dst in ((0, q_rows), (6, k_rows)):
        jobs.append(([S.qk[:, src + f, SEQ:T] for f in range(4)], TS, [(0, TS, 512, dst[:, 0:512])]))
        jobs.append(([S.qk[:, src + f, SEQ:T] for f in range(4, 6)], TS, [(0, TS, 256, dst[:, 512:768])]))
    for g, name in enumerate(("win128_p", "win512_p", "win2048_p")):
        keep = min(WINDOWS[g], SEQ)
        rows = o[name][0, 0].rearrange("t a h d -> t a (h d)")
        for t in range(keep // P):
            at = SEQ - keep + t * P
            jobs.append(([S.qk[:, 6 + 2 * g + f, at:at + P] for f in range(2)], P, [(0, P, 256, rows[t * P:(t + 1) * P, 0, :])]))
    direct = [(v_rows.rearrange("t (g x) -> t g x", g=3), v_new[:, :, :])]
    for g, name in enumerate(("win128_p", "win512_p", "win2048_p")):
        rows = o[name][0, 0].rearrange("t a h d -> t a (h d)")
        if g == 0:
            direct.append((rows[:, 1, :], vS[:, 0, QT - 1, :]))
        elif g == 1:
            direct += [(rows.rearrange("(j r) a x -> r j a x", r=4)[r, :, 1, :], vS[:, 1, 2 * r + 1, :]) for r in range(4)]
        else:
            direct += [(rows.rearrange("(j r) a x -> r j a x", r=8)[r, :, 1, :], vS[:, 2, r, :]) for r in range(8)]
    turn_and_store(nc, S, "ab", jobs, direct)

    with ExitStack() as ctx:
        (new_rows,) = add_sems(nc, "new_rows_out")
        block = ctx.enter_context(nc.Block())

        @block.sync
        def _(sp):
            count = 0
            for g, name in enumerate(("win128_s", "win512_s", "win2048_s")):
                out = o[name][0].rearrange("n t a h d -> n t a (h d)")
                keep = out.shape[1]
                for a, rows in ((0, k_rows), (1, v_rows)):
                    sp.dma_start(out[:, keep - L_NEW:keep, a, :], rows[:, g * GW:(g + 1) * GW].rearrange("(n l) x -> n l x", n=N_SEQ)).then_inc(new_rows, 16)
                    count += 1
            sp.wait_ge(new_rows, 16 * count)


def dilated_prompt(nc, S, vS):
    with ExitStack() as ctx:
        sb = lambda n, s: ctx.enter_context(nc.sbuf_tensor(n, s, F32))
        toep = sb("toep", [P, 3, HPG, 256])
        sc = sb("sc", [P, 3, HPG, 256])
        pT = sb("pT", [P, 2, HPG, 256])
        row = sb("part_row", [P, 4, HPG, HEAD_ROW])
        toep_in, scored, biased, row_in, cache_out = add_sems(nc, "toep_in", "scored", "biased", "maxima_ready", "cache_out")
        exps, turned, kept, summed, sums_copied = add_sems(nc, "exps_done", "probs_turned", "probs_kept", "pv_summed", "sums_copied")
        stored = add_sems(nc, *(f"part_stored{i}" for i in range(4)))
        s_ps = S.ps[:, 0:2048].rearrange("p (b h k) -> p b h k", b=2, h=HPG)
        t_ps = S.ps[:, 2048:3072].rearrange("p (h k) -> p h k", h=HPG)
        o_ps = S.ps[:, 3072:4096].rearrange("p (b c) -> p b c", b=2)
        blocks = [(g, b) for g in range(3) for b in range(QT)]
        place = lambda h: 2 * (h % 2) + h // 2
        block = ctx.enter_context(nc.Block())

        @block.sync
        def _(sp):
            sp.wait_ge(S.ab_lines, 16 * HPG)
            for g, n in enumerate((256, 256, P)):
                for odd in range(2):
                    sp.dma_start(toep[:, g, 2 * odd:2 * odd + 2, 0:n],
                                 toeplitz(S.ab_copies, AB_LINE, LINES[g][0], slice(odd, odd + 4), 2, n)).then_inc(toep_in, 16)
            for i, (g, b) in enumerate(blocks):
                sp.wait_ge(sums_copied, i + 1)
                sp.wait_ge(exps, i + 1)
                dst = dram_rows(g, b, S.part_rows[g, 0:SEQ].rearrange("t h x -> t (h x)"))
                sp.dma_start(dst, row[:, i % 4, :, :].rearrange("p h x -> p (h x)")).then_inc(stored[i % 4], 16)
            for j in range(4):
                sp.wait_ge(stored[j], 16 * len(blocks) // 4)

        @block.tensor
        def _(pe):
            def scores(i):
                g, b = blocks[i]
                nk = 256 if has_previous(g, b) else P
                if i >= 2:
                    pe.wait_ge(biased, i - 1)
                for h in range(HPG):
                    f, base = 2 * g + h // 2, DH * (h % 2)
                    last = pe.matmul(s_ps[:, i % 2, place(h), 0:nk], block_tokens(g, b, S.qk[base:base + DH, f, 0:SEQ]),
                                     block_keys(g, b, S.qk[base:base + DH, 6 + f, 0:SEQ]), start=True, stop=True)
                last.then_inc(scored, 1)

            scores(0)
            scores(1)
            for i, (g, b) in enumerate(blocks):
                pe.wait_ge(exps, i + 1)
                if i:
                    pe.wait_ge(kept, i)
                kts = 2 if has_previous(g, b) else 1
                for h in range(HPG):
                    for kt in range(kts):
                        last = pe.transpose(t_ps[:, h, kt * P:(kt + 1) * P], sc[:, i % 3, place(h), kt * P:(kt + 1) * P], S.ident[:, :])
                last.then_inc(turned, 1)
                if i + 2 < len(blocks):
                    scores(i + 2)
                pe.wait_ge(kept, i + 1)
                if i >= 2:
                    pe.wait_ge(sums_copied, i - 1)
                for h in range(HPG):
                    for kt in range(kts):
                        v = vS[:, g, b - (kts - 1) + kt, h * DH:(h + 1) * DH]
                        last = pe.matmul(o_ps[:, i % 2, h * DH:(h + 1) * DH], pT[:, i % 2, h, kt * P:(kt + 1) * P], v,
                                         start=kt == 0, stop=kt == kts - 1)
                last.then_inc(summed, 1)

        @block.vector
        def _(dve):
            def copy_sums(i):
                dve.wait_ge(summed, i + 1)
                dve.tensor_copy(row[:, i % 4, :, 0:DH], o_ps[:, i % 2, 0:GW].rearrange("p (h d) -> p h d", h=HPG)).then_inc(sums_copied, 1)

            dve.wait_ge(toep_in, 96)
            for i, (g, b) in enumerate(blocks):
                nk = 256 if has_previous(g, b) else P
                off = 0 if nk == 256 or g == 2 else P
                dve.wait_ge(scored, i + 1)
                if i >= 3:
                    dve.wait_ge(turned, i - 2)
                dve.scalar_tensor_tensor(sc[:, i % 3, :, 0:nk], s_ps[:, i % 2, :, 0:nk], DH ** -0.5, toep[:, g, :, off:off + nk],
                                         ALU.mult, ALU.add).then_inc(biased, 1)
                dve.wait_ge(biased, i + 1)
                if i >= 4:
                    dve.wait_ge(stored[i % 4], 16 * (i // 4))
                dve.tensor_reduce(row[:, i % 4, :, AT_M].rearrange("p (b a) -> p a b", a=2), sc[:, i % 3, :, 0:nk], AX.X, ALU.max, negate=True).then_inc(row_in, 1)
                if i >= 2:
                    copy_sums(i - 2)
            for i in range(len(blocks) - 2, len(blocks)):
                copy_sums(i)

        @block.scalar
        def _(act):
            def exponentials(i):
                g, b = blocks[i]
                kts = 2 if has_previous(g, b) else 1
                act.wait_ge(row_in, i + 1)
                for h in range(HPG):
                    last = act.activation(sc[:, i % 3, place(h), 0:kts * P], sc[:, i % 3, place(h), 0:kts * P], ACT.Exp,
                                          bias=row[:, i % 4, h, AT_M:AT_M + 1], accum_out=row[:, i % 4, h, AT_L:AT_L + 1])
                    if h == HPG - 1:
                        last.then_inc(exps, 1)

            exponentials(0)
            for i, (g, b) in enumerate(blocks):
                kts = 2 if has_previous(g, b) else 1
                name, cache = ("win128_s", "win512_s", "win2048_s")[g], S.d[("cache_win128", "cache_win512", "cache_win2048")[g]][0]
                old = cache.shape[1]
                keep = min(WINDOWS[g], old + L_NEW) - L_NEW
                act.dma_start(S.o[name][0, b, 0:keep].rearrange("t a h d -> t (a h d)"),
                              cache[b, old - keep:old].rearrange("t a h d -> t (a h d)")).then_inc(cache_out, 16)
                if i + 1 < len(blocks):
                    exponentials(i + 1)
                act.wait_ge(turned, i + 1)
                if i >= 2:
                    act.wait_ge(summed, i - 1)
                act.activation(pT[:, i % 2, :, 0:kts * P], t_ps[:, :, 0:kts * P], ACT.Copy).then_inc(kept, 1)
            act.wait_ge(cache_out, 16 * len(blocks))


def dilated_sample(nc, S, g, q_rows, v_rows_sb, make_beside):
    nk = 64 if g == 2 else P
    dil = DILS[g]
    cache = S.d[("cache_win128", "cache_win512", "cache_win2048")[g]][0]
    with ExitStack() as ctx:
        tag = f"g{g}"
        sb = lambda n, s: ctx.enter_context(nc.sbuf_tensor(f"{n}_{tag}", s, F32))
        lk = 1 if g == 0 else L_NEW
        HN = N_SEQ // 2
        kt = sb("kt", [nk, N_SEQ, lk, GW])
        vt = sb("vt", [nk, N_SEQ, lk, GW])
        qb = sb("qb", [nk, N_SEQ, L_NEW, GW])
        UNITS = N_SEQ * lk
        OWN = P // UNITS
        spread = qb[:, :, :, :].rearrange("k n l x -> k (n l x)")[:, 0:UNITS * (P + OWN)]
        hot = sb("shot", [NB, L_NEW, nk + TS])
        tabr = sb("tabr", [NB, L_NEW, P])
        other = sb("other", [P, TS])
        fh = sb("fh", [P, 2, HPG])
        rh = sb("rh", [P, HPG])
        qx = sb("qx", [P, 2, P])
        cs = sb("cs", [nk, P])
        bias = sb("bias", [P, nk + TS])
        sc = sb("ssc", [P, nk + TS])
        pT = sb("spT", [TS, P])
        new = sb("snew", [P, HPG, DH])
        row = sb("srow", [P, HEAD_ROW])
        beside = make_beside(ctx)
        u, neg_max, sum_p = row[:, 0:DH], row[:, AT_M:AT_M + 1], row[:, AT_L:AT_L + 1]
        keys_in = add_sems(nc, f"keys_in0_{tag}", f"keys_in1_{tag}")
        cin, vin, step, pstep, astep, out_done, others_masked, zeroed = add_sems(
            nc, *(f"{x}_{tag}" for x in ("consts_in", "values_in", "vector_step", "tensor_step", "exps_step", "rows_out", "others_masked", "spread_zeroed")))
        block = ctx.enter_context(nc.Block())
        b_ps = S.ps[:, 0:nk + TS]
        s_ps = S.ps[:, 512:512 + nk + TS]
        t_ps = S.ps[:, 1024:1024 + 2 * P]
        n_ps = S.ps[:, 2048:2048 + GW]

        def rows_of(n, a):
            c = cache[n].rearrange("t a h d -> t a (h d)")[:, a, :]
            if g == 0:
                return c
            return c.rearrange("(j r) x -> j r x", r=dil)[:, 0:L_NEW, :]

        @block.sync
        def _(sp):
            beside.sync(sp)
            for half in range(2):
                src = q_rows[half * HN * L_NEW:(half + 1) * HN * L_NEW, g * GW:(g + 1) * GW]
                sp.dma_start(qb[:, half * HN:(half + 1) * HN].rearrange("k n l x -> k (n l) x"),
                             bass.AP(src.tensor, src.offset, [[0, nk]] + [list(x) for x in src.ap])).then_inc(keys_in[half], 16)
                for n in range(half * HN, (half + 1) * HN):
                    sp.dma_start(kt[:, n, 0, :] if g == 0 else kt[:, n, :, :], rows_of(n, 0)).then_inc(keys_in[half], 16)
            for n in range(N_SEQ):
                sp.dma_start(vt[:, n, 0, :] if g == 0 else vt[:, n, :, :], rows_of(n, 1)).then_inc(vin, 16)

        @block.scalar
        def _(act):
            act.dma_start(hot[:, :, :], S.c[f"sample_hot{g}"]).then_inc(cin, 16)
            act.dma_start(other[:, :], S.c["other_seq"]).then_inc(cin, 16)
            act.dma_start(fh[:, :, :], S.c["feat_head"]).then_inc(cin, 16)
            act.dma_start(rh[:, :], S.c["row_head"]).then_inc(cin, 16)
            beside.scalar(act)
            act.wait_ge(step, 9)
            act.activation(sc[:, :], sc[:, :], ACT.Exp, bias=neg_max, accum_out=sum_p).then_inc(astep, 1)
            act.wait_ge(step, 12)
            act.wait_ge(astep, 1)
            act.dma_start(S.part_rows[g, SEQ:T].rearrange("t h x -> (t h) x"), row[:, :]).then_inc(out_done, 16)
            act.wait_ge(out_done, 16)

        @block.vector
        def _(dve):
            beside.vector(dve)
            done = chain(dve, step)
            for half in range(2):
                dve.wait_ge(keys_in[half], 16 * (HN + 1))
                own = slice(half * HN, (half + 1) * HN)
                kk = kt[:, own, 0:1, :].broadcast_to([nk, HN, L_NEW, GW]) if g == 0 else kt[:, own]
                done(dve.tensor_tensor(qb[:, own], qb[:, own], kk, ALU.mult))
                if half == 0:
                    done(dve.tensor_reduce(cs[:, 0:64], qb[:, own].rearrange("k n l (h d) -> k (n l h) d", h=HPG), AX.X, ALU.add))
                    done(dve.memset(tabr[:, :, :], 0.0))
                else:
                    done(dve.tensor_reduce(cs[:, 64:128], qb[:, own].rearrange("k n l (h d) -> k (n l h) d", h=HPG), AX.X, ALU.add))
            for l in range(L_NEW):
                dve.tensor_copy(tabr[:, l, :].rearrange("b (n l h) -> b n l h", n=N_SEQ, l=L_NEW)[:, :, l, :],
                                S.tab[:, g * HPG:(g + 1) * HPG].unsqueeze(1).broadcast_to([NB, N_SEQ, HPG]))
            dve.wait_ge(cin, 64)
            for f in range(2):
                ins = dve.tensor_tensor(qx[:, f, :].rearrange("p (t h) -> p t h", h=HPG),
                                        S.qk[:, 2 * g + f, SEQ:T].unsqueeze(2).broadcast_to([P, TS, HPG]),
                                        fh[:, f:f + 1, :].broadcast_to([P, TS, HPG]), ALU.mult)
            done(ins)
            dve.wait_ge(pstep, 2)
            done(dve.tensor_copy(bias[:, :], b_ps))
            done(dve.scalar_tensor_tensor(sc[:, :], s_ps, DH ** -0.5, bias[:, :], ALU.mult, ALU.add))
            dve.tensor_tensor(sc[:, nk:], sc[:, nk:], other[:, :], ALU.add).then_inc(others_masked, 1)
            dve.wait_ge(others_masked, 1)
            done(dve.tensor_reduce(neg_max, sc[:, :], AX.X, ALU.max, negate=True))
            dve.wait_ge(pstep, 3)
            dve.wait_ge(zeroed, 1)
            dve.tensor_copy(spread.rearrange("k (u x) -> k u x", x=P + OWN)[:, :, 0:OWN], t_ps[0:nk, 0:P].rearrange("k (u x) -> k u x", x=OWN))
            done(dve.tensor_copy(pT[:, :], t_ps[0:TS, P:2 * P]))
            dve.wait_ge(pstep, 4)
            done(dve.tensor_tensor(new[:, :, :], n_ps.rearrange("p (h d) -> p h d", h=HPG),
                                   rh[:, :].unsqueeze(2).broadcast_to([P, HPG, DH]), ALU.mult))
            done(dve.tensor_reduce(u, new[:, :, :].rearrange("p h d -> p d h"), AX.X, ALU.add))

        @block.gpsimd
        def _(pool):
            pool.wait_ge(step, 5)
            pool.memset(spread, 0.0).then_inc(zeroed, 1)

        @block.tensor
        def _(pe):
            beside.tensor(pe)
            pe.wait_ge(step, 6)
            for l in range(L_NEW):
                last = pe.matmul(b_ps, tabr[:, l, :], hot[:, l, :], start=l == 0, stop=l == L_NEW - 1)
            last.then_inc(pstep, 1)
            pe.transpose(s_ps[:, 0:nk], cs[:, :], S.ident[0:nk, 0:nk])
            for f in range(2):
                last = pe.matmul(s_ps[:, nk:], qx[:, f, :], S.qk[:, 6 + 2 * g + f, SEQ:T], start=f == 0, stop=f == 1)
            last.then_inc(pstep, 1)
            pe.wait_ge(astep, 1)
            pe.transpose(t_ps[0:nk, 0:P], sc[:, 0:nk], S.ident[:, :])
            pe.transpose(t_ps[0:TS, P:2 * P], sc[:, nk:], S.ident[:, :]).then_inc(pstep, 1)
            pe.wait_ge(step, 10)
            pe.wait_ge(vin, 16 * N_SEQ)
            for unit in range(UNITS):
                pe.matmul(n_ps, spread[:, unit * P:(unit + 1) * P], vt[:, unit // lk, unit % lk, :], start=unit == 0, stop=False)
            pe.matmul(n_ps, pT[:, :], v_rows_sb[:, g, :], start=False, stop=True).then_inc(pstep, 1)


class CombineWindows:

    def __init__(self, nc, S, ctx, tag, tiles, bT):
        sb = lambda n, s: ctx.enter_context(nc.sbuf_tensor(f"cw_{n}_{tag}", s, F32))
        self.S, self.bT = S, bT
        self.tiles = [(t, P if t < QT else TS) for t in tiles]
        self.rows = sb("rows", [P, len(self.tiles), 3, HPG, HEAD_ROW])
        self.nM, self.e, self.el, self.den = sb("max", [P, HPG]), sb("e", [P, 2, 3, HPG]), sb("el", [P, 3, HPG]), sb("den", [P, HPG])
        self.b = sb("b", [P, 2, GW])
        self.diffed, self.exped, self.mixed, self.turned, self.kept, self.step = add_sems(
            nc, *(f"cw_{x}_{tag}" for x in ("diffed", "exped", "mixed", "turned", "kept", "step")))
        self.loaded = add_sems(nc, *(f"cw_loaded{i}_{tag}" for i in range(len(self.tiles))))

    def sync(self, sp):
        for i, (t, n) in enumerate(self.tiles):
            sp.dma_start(self.rows[0:n, i].rearrange("t g h x -> t g (h x)"),
                         self.S.part_rows[:, t * P:t * P + n].rearrange("g t h x -> t g (h x)")).then_inc(self.loaded[i], 16)

    def vector(self, dve):
        done = chain(dve, self.step)
        for i, (t, n) in enumerate(self.tiles):
            r, e, el, den = self.rows[0:n, i], self.e[0:n, i % 2], self.el[0:n], self.den[0:n, :]
            dve.wait_ge(self.loaded[i], 16)
            m = r[:, :, :, AT_M]
            done(dve.tensor_reduce(self.nM[0:n, :], m.rearrange("p g h -> p h g"), AX.X, ALU.min))
            dve.tensor_tensor(e, self.nM[0:n, :].unsqueeze(1).broadcast_to([n, 3, HPG]), m, ALU.subtract).then_inc(self.diffed, 1)
            dve.wait_ge(self.exped, i + 1)
            done(dve.tensor_tensor(el, e, r[:, :, :, AT_L], ALU.mult))
            done(dve.tensor_reduce(den, el.rearrange("p g h -> p h g"), AX.X, ALU.add))
            done(dve.reciprocal(den, den))
            done(dve.tensor_tensor(el, e, den.unsqueeze(1).broadcast_to([n, 3, HPG]), ALU.mult))
            for g in range(3):
                u = r[:, g, :, 0:DH]
                ins = dve.tensor_tensor(u, u, el[:, g, :].unsqueeze(2).broadcast_to([n, HPG, DH]), ALU.mult)
            done(ins)
            if i >= 2:
                dve.wait_ge(self.turned, i - 1)
            bt = self.b[0:n, i % 2, :].rearrange("p (h d) -> p h d", h=HPG)
            done(dve.tensor_tensor(bt, r[:, 0, :, 0:DH], r[:, 1, :, 0:DH], ALU.add))
            dve.tensor_tensor(bt, bt, r[:, 2, :, 0:DH], ALU.add).then_inc(self.mixed, 1)

    def tensor(self, pe):
        ps, ident = self.S.ps, self.S.ident
        for i, (t, n) in enumerate(self.tiles):
            pe.wait_ge(self.mixed, i + 1)
            if i >= 2:
                pe.wait_ge(self.kept, i - 1)
            for f in range(2):
                last = pe.transpose(ps[:, (i % 2) * BANK + f * P:(i % 2) * BANK + f * P + n], self.b[0:n, i % 2, f * P:(f + 1) * P], ident[0:n, 0:n])
            last.then_inc(self.turned, 1)
        pe.wait_ge(self.kept, len(self.tiles))

    def scalar(self, act):
        for i, (t, n) in enumerate(self.tiles):
            act.wait_ge(self.diffed, i + 1)
            act.activation(self.e[0:n, i % 2], self.e[0:n, i % 2], ACT.Exp).then_inc(self.exped, 1)
            act.wait_ge(self.turned, i + 1)
            act.activation(self.bT[:, :, t * P:t * P + n],
                           self.S.ps[:, (i % 2) * BANK:(i % 2) * BANK + 2 * P].rearrange("p (f t) -> p f t", f=2)[:, :, 0:n], ACT.Copy).then_inc(self.kept, 1)


class ConvNorm:

    def __init__(self, nc, S, ctx, yT):
        sb = lambda n, s: ctx.enter_context(nc.sbuf_tensor(n, s, F32))
        self.S, self.yT = S, yT
        self.sq, self.mean, self.rstd, self.gb = sb("ln_sq", [P, 2, T]), sb("ln_mean", [P, T]), sb("ln_rstd", [P, T]), sb("ln_gb", [P, 2, CC])
        self.loaded, self.meaned, self.centred, self.squared, self.varied, self.rstd_step, self.scaled, self.sig, self.mean_kept = add_sems(
            nc, *("ln_" + x for x in ("loaded", "meaned", "centred", "squared", "varied", "rstd_step", "scaled", "sigmoid", "mean_kept")))

    def sync(self, sp):
        for i, name in enumerate(("conv_ln_g", "conv_ln_b")):
            sp.dma_start(self.gb[:, i, :], self.S.d[name][0].rearrange("(c p) -> p c", p=P)).then_inc(self.loaded, 16)

    def tensor(self, pe):
        S, yT = self.S, self.yT
        for c in range(CC):
            for at, t, n in PIECES:
                last = pe.matmul(S.ps[:, at:at + n], S.ones[:, :], yT[:, c, t:t + n], start=c == 0, stop=c == CC - 1)
        last.then_inc(self.meaned, 1)
        for c in range(CC):
            pe.wait_ge(self.squared, c + 1)
            for at, t, n in PIECES:
                last = pe.matmul(S.ps[:, 1536 + at:1536 + at + n], S.ones[:, :], self.sq[:, c % 2, t:t + n], start=c == 0, stop=c == CC - 1)
            last.then_inc(self.varied, 1)

    def vector(self, dve):
        S, yT, gb = self.S, self.yT, self.gb
        dve.wait_ge(self.meaned, 1)
        dve.tensor_scalar(by3(self.mean[:, :]), slot(S, 0), 1.0 / CONV_CH, None, ALU.mult).then_inc(self.mean_kept, 1)
        dve.wait_ge(self.mean_kept, 1)
        for c in range(CC):
            dve.tensor_tensor(yT[:, c, :], yT[:, c, :], self.mean[:, :], ALU.subtract).then_inc(self.centred, 1)
        dve.wait_ge(self.rstd_step, 2)
        dve.wait_ge(self.loaded, 32)
        for c in range(CC):
            dve.wait_ge(self.centred, c + 1)
            dve.tensor_tensor(yT[:, c, :], yT[:, c, :], self.rstd[:, :], ALU.mult).then_inc(self.centred, 1)
            dve.wait_ge(self.centred, CC + c + 1)
            dve.tensor_scalar(yT[:, c, :], yT[:, c, :], gb[:, 0, c:c + 1], gb[:, 1, c:c + 1], ALU.mult, ALU.add).then_inc(self.scaled, 1)
        for c in range(CC):
            dve.wait_ge(self.sig, c + 1)
            dve.tensor_tensor(yT[:, c, :], yT[:, c, :], self.sq[:, c % 2, :], ALU.mult).then_inc(self.scaled, 1)

    def scalar(self, act):
        S, yT = self.S, self.yT
        for c in range(CC):
            act.wait_ge(self.centred, c + 1)
            if c >= 2:
                act.wait_ge(self.varied, c - 1)
            act.activation(self.sq[:, c % 2, :], yT[:, c, :], ACT.Square).then_inc(self.squared, 1)
        act.wait_ge(self.varied, CC)
        act.activation(by3(self.rstd[:, :]), slot(S, 1), ACT.Ln, scale=1.0 / CONV_CH, bias=S.eps[:, :]).then_inc(self.rstd_step, 1)
        act.wait_ge(self.rstd_step, 1)
        act.activation(self.rstd[:, :], self.rstd[:, :], ACT.Exp, scale=-0.5).then_inc(self.rstd_step, 1)
        for c in range(CC):
            act.wait_ge(self.scaled, c + 1 if c < 2 else CC + c - 1)
            act.activation(self.sq[:, c % 2, :], yT[:, c, :], ACT.Sigmoid).then_inc(self.sig, 1)


def combine_last(nc, S, bT):
    with ExitStack() as ctx:
        combine = CombineWindows(nc, S, ctx, "sample", [QT], bT)
        block = ctx.enter_context(nc.Block())

        @block.sync
        def _(sp):
            combine.sync(sp)

        @block.scalar
        def _(act):
            combine.scalar(act)

        @block.tensor
        def _(pe):
            combine.tensor(pe)

        @block.vector
        def _(dve):
            combine.vector(dve)


def project_back(nc, S, tag, w, kt, operand):
    with ExitStack() as ctx:
        S.h = Parts(nc, ctx, f"operand_{tag}", [kt, T])
        W = Weights(nc, ctx, tag)
        hi_made, lo_made, x_in = add_sems(nc, *(f"{x}_{tag}" for x in ("operand_hi_made", "operand_lo_made", "x_in")))
        block = ctx.enter_context(nc.Block())
        PAIRS = KD // 2
        v = w.rearrange("(k p) m -> p k m", p=P)

        @block.sync
        def _(sp):
            for j in range(2):
                W.load(sp, j, 1, kt, v[:, 0:kt, j * P:(j + 1) * P])
            sp.wait_ge(lo_made, kt)
            sp.dma_start(S.xT, S.x_spill).then_inc(x_in, 16)
            load_weight_pairs(sp, W, kt, PAIRS - 1, *w_pairs(w, 2 * P), before=1)

        @block.tensor
        def _(pe):
            multiply_pairs(pe, S, W, kt, PAIRS, S.h, made=(lo_made, 0))

        @block.scalar
        def _(act):
            for k in range(kt):
                act.activation(S.h.hi[:, k, :], operand(k), ACT.Copy).then_inc(hi_made, 1)
                if k < 2:
                    W.high(act, k, 1, kt)
            with act.Fori(0, PAIRS - 1) as i:
                for j in range(2):
                    W.high(act, j, i + 2, kt)

        @block.vector
        def _(dve):
            def add(i, j):
                dve.wait_ge(W.product[j], i + 2)
                x = S.xT[:, bass.ds(i * 2 + j, 1), :].rearrange("p a (c t) -> p (a c) t", c=3)
                dve.tensor_tensor(x, x, slot(S, j), ALU.add).then_inc(W.free[j], 1)

            for j in range(2):
                dve.sem_inc(W.free[j], 1)
                dve.sem_inc(W.lo_made[j], 1)
            for k in range(kt):
                dve.wait_ge(hi_made, k + 1)
                dve.tensor_tensor(S.h.lo[:, k, :], operand(k), S.h.hi[:, k, :], ALU.subtract).then_inc(lo_made, 1)
                if k < 2:
                    W.low(dve, k, 1, kt)
            dve.wait_ge(x_in, 16)
            with dve.Fori(0, PAIRS - 1) as i:
                for j in range(2):
                    add(i, j)
                    W.low(dve, j, i + 2, kt)
            for j in range(2):
                add(PAIRS - 1, j)


def ffn(nc, S, layer):
    RUNS = ((0, 8), (8, 7), (15, 7))
    PAIRS = KD // 2
    with ExitStack() as ctx:
        tag = f"ffn{layer}"
        S.h = Parts(nc, ctx, f"h_{tag}", [KD, T])
        W = Weights(nc, ctx, tag)
        w_gate, w_up, w_down = (S.d[n][layer].rearrange("(k p) m -> p k m", p=P) for n in ("w_ffn_gate", "w_ffn_up", "w_ffn_down"))
        with nc.sbuf_tensor(f"norm_{tag}", [P, 5, T], F32) as scratch:
            rms_norm(nc, S, tag, S.g_ffn[:, layer, :], S.xT, S.h, scratch, W=W, first=(w_gate[:, :, 0:P], w_up[:, :, 0:P]))
        hidden = Parts(nc, ctx, f"hidden_{tag}", [KD, T])
        gate, whole = S.home[:, KD, :], S.home[:, KD + 1, :]
        sigmoid_made, hi_made, lo_made = add_sems(nc, *(f"{x}_{tag}" for x in ("sigmoid_made", "hidden_hi_made", "hidden_lo_made")))
        block = ctx.enter_context(nc.Block())

        @block.sync
        def _(sp):
            before = 0
            for first, tiles in RUNS:
                load_weight_pairs(sp, W, KD, tiles, (w_gate, P, first * P), (w_up, P, first * P), before, there=0 if before else 1)
                rows = w_down[:, first:first + tiles, :]
                load_weight_pairs(sp, W, tiles, PAIRS, (rows, 2 * P, 0), (rows, 2 * P, P), before + tiles)
                before += tiles + PAIRS

        @block.tensor
        def _(pe):
            before = 0
            for first, tiles in RUNS:
                multiply_pairs(pe, S, W, KD, tiles, S.h, before)
                multiply_pairs(pe, S, W, tiles, PAIRS, hidden, before + tiles, made=(lo_made, first + 1))
                before += tiles + PAIRS

        @block.scalar
        def _(act):
            def tile_of_hidden(i, before, first, next_kt):
                W.high(act, 0, i + (before + 2), next_kt)
                act.wait_ge(W.product[0], i + (before + 2))
                act.wait_ge(W.free[1], i + (before + 1))
                act.activation(by3(gate), slot(S, 0), ACT.Sigmoid).then_inc(sigmoid_made, 1)
                W.high(act, 1, i + (before + 2), next_kt)
                act.wait_ge(W.free[1], i + (before + 2))
                act.activation(hidden.hi[:, bass.ds(i, 1), :].rearrange("p a t -> p (a t)"), whole, ACT.Copy).then_inc(hi_made, 1)

            before = 0
            for first, tiles in RUNS:
                with act.Fori(0, tiles - 1) as i:
                    tile_of_hidden(i, before, first, KD)
                tile_of_hidden(tiles - 1, before, first, tiles)
                before += tiles
                with act.Fori(0, PAIRS - 1) as i:
                    for j in range(2):
                        W.high(act, j, i + (before + 2), tiles)
                before += PAIRS
                if (first, tiles) != RUNS[-1]:
                    for j in range(2):
                        W.high(act, j, before + 1, KD)

        @block.vector
        def _(dve):
            def tile_of_hidden(i, before, first, next_kt):
                W.low(dve, 0, i + (before + 2), next_kt)
                dve.wait_ge(sigmoid_made, i + (first + 1))
                dve.tensor_tensor(by3(gate), by3(gate), slot(S, 0), ALU.mult).then_inc(W.free[0], 1)
                W.low(dve, 1, i + (before + 2), next_kt)
                dve.wait_ge(W.product[1], i + (before + 2))
                dve.wait_ge(W.free[0], i + (before + 2))
                dve.wait_ge(lo_made, i + (first + 1))
                dve.tensor_tensor(by3(whole), by3(gate), slot(S, 1), ALU.mult).then_inc(W.free[1], 1)
                dve.wait_ge(hi_made, i + (first + 1))
                dve.tensor_tensor(hidden.lo[:, bass.ds(i, 1), :].rearrange("p a t -> p (a t)"), whole,
                                  hidden.hi[:, bass.ds(i, 1), :].rearrange("p a t -> p (a t)"), ALU.subtract).then_inc(lo_made, 1)

            def add(i, j, before):
                dve.wait_ge(W.product[j], i + (before + 2))
                x = S.xT[:, bass.ds(i * 2 + j, 1), :].rearrange("p a (c t) -> p (a c) t", c=3)
                dve.tensor_tensor(x, x, slot(S, j), ALU.add).then_inc(W.free[j], 1)

            dve.sem_inc(lo_made, 1)
            for j in range(2):
                dve.sem_inc(W.free[j], 1)
            before = 0
            for first, tiles in RUNS:
                with dve.Fori(0, tiles - 1) as i:
                    tile_of_hidden(i, before, first, KD)
                tile_of_hidden(tiles - 1, before, first, tiles)
                before += tiles
                with dve.Fori(0, PAIRS - 1) as i:
                    for j in range(2):
                        add(i, j, before)
                        W.low(dve, j, i + (before + 2), tiles)
                for j in range(2):
                    add(PAIRS - 1, j, before)
                    if (first, tiles) != RUNS[-1]:
                        W.low(dve, j, before + PAIRS + 1, KD)
                before += PAIRS


def store_y(nc, S):
    with ExitStack() as ctx:
        rows = ctx.enter_context(nc.sbuf_tensor("y_rows", [P, 3, D_MODEL], F32))
        turned, kept = add_sems(nc, "y_turned", "y_kept")
        stored = add_sems(nc, "y_stored0", "y_stored1", "y_stored2")
        block = ctx.enter_context(nc.Block())
        N = [P] * QT + [TS]

        @block.tensor
        def _(pe):
            for t, n in enumerate(N):
                if t >= 2:
                    pe.wait_ge(kept, t - 1)
                for k in range(KD):
                    last = pe.transpose(S.ps[0:n, (t % 2) * D_MODEL + k * P:(t % 2) * D_MODEL + (k + 1) * P], S.xT[:, k, t * P:t * P + n], S.ident[:, :])
                last.then_inc(turned, 1)

        @block.vector
        def _(dve):
            for t, n in enumerate(N):
                dve.wait_ge(turned, t + 1)
                if t >= 3:
                    dve.wait_ge(stored[t % 3], 16 * (t // 3))
                dve.tensor_copy(rows[0:n, t % 3, :], S.ps[0:n, (t % 2) * D_MODEL:(t % 2 + 1) * D_MODEL]).then_inc(kept, 1)

        @block.sync
        def _(sp):
            for t, n in enumerate(N):
                sp.wait_ge(kept, t + 1)
                dst = S.o["y_prompt"][0, t * P:(t + 1) * P, :] if t < QT else S.o["y_sample"].rearrange("n l d -> (n l) d")
                sp.dma_start(dst, rows[0:n, t % 3, :]).then_inc(stored[t % 3], 16)
            for s in range(3):
                sp.wait_ge(stored[s], 48)


WORK_AT = [None, None] + [sum((t + 1) * P for t in range(2, u)) for u in range(2, QT)]
WORK = sum((t + 1) * P for t in range(2, QT))
S_KEYS = PAST + L_NEW
NEW_AT = PAST
S_COLS = PAST + TS


LR_AT = 96


def index_products(nc, S, iqT, ikT, iw, bT):
    with ExitStack() as ctx:
        W = Weights(nc, ctx, "index")
        gap_zeroed, kept, turned, rows_kept, doubled, stored = add_sems(
            nc, *("index_" + x for x in ("gap_zeroed", "key_kept", "turned", "rows_kept", "key_doubled", "kidx_stored")))
        w = S.d["w_in_cd"][0].rearrange("(k p) m -> p k m", p=P)
        KW, M = DH + IDX_H, LR_AT + GLA_RANK
        turn = S.ps[:, 3072:4096].rearrange("p (b c) -> p b c", b=2)
        block = ctx.enter_context(nc.Block())

        @block.sync
        def _(sp):
            for j in range(2):
                W.load(sp, j, 1, KD, w[:, :, IQ + j * P:IQ + (j + 1) * P])
            sp.wait_ge(gap_zeroed, 1)
            sp.dma_start(W.raw[:, :, 0, 0:KW], w[:, :, IK:IK + KW]).then_inc(W.loaded[0], 16)
            sp.dma_start(W.raw[:, :, 0, LR_AT:M], w[:, :, CLR:CLR + GLA_RANK]).then_inc(W.loaded[0], 16)
            sp.wait_ge(turned, QT + 1)
            sp.dma_start(ikT[DH:P, :], ikT[0:DH, :]).then_inc(doubled, 16)
            sp.wait_ge(rows_kept, QT + 1)
            sp.dma_start(S.o["dsa_kidx_p"][0, 0].rearrange("t p d -> p t d"), iw[:, 0:QT, 0:DH]).then_inc(stored, 16)
            sp.dma_start(S.o["dsa_kidx_s"][0].rearrange("n l d -> (n l) d"), iw[0:TS, QT, 0:DH]).then_inc(stored, 16)
            sp.wait_ge(stored, 32)
            sp.wait_ge(doubled, 16)

        @block.gpsimd
        def _(pool):
            pool.wait_ge(W.lo_made[0], 2)
            pool.memset(W.raw[:, :, 0, KW:LR_AT], 0.0).then_inc(gap_zeroed, 1)

        @block.tensor
        def _(pe):
            for n, (j, m) in enumerate(((0, P), (1, P), (0, M))):
                pe.wait_ge(W.lo_made[j], n // 2 + 2)
                if n == 2:
                    pe.wait_ge(W.free[0], 1)
                for k in range(KD):
                    for i, (wp, xp) in enumerate(passes(W.parts, S.h)):
                        for c, (at, t, size) in enumerate(PIECES):
                            last = pe.matmul(S.ps[0:m, j * 1536 + at:j * 1536 + at + size], wp[:, k, j, 0:m], xp[:, k, t:t + size],
                                             start=k == 0 and i == 0, stop=k == KD - 1 and i == 2)
                last.then_inc(W.product[j], 1)
            pe.wait_ge(kept, 1)
            for t in range(QT + 1):
                n = P if t < QT else TS
                if t >= 2:
                    pe.wait_ge(rows_kept, t - 1)
                pe.transpose(turn[0:n, t % 2, 0:KW], ikT[0:KW, t * P:t * P + n], S.ident[0:KW, 0:KW]).then_inc(turned, 1)

        @block.scalar
        def _(act):
            for j in range(2):
                W.high(act, j, 1, KD)
            act.wait_ge(W.loaded[0], 48)
            act.wait_ge(W.product[0], 2)
            act.activation(W.parts.hi[:, :, 0, 0:M], W.raw[:, :, 0, 0:M], ACT.Copy).then_inc(W.hi_made[0], 1)
            act.activation(by3(iqT[:, 0, :]), slot(S, 0), ACT.Copy).then_inc(W.free[0], 1)
            act.wait_ge(W.product[1], 2)
            act.activation(by3(iqT[:, 1, :]), slot(S, 1), ACT.Copy)
            act.wait_ge(W.product[0], 3)
            act.activation(by3(ikT[0:KW, :]), slot(S, 0)[0:KW], ACT.Copy).then_inc(kept, 1)
            act.activation(by3(bT[LR_AT:M, 1, :]), slot(S, 0)[LR_AT:M], ACT.Copy)
            for t in range(QT + 1):
                n = P if t < QT else TS
                act.wait_ge(turned, t + 1)
                act.activation(iw[0:n, t, :], turn[0:n, t % 2, 0:KW], ACT.Copy).then_inc(rows_kept, 1)

        @block.vector
        def _(dve):
            for j in range(2):
                dve.sem_inc(W.lo_made[j], 1)
                W.low(dve, j, 1, KD)
            dve.wait_ge(W.hi_made[0], 2)
            dve.tensor_tensor(W.parts.lo[:, :, 0, 0:M], W.raw[:, :, 0, 0:M], W.parts.hi[:, :, 0, 0:M], ALU.subtract).then_inc(W.lo_made[0], 1)


def index_scores_prompt(nc, S, iqT, ikT, iw, work, pages, page_keys, page_loaded):
    with ExitStack() as ctx:
        sb = lambda n, s: ctx.enter_context(nc.sbuf_tensor(n, s, F32))
        relu = sb("relu", [P, 2, SEQ])
        wgt = sb("head_w", [P, QT, IDX_H])
        tri = sb("tri", [P, P])
        table_in, loaded, dots, rectified, step = add_sems(nc, "is_table_in", "tri_loaded", "dots_done", "rectified", "index_step")
        units = [(t, h) for t in range(2, QT) for h in range(IDX_H)]
        block = ctx.enter_context(nc.Block())

        @block.sync
        def _(sp):
            sp.dma_start(pages[:, :], S.d["page_table"].rearrange("n (a g) -> a (n g)", a=1)).then_inc(table_in, 16)
            sp.dma_start(tri[:, :], S.c["tri"]).then_inc(loaded, 16)
            sp.wait_ge(table_in, 16)
            pool_keys = S.d["cache_dsa_kidx"][0]
            for n in range(N_SEQ):
                for g in range(N_PAGES):
                    page = sp.value_load(pages[0:1, n * N_PAGES + g:n * N_PAGES + g + 1], min_val=0, max_val=pool_keys.shape[0] - 1)
                    sp.dma_start(page_keys[:, n, g, :], pool_keys[bass.ds(page, 1)].rearrange("a s d -> s (a d)")).then_inc(page_loaded[n], 16)

        @block.tensor
        def _(pe):
            for u, (t, h) in enumerate(units):
                if u >= 4:
                    pe.wait_ge(rectified, u - 3)
                base = DH * (h % 2)
                for at in range(0, (t + 1) * P, BANK):
                    n = min(BANK, (t + 1) * P - at)
                    last = pe.matmul(S.ps[:, (u % 4) * 1024 + at:(u % 4) * 1024 + at + n], iqT[base:base + DH, h // 2, t * P:(t + 1) * P],
                                     ikT[base:base + DH, at:at + n], start=True, stop=True)
                last.then_inc(dots, 1)

        @block.scalar
        def _(act):
            for u, (t, h) in enumerate(units):
                act.wait_ge(dots, u + 1)
                if u >= 2:
                    act.wait_ge(step, u)
                act.activation(relu[:, u % 2, 0:(t + 1) * P], S.ps[:, (u % 4) * 1024:(u % 4) * 1024 + (t + 1) * P], ACT.Relu).then_inc(rectified, 1)

        @block.vector
        def _(dve):
            done = chain(dve, step)
            done(dve.tensor_scalar(wgt[:, :, :], iw[:, 0:QT, DH:DH + IDX_H], DH ** -0.5 * IDX_H ** -0.5, None, ALU.mult))
            for u, (t, h) in enumerate(units):
                n = (t + 1) * P
                dst = work[:, WORK_AT[t]:WORK_AT[t] + n]
                dve.wait_ge(rectified, u + 1)
                if h == 0:
                    done(dve.tensor_scalar(dst, relu[:, u % 2, 0:n], wgt[:, t, h:h + 1], None, ALU.mult))
                else:
                    done(dve.scalar_tensor_tensor(dst, relu[:, u % 2, 0:n], wgt[:, t, h:h + 1], dst, ALU.mult, ALU.add))
            dve.wait_ge(loaded, 16)
            for t in range(2, QT):
                own = work[:, WORK_AT[t] + t * P:WORK_AT[t] + (t + 1) * P]
                dve.tensor_tensor(own, own, tri[:, :], ALU.add)


def index_scores_sample(nc, S, iqT, ikT, iw, work_s, keys, loaded):
    with ExitStack() as ctx:
        sb = lambda n, s: ctx.enter_context(nc.sbuf_tensor(n, s, F32))
        kT = sb("kidx_T", [P, 2, 4, P])
        iqs = sb("iq_s", [P, N_SEQ, 32])
        rows = sb("index_rows", [TS, 2, P])
        wx = sb("wx", [TS, 2, P])
        wsel = sb("wsel", [P, 2, TS])
        relu = sb("relu_s", [P, S_KEYS])
        nmask = sb("new_mask", [TS, L_NEW])
        consts, spread, turned, copied, dotted, relued, wstep, summed, final = add_sems(
            nc, *("is_" + x for x in ("consts", "queries_spread", "keys_turned", "keys_copied", "dots", "rectified",
                                      "weights_step", "summed", "kept")))
        dots_ps = S.ps[:, 0:1536]
        sum_ps = S.ps[0:TS, 1536:3072]
        turn_ps = S.ps[:, 3072:4096].rearrange("p (b x) -> p b x", b=2)
        block = ctx.enter_context(nc.Block())

        @block.sync
        def _(sp):
            sp.dma_start(rows[:, :, :], S.c["index_rows"]).then_inc(consts, 16)
            sp.dma_start(nmask[:, :], S.c["new_mask"]).then_inc(consts, 16)

        @block.vector
        def _(dve):
            dve.memset(iqs[:, :, :], 0.0).then_inc(spread, 1)
            dve.wait_ge(spread, 1)
            for h in range(IDX_H):
                src = iqT[DH * (h % 2):DH * (h % 2) + DH, h // 2, SEQ:T].rearrange("p (n l) -> p n l", l=L_NEW)
                for half in range(2):
                    ins = dve.tensor_copy(iqs[half * DH:(half + 1) * DH, :, h * L_NEW:(h + 1) * L_NEW], src)
            ins.then_inc(spread, 1)
            dve.wait_ge(consts, 32)
            for g in range(2):
                for h in range(IDX_H):
                    v = lambda x: x[:, g, :].rearrange("t (n a h l) -> t n a h l", n=4, a=2, h=4)
                    ins = dve.tensor_scalar(v(wx)[:, :, :, h, :], v(rows)[:, :, :, h, :], iw[0:TS, QT, DH + h:DH + h + 1], DH ** -0.5 * IDX_H ** -0.5,
                                            ALU.mult, ALU.mult)
            ins.then_inc(wstep, 1)
            dve.wait_ge(wstep, 2)
            dve.tensor_copy(wsel[:, :, :], turn_ps[:, 0, 0:2 * TS].rearrange("p (g t) -> p g t", g=2)).then_inc(wstep, 1)
            for n in range(N_SEQ):
                dve.wait_ge(turned, n + 1)
                if n >= 2:
                    dve.wait_ge(dotted, n - 1)
                dve.tensor_copy(kT[:, n % 2, :, :], turn_ps[:, n % 2, :].rearrange("p (c s) -> p c s", c=4)).then_inc(copied, 1)
            dve.wait_ge(summed, 1)
            dve.tensor_copy(work_s[:, 0:PAST], sum_ps[:, 0:PAST])
            dve.tensor_tensor(work_s[:, PAST:S_KEYS], sum_ps[:, PAST:S_KEYS], nmask[:, :], ALU.add)

        @block.tensor
        def _(pe):
            pe.wait_ge(wstep, 1)
            for g in range(2):
                last = pe.transpose(turn_ps[:, 0, g * TS:(g + 1) * TS], wx[:, g, :], S.ident[0:TS, 0:TS])
            last.then_inc(wstep, 1)
            pe.wait_ge(wstep, 3)
            pe.wait_ge(spread, 2)

            def turn(n):
                pe.wait_ge(loaded[n], 16 * N_PAGES)
                if n >= 2:
                    pe.wait_ge(copied, n - 1)
                for c in range(4):
                    last = pe.transpose(turn_ps[:, n % 2, c * P:(c + 1) * P], keys[:, n, 2 * c:2 * c + 2, :].rearrange("s g d -> s (g d)"), S.ident[:, :])
                last.then_inc(turned, 1)

            turn(0)
            for n in range(N_SEQ):
                if n + 1 < N_SEQ:
                    turn(n + 1)
                pe.wait_ge(copied, n + 1)
                if n == 4:
                    pe.wait_ge(relued, 1)
                q = 32 * (n % 4)
                for half in range(2):
                    for c in range(4):
                        at = half * BANK + c * P
                        pe.matmul(dots_ps[q:q + 32, at:at + P], iqs[half * DH:(half + 1) * DH, n, :], kT[half * DH:(half + 1) * DH, n % 2, c, :],
                                  start=True, stop=True)
                pe.matmul(dots_ps[q:q + 32, PAST:S_KEYS], iqs[0:DH, n, :], ikT[0:DH, SEQ + n * L_NEW:SEQ + (n + 1) * L_NEW],
                          start=True, stop=True).then_inc(dotted, 1)
                if n % 4 == 3:
                    g = n // 4
                    pe.wait_ge(relued, g + 1)
                    for at, size in ((0, BANK), (BANK, BANK), (PAST, L_NEW)):
                        last = pe.matmul(sum_ps[:, at:at + size], wsel[:, g, :], relu[:, at:at + size], start=g == 0, stop=g == 1)
                    last.then_inc(summed if g else final, 1)

        @block.scalar
        def _(act):
            for g in range(2):
                act.wait_ge(dotted, 4 * g + 4)
                if g:
                    act.wait_ge(final, 1)
                act.activation(relu[:, 0:PAST].rearrange("p (c b s) -> p b c s", b=2, s=P),
                               dots_ps[:, 0:PAST].rearrange("p (b c s) -> p b c s", b=2, s=P), ACT.Relu)
                act.activation(relu[:, PAST:S_KEYS], dots_ps[:, PAST:S_KEYS], ACT.Relu).then_inc(relued, 1)


class BestKeys:
    ROUNDS = TOPK // 8
    BESIDE_PRODUCTS, BESIDE_GLA, BESIDE_SAMPLE = 20, QT, 1

    def __init__(self, nc, ctx, work, work_s):
        self.best = ctx.enter_context(nc.sbuf_tensor("best", [P, 7, 8], F32))
        self.tick = ctx.enter_context(nc.sbuf_tensor("tick", [1, 2], F32))
        self.lines = [work[:, WORK_AT[t]:WORK_AT[t] + (t + 1) * P] for t in range(QT - 1, 1, -1)] + [work_s[:, :]]
        self.rows = [P] * 6 + [TS]

    def start(self, dve, step):
        dve.memset(self.tick[:, :], 0.0).then_inc(step, len(self.lines))

    def largest(self, dve, step, i):
        n = len(self.lines)
        dve.wait_ge(step, i * (2 * n) + n)
        dve.tensor_copy(self.tick[:, 0:1], self.tick[:, 1:2])
        for j, line in enumerate(self.lines):
            dve.max(self.best[0:self.rows[j], j, :], line).then_inc(step, 1)

    def take(self, dve, step, i):
        n = len(self.lines)
        dve.wait_ge(step, i * (2 * n) + 2 * n)
        dve.tensor_copy(self.tick[:, 0:1], self.tick[:, 1:2])
        for j, line in enumerate(self.lines):
            dve.match_replace(line, self.best[0:self.rows[j], j, :], line, TAKEN).then_inc(step, 1)

    def masks(self, dve, step, rounds):
        n = len(self.lines)
        for j, line in enumerate(self.lines):
            dve.wait_ge(step, 2 * n * rounds + j + 1)
            dve.tensor_scalar(line, line, TAKEN, MASKED, ALU.not_equal, ALU.mult)


def big_products(nc, S, gT, big, gvS, keys):
    with ExitStack() as ctx:
        W = Weights(nc, ctx, "cd")
        v_product, v_kept, round_step = add_sems(nc, "cv_product", "cv_kept", "topk_step")
        w = S.d["w_in_cd"][0]
        vps = S.ps[:, 3072:4096].rearrange("p (b c) -> p b c", b=2)
        block = ctx.enter_context(nc.Block())

        @block.sync
        def _(sp):
            load_weight_pairs(sp, W, KD, 2, *w_pairs(w, CQ))
            load_weight_pairs(sp, W, KD, 6, *w_pairs(w, CG), before=2)
            load_weight_pairs(sp, W, KD, 2, *w_pairs(w, CV), before=8)

        @block.tensor
        def _(pe):
            multiply_pairs(pe, S, W, KD, 2, S.h)
            multiply_pairs(pe, S, W, KD, 6, S.h, before=2)
            value_products(pe, S, W, vps, v_product, v_kept, 2, 8, token_tile)

        @block.scalar
        def _(act):
            for j in range(2):
                act.sem_inc(W.free[j], 1)
                W.high(act, j, 1, KD)
            for dst, iters, before in ((gT, 2, 0), (big, 6, 2)):
                with act.Fori(0, iters) as i:
                    for j in range(2):
                        act.wait_ge(W.product[j], i + (2 + before))
                        act.activation(dst[:, bass.ds(i * 2 + j, 1), :].rearrange("p a (c t) -> p (a c) t", c=3), slot(S, j), ACT.Copy).then_inc(W.free[j], 1)
                        W.high(act, j, i + (2 + before), KD)
            keep_values(act, W, vps, lambda g, t: gvS[:, t, g * GW:(g + 1) * GW], v_product, v_kept, 2, 8)

        @block.gpsimd
        def _(pool):
            for j in range(2):
                pool.sem_inc(W.lo_made[j], 1)
            with pool.Fori(1, 11) as n:
                for j in range(2):
                    W.low(pool, j, n, KD)

        @block.vector
        def _(dve):
            keys.start(dve, round_step)
            with dve.Fori(0, keys.BESIDE_PRODUCTS) as i:
                keys.largest(dve, round_step, i)
                keys.take(dve, round_step, i)


def token_tile(g, t, line):
    return line[:, t * P:t * P + P] if t < QT else line[:, SEQ:T]


def dsa_value_products(nc, S, dvS, dv_new, keys):
    with ExitStack() as ctx:
        W = Weights(nc, ctx, "dv")
        product, kept, round_step = add_sems(nc, "dv_product", "dv_kept", "topk_step_dv")
        vps = S.ps[:, 3072:4096].rearrange("p (b c) -> p b c", b=2)
        block = ctx.enter_context(nc.Block())

        @block.sync
        def _(sp):
            load_weight_pairs(sp, W, KD, 2, *w_pairs(S.d["w_in_cd"][0], DV_))

        @block.tensor
        def _(pe):
            value_products(pe, S, W, vps, product, kept, 2, 0, token_tile)

        @block.scalar
        def _(act):
            for j in range(2):
                W.high(act, j, 1, KD)
            keep_values(act, W, vps, lambda g, t: (dvS[:, t] if t < QT else dv_new)[:, g * GW:(g + 1) * GW], product, kept, 2, 0)

        @block.vector
        def _(dve):
            for j in range(2):
                dve.sem_inc(W.lo_made[j], 1)
                W.low(dve, j, 1, KD)
            for j in range(2):
                W.low(dve, j, 2, KD)
            rounds = keys.ROUNDS - keys.BESIDE_PRODUCTS - keys.BESIDE_GLA - keys.BESIDE_SAMPLE
            keys.start(dve, round_step)
            with dve.Fori(0, rounds) as i:
                keys.largest(dve, round_step, i)
                keys.take(dve, round_step, i)
            keys.masks(dve, round_step, rounds)


def gla_decays(nc, S, bT):
    with ExitStack() as ctx:
        sb = lambda n, s: ctx.enter_context(nc.sbuf_tensor(n, s, F32))
        wa_all, ba, inside, e = sb("wa2", [LR_AT + GLA_RANK, 2, P]), sb("ba", [P, 2]), sb("inside", [P, T]), sb("gla_e", [P, T])
        low_rank = slice(LR_AT, LR_AT + GLA_RANK)
        wa, lrT = wa_all[low_rank], bT[low_rank, 1, :]
        loaded, product, z_ready, a_step, v_step = add_sems(nc, "gate_loaded", "gate_product", "gate_z", "gate_log_step", "gate_step")
        block = ctx.enter_context(nc.Block())

        @block.sync
        def _(sp):
            sp.dma_start(wa, S.d["gla_wa2"][0].rearrange("r (f p) -> r f p", p=P)).then_inc(loaded, 16)
            sp.dma_start(ba[:, :], S.d["gla_ba"][0].rearrange("(f p) -> p f", p=P)).then_inc(loaded, 16)
            sp.dma_start(inside[:, :], S.c["chunk_inside"].broadcast_to([P, T])).then_inc(loaded, 16)

        @block.tensor
        def _(pe):
            pe.wait_ge(loaded, 48)
            for f in range(2):
                for at, t, n in PIECES:
                    last = pe.matmul(S.ps[:, f * 1536 + at:f * 1536 + at + n], wa[:, f, :], lrT[:, t:t + n], start=True, stop=True)
                last.then_inc(product, 1)

        @block.scalar
        def _(act):
            for f in range(2):
                act.wait_ge(z_ready, f + 1)
                if f:
                    act.wait_ge(v_step, 1)
                for func, scale, bias in ((ACT.Abs, 1.0, 0.0), (ACT.Exp, -1.0, 0.0), (ACT.Ln, 1.0, S.ones[:, 0:1])):
                    act.activation(e[:, :], bT[:, f, :] if func is ACT.Abs else e[:, :], func, scale=scale, bias=bias).then_inc(a_step, 1)
                    act.wait_ge(a_step, 3 * f + {ACT.Abs: 1, ACT.Exp: 2}.get(func, 3))

        @block.vector
        def _(dve):
            for f in range(2):
                dve.wait_ge(product, 2)
                dve.tensor_scalar(by3(bT[:, f, :]), slot(S, f), ba[:, f:f + 1], None, ALU.add).then_inc(z_ready, 1)
            for f in range(2):
                dve.wait_ge(a_step, 3 * f + 3)
                dve.scalar_tensor_tensor(bT[:, f, :], bT[:, f, :], 0.0, e[:, :], ALU.min, ALU.subtract).then_inc(v_step, 1)
                dve.wait_ge(v_step, 3 * f + 1)
                dve.tensor_scalar(bT[:, f, :], bT[:, f, :], 1.0 / GLA_TAU, None, ALU.mult).then_inc(v_step, 1)
                dve.wait_ge(v_step, 3 * f + 2)
                dve.tensor_tensor_scan(bT[:, f, :], inside[:, :], bT[:, f, :], 0.0, ALU.mult, ALU.add).then_inc(v_step, 1)


SUB = 32


def gla_prompt(nc, S, gT, bT, gvS, keys):
    with ExitStack() as ctx:
        sb = lambda n, s: ctx.enter_context(nc.sbuf_tensor(n, s, F32))
        NS = P // SUB
        nb = sb("neg_mid", [P, 2, QT * NS])
        eq, ek = sb("eq", [P, 2, 2, P]), sb("ek", [P, 2, 2, NS, P])
        ei, ed = sb("ei", [P, 2, 2, P]), sb("ed", [P, 2, 2, P])
        el = sb("el", [P, 2, QT])
        A = sb("A_T", [P, 2, GLA_H, P])
        kd = sb("kd", [P, 2, 2, P])
        st = sb("gla_state", [P, 2, GLA_DV])
        causal = sb("causal_T", [P, P])
        loaded, ready, exps, mixed, scored, masked, turned, copied, outs, outs_kept, states, stepped, stored, round_step = add_sems(
            nc, *("gp_" + x for x in ("loaded", "start", "exps", "mixed", "scored", "masked", "turned", "kd_copied", "outs", "outs_kept",
                                      "state_sums", "stepped", "stored", "topk_step")))
        a_ps = S.ps[:, 0:1024].rearrange("p (b f i) -> p b f i", b=2, f=4)
        o_ps = S.ps[:, 1024:2048].rearrange("p (b f i) -> p b f i", b=2, f=4)
        k_ps = S.ps[:, 2048:2048 + 2 * P].rearrange("p (f x) -> p f x", f=2)
        s_ps = S.ps[:, 2560:2560 + 2 * P].rearrange("p (f x) -> p f x", f=2)
        block = ctx.enter_context(nc.Block())

        @block.sync
        def _(sp):
            sp.dma_start(causal[:, :], S.c["causal_T"]).then_inc(loaded, 16)
            sp.wait_ge(stepped, QT + 1)
            for f in range(2):
                sp.dma_start(S.o["gla_p"][0, 0, 2 * f:2 * f + 2].rearrange("h k v -> (h k) v"), st[:, f, :]).then_inc(stored, 16)
            sp.wait_ge(stored, 32)

        @block.scalar
        def _(act):
            def exponentials(c):
                if c >= 2:
                    act.wait_ge(outs, c - 1)
                for f in range(2):
                    b = lambda at, n: bT[:, f, c * P + at:c * P + at + n]
                    for s in range(NS):
                        at = s * SUB
                        act.activation(eq[:, c % 2, f, at:at + SUB], b(at, SUB), ACT.Exp, bias=nb[:, f, c * NS + s:c * NS + s + 1])
                        act.activation(ek[:, c % 2, f, s, 0:at + SUB], b(0, at + SUB), ACT.Exp, scale=-1.0, bias=b(at + SUB // 2, 1))
                    act.activation(ei[:, c % 2, f, :], b(0, P), ACT.Exp)
                    last = act.activation(ed[:, c % 2, f, :], b(0, P), ACT.Exp, scale=-1.0, bias=b(P - 1, 1))
                last.then_inc(exps, 1)

            act.wait_ge(ready, 1)
            act.activation(el[:, :, :], bT[:, :, P - 1:SEQ:P], ACT.Exp)
            exponentials(0)
            for c in range(QT):
                if c + 1 < QT:
                    exponentials(c + 1)
                act.wait_ge(turned, c + 1)
                if c >= 2:
                    act.wait_ge(states, c - 1)
                act.activation(kd[:, c % 2, :, :], k_ps, ACT.Copy).then_inc(copied, 1)

        @block.vector
        def _(dve):
            def mix(c):
                cols = slice(c * P, (c + 1) * P)
                dve.wait_ge(exps, c + 1)
                q, k = gT[:, 0:2, cols], gT[:, 2:4, cols]
                dve.scalar_tensor_tensor(eq[:, c % 2], eq[:, c % 2], GLA_DK ** -0.5, q, ALU.mult, ALU.mult)
                for f in range(2):
                    dve.tensor_tensor(ek[:, c % 2, f], ek[:, c % 2, f], gT[:, 2 + f, cols].unsqueeze(1).broadcast_to([P, NS, P]), ALU.mult)
                dve.scalar_tensor_tensor(ei[:, c % 2], ei[:, c % 2], GLA_DK ** -0.5, q, ALU.mult, ALU.mult)
                dve.tensor_tensor(ed[:, c % 2], ed[:, c % 2], k, ALU.mult).then_inc(mixed, 1)

            def mask(c):
                dve.wait_ge(scored, c + 1)
                for b in range(2):
                    last = dve.tensor_tensor(A[:, c % 2].rearrange("p (f b) i -> p b f i", b=2)[:, b], a_ps[:, b, 0:2, :],
                                             causal[:, :].unsqueeze(1).broadcast_to([P, 2, P]), ALU.mult)
                last.then_inc(masked, 1)

            keys.start(dve, round_step)
            dve.tensor_scalar(nb[:, :, :], bT[:, :, SUB // 2:SEQ:SUB], -1.0, None, ALU.mult)
            dve.memset(st[:, :, :], 0.0).then_inc(stepped, 1)
            dve.memset(ek[:, :, :, :, :], 0.0).then_inc(ready, 1)
            dve.wait_ge(loaded, 16)
            mix(0)
            mask(0)
            for c in range(QT):
                if c + 1 < QT:
                    mix(c + 1)
                dve.wait_ge(outs, c + 1)
                for b in range(2):
                    last = dve.tensor_copy(gT[:, b:4:2, c * P:(c + 1) * P], o_ps[:, b, 0:2, :])
                last.then_inc(outs_kept, 1)
                keys.largest(dve, round_step, c)
                dve.wait_ge(states, c + 1)
                for f in range(2):
                    last = dve.scalar_tensor_tensor(st[:, f, :], st[:, f, :], el[:, f, c:c + 1], s_ps[:, f, :], ALU.mult, ALU.add)
                last.then_inc(stepped, 1)
                if c + 1 < QT:
                    mask(c + 1)
                keys.take(dve, round_step, c)

        @block.tensor
        def _(pe):
            def scores(c):
                pe.wait_ge(mixed, c + 1)
                if c:
                    pe.wait_ge(masked, c)
                for h in range(GLA_H):
                    f, b = h // 2, h % 2
                    half = slice(b * DH, b * DH + DH)
                    for s in range(NS):
                        last = pe.matmul(a_ps[:, b, f, s * SUB:(s + 1) * SUB], ek[half, c % 2, f, s, :], eq[half, c % 2, f, s * SUB:(s + 1) * SUB], start=True, stop=True)
                last.then_inc(scored, 1)
                if c:
                    pe.wait_ge(copied, c)
                for f in range(2):
                    last = pe.transpose(k_ps[:, f, :], ed[:, c % 2, f, :], S.ident[:, :])
                last.then_inc(turned, 1)

            scores(0)
            for c in range(QT):
                pe.wait_ge(masked, c + 1)
                pe.wait_ge(stepped, c + 1)
                if c:
                    pe.wait_ge(outs_kept, c)
                for h in range(GLA_H):
                    f, b = h // 2, h % 2
                    half = slice(b * DH, b * DH + DH)
                    pe.matmul(o_ps[:, b, f, :], st[half, f, :], ei[half, c % 2, f, :], start=True, stop=False)
                    last = pe.matmul(o_ps[:, b, f, :], gvS[:, c, h * P:(h + 1) * P], A[:, c % 2, h, :], start=False, stop=True)
                last.then_inc(outs, 1)
                pe.wait_ge(copied, c + 1)
                for h in range(GLA_H):
                    f, b = h // 2, h % 2
                    last = pe.matmul(s_ps[b * DH:(b + 1) * DH, f, :], kd[:, c % 2, f, b * DH:(b + 1) * DH], gvS[:, c, h * P:(h + 1) * P], start=True, stop=True)
                last.then_inc(states, 1)
                if c + 1 < QT:
                    scores(c + 1)


def gla_sample(nc, S, gT, bT, gvS, keys):
    with ExitStack() as ctx:
        sb = lambda n, s: ctx.enter_context(nc.sbuf_tensor(n, s, F32))
        s0 = sb("s0", [P, 2, N_SEQ, GLA_DV])
        new = s0
        e, q, k, kd, diff = sb("gs_e", [P, 4, 2, TS]), sb("gs_q", [P, 2, TS]), sb("gs_k", [P, 2, TS]), sb("gs_kd", [P, 2, TS]), sb("gs_diff", [P, 2, TS])
        el = sb("gs_el", [P, 2, N_SEQ])
        A = sb("gs_A", [TS, GLA_H, TS])
        kdT = sb("gs_kdT", [TS, 2, P])
        km = sb("gs_km", [TS, N_SEQ, P])
        mask, seq = sb("gs_mask", [TS, TS]), sb("gs_seq", [TS, N_SEQ])
        round_step, loaded, diffed, exped, mixed, scored, step, outs, kept, states, finished, stored = add_sems(
            nc, *("gs_" + x for x in ("topk_step", "loaded", "diffed", "exped", "mixed", "scored", "step", "outs", "kept", "states", "finished", "stored")))
        a_ps = S.ps[0:TS, 0:1024].rearrange("p (b f i) -> p b f i", b=2, f=16)
        k_ps = S.ps[0:TS, 1024:1024 + 2 * P].rearrange("p (f x) -> p f x", f=2)
        inter_ps = S.ps[:, 1536:2560].rearrange("p (b f i) -> p b f i", b=2, f=16)
        intra_ps = S.ps[:, 2560:2560 + GLA_H * TS].rearrange("p (h i) -> p h i", h=GLA_H)
        s_ps = S.ps[:, 3072:4096].rearrange("p (n v) -> p n v", n=N_SEQ)
        block = ctx.enter_context(nc.Block())
        last_b = bT[:, :, SEQ + L_NEW - 1:T:L_NEW]

        @block.sync
        def _(sp):
            for n in range(N_SEQ):
                sp.dma_start(s0[:, :, n, :], S.d["state_gla"][0, n].rearrange("(f b) k v -> (b k) f v", b=2)).then_inc(loaded, 16)
            sp.dma_start(mask[:, :], S.c["sample_causal_T"]).then_inc(loaded, 16)
            sp.dma_start(seq[:, :], S.c["seq_of"]).then_inc(loaded, 16)
            sp.wait_ge(finished, 2)
            for n in range(N_SEQ):
                sp.dma_start(S.o["gla_s"][0, n].rearrange("(f b) k v -> (b k) f v", b=2), new[:, :, n, :]).then_inc(stored, 16)
            sp.wait_ge(stored, 16 * N_SEQ)

        @block.scalar
        def _(act):
            b = bT[:, :, SEQ:T]
            act.activation(e[:, 0], b, ACT.Exp)
            act.activation(e[:, 1], b, ACT.Exp, scale=-1.0)
            act.activation(el[:, :, :], last_b, ACT.Exp)
            act.wait_ge(diffed, 1)
            act.activation(e[:, 2], diff[:, :, :], ACT.Exp).then_inc(exped, 1)
            act.wait_ge(outs, 1)
            for b in range(2):
                last = act.activation(gT[:, b:4:2, SEQ:T], inter_ps[:, b, 0:2, :], ACT.Copy)
            last.then_inc(kept, 1)

        @block.vector
        def _(dve):
            done = chain(dve, step)
            dve.tensor_tensor(diff[:, :, :].rearrange("p f (n l) -> p f n l", l=L_NEW), last_b.unsqueeze(3).broadcast_to([P, 2, N_SEQ, L_NEW]),
                              bT[:, :, SEQ:T].rearrange("p f (n l) -> p f n l", l=L_NEW), ALU.subtract).then_inc(diffed, 1)
            dve.wait_ge(exped, 1)
            dve.scalar_tensor_tensor(q[:, :, :], e[:, 0], GLA_DK ** -0.5, gT[:, 0:2, SEQ:T], ALU.mult, ALU.mult)
            dve.tensor_tensor(k[:, :, :], e[:, 1], gT[:, 2:4, SEQ:T], ALU.mult)
            dve.tensor_tensor(kd[:, :, :], e[:, 2], gT[:, 2:4, SEQ:T], ALU.mult).then_inc(mixed, 1)
            keys.start(dve, round_step)
            for i in range(keys.BESIDE_SAMPLE):
                keys.largest(dve, round_step, i)
                keys.take(dve, round_step, i)
            dve.wait_ge(loaded, 16 * (N_SEQ + 2))
            dve.wait_ge(scored, 1)
            for b in range(2):
                dve.tensor_tensor(A[:, :, :].rearrange("p (f b) i -> p b f i", b=2)[:, b], a_ps[:, b, 0:2, :], mask[:, :].unsqueeze(1).broadcast_to([TS, 2, TS]), ALU.mult)
            done(dve.tensor_copy(kdT[:, :, :], k_ps))
            keys_of_sequences = lambda f: dve.tensor_tensor(km[:, :, :], kdT[:, f, :].unsqueeze(1).broadcast_to([TS, N_SEQ, P]),
                                                            seq[:, :].unsqueeze(2).broadcast_to([TS, N_SEQ, P]), ALU.mult)
            done(keys_of_sequences(0))
            dve.wait_ge(kept, 1)
            for f in range(2):
                ins = dve.tensor_tensor(new[:, f], s0[:, f], el[:, f, :].unsqueeze(2).broadcast_to([P, N_SEQ, GLA_DV]), ALU.mult)
            done(ins)
            dve.tensor_tensor(gT[:, :, SEQ:T], gT[:, :, SEQ:T], intra_ps, ALU.add)
            for f in range(2):
                dve.wait_ge(states, f + 1)
                if f == 0:
                    done(keys_of_sequences(1))
                dve.tensor_tensor(new[:, f], new[:, f], s_ps, ALU.add).then_inc(finished, 1)

        @block.tensor
        def _(pe):
            pe.wait_ge(mixed, 1)
            for h in range(GLA_H):
                f, b = h // 2, h % 2
                half = slice(b * DH, b * DH + DH)
                pe.matmul(a_ps[:, b, f, :], k[half, f, :], q[half, f, :], start=True, stop=True)
            for f in range(2):
                last = pe.transpose(k_ps[:, f, :], kd[:, f, :], S.ident[:, :])
            last.then_inc(scored, 1)
            pe.wait_ge(loaded, 16 * (N_SEQ + 2))
            for h in range(GLA_H):
                f, b = h // 2, h % 2
                half = slice(b * DH, b * DH + DH)
                for n in range(N_SEQ):
                    pe.matmul(inter_ps[:, b, f, n * L_NEW:(n + 1) * L_NEW], s0[half, f, n, :], q[half, f, n * L_NEW:(n + 1) * L_NEW], start=True, stop=True)
            pe.wait_ge(step, 2)
            for h in range(GLA_H):
                last = pe.matmul(intra_ps[:, h, :], gvS[0:TS, QT, h * P:(h + 1) * P], A[:, h, :], start=True, stop=True)
            last.then_inc(outs, 1)
            for f in range(2):
                if f:
                    pe.wait_ge(finished, 1)
                    pe.wait_ge(step, 4)
                for n in range(N_SEQ):
                    for b in range(2):
                        last = pe.matmul(s_ps[b * DH:(b + 1) * DH, n, :], km[:, n, b * DH:(b + 1) * DH],
                                         gvS[0:TS, QT, (2 * f + b) * P:(2 * f + b + 1) * P], start=True, stop=True)
                last.then_inc(states, 1)


def gate_outputs(nc, S, gT, cg):
    with ExitStack() as ctx:
        sig = ctx.enter_context(nc.sbuf_tensor("cg_sig", [P, 2, T], F32))
        made, gated = add_sems(nc, "cg_sigmoid", "cg_gated")
        block = ctx.enter_context(nc.Block())

        @block.scalar
        def _(act):
            for h in range(GLA_H):
                if h >= 2:
                    act.wait_ge(gated, 2 * (h - 1))
                act.activation(sig[:, h % 2, :], cg[:, h, :], ACT.Sigmoid).then_inc(made, 1)

        @block.vector
        def _(dve):
            for h in range(GLA_H):
                dve.wait_ge(made, h + 1)
                dve.tensor_tensor(cg[:, h, :], cg[:, h, :], sig[:, h % 2, :], ALU.mult).then_inc(gated, 1)
                dve.wait_ge(gated, 2 * h + 1)
                dve.tensor_tensor(cg[:, h, :], cg[:, h, :], gT[:, h, :], ALU.mult).then_inc(gated, 1)


def dsa_prompt(nc, S, big, work, dvS):
    with ExitStack() as ctx:
        sb = lambda n, s: ctx.enter_context(nc.sbuf_tensor(n, s, F32))
        toep = sb("toep_dsa", [P, 4, SEQ])
        sc = sb("sc_dsa", [P, 3, SEQ])
        pT = sb("pT_dsa", [P, 2, BANK])
        osb = sb("o_dsa", [P, 2, P])
        stat = sb("stat_dsa", [P, 3, 4])
        scored, biased, vstep, maxed, exps, turned, kept, summed, scaled, pair_turned, pair_kept = add_sems(
            nc, *("dp_" + x for x in ("scored", "biased", "vector_step", "maxima", "exps", "turned",
                                      "probs_kept", "summed", "scaled", "pair_turned", "pair_kept")))
        toep_in = add_sems(nc, *(f"dp_toep_in{i}" for i in range(4)))
        units = [(f, t, b) for f in range(DSA_H // 2) for t in range(QT) for b in range(2)]
        groups = [(u, list(range(at, min(at + 4, units[u][1] + 1)))) for u in range(len(units)) for at in range(0, units[u][1] + 1, 4)]
        groups_to = [sum(1 for g in groups if g[0] <= u) for u in range(len(units))]
        s_ps = S.ps[:, 0:2048].rearrange("p (b k) -> p b k", b=2)
        t_ps = S.ps[:, 2048:3072].rearrange("p (b k) -> p b k", b=2)
        o_ps = S.ps[:, 3072:4096].rearrange("p (b d) -> p b d", b=2)[:, :, 0:DH]
        oT_ps = S.ps[:, 3584 + P:3584 + 2 * P]
        block = ctx.enter_context(nc.Block())

        @block.sync
        def _(sp):
            sp.wait_ge(S.dsa_lines, 16 * DSA_H)
            for h in range(DSA_H):
                if h >= 4:
                    sp.wait_ge(biased, (h - 4) // 2 * 2 * QT + 2 * QT)
                sp.dma_start(toep[:, h % 4:h % 4 + 1, :], toeplitz(S.dsa_copies, DSA_LINE, 0, slice(h, h + 1), 1, SEQ)).then_inc(toep_in[h % 4], 16)

        @block.tensor
        def _(pe):
            def scores(u):
                f, t, b = units[u]
                if u >= 2:
                    pe.wait_ge(biased, u - 1)
                half = slice(b * DH, b * DH + DH)
                for at in range(0, (t + 1) * P, BANK):
                    n = min(BANK, (t + 1) * P - at)
                    last = pe.matmul(s_ps[:, u % 2, at:at + n], big[half, 4 + f, t * P:(t + 1) * P], big[half, 8 + f, at:at + n], start=True, stop=True)
                last.then_inc(scored, 1)

            def turn_probs(g):
                u, kts = groups[g]
                pe.wait_ge(exps, u + 1)
                if g >= 2:
                    pe.wait_ge(kept, g - 1)
                for i, kt in enumerate(kts):
                    last = pe.transpose(t_ps[:, g % 2, i * P:(i + 1) * P], sc[:, u % 3, kt * P:(kt + 1) * P], S.ident[:, :])
                last.then_inc(turned, 1)

            def weigh_values(g):
                u, kts = groups[g]
                f, t, b = units[u]
                pe.wait_ge(kept, g + 1)
                if kts[0] == 0 and u >= 2:
                    pe.wait_ge(scaled, u - 1)
                if kts[0] == 0 and u % 2 == 1 and u >= 3:
                    pe.wait_ge(pair_kept, (u - 3) // 2 + 1)
                h = 2 * f + b
                for i, kt in enumerate(kts):
                    last = pe.matmul(o_ps[:, u % 2, :], pT[:, g % 2, i * P:(i + 1) * P], dvS[:, kt, h * DH:(h + 1) * DH], start=kt == 0, stop=kt == t)
                if kts[-1] == t:
                    last.then_inc(summed, 1)

            def turn_pair(k):
                pe.wait_ge(scaled, 2 * k + 2)
                if k:
                    pe.wait_ge(pair_kept, k)
                pe.transpose(oT_ps, osb[:, k % 2, :], S.ident[:, :]).then_inc(pair_turned, 1)

            scores(0)
            scores(1)
            for g, (u, kts) in enumerate(groups):
                if kts[0] == 0:
                    if u + 2 < len(units):
                        scores(u + 2)
                turn_probs(g)
                if g:
                    weigh_values(g - 1)
                if kts[0] == 0 and u % 2 == 1 and u >= 3:
                    turn_pair((u - 3) // 2)
            weigh_values(len(groups) - 1)
            turn_pair(len(units) // 2 - 1)

        @block.vector
        def _(dve):
            done = chain(dve, vstep)
            def scale(u):
                dve.wait_ge(exps, u + 1)
                done(dve.reciprocal(stat[:, u % 3, 3:4], stat[:, u % 3, 2:3]))
                dve.wait_ge(summed, u + 1)
                if u % 2 == 0 and u >= 4:
                    dve.wait_ge(pair_turned, (u - 4) // 2 + 1)
                dve.tensor_scalar(osb[:, (u // 2) % 2, (u % 2) * DH:(u % 2 + 1) * DH], o_ps[:, u % 2, :], stat[:, u % 3, 3:4], None,
                                  ALU.mult).then_inc(scaled, 1)

            for u, (f, t, b) in enumerate(units):
                h, n = 2 * f + b, (t + 1) * P
                if t == 0:
                    dve.wait_ge(toep_in[h % 4], 16 * (h // 4 + 1))
                dve.wait_ge(scored, u + 1)
                if u >= 3:
                    dve.wait_ge(turned, groups_to[u - 3])
                bias = toep[:, h % 4, SEQ - n:SEQ]
                st = stat[:, u % 3, :]
                if t < 2:
                    dve.tensor_tensor_reduce(sc[:, u % 3, 0:n], s_ps[:, u % 2, 0:n], bias, 1.0, TAKEN, ALU.add, ALU.max, st[:, 0:1]).then_inc(biased, 1)
                    dve.wait_ge(biased, u + 1)
                else:
                    dve.tensor_tensor(sc[:, u % 3, 0:n], s_ps[:, u % 2, 0:n], bias, ALU.add).then_inc(biased, 1)
                    dve.wait_ge(biased, u + 1)
                    done(dve.tensor_tensor_reduce(sc[:, u % 3, 0:n], sc[:, u % 3, 0:n], work[:, WORK_AT[t]:WORK_AT[t] + n], 1.0, TAKEN,
                                                  ALU.add, ALU.max, st[:, 0:1]))
                dve.tensor_scalar(st[:, 1:2], st[:, 0:1], -1.0, None, ALU.mult).then_inc(maxed, 1)
                if u >= 2:
                    scale(u - 2)
            for u in range(len(units) - 2, len(units)):
                scale(u)

        @block.scalar
        def _(act):
            def keep_pair(k):
                f, t, _ = units[2 * k]
                act.wait_ge(pair_turned, k + 1)
                act.activation(big[:, 4 + f, t * P:(t + 1) * P], oT_ps, ACT.Copy).then_inc(pair_kept, 1)

            def exponentials(u):
                act.wait_ge(maxed, u + 1)
                n = (units[u][1] + 1) * P
                act.activation(sc[:, u % 3, 0:n], sc[:, u % 3, 0:n], ACT.Exp, bias=stat[:, u % 3, 1:2], accum_out=stat[:, u % 3, 2:3]).then_inc(exps, 1)

            g = 0
            exponentials(0)
            for u in range(len(units)):
                if u + 1 < len(units):
                    exponentials(u + 1)
                while g < len(groups) and groups[g][0] == u:
                    m = len(groups[g][1]) * P
                    act.wait_ge(turned, g + 1)
                    if g >= 2:
                        act.wait_ge(kept, g - 1)
                    act.activation(pT[:, g % 2, 0:m], t_ps[:, g % 2, 0:m], ACT.Copy).then_inc(kept, 1)
                    g += 1
                if u % 2 == 1 and u >= 3:
                    keep_pair((u - 3) // 2)
            keep_pair(len(units) // 2 - 1)


KV_SLOTS = 5


def dsa_sample(nc, S, big, work, work_s, dv_new):
    sc, bias = work[:, 0:S_COLS], work[:, S_COLS:2 * S_COLS]
    mask = work[0:TS, 2 * S_COLS:3 * S_COLS]
    with ExitStack() as outer:
        sb = lambda n, s: outer.enter_context(nc.sbuf_tensor(n, s, F32))
        pages = outer.enter_context(nc.sbuf_tensor("pages_kv", [1, N_SEQ * N_PAGES], I32))
        qb = sb("qb_dsa", [P, 4, N_SEQ, 32])
        tabr = sb("tabr_dsa", [NB, L_NEW, P])
        slots = [sb(f"kv_slot{i}", [P, N_PAGES, BANK]) for i in range(KV_SLOTS)]
        for half in range(2):
            with ExitStack() as ctx:
                tag = f"ds{half}"
                sb2 = lambda n, s: ctx.enter_context(nc.sbuf_tensor(f"{n}_{tag}", s, F32))
                hot, hot_new = sb2("hot_s", [NB, L_NEW, PAST]), sb2("hot_new_s", [NB, L_NEW, TS])
                sel = sb2("dsa_rows", [TS, P])
                other = sb2("dsa_other", [P, TS])
                own_head = sb2("own_head", [P, DSA_H])
                heads = sb2("all_heads", [P, DSA_H, DH])
                out = sb2("out_rows", [P, 2, DH])
                kT = sb2("kT", [P, 2, BANK])
                pT = sb2("pT_s", [P, N_PAGES + 1, P])
                stat = sb2("stat_s", [P, 3])
                consts, table_in, prep, hot_in, biased, scored, step, exps, turned, copied, probs_turned, probs_kept, summed = add_sems(
                    nc, *(f"{x}_{tag}" for x in ("consts", "table_in", "prepared", "hot_in", "bias_made", "scored", "step", "exps", "keys_turned",
                                                 "keys_copied", "probs_turned", "probs_kept", "summed")))
                kv_in = add_sems(nc, *(f"kv_in{i}_{tag}" for i in range(KV_SLOTS)))
                s_ps = S.ps[:, 0:S_COLS]
                b_ps = S.ps[:, 1536:1536 + S_COLS]
                t_ps = S.ps[:, 3072:4096].rearrange("p (b x) -> p b x", b=2)
                p_ps = S.ps[:, 0:(N_PAGES + 1) * P].rearrange("p (g x) -> p g x", g=N_PAGES + 1)
                o_ps = S.ps[:, 1536:1536 + BANK]
                oT_ps = S.ps[:, 2048:2048 + P].rearrange("p (n f b l) -> p n f b l", n=4, f=4, b=2)
                pool_kv = S.d["cache_dsa_kv"][0]
                block = ctx.enter_context(nc.Block())

                @block.sync
                def _(sp):
                    if half == 0:
                        sp.dma_start(pages[:, :], S.d["page_table"].rearrange("n (a g) -> a (n g)", a=1)).then_inc(table_in, 16)
                    if half == 0:
                        sp.wait_ge(table_in, 16)
                    for i in range(8):
                        n, what = 4 * half + i % 4, i // 4
                        if i >= KV_SLOTS:
                            sp.wait_ge(turned, N_PAGES * (i - KV_SLOTS + 1))
                        for g in range(N_PAGES):
                            page = sp.value_load(pages[0:1, n * N_PAGES + g:n * N_PAGES + g + 1], min_val=0, max_val=pool_kv.shape[0] - 1)
                            sp.dma_start(slots[i % KV_SLOTS][:, g, :], pool_kv[bass.ds(page, 1)].rearrange("a s c h d -> s (a c) (h d)")[:, what, :]).then_inc(kv_in[i % KV_SLOTS], 16)

                @block.scalar
                def _(act):
                    act.dma_start(sel[:, :], S.c["dsa_rows"][:, half, :]).then_inc(consts, 16)
                    act.dma_start(other[:, :], S.c["dsa_other"][:, half, :]).then_inc(consts, 16)
                    act.dma_start(own_head[:, :], S.c["dsa_row_head"]).then_inc(consts, 16)
                    act.dma_start(hot[:, :, 0:BANK], S.c["dsa_hot"][:, :, 0:BANK]).then_inc(hot_in, 16)
                    act.dma_start(hot_new[:, :, :], S.c["dsa_hot_new"]).then_inc(hot_in, 16)
                    act.dma_start(hot[:, :, BANK:PAST], S.c["dsa_hot"][:, :, BANK:PAST]).then_inc(hot_in, 16)
                    for i in range(4 * N_PAGES):
                        act.wait_ge(turned, i + 1)
                        if i >= 2:
                            act.wait_ge(scored, i - 1)
                        act.activation(kT[:, i % 2, :], t_ps[:, i % 2, :], ACT.Copy).then_inc(copied, 1)
                    act.wait_ge(step, 3)
                    act.activation(sc, sc, ACT.Exp, bias=stat[:, 0:1], accum_out=stat[:, 1:2]).then_inc(exps, 1)

                @block.vector
                def _(dve):
                    done = chain(dve, step)
                    if half == 0:
                        dve.memset(qb[:, :, :, :], 0.0).then_inc(prep, 1)
                        dve.memset(tabr[:, :, :], 0.0).then_inc(prep, 1)
                        dve.wait_ge(prep, 2)
                        for h in range(DSA_H):
                            rows, f = slice(DH * (h % 2), DH * (h % 2) + DH), h // 2
                            dve.tensor_copy(qb[rows, f, :, h * L_NEW:(h + 1) * L_NEW],
                                            big[rows, 4 + f, SEQ:T].rearrange("p (n l) -> p n l", l=L_NEW))
                        for l in range(L_NEW):
                            dve.tensor_copy(tabr[:, l, :].rearrange("b (n h l) -> b n h l", n=4, h=DSA_H)[:, :, :, l],
                                            S.tab[:, 12:12 + DSA_H].unsqueeze(1).broadcast_to([NB, 4, DSA_H]))
                        dve.tensor_copy(mask[:, 0:PAST], work_s[:, 0:PAST])
                        dve.tensor_copy(mask[:, PAST:S_COLS].rearrange("t (n l) -> t n l", n=N_SEQ),
                                        work_s[:, PAST:S_KEYS].unsqueeze(1).broadcast_to([TS, N_SEQ, L_NEW])).then_inc(prep, 1)
                    dve.wait_ge(consts, 48)
                    dve.wait_ge(biased, 3)
                    dve.tensor_copy(bias[:, 0:PAST], b_ps[:, 0:PAST])
                    done(dve.tensor_tensor(bias[:, PAST:S_COLS], b_ps[:, PAST:S_COLS], other[:, :], ALU.add))
                    dve.wait_ge(scored, 4 * N_PAGES + 1)
                    done(dve.tensor_tensor(sc, s_ps, bias, ALU.add))
                    done(dve.tensor_reduce(stat[:, 0:1], sc, AX.X, ALU.max, negate=True))
                    dve.wait_ge(exps, 1)
                    done(dve.reciprocal(stat[:, 2:3], stat[:, 1:2]))
                    done(dve.tensor_scalar(sc, sc, stat[:, 2:3], None, ALU.mult))
                    dve.wait_ge(probs_turned, 1)
                    dve.tensor_copy(pT[:, 0:N_PAGES, :], p_ps[:, 0:N_PAGES, :])
                    dve.tensor_copy(pT[0:TS, N_PAGES, :], p_ps[0:TS, N_PAGES, :]).then_inc(probs_kept, 1)
                    dve.wait_ge(summed, 1)
                    done(dve.tensor_tensor(heads[:, :, :], o_ps.rearrange("p (h d) -> p h d", h=DSA_H),
                                           own_head[:, :].unsqueeze(2).broadcast_to([P, DSA_H, DH]), ALU.mult))
                    for b in range(2):
                        done(dve.tensor_reduce(out[:, b, :], heads[:, :, :].rearrange("p h d -> p d h"), AX.X, ALU.add))
                    dve.wait_ge(summed, 2)
                    for b in range(2):
                        rows = slice(b * DH, b * DH + DH)
                        dve.tensor_copy(big[rows, 4:8, SEQ + 16 * half:SEQ + 16 * (half + 1)].rearrange("p f (n l) -> p f n l", n=4),
                                        oT_ps[rows, :, :, b, :].rearrange("p n f l -> p f n l"))

                @block.tensor
                def _(pe):
                    if half == 0:
                        pe.wait_ge(prep, 3)

                    def turn_keys(i):
                        n, g = divmod(i, N_PAGES)
                        pe.wait_ge(kv_in[n % KV_SLOTS], 16 * N_PAGES * (n // KV_SLOTS + 1))
                        if i >= 2:
                            pe.wait_ge(copied, i - 1)
                        for f in range(4):
                            last = pe.transpose(t_ps[:, i % 2, f * P:(f + 1) * P], slots[n % KV_SLOTS][:, g, f * P:(f + 1) * P], S.ident[:, :])
                        last.then_inc(turned, 1)
                        if g == N_PAGES - 1:
                            return last
                    turn_keys(0)
                    for i in range(4 * N_PAGES):
                        if i + 1 < 4 * N_PAGES:
                            turn_keys(i + 1)
                        pe.wait_ge(copied, i + 1)
                        n, g = divmod(i, N_PAGES)
                        for f in range(4):
                            last = pe.matmul(s_ps[32 * n:32 * n + 32, g * P:(g + 1) * P], qb[:, f, 4 * half + n, :], kT[:, i % 2, f * P:(f + 1) * P],
                                             start=f == 0, stop=f == 3)
                        last.then_inc(scored, 1)
                    for n in range(4):
                        for f in range(4):
                            last = pe.matmul(s_ps[32 * n:32 * n + 32, NEW_AT:NEW_AT + TS], qb[:, f, 4 * half + n, :], big[:, 8 + f, SEQ:T],
                                             start=f == 0, stop=f == 3)
                    last.then_inc(scored, 1)
                    pe.wait_ge(consts, 48)
                    pe.wait_ge(hot_in, 48)
                    for at, n in ((0, BANK), (BANK, BANK), (PAST, TS)):
                        for l in range(L_NEW):
                            of = hot[:, l, at:at + n] if at < PAST else hot_new[:, l, :]
                            pe.matmul(b_ps[:, at:at + n], tabr[:, l, :], of, start=l == 0, stop=False)
                        pe.matmul(b_ps[:, at:at + n], sel[:, :], mask[:, at:at + n], start=False, stop=True).then_inc(biased, 1)
                    pe.wait_ge(step, 5)
                    for g in range(N_PAGES):
                        pe.transpose(p_ps[:, g, :], sc[:, g * P:(g + 1) * P], S.ident[:, :])
                    pe.transpose(p_ps[0:TS, N_PAGES, :], sc[:, PAST:S_COLS], S.ident[:, :]).then_inc(probs_turned, 1)
                    pe.wait_ge(probs_kept, 1)
                    for n in range(4):
                        i = 4 + n
                        pe.wait_ge(kv_in[i % KV_SLOTS], 16 * N_PAGES * (i // KV_SLOTS + 1))
                        own = slice(n * 32, n * 32 + 32)
                        for g in range(N_PAGES):
                            pe.matmul(o_ps[own, :], pT[:, g, own], slots[i % KV_SLOTS][:, g, :], start=g == 0, stop=False)
                        last = pe.matmul(o_ps[own, :], pT[0:TS, N_PAGES, own], dv_new[:, :], start=False, stop=True)
                    last.then_inc(summed, 1)
                    pe.wait_ge(step, 8)
                    pe.transpose(oT_ps.rearrange("p n f b l -> p (n f b l)"), out[:, :, :].rearrange("p b d -> p (b d)"), S.ident[:, :]).then_inc(summed, 1)


def layer1_states(nc, S, big, dvS, dv_new):
    o = S.o
    rows_p = o["dsa_kv_p"][0, 0].rearrange("t p c h d -> t p c (h d)")
    rows_s = o["dsa_kv_s"][0].rearrange("n l c h d -> (n l) c (h d)")
    jobs = [([big[:, 8 + f, t * P:(t + 1) * P] for f in range(4)], P, [(0, P, 512, rows_p[t, :, 0, :])]) for t in range(QT)]
    jobs.append(([big[:, 8 + f, SEQ:T] for f in range(4)], TS, [(0, TS, 512, rows_s[:, 0, :])]))
    direct = [(rows_p[t, :, 1, :], dvS[:, t, :]) for t in range(QT)] + [(rows_s[:, 1, :], dv_new[:, :])]
    turn_and_store(nc, S, "cd", jobs, direct)


def layer1(nc, S):
    with ExitStack() as layer:
        keep = lambda n, s: layer.enter_context(nc.sbuf_tensor(n, s, F32))
        big = S.home
        with ExitStack() as mixing:
            keep1 = lambda n, s: mixing.enter_context(nc.sbuf_tensor(n, s, F32))
            dv_new = keep1("dv_new", [TS, BANK])
            work, work_s = keep1("work", [P, WORK]), keep1("work_s", [TS, S_KEYS])
            keys = BestKeys(nc, mixing, work, work_s)
            heads = mixing.enter_context(ExitStack())
            S.h = Parts(nc, heads, "h1", [KD, T])
            with nc.sbuf_tensor("norm1", [P, 5, T], F32) as scratch:
                rms_norm(nc, S, "mix1", S.g_mix[:, 1, :], S.xT, S.h, scratch, spill=S.x_spill)
            with ExitStack() as gla:
                keep2 = lambda n, s: gla.enter_context(nc.sbuf_tensor(n, s, F32))
                bT = keep2("decays", [P, 2, T])
                with ExitStack() as index:
                    iw = index.enter_context(nc.sbuf_tensor("iw", [P, QT + 1, DH + IDX_H], F32))
                    iqT = index.enter_context(nc.sbuf_tensor("iqT", [P, 2, T], F32))
                    ikT = index.enter_context(nc.sbuf_tensor("ikT", [P, T], F32))
                    index_products(nc, S, iqT, ikT, iw, bT)
                    pages = index.enter_context(nc.sbuf_tensor("pages_i", [1, N_SEQ * N_PAGES], I32))
                    page_keys = index.enter_context(nc.sbuf_tensor("page_keys", [P, N_SEQ, N_PAGES, DH], F32))
                    page_loaded = add_sems(nc, *(f"is_loaded{n}" for n in range(N_SEQ)))
                    index_scores_prompt(nc, S, iqT, ikT, iw, work, pages, page_keys, page_loaded)
                    index_scores_sample(nc, S, iqT, ikT, iw, work_s, page_keys, page_loaded)
                gT = keep2("gT", [P, 4, T])
                gvS = keep2("gvS", [P, QT + 1, BANK])
                big_products(nc, S, gT, big, gvS, keys)
                gla_decays(nc, S, bT)
                gla_prompt(nc, S, gT, bT, gvS, keys)
                gla_sample(nc, S, gT, bT, gvS, keys)
                head_norms(nc, S, "gla", gT, [0, 1, 2, 3], [S.g_gla[:, 0:1]] * 4, S.ones, GLA_DV)
                gate_outputs(nc, S, gT, big)
            recycle_semaphores(nc)
            dvS = heads.enter_context(nc.sbuf_tensor("dvS", [P, QT, BANK], F32))
            dsa_value_products(nc, S, dvS, dv_new, keys)
            head_norms(nc, S, "qk1", big, list(range(4, 12)), [S.g_qk[:, 2:3]] * 4 + [S.g_qk[:, 3:4]] * 4, S.head_ones, DH)
            layer1_states(nc, S, big, dvS, dv_new)
            dsa_prompt(nc, S, big, work, dvS)
            heads.close()
            dsa_sample(nc, S, big, work, work_s, dv_new)
        recycle_semaphores(nc)
        project_back(nc, S, "out1", S.d["w_out_cd"][0], KD, lambda k: big[:, k, :])


def build_kernel(nc, d, c, o, stop=99):
    S = Stage()
    LIVE_SEMAPHORES.clear()
    S.d, S.c, S.o = d, c, o
    dram = lambda n, s: nc.dram_tensor(n, s, F32, kind="Internal").ap()
    S.x_spill = dram("x_spill", [P, KD, T])
    S.part_rows = dram("part_rows", [3, T, HPG, HEAD_ROW])
    S.ab_line, S.dsa_line = dram("ab_line", [HPG, AB_LINE]), dram("dsa_line", [DSA_H, DSA_LINE])
    S.ab_copies, S.dsa_copies = dram("ab_copies", [HPG, P, AB_LINE]), dram("dsa_copies", [DSA_H, P, DSA_LINE])
    S.ab_lines, S.dsa_lines = nc.alloc_semaphore("ab_lines_copied"), nc.alloc_semaphore("dsa_lines_copied")
    q_rows, k_rows, v_rows = (dram(n, [TS, 3 * GW]) for n in ("q_rows", "k_rows", "v_rows"))
    with ExitStack() as ctx, nc.allow_non_contiguous_dma(reason="columns of gains and rows of a few floats"):
        sb = lambda n, s: ctx.enter_context(nc.sbuf_tensor(n, s, F32))
        S.ps = ctx.enter_context(nc.psum_tensor("ps", [P, 4096], F32))
        S.ident, S.head_ones, S.ones = sb("ident", [P, P]), sb("head_ones", [P, P]), sb("ones", [P, P])
        S.g_mix, S.g_ffn, S.g_qk = sb("g_mix", [P, 2, KD]), sb("g_ffn", [P, 2, KD]), sb("g_qk", [P, 4])
        S.tab, S.eps, S.g_gla = sb("tab", [NB, 20]), sb("eps", [P, 1]), sb("g_gla", [P, 1])
        S.home = sb("home", [P, 12, T])
        S.xT = S.home[:, 0:KD, :]
        load_inputs(nc, S, S.xT)
        bias_lines(nc, S)
        with ExitStack() as layer0:
            keep = lambda n, s: layer0.enter_context(nc.sbuf_tensor(n, s, F32))
            yT = keep("yT", [P, CC, T])
            v_new = keep("v_new", [TS, 3, GW])
            with ExitStack() as attention:
                keep2 = lambda n, s: attention.enter_context(nc.sbuf_tensor(n, s, F32))
                S.qk = S.home
                vS = keep2("vS", [P, 3, QT, GW])
                with ExitStack() as projections:
                    uT = projections.enter_context(nc.sbuf_tensor("uT", [P, CC, U_LEN], F32))
                    taps = projections.enter_context(nc.sbuf_tensor("taps", [P, CC, TAPS], F32))
                    scratch = vS[:, :, :, :].rearrange("p g b c -> p (g b c)")[:, 0:5 * T].rearrange("p (l t) -> p l t", l=5)
                    with ExitStack() as normed:
                        S.h = Parts(nc, normed, "h0", [KD, T])
                        w = S.d["w_in_ab"][0].rearrange("(k p) m -> p k m", p=P)
                        with ExitStack() as first_products:
                            W = Weights(nc, first_products, "glu")
                            rms_norm(nc, S, "mix0", S.g_mix[:, 0, :], S.xT, S.h, scratch, spill=S.x_spill, W=W,
                                     first=(w[:, :, CONV_CH:CONV_CH + P], w[:, :, 0:P]))
                            glu_products(nc, S, W, uT, taps, S.home)
                        qkv_products(nc, S, uT, taps, yT, vS, v_new)
                    head_norms(nc, S, "qk0", S.qk, list(range(12)), [S.g_qk[:, 0:1]] * 6 + [S.g_qk[:, 1:2]] * 6, S.head_ones, DH)
                    layer0_states(nc, S, uT, vS, v_new, q_rows, k_rows, v_rows)
                dilated_prompt(nc, S, vS)
            merged = keep("bT", [P, 2, T])
            dilated_sample(nc, S, 0, q_rows, v_new, lambda ctx: ConvNorm(nc, S, ctx, yT))
            dilated_sample(nc, S, 1, q_rows, v_new, lambda ctx: CombineWindows(nc, S, ctx, "first", range(0, 4), merged))
            dilated_sample(nc, S, 2, q_rows, v_new, lambda ctx: CombineWindows(nc, S, ctx, "second", range(4, QT), merged))
            combine_last(nc, S, merged)
            recycle_semaphores(nc)
            project_back(nc, S, "out0", S.d["w_out_ab"][0], 6, lambda k: yT[:, k, :] if k < CC else merged[:, k - CC, :])
        ffn(nc, S, 0)
        recycle_semaphores(nc)
        if stop > 1:
            layer1(nc, S)
            recycle_semaphores(nc)
            ffn(nc, S, 1)
        store_y(nc, S)


_OUTS = [("y_prompt", (1, SEQ, D_MODEL)), ("y_sample", (N_SEQ, L_NEW, D_MODEL)),
         ("conv_p", (1, 1, HIST, CONV_CH)), ("conv_s", (1, N_SEQ, HIST, CONV_CH)),
         ("win128_p", (1, 1, 128, 2, HPG, DH)), ("win128_s", (1, N_SEQ, 128, 2, HPG, DH)),
         ("win512_p", (1, 1, 512, 2, HPG, DH)), ("win512_s", (1, N_SEQ, 512, 2, HPG, DH)),
         ("win2048_p", (1, 1, SEQ, 2, HPG, DH)), ("win2048_s", (1, N_SEQ, PAST + L_NEW, 2, HPG, DH)),
         ("gla_p", (1, 1, GLA_H, GLA_DK, GLA_DV)), ("gla_s", (1, N_SEQ, GLA_H, GLA_DK, GLA_DV)),
         ("dsa_kv_p", (1, 1, QT, PAGE, 2, DSA_H, DH)), ("dsa_kv_s", (1, N_SEQ, L_NEW, 2, DSA_H, DH)),
         ("dsa_kidx_p", (1, 1, QT, PAGE, DH)), ("dsa_kidx_s", (1, N_SEQ, L_NEW, DH))]


def kernel(**inputs):
    import concourse.bacc as _bacc
    from concourse.bass_utils import run_bass_kernel_spmd as _run

    nc = _bacc.Bacc("TRN2", target_bir_lowering=False, num_devices=1)
    arrays, d, c, o = {}, {}, {}, {}
    for name, a in inputs.items():
        arrays[f"in_{name}"] = np.ascontiguousarray(a)
        d[name] = nc.dram_tensor(f"in_{name}", a.shape, mybir.dt.from_np(arrays[f"in_{name}"].dtype), kind="ExternalInput").ap()
    for name, a in shape_constants().items():
        arrays[f"const_{name}"] = np.ascontiguousarray(a)
        c[name] = nc.dram_tensor(f"const_{name}", a.shape, mybir.dt.from_np(a.dtype), kind="ExternalInput").ap()
    for name, shape in _OUTS:
        o[name] = nc.dram_tensor(f"out_{name}", shape, F32, kind="ExternalOutput").ap()
    build_kernel(nc, d, c, o)
    r = _run(nc, [arrays], core_ids=[0])
    return tuple(r.results[0][f"out_{name}"] for name, _ in _OUTS)
```
